# Optimizing a Trainium2 kernel written in Bass

```python
import math
import jax, jax.numpy as jnp
from jax import lax
import numpy as np

D_MODEL = 1024
BATCH = 1
SEQ = 1024
DEPTH = 1
DEC_BATCH = 8
DEC_SEQ = 1
PAST_LEN = 2048
PAGE_SIZE = 128

SSD_EXPAND = 2
D_INNER = SSD_EXPAND * D_MODEL
SSD_HEAD_DIM = 64
SSD_HEADS = D_INNER // SSD_HEAD_DIM
SSD_GROUPS = 4
SSD_HPG = SSD_HEADS // SSD_GROUPS
SSD_STATE = 128
CONV_K = 4
CONV_DIM = D_INNER + 2 * SSD_GROUPS * SSD_STATE
SSD_CHUNK = 128
HEAD_DIM = 64
N_HEADS = D_MODEL // HEAD_DIM
N_KV = 4
GQA = N_HEADS // N_KV
ATTN_WIDTH = N_HEADS * HEAD_DIM
KV_WIDTH = N_KV * HEAD_DIM
WINDOW = 128
MEM_LEN = 256
C_HEADS = 4
C_HEAD_DIM = 128
C_WIDTH = C_HEADS * C_HEAD_DIM
N_GROUPS = 4
EXP_PER_GROUP = 8
N_EXPERTS = N_GROUPS * EXP_PER_GROUP
TOP_K = 2
D_EXPERT = D_MODEL // 2
MOE_BLOCK = 128
IN_WIDTHS = (D_INNER, CONV_DIM, SSD_HEADS, ATTN_WIDTH, KV_WIDTH, KV_WIDTH, D_MODEL, D_MODEL)
IN_COLS = D_INNER + CONV_DIM + SSD_HEADS + ATTN_WIDTH + 2 * KV_WIDTH + 2 * D_MODEL
EPS = 1e-6
NEG_INF = -1e30

kernel_name = 'hybrid_ssd_swa_hmoe_step'

def rms_norm(x, g):
    xf = x.astype(jnp.float32)
    y = xf * lax.rsqrt(jnp.mean(xf * xf, axis=-1, keepdims=True) + EPS)
    return (y * g.astype(jnp.float32)).astype(x.dtype)

def alibi_slopes():
    return jnp.exp2(-8.0 * jnp.arange(1, N_HEADS + 1, dtype=jnp.float32) / N_HEADS)

def causal_conv(u, buf, w, b):
    up = jnp.concatenate([buf.astype(u.dtype), u], axis=1)
    L = u.shape[1]
    out = b + sum(w[k] * up[:, k:k + L] for k in range(CONV_K))
    return jax.nn.silu(out), up[:, L:]

def ssd_scan(x, dt, a, bm, cm, h0):
    b, L = x.shape[:2]
    lc = SSD_CHUNK if L % SSD_CHUNK == 0 else L
    nc = L // lc

    def to_chunks(t):
        return jnp.moveaxis(t.reshape((b, nc, lc) + t.shape[2:]), 1, 0)

    xc = to_chunks(x.reshape(b, L, SSD_GROUPS, SSD_HPG, SSD_HEAD_DIM))
    dtc = to_chunks(dt.reshape(b, L, SSD_GROUPS, SSD_HPG))
    bc, cc = to_chunks(bm), to_chunks(cm)
    a_g = a.reshape(SSD_GROUPS, SSD_HPG)
    causal = jnp.tril(jnp.ones((lc, lc), bool))[None, :, :, None, None]

    def step(h, inp):
        xk, dk, bk, ck = inp
        acum = jnp.cumsum(dk * a_g, axis=1)
        seg = acum[:, :, None] - acum[:, None, :]
        decay = jnp.exp(jnp.where(causal, seg, NEG_INF))
        cb = jnp.einsum('blgn,bsgn->blsg', ck, bk)
        y = jnp.einsum('blsgr,bsgrp->blgrp', cb[..., None] * decay * dk[:, None], xk)
        y = y + jnp.einsum('blgn,bgrpn->blgrp', ck, h) * jnp.exp(acum)[..., None]
        w_tail = jnp.exp(acum[:, -1:] - acum) * dk
        h = h * jnp.exp(acum[:, -1])[..., None, None] + jnp.einsum('bsgn,bsgr,bsgrp->bgrpn', bk, w_tail, xk)
        return h, y

    h0g = h0.reshape(b, SSD_GROUPS, SSD_HPG, SSD_HEAD_DIM, SSD_STATE)
    h, ys = lax.scan(step, h0g, (xc, dtc, bc, cc))
    y = jnp.moveaxis(ys, 0, 1).reshape(b, L, SSD_HEADS, SSD_HEAD_DIM)
    return y, h.reshape(b, SSD_HEADS, SSD_HEAD_DIM, SSD_STATE)

def window_attend(q, k, v, key_valid, sinks):
    lq, lk = q.shape[-3], k.shape[-3]
    qg = q.reshape(q.shape[:-2] + (N_KV, GQA, HEAD_DIM))
    s = jnp.einsum('...qkgd,...skd->...kgqs', qg, k.astype(q.dtype)).astype(jnp.float32) * (HEAD_DIM ** -0.5)
    dist = (jnp.arange(lq)[:, None] + (lk - lq) - jnp.arange(lk)[None, :]).astype(jnp.float32)
    slopes = alibi_slopes().reshape(N_KV, GQA, 1, 1)
    allowed = (dist >= 0) & (dist <= WINDOW) & key_valid[..., None, None, None, :]
    s = jnp.where(allowed, s - slopes * dist, NEG_INF)
    sink = sinks.astype(jnp.float32).reshape(N_KV, GQA, 1, 1)
    m = jnp.maximum(jnp.max(s, axis=-1, keepdims=True), sink)
    p = jnp.exp(s - m)
    denom = jnp.sum(p, axis=-1, keepdims=True) + jnp.exp(sink - m)
    o = jnp.einsum('...kgqs,...skd->...qkgd', p / denom, v.astype(jnp.float32))
    return o.reshape(q.shape[:-2] + (ATTN_WIDTH,)).astype(q.dtype)

def swa_banded(q, k, v, sinks):
    b, L = q.shape[:2]
    nb = L // WINDOW
    qb = q.reshape(b, nb, WINDOW, N_HEADS, HEAD_DIM)

    def band(t):
        tp = jnp.concatenate([jnp.zeros_like(t[:, :WINDOW]), t], axis=1)
        tp = tp.reshape(b, nb + 1, WINDOW, N_KV, HEAD_DIM)
        return jnp.concatenate([tp[:, :-1], tp[:, 1:]], axis=2)

    valid = (jnp.arange(nb)[:, None] > 0) | (jnp.arange(2 * WINDOW)[None, :] >= WINDOW)
    o = window_attend(qb, band(k), band(v), valid, sinks)
    return o.reshape(b, L, ATTN_WIDTH)

def parallel_mixers(xn, conv_buf, ssd_h, k_buf, v_buf, w_in, conv_w, conv_b, dt_bias, a_log, d_skip,
                    g_ssd, w_ssd_down, attn_sinks, w_mix_out):
    b, L, _ = xn.shape
    f32 = jnp.float32
    cuts = [int(c) for c in np.cumsum(IN_WIDTHS)[:-1]]
    z, xbc, dt_raw, q, k, v, g_s, g_a = jnp.split(xn @ w_in, cuts, axis=-1)
    xbc, conv_new = causal_conv(xbc, conv_buf, conv_w, conv_b)
    xs, bm, cm = jnp.split(xbc.astype(f32), [D_INNER, D_INNER + SSD_GROUPS * SSD_STATE], axis=-1)
    xs = xs.reshape(b, L, SSD_HEADS, SSD_HEAD_DIM)
    dt = jax.nn.softplus(dt_raw.astype(f32) + dt_bias.astype(f32))
    a = -jnp.exp(a_log.astype(f32))
    y, h_new = ssd_scan(xs, dt, a, bm.reshape(b, L, SSD_GROUPS, SSD_STATE),
                        cm.reshape(b, L, SSD_GROUPS, SSD_STATE), ssd_h.astype(f32))
    y = (y + d_skip.astype(f32)[:, None] * xs).reshape(b, L, D_INNER) * jax.nn.silu(z.astype(f32))
    y = rms_norm(y.reshape(b, L, SSD_GROUPS, D_INNER // SSD_GROUPS), g_ssd.reshape(SSD_GROUPS, -1))
    y_ssd = y.reshape(b, L, D_INNER).astype(xn.dtype) @ w_ssd_down
    q = q.reshape(b, L, N_HEADS, HEAD_DIM)
    k = k.reshape(b, L, N_KV, HEAD_DIM)
    v = v.reshape(b, L, N_KV, HEAD_DIM)
    if k_buf is None:
        y_att = swa_banded(q, k, v, attn_sinks)
        k_new, v_new = k[:, -WINDOW:], v[:, -WINDOW:]
    else:
        k_all = jnp.concatenate([k_buf.astype(k.dtype), k], axis=1)
        v_all = jnp.concatenate([v_buf.astype(v.dtype), v], axis=1)
        y_att = window_attend(q, k_all, v_all, jnp.ones((k_all.shape[1],), bool), attn_sinks).reshape(b, L, ATTN_WIDTH)
        k_new, v_new = k_all[:, -k_buf.shape[1]:], v_all[:, -v_buf.shape[1]:]
    merged = jax.nn.sigmoid(g_s) * y_ssd + jax.nn.sigmoid(g_a) * y_att
    return merged @ w_mix_out, (h_new.astype(xn.dtype), conv_new, k_new, v_new)

def memory_kv(mem, g_mem, w_ckv):
    b, m, _ = mem.shape
    mk, mv = jnp.split(rms_norm(mem, g_mem) @ w_ckv, 2, axis=-1)
    return mk.reshape(b, m, C_HEADS, C_HEAD_DIM), mv.reshape(b, m, C_HEADS, C_HEAD_DIM)

def cross_attend(xn, mem_k, mem_v, w_cq, w_co):
    b, L, _ = xn.shape
    q = (xn @ w_cq).reshape(b, L, C_HEADS, C_HEAD_DIM)
    s = jnp.einsum('bqhd,bmhd->bhqm', q, mem_k.astype(q.dtype)).astype(jnp.float32) * (C_HEAD_DIM ** -0.5)
    o = jnp.einsum('bhqm,bmhd->bqhd', jax.nn.softmax(s, axis=-1), mem_v.astype(jnp.float32))
    return o.reshape(b, L, C_WIDTH).astype(xn.dtype) @ w_co

def routed_experts(xf, expert, gate, w_gate, w_up, w_down):
    t = xf.shape[0]
    n_assign = t * TOP_K
    flat_e = expert.reshape(-1)
    order = jnp.argsort(flat_e)
    e_sorted = flat_e[order]
    tok_sorted = (order // TOP_K).astype(jnp.int32)
    counts = jnp.bincount(flat_e, length=N_EXPERTS)
    padded = (counts + MOE_BLOCK - 1) // MOE_BLOCK * MOE_BLOCK
    pad_end = jnp.cumsum(padded)
    rank = jnp.arange(n_assign) - (jnp.cumsum(counts) - counts)[e_sorted]
    dest = (pad_end - padded)[e_sorted] + rank
    n_blocks = -(-n_assign // MOE_BLOCK) + N_EXPERTS
    row_tok = jnp.zeros((n_blocks * MOE_BLOCK,), jnp.int32).at[dest].set(tok_sorted)
    xb = xf[row_tok].reshape(n_blocks, MOE_BLOCK, D_MODEL)
    block_e = jnp.minimum(jnp.searchsorted(pad_end, jnp.arange(n_blocks) * MOE_BLOCK, side='right'), N_EXPERTS - 1)

    def expert_mlp(args):
        xk, e = args
        return (jax.nn.silu(xk @ w_gate[e]) * (xk @ w_up[e])) @ w_down[e]

    yb = lax.map(expert_mlp, (xb, block_e)).reshape(-1, D_MODEL)
    contrib = yb[dest].astype(jnp.float32) * gate.reshape(-1)[order][:, None]
    return jax.ops.segment_sum(contrib, tok_sorted, num_segments=t).astype(xf.dtype)

def hier_moe(xn, w_rg, b_rg, w_re, b_re, w_gate, w_up, w_down):
    shp = xn.shape
    xf = xn.reshape(-1, D_MODEL)
    t = xf.shape[0]
    lg = (xf @ w_rg).astype(jnp.float32) + b_rg.astype(jnp.float32)
    grp = jnp.argmax(lg, axis=-1)
    p_grp = jnp.take_along_axis(jax.nn.softmax(lg, axis=-1), grp[:, None], axis=1)
    le = ((xf @ w_re).astype(jnp.float32) + b_re.astype(jnp.float32)).reshape(t, N_GROUPS, EXP_PER_GROUP)
    le = jnp.take_along_axis(le, grp[:, None, None], axis=1)[:, 0]
    top_p, top_i = lax.top_k(jax.nn.softmax(le, axis=-1), TOP_K)
    gate = p_grp * top_p / jnp.sum(top_p, axis=-1, keepdims=True)
    expert = (grp[:, None] * EXP_PER_GROUP + top_i).astype(jnp.int32)
    return routed_experts(xf, expert, gate, w_gate, w_up, w_down).reshape(shp)

def decoder_layer(x, conv_buf, ssd_h, k_buf, v_buf, mem_k, mem_v, lw):
    (g_mix, w_in, conv_w, conv_b, dt_bias, a_log, d_skip, g_ssd, w_ssd_down, attn_sinks, w_mix_out,
     g_cross, w_cq, w_co, g_moe, w_rg, b_rg, w_re, b_re, w_gate, w_up, w_down) = lw
    mix, state = parallel_mixers(rms_norm(x, g_mix), conv_buf, ssd_h, k_buf, v_buf, w_in, conv_w, conv_b,
                                 dt_bias, a_log, d_skip, g_ssd, w_ssd_down, attn_sinks, w_mix_out)
    x = x + mix
    x = x + cross_attend(rms_norm(x, g_cross), mem_k, mem_v, w_cq, w_co)
    x = x + hier_moe(rms_norm(x, g_moe), w_rg, b_rg, w_re, b_re, w_gate, w_up, w_down)
    return x, state

def setup_inputs(seed: int = 0) -> dict:
    key = jax.random.key(seed)
    keys = iter(list(jax.random.split(key, 64)))

    def nrm(shape, scale):
        return scale * jax.random.normal(next(keys), shape, jnp.float32)

    win_buf = min(WINDOW, PAST_LEN)
    dt0 = jnp.exp(jax.random.uniform(next(keys), (DEPTH, SSD_HEADS), jnp.float32, math.log(1e-3), math.log(1e-1)))
    dt_bias = dt0 + jnp.log(-jnp.expm1(-dt0))
    a_log = jnp.log(jax.random.uniform(next(keys), (DEPTH, SSD_HEADS), jnp.float32, 1.0, 16.0))
    return {
        'x_prompt': nrm((BATCH, SEQ, D_MODEL), 1.0),
        'x_sample': nrm((DEC_BATCH, DEC_SEQ, D_MODEL), 1.0),
        'state_ssd': nrm((DEPTH, DEC_BATCH, SSD_HEADS, SSD_HEAD_DIM, SSD_STATE), 0.5),
        'state_conv': nrm((DEPTH, DEC_BATCH, CONV_K - 1, CONV_DIM), 1.0),
        'cache_win_k': nrm((DEPTH, DEC_BATCH, win_buf, N_KV, HEAD_DIM), 1.0),
        'cache_win_v': nrm((DEPTH, DEC_BATCH, win_buf, N_KV, HEAD_DIM), 1.0),
        'cache_mem_k': nrm((DEPTH, DEC_BATCH, MEM_LEN, C_HEADS, C_HEAD_DIM), 1.0),
        'cache_mem_v': nrm((DEPTH, DEC_BATCH, MEM_LEN, C_HEADS, C_HEAD_DIM), 1.0),
        'mem_prompt': nrm((BATCH, MEM_LEN, D_MODEL), 1.0),
        'g_mix': 1.0 + nrm((DEPTH, D_MODEL), 0.02),
        'w_in': nrm((DEPTH, D_MODEL, IN_COLS), D_MODEL ** -0.5),
        'conv_w': nrm((DEPTH, CONV_K, CONV_DIM), CONV_K ** -0.5),
        'conv_b': nrm((DEPTH, CONV_DIM), 0.02),
        'dt_bias': dt_bias,
        'a_log': a_log,
        'd_skip': 1.0 + nrm((DEPTH, SSD_HEADS), 0.1),
        'g_ssd': 1.0 + nrm((DEPTH, D_INNER), 0.02),
        'w_ssd_down': nrm((DEPTH, D_INNER, D_MODEL), D_INNER ** -0.5),
        'attn_sinks': nrm((DEPTH, N_HEADS), 1.0),
        'w_mix_out': nrm((DEPTH, D_MODEL, D_MODEL), D_MODEL ** -0.5),
        'g_cross': 1.0 + nrm((DEPTH, D_MODEL), 0.02),
        'g_mem': 1.0 + nrm((DEPTH, D_MODEL), 0.02),
        'w_cq': nrm((DEPTH, D_MODEL, C_WIDTH), D_MODEL ** -0.5),
        'w_ckv': nrm((DEPTH, D_MODEL, 2 * C_WIDTH), D_MODEL ** -0.5),
        'w_co': nrm((DEPTH, C_WIDTH, D_MODEL), C_WIDTH ** -0.5),
        'g_moe': 1.0 + nrm((DEPTH, D_MODEL), 0.02),
        'w_route_group': nrm((DEPTH, D_MODEL, N_GROUPS), D_MODEL ** -0.5),
        'b_route_group': nrm((DEPTH, N_GROUPS), 0.01),
        'w_route_expert': nrm((DEPTH, D_MODEL, N_EXPERTS), D_MODEL ** -0.5),
        'b_route_expert': nrm((DEPTH, N_EXPERTS), 0.01),
        'w_e_gate': nrm((DEPTH, N_EXPERTS, D_MODEL, D_EXPERT), D_MODEL ** -0.5),
        'w_e_up': nrm((DEPTH, N_EXPERTS, D_MODEL, D_EXPERT), D_MODEL ** -0.5),
        'w_e_down': nrm((DEPTH, N_EXPERTS, D_EXPERT, D_MODEL), D_EXPERT ** -0.5),
        'g_final': 1.0 + nrm((D_MODEL,), 0.02),
    }

def reference(x_prompt, x_sample, state_ssd, state_conv, cache_win_k, cache_win_v, cache_mem_k, cache_mem_v,
              mem_prompt, g_mix, w_in, conv_w, conv_b, dt_bias, a_log, d_skip, g_ssd, w_ssd_down, attn_sinks,
              w_mix_out, g_cross, g_mem, w_cq, w_ckv, w_co, g_moe, w_route_group, b_route_group,
              w_route_expert, b_route_expert, w_e_gate, w_e_up, w_e_down, g_final):
    b = x_prompt.shape[0]
    xp, xs = x_prompt, x_sample
    p_ssd, p_conv, p_wk, p_wv, p_mk, p_mv = [], [], [], [], [], []
    s_ssd, s_conv, s_wk, s_wv = [], [], [], []
    for l in range(DEPTH):
        lw = (g_mix[l], w_in[l], conv_w[l], conv_b[l], dt_bias[l], a_log[l], d_skip[l], g_ssd[l], w_ssd_down[l],
              attn_sinks[l], w_mix_out[l], g_cross[l], w_cq[l], w_co[l], g_moe[l], w_route_group[l],
              b_route_group[l], w_route_expert[l], b_route_expert[l], w_e_gate[l], w_e_up[l], w_e_down[l])
        mk, mv = memory_kv(mem_prompt, g_mem[l], w_ckv[l])
        zero_conv = jnp.zeros((b, CONV_K - 1, CONV_DIM), xp.dtype)
        zero_h = jnp.zeros((b, SSD_HEADS, SSD_HEAD_DIM, SSD_STATE), xp.dtype)
        xp, (h_p, c_p, k_p, v_p) = decoder_layer(xp, zero_conv, zero_h, None, None, mk, mv, lw)
        xs, (h_s, c_s, k_s, v_s) = decoder_layer(xs, state_conv[l], state_ssd[l], cache_win_k[l], cache_win_v[l],
                                                 cache_mem_k[l], cache_mem_v[l], lw)
        p_ssd.append(h_p); p_conv.append(c_p); p_wk.append(k_p); p_wv.append(v_p)
        p_mk.append(mk); p_mv.append(mv)
        s_ssd.append(h_s); s_conv.append(c_s); s_wk.append(k_s); s_wv.append(v_s)
    y_prompt = rms_norm(xp, g_final)
    y_sample = rms_norm(xs, g_final)
    return (y_prompt, y_sample,
            jnp.stack(p_ssd), jnp.stack(p_conv), jnp.stack(p_wk), jnp.stack(p_wv), jnp.stack(p_mk), jnp.stack(p_mv),
            jnp.stack(s_ssd), jnp.stack(s_conv), jnp.stack(s_wk), jnp.stack(s_wv))


_drawn_inputs = setup_inputs


def setup_inputs(seed=0):
    import zlib

    import numpy as np

    out = dict(_drawn_inputs(seed))
    spreads = {}
    factors = {'g_ssd': 3.042,
     'g_cross': 4.692,
     'g_mem': 2.752,
     'b_route_group': 17.706,
     'b_route_expert': 20.583,
     'g_final': 8.056,
     'g_moe': 4.068}
    for name, (base, spread) in spreads.items():
        noise = np.random.default_rng([zlib.crc32(name.encode()), seed]).standard_normal(out[name].shape)
        drawn = base * np.exp(spread * noise) if base else spread * noise
        out[name] = __import__('jax').numpy.asarray(drawn.astype(out[name].dtype))
    for name, factor in factors.items():
        out[name] = (out[name] * factor).astype(out[name].dtype)
    return out
```

```python
from contextlib import ExitStack, contextmanager

import concourse.bass as bass
from concourse import mybir

F32 = mybir.dt.float32
I32 = mybir.dt.int32
U32 = mybir.dt.uint32
ALU = mybir.AluOpType
ACT = mybir.ActivationFunctionType
AX = mybir.AxisListType

P = 128
D = 1024
KD = D // P
SEQ = 1024
NB = 8
NT = SEQ // P
TILES = NT + 1
T = SEQ + NB
TP = TILES * P
NSPLIT = 3
NW = T // NSPLIT
DI = 2048
HS, HP, NG, NS = 32, 64, 4, 128
HPG = HS // NG
CD = DI + 2 * NG * NS
CT = CD // P
XT = DI // P
XBT = XT + NG
CK = 4
NH, NKV, HD = 16, 4, 64
GQA = NH // NKV
W = 128
MEM, CH, CHD = 256, 4, 128
CW = CH * CHD
MT = MEM // P
NGR, EPG = 4, 8
NE = NGR * EPG
DE = 512
EPS = 1e-6
NEG = -1e30
Z0 = 0
XBC0 = DI
DT0 = XBC0 + CD
Q0 = DT0 + HS
K0 = Q0 + NH * HD
V0 = K0 + NKV * HD
GS0 = V0 + NKV * HD
VDT = NKV * HD + HS
QKT = (NH + NKV) * HD // P
GT = 2 * D // P

G_MIX, G_CROSS, G_MOE, G_MEM, G_SSD = 0, KD, 2 * KD, 3 * KD, 4 * KD
G_ROWS = 4 * KD + XT
CR_STATE, CR_W, CR_B = 0, NB * (CK - 1), NB * (CK - 1) + CK
CR = CR_B + 1


class Env:

    def __init__(self, nc, ctx, a, o):
        self.nc, self.ctx, self.a, self.o = nc, ctx, a, o

        self.stage_sems = []

    def sem(self, name):
        sem = self.nc.alloc_semaphore(name)
        self.stage_sems.append(sem)
        return sem

    @contextmanager
    def stage(self):
        self.stage_sems = []
        yield
        self.nc.clear_and_free_semaphores(self.stage_sems)
        self.nc.all_engine_barrier()

    def dram(self, name, shape, dt=F32):
        return self.nc.dram_tensor(name, shape, dt, kind="Internal").ap()


def bc(ap, shape):
    return ap.to_broadcast(shape)


def constants(e):
    nc, a = e.nc, e.a
    keep = lambda n, s, dt=F32: e.ctx.enter_context(nc.sbuf_tensor(n, s, dt))
    e.ident = keep("ident", [P, P])
    e.tri = keep("tri", [P, P])
    e.below = keep("below", [P, P])
    e.ones = keep("ones", [P, P])
    e.mhalf = keep("mhalf", [P, 16])
    e.eps = keep("eps", [P, 16])
    e.gvec = keep("gvec", [P, G_ROWS])
    e.cvec = keep("cvec", [P, CT, CR])
    e.tails = keep("tails", [P, CT, CK - 1 + NB])
    e.ps = e.ctx.enter_context(nc.psum_tensor("ps", [P, 8, 512], F32))
    ps = e.ps
    made, loaded, turned, copied = e.sem("const_made"), e.sem("const_loaded"), e.sem("const_turned"), e.sem("const_copied")
    with nc.sbuf_tensor("grows", [G_ROWS, P], F32) as grows, nc.sbuf_tensor("crows", [CR, CD], F32) as crows, \
            nc.Block() as block:
        @block.sync
        def _(sp):
            for n, (name, row, rows) in enumerate((("g_mix", G_MIX, KD), ("g_cross", G_CROSS, KD), ("g_moe", G_MOE, KD),
                                                   ("g_mem", G_MEM, KD), ("g_ssd", G_SSD, XT))):
                sp.dma_start(grows[row:row + rows, :], a[name].rearrange("o (k p) -> (o k) p", p=P)).then_inc(loaded, 16)
            sp.dma_start(crows[CR_STATE:CR_W, :], a["state_conv"].rearrange("o b k c -> (o b k) c")).then_inc(loaded, 16)
            sp.dma_start(crows[CR_W:CR_B, :], a["conv_w"][0]).then_inc(loaded, 16)
            sp.dma_start(crows[CR_B:CR, :], a["conv_b"]).then_inc(loaded, 16)

        @block.gpsimd
        def _(pool):
            pool.memset(e.ident[:, :], 0.0)
            pool.memset(e.tri[:, :], 1.0)
            pool.memset(e.below[:, :], 1.0)
            pool.memset(e.ones[:, :], 1.0)
            pool.memset(e.mhalf[:, :], -0.5)
            pool.memset(e.eps[:, :], EPS)
            pool.drain()
            pool.affine_select(out=e.ident[:, :], in_=e.ident[:, :], compare_op=ALU.not_equal, fill=1.0,
                               base=0, pattern=[[-1, P]], channel_multiplier=1)
            pool.affine_select(out=e.tri[:, :], in_=e.tri[:, :], compare_op=ALU.is_ge, fill=0.0,
                               base=0, pattern=[[1, P]], channel_multiplier=-1)
            pool.affine_select(out=e.below[:, :], in_=e.below[:, :], compare_op=ALU.is_ge, fill=0.0,
                               base=-1, pattern=[[-1, P]], channel_multiplier=1)
            pool.drain()
            pool.sem_inc(made, 1)

        @block.tensor
        def _(pe):
            pe.wait_ge(made, 1)
            pe.wait_ge(loaded, 8 * 16)
            pe.transpose(ps[:, 0, 0:G_ROWS], grows[:, :], e.ident[0:G_ROWS, 0:G_ROWS])
            for c in range(CT):
                last = pe.transpose(ps[:, 1 + c // 12, (c % 12) * 32:(c % 12) * 32 + CR],
                                    crows[:, c * P:(c + 1) * P], e.ident[0:CR, 0:CR])
            last.then_inc(turned, 1)

        @block.vector
        def _(dve):
            dve.wait_ge(turned, 1)
            dve.tensor_copy(e.gvec[:, :], ps[:, 0, 0:G_ROWS])
            for h in range(2):
                dve.tensor_copy(e.cvec[:, 12 * h:12 * h + 12, :],
                                ps[:, 1 + h, 0:12 * 32].rearrange("p (c r) -> p c r", r=32)[:, :, 0:CR])


def rms_tiles(e, name, x, n_tiles, out_turned, grow=None, load=None, gtok=None, store=None):
    nc, ps = e.nc, e.ps
    loaded, squared, meaned, rooted = (e.sem(f"{name}_{x}") for x in ("loaded", "squared", "meaned", "rooted"))
    scaled, turned, low_freed, high_freed = (e.sem(f"{name}_{x}") for x in ("scaled", "turned", "low_freed", "high_freed"))
    stored = [e.sem(f"{name}_stored{i}") for i in range(2)]
    with nc.sbuf_tensor(name + "_xn", [P, 2, D], F32) as xn, nc.sbuf_tensor(name + "_sq", [P, D], F32) as sq, \
            nc.sbuf_tensor(name + "_ss", [P, n_tiles], F32) as ss, nc.sbuf_tensor(name + "_rs", [P, n_tiles], F32) as rs, \
            nc.Block() as block:
        n_loads = len(load or [])

        @block.sync
        def _(sp):
            for dst, src in load or []:
                sp.dma_start(dst, src).then_inc(loaded, 16)
            if store is not None:
                for t in range(n_tiles):
                    sp.wait_ge(scaled, t + 1)
                    sp.dma_start(store[t * P:(t + 1) * P, :], xn[:, t % 2, :]).then_inc(stored[t % 2], 16)
                for b in range(2):
                    sp.wait_ge(stored[b], 16 * ((n_tiles + 1 - b) // 2))

        @block.scalar
        def _(act):
            if n_loads:
                act.wait_ge(loaded, 16 * n_loads)
            for t in range(n_tiles):
                act.activation(sq[:, :], x[:, t, :], ACT.Square, accum_out=ss[:, t:t + 1]).then_inc(squared, 1)
                act.drain()
            for t in range(n_tiles):
                act.wait_ge(turned, 2 * t + 2)
                for k in range(4, KD):
                    src, dst = ps[:, 2 * (t % 2) + 1, (k - 4) * P:(k - 3) * P], out_turned[:, k, t * P:(t + 1) * P]
                    if gtok is None:
                        last = act.activation(dst, src, ACT.Copy, scale=e.gvec[:, grow + k:grow + k + 1])
                    else:
                        last = act.activation(dst, src, ACT.Copy)
                last.then_inc(high_freed, 1)

        @block.gpsimd
        def _(pool):
            pool.wait_ge(meaned, 1)
            pool.tensor_tensor(rs[:, :], ss[:, :], e.mhalf[:, 0:n_tiles], ALU.pow).then_inc(rooted, 1)

        @block.vector
        def _(dve):
            if n_loads:
                dve.wait_ge(loaded, 16 * n_loads)
            dve.wait_ge(squared, n_tiles)
            dve.tensor_scalar(ss[:, :], ss[:, :], 1.0 / D, EPS, ALU.mult, ALU.add).then_inc(meaned, 1)
            dve.wait_ge(rooted, 1)

            def scale(t):
                if t >= 2:
                    dve.wait_ge(turned, 2 * (t - 1))
                    if store is not None:
                        dve.wait_ge(stored[t % 2], 16 * (t // 2))
                last = dve.tensor_scalar(xn[:, t % 2, :], x[:, t, :], rs[:, t:t + 1], None, ALU.mult)
                if gtok is not None:
                    dve.drain()
                    last = dve.tensor_tensor(xn[:, t % 2, :], xn[:, t % 2, :], gtok, ALU.mult)
                last.then_inc(scaled, 1)

            scale(0)
            for t in range(n_tiles):
                if t + 1 < n_tiles:
                    scale(t + 1)
                dve.wait_ge(turned, 2 * t + 1)
                src = ps[:, 2 * (t % 2), :].rearrange("p (k n) -> p k n", k=4)
                dst = out_turned[:, 0:4, t * P:(t + 1) * P]
                if gtok is None:
                    last = dve.tensor_tensor(dst, src, bc(e.gvec[:, grow:grow + 4].unsqueeze(2), [P, 4, P]), ALU.mult)
                else:
                    last = dve.tensor_copy(dst, src)
                last.then_inc(low_freed, 1)

        @block.tensor
        def _(pe):
            for t in range(n_tiles):
                pe.wait_ge(scaled, t + 1)
                if t >= 2:
                    pe.wait_ge(low_freed, t - 1)
                    pe.wait_ge(high_freed, t - 1)
                for k in range(KD):
                    last = pe.transpose(ps[:, 2 * (t % 2) + k // 4, (k % 4) * P:(k % 4 + 1) * P],
                                        xn[:, t % 2, k * P:(k + 1) * P], e.ident[:, :])
                    if k % 4 == 3:
                        last.then_inc(turned, 1)


def project(e, x_turned):
    nc, a, ps = e.nc, e.a, e.ps
    w_in = a["w_in"][0]
    e.xb_rows = e.dram("xb_rows", [SEQ, XBT * P])
    e.bc_cols = e.dram("bc_cols", [2 * NG, P, SEQ])
    e.qk_cols = e.dram("qk_cols", [QKT, P, T])
    e.gate_cols = e.dram("gate_cols", [GT, P, T])
    e.z_rows = e.dram("z_rows", [TP, DI])
    e.vdt_rows = e.dram("vdt_rows", [TP, VDT])

    w_ready, w_free = [e.sem(f"proj_w_ready{i}") for i in range(4)], e.sem("proj_w_free")
    ps_ready, ps_free = e.sem("proj_ps_ready"), e.sem("proj_ps_free")
    u_ready, u_free = e.sem("conv_u_ready"), e.sem("conv_u_free")
    conv_ready, conv_free = e.sem("conv_ready"), e.sem("conv_free")
    act_ready = e.sem("conv_act_ready")
    turned, turn_free = e.sem("conv_turned"), e.sem("conv_turn_free")
    rows_ready, rows_stored = e.sem("conv_rows_ready"), [e.sem(f"conv_rows_stored{i}") for i in range(2)]
    cols_stored = [e.sem(f"conv_cols_stored{i}") for i in range(2)]
    plain_ready, plain_stored = e.sem("plain_ready"), [e.sem(f"plain_stored{i}") for i in range(2)]
    zw_ready = [e.sem(f"zw_ready{i}") for i in range(3)]
    zw_free, z_ps, z_free = e.sem("zw_free"), e.sem("z_ps_ready"), e.sem("z_ps_free")
    z_out, z_stored = e.sem("z_out_ready"), [e.sem(f"z_stored{i}") for i in range(3)]

    WS = 4
    ZN = DI // 512
    N_FEAT = CT + QKT + GT
    with ExitStack() as st:
        sb = lambda n, s: st.enter_context(nc.sbuf_tensor(n, s, F32))
        wring = sb("wring", [P, WS, KD, P])
        zring = sb("zring", [P, 2, KD, 512])
        wv = sb("wv", [P, KD, VDT])
        u = sb("conv_u", [P, 2, CK - 1 + T])
        acc = sb("conv_acc", [P, 2, SEQ])
        y = sb("conv_y", [P, 2, SEQ])
        rows = sb("conv_rows", [P, 2, NT, P])
        plain = sb("plain", [P, 2, T])
        zout = sb("zout", [P, 3, 512])
        block = st.enter_context(nc.Block())

        def cols(c):
            return w_in[:, c].rearrange("(k p) c -> p k c", p=P)

        @block.sync
        def _(sp):
            def load(slot, n, col):
                sp.wait_ge(w_free, n + 1)
                sp.dma_start(wring[:, slot], cols(bass.ds(col, P))).then_inc(w_ready[slot], 16)
            with sp.Fori(0, CT // WS) as i:
                for j in range(WS):
                    load(j, i * WS + j, i * (WS * P) + (XBC0 + j * P))
            with sp.Fori(0, QKT // WS) as i:
                for j in range(WS):
                    load(j, i * WS + (CT + j), i * (WS * P) + (Q0 + j * P))
            for m in range(QKT // WS * WS, QKT):
                load((CT + m) % WS, CT + m, Q0 + m * P)
            with sp.Fori(0, GT // WS) as i:
                for j in range(WS):
                    load((CT + QKT + j) % WS, i * WS + (CT + QKT + j), i * (WS * P) + (GS0 + j * P))
            with sp.Fori(0, ZN // 2) as i:
                for j in range(2):
                    sp.wait_ge(zw_free, i * 2 + (j + 1))
                    sp.dma_start(zring[:, j], cols(bass.ds(i * 1024 + (Z0 + j * 512), 512))).then_inc(zw_ready[j], 16)
            sp.dma_start(wv[:, :, 0:V0 + NKV * HD - V0], cols(slice(V0, V0 + NKV * HD))).then_inc(zw_ready[2], 16)
            sp.dma_start(wv[:, :, NKV * HD:VDT], cols(slice(DT0, DT0 + HS))).then_inc(zw_ready[2], 16)

        @block.tensor
        def _(pe):
            pe.sem_inc(w_free, WS)
            pe.sem_inc(zw_free, 2)

            def product(slot, par, n, turn_of_slot):
                pe.wait_ge(w_ready[slot], turn_of_slot * 16 + 16)
                pe.wait_ge(ps_free, n + 1)
                for k in range(KD):
                    for s in range(NSPLIT):
                        last = pe.matmul(ps[:, 3 * par + s, 0:NW], wring[:, slot, k], x_turned[:, k, s * NW:(s + 1) * NW],
                                         start=(k == 0), stop=(k == KD - 1))
                last.then_inc(ps_ready, 1)
                pe.drain().then_inc(w_free, 1)

            def turn(par, n):
                pe.wait_ge(act_ready, n + 1)
                pe.wait_ge(turn_free, n + 1)
                for t in range(NT):
                    last = pe.transpose(ps[:, 6 + t // 4, (t % 4) * P:(t % 4 + 1) * P], y[:, par, t * P:(t + 1) * P], e.ident[:, :])
                last.then_inc(turned, 1)

            product(0, 0, 0, 0)
            with pe.Fori(0, XBT // WS) as i:
                for j in range(WS):
                    product((j + 1) % WS, (j + 1) % 2, i * WS + (j + 1), i + (j + 1) // WS)
                    turn(j % 2, i * WS + j)
            for n in range(XBT + 1, CT):
                product(n % WS, n % 2, n, n // WS)
            with pe.Fori(0, QKT // WS) as i:
                for j in range(WS):
                    product(j, j % 2, i * WS + (CT + j), i + CT // WS)
            for m in range(QKT // WS * WS, QKT):
                product((CT + m) % WS, m % 2, CT + m, (CT + m) // WS)
            with pe.Fori(0, GT // WS) as i:
                for j in range(WS):
                    product((CT + QKT + j) % WS, (QKT + j) % 2, i * WS + (CT + QKT + j), i + (CT + QKT + j) // WS)

            def row_product(bank, unit, t, w, width):
                pe.wait_ge(z_free, unit + 1)
                for k in range(KD):
                    last = pe.matmul(ps[:, bank, 0:width], x_turned[:, k, t * P:(t + 1) * P], w[:, k], start=(k == 0), stop=(k == KD - 1))
                last.then_inc(z_ps, 1)

            with pe.Fori(0, ZN // 2) as i:
                for j in range(2):
                    pe.wait_ge(zw_ready[j], i * 16 + 16)
                    for t in range(TILES):
                        row_product((j * TILES + t) % 6, i * (2 * TILES) + (j * TILES + t), t, zring[:, j], 512)
                    pe.drain().then_inc(zw_free, 1)
            pe.wait_ge(zw_ready[2], 32)
            for t in range(TILES):
                row_product((ZN * TILES + t) % 6, ZN * TILES + t, t, wv, VDT)

        @block.scalar
        def _(act):
            act.sem_inc(ps_free, 2)
            act.sem_inc(conv_free, 2)

            def empty(par, dst, func=ACT.Copy):
                for s in range(NSPLIT):
                    last = act.activation(dst[:, s * NW:(s + 1) * NW], ps[:, 3 * par + s, 0:NW], func)
                return last

            def conv_tile(par, n):
                act.wait_ge(ps_ready, n + 1)
                act.wait_ge(u_free, n + 1)
                empty(par, u[:, par, CK - 1:]).then_inc(u_ready, 1)
                act.drain().then_inc(ps_free, 1)
                act.wait_ge(conv_ready, n + 1)
                act.activation(y[:, par], acc[:, par], ACT.Silu).then_inc(act_ready, 1)
                act.drain().then_inc(conv_free, 1)

            def x_tile(par, n, first):
                if not first:
                    act.wait_ge(turned, n + (-1))
                conv_tile(par, n)
            x_tile(0, 0, True)
            x_tile(1, 1, True)
            for n in (2, 3):
                x_tile(n % 2, n, False)
            with act.Fori(1, XT // WS) as i:
                for j in range(WS):
                    x_tile(j % 2, i * WS + j, False)
            for n in range(XT, CT):
                if n - 2 < XBT:
                    act.wait_ge(turned, n - 1)
                if n - 2 >= XT:
                    act.wait_ge(cols_stored[n % 2], 16 * ((n - XT) // 2))
                conv_tile(n % 2, n)
                act.wait_ge(act_ready, n + 1)
                act.dma_start(e.bc_cols[n - XT], y[:, n % 2]).then_inc(cols_stored[n % 2], 16)

            def plain_tile(par, n, earlier, dst, func):
                act.wait_ge(ps_ready, n + (CT + 1))
                act.wait_ge(plain_stored[par], earlier * 16)
                empty(par, plain[:, par], func).then_inc(plain_ready, 1)
                act.drain().then_inc(ps_free, 1)
                act.dma_start(dst, plain[:, par]).then_inc(plain_stored[par], 16)

            with act.Fori(0, QKT // WS) as i:
                for j in range(WS):
                    plain_tile(j % 2, i * WS + j, i * 2 + j // 2, e.qk_cols[bass.ds(i * WS + j, 1)].rearrange("o p t -> (o p) t"), ACT.Copy)
            for m in range(QKT // WS * WS, QKT):
                plain_tile(m % 2, m, m // 2, e.qk_cols[m], ACT.Copy)
            with act.Fori(0, GT // WS) as i:
                for j in range(WS):
                    plain_tile((QKT + j) % 2, i * WS + (QKT + j), i * 2 + (QKT + j) // 2, e.gate_cols[bass.ds(i * WS + j, 1)].rearrange("o p t -> (o p) t"), ACT.Sigmoid)
            act.drain().then_inc(z_free, 6)

            def row_tile(bank, buf, unit, earlier, dst, width, func):
                act.wait_ge(z_ps, unit + 1)
                act.wait_ge(z_stored[buf], earlier * 16)
                act.activation(zout[:, buf, 0:width], ps[:, bank, 0:width], func).then_inc(z_out, 1)
                act.drain().then_inc(z_free, 1)
                act.dma_start(dst, zout[:, buf, 0:width]).then_inc(z_stored[buf], 16)

            with act.Fori(0, ZN // 2) as i:
                for j in range(2):
                    for t in range(TILES):
                        n = j * TILES + t
                        row_tile(n % 6, n % 3, i * (2 * TILES) + n, i * (2 * TILES // 3) + n // 3, e.z_rows[t * P:(t + 1) * P, bass.ds(i * 1024 + j * 512, 512)], 512, ACT.Silu)
            for t in range(TILES):
                n = ZN * TILES + t
                row_tile(n % 6, n % 3, n, n // 3, e.vdt_rows[t * P:(t + 1) * P, :], VDT, ACT.Copy)
            for b in range(2):
                act.wait_ge(cols_stored[b], 16 * (CT - XT) // 2)
                act.wait_ge(plain_stored[b], 16 * (QKT + GT) // 2)
            for b in range(3):
                act.wait_ge(z_stored[b], 16 * (ZN + 1) * TILES // 3)

        @block.vector
        def _(dve):
            dve.memset(u[:, :, 0:CK - 1], 0.0)
            dve.drain().then_inc(u_free, 2)
            dve.sem_inc(turn_free, 1)

            def conv(par, n):
                dve.wait_ge(u_ready, n + 1)
                dve.wait_ge(conv_free, n + 1)
                cv = e.cvec[:, bass.ds(n, 1), :].rearrange("p o r -> p (o r)")
                dve.tensor_scalar(acc[:, par], u[:, par, CK - 1:CK - 1 + SEQ], cv[:, CR_W + CK - 1:CR_W + CK], cv[:, CR_B:CR], ALU.mult, ALU.add)
                for k in range(CK - 1):
                    dve.drain()
                    last = dve.scalar_tensor_tensor(out=acc[:, par], in0=u[:, par, k:k + SEQ], scalar=cv[:, CR_W + k:CR_W + k + 1],
                                                    in1=acc[:, par], op0=ALU.mult, op1=ALU.add)
                last.then_inc(conv_ready, 1)
                dve.tensor_copy(e.tails[:, bass.ds(n, 1), :].rearrange("p o r -> p (o r)"), u[:, par, SEQ:SEQ + CK - 1 + NB])
                dve.drain().then_inc(u_free, 1)

            def rows_out(par, n, earlier):
                dve.wait_ge(turned, n + 1)
                dve.wait_ge(rows_stored[par], earlier * 16)
                dve.tensor_copy(rows[:, par], ps[:, 6:8, :].rearrange("p b (t c) -> p (b t) c", c=P)).then_inc(rows_ready, 1)
                dve.drain().then_inc(turn_free, 1)

            conv(0, 0)
            with dve.Fori(0, XBT // WS) as i:
                for j in range(WS):
                    conv((j + 1) % 2, i * WS + (j + 1))
                    rows_out(j % 2, i * WS + j, i * 2 + j // 2)
            for n in range(XBT + 1, CT):
                conv(n % 2, n)

        @block.gpsimd
        def _(pool):
            with pool.Fori(0, XBT // WS) as i:
                for j in range(WS):
                    pool.wait_ge(rows_ready, i * WS + (j + 1))
                    pool.dma_start(e.xb_rows[:, bass.ds(i * (WS * P) + j * P, P)].rearrange("(t p) c -> p t c", p=P),
                                   rows[:, j % 2]).then_inc(rows_stored[j % 2], 16)
            for b in range(2):
                pool.wait_ge(rows_stored[b], 16 * XBT // 2)


def mixer_norm(e, x_turned):
    nc, a = e.nc, e.a
    zeroed = e.sem("mixer_zeroed")
    with nc.sbuf_tensor("x_rows", [P, TILES, D], F32) as x:
        with nc.Block() as block:
            @block.vector
            def _(dve):
                dve.memset(x[:, NT, :], 0.0)
        rms_tiles(e, "mixer", x, TILES, x_turned, grow=G_MIX, load=x_loads(e, x))


def x_loads(e, x):
    return [(x[:, 0:NT, :], e.a["x_prompt"][0].rearrange("(t p) d -> p t d", p=P)),
            (x[0:NB, NT, :], e.a["x_sample"][:, 0, :])]


def ssd_steps(e):
    nc, a = e.nc, e.a
    keep = lambda n, s: e.ctx.enter_context(nc.sbuf_tensor(n, s, F32))
    e.dt = keep("dt", [P, TILES, HS])
    e.da = keep("da", [P, TILES, HS])
    e.d_skip = keep("d_skip", [P, HS])
    loaded, s_v, s_a = e.sem("dt_loaded"), e.sem("dt_vector_step"), e.sem("dt_scalar_step")
    with ExitStack() as st:
        sb = lambda n, s: st.enter_context(nc.sbuf_tensor(n, s, F32))
        raw, e1, ln = sb("dt_raw", [P, TILES, HS]), sb("dt_exp", [P, TILES, HS]), sb("dt_ln", [P, TILES, HS])
        u, d = sb("dt_u", [P, TILES, HS]), sb("dt_d", [P, TILES, HS])
        bias, alog = sb("dt_bias_all", [P, HS]), sb("a_log_all", [P, HS])
        block = st.enter_context(nc.Block())

        @block.sync
        def _(sp):
            sp.dma_start(raw[:, :, :], e.vdt_rows[:, NKV * HD:VDT].rearrange("(t p) c -> p t c", p=P)).then_inc(loaded, 16)
            for name, dst in (("dt_bias", bias), ("a_log", alog), ("d_skip", e.d_skip)):
                sp.dma_start(dst[:, :], a[name].to_broadcast([P, HS])).then_inc(loaded, 16)

        @block.scalar
        def _(act):
            act.wait_ge(loaded, 64)
            act.activation(alog[:, :], alog[:, :], ACT.Exp).then_inc(s_a, 1)
            act.wait_ge(s_v, 1)
            act.activation(e1[:, :, :], d[:, :, :], ACT.Exp).then_inc(s_a, 1)
            act.wait_ge(s_v, 2)
            act.activation(ln[:, :, :], u[:, :, :], ACT.Ln).then_inc(s_a, 1)

        @block.vector
        def _(dve):
            dve.wait_ge(loaded, 64)
            dve.tensor_tensor(raw[:, :, :], raw[:, :, :], bc(bias[:, :].unsqueeze(1), [P, TILES, HS]), ALU.add)
            dve.drain()
            dve.tensor_scalar(u[:, :, :], raw[:, :, :], -1.0, None, ALU.mult)
            dve.drain()
            dve.tensor_tensor(d[:, :, :], raw[:, :, :], u[:, :, :], ALU.min).then_inc(s_v, 1)
            dve.wait_ge(s_a, 2)
            dve.tensor_scalar(u[:, :, :], e1[:, :, :], 1.0, None, ALU.add).then_inc(s_v, 1)
            dve.drain()
            dve.tensor_scalar(d[:, :, :], u[:, :, :], -1.0, None, ALU.add)
            dve.drain()
            dve.tensor_scalar(e.dt[:, :, :], d[:, :, :], 0.0, None, ALU.is_equal)
            dve.tensor_scalar(raw[:, :, :], raw[:, :, :], 0.0, None, ALU.max)
            dve.drain()
            dve.tensor_tensor(d[:, :, :], d[:, :, :], e.dt[:, :, :], ALU.add)
            dve.tensor_tensor(e.dt[:, :, :], e.dt[:, :, :], e1[:, :, :], ALU.mult)
            dve.drain()
            dve.reciprocal(d[:, :, :], d[:, :, :])
            dve.tensor_tensor(raw[:, :, :], raw[:, :, :], e.dt[:, :, :], ALU.add)
            dve.drain()
            dve.tensor_tensor(d[:, :, :], d[:, :, :], e1[:, :, :], ALU.mult)
            dve.drain()
            dve.wait_ge(s_a, 3)
            dve.tensor_tensor(d[:, :, :], d[:, :, :], ln[:, :, :], ALU.mult)
            dve.tensor_scalar(alog[:, :], alog[:, :], -1.0, None, ALU.mult)
            dve.drain()
            dve.tensor_tensor(e.dt[:, :, :], raw[:, :, :], d[:, :, :], ALU.add)
            dve.drain()
            dve.tensor_tensor(e.da[:, :, :], e.dt[:, :, :], bc(alog[:, :].unsqueeze(1), [P, TILES, HS]), ALU.mult)


def ssd_chunks(e):
    nc, a, ps = e.nc, e.a, e.ps
    e.y_cols = e.dram("y_cols", [XT, P, T])
    names = ("in_ready0", "in_ready1", "in_pe", "in_pool", "in_dve", "sums", "decays", "decays_pool", "decays_dve",
             "rtri_ready", "rtri_free", "seg_ready", "seg_free", "e_ready", "e_free", "cb_ready", "cb_free", "cbm_ready",
             "m_ready", "m_free", "xdt_ready", "xdt_free", "xw_ready", "xw_free", "xd_ready", "xd_free",
             "inter", "inter_free", "intra", "intra_free", "scaled", "upd", "state_ready", "gated", "gated_free", "sums_free", "upd_free",
             "squared", "rooted", "normed", "normed_free", "turned", "turn_free", "cols_ready", "y_stored0", "y_stored1")
    s = {n: e.sem("ssd_" + n) for n in names}
    XW = XBT * P
    with ExitStack() as st:
        sb = lambda n, sh: st.enter_context(nc.sbuf_tensor(n, sh, F32))
        xb = sb("ssd_xb", [P, 2, XW])
        bcc = sb("ssd_bc", [P, 2, 2 * NG, P])
        z = sb("ssd_z", [P, 2, DI])
        rtri = sb("ssd_rtri", [P, 2, HPG, P])
        ee = sb("ssd_e", [P, 2, HPG, P])
        mm = sb("ssd_m", [P, 2, HPG, P])
        cbm = sb("ssd_cbm", [P, NG, P])
        dec = sb("ssd_dec", [P, 2, 3 * HS])
        wdt = sb("ssd_wdt", [P, HS])
        xdt = sb("ssd_xdt", [P, 2, HS, HP])
        xw = sb("ssd_xw", [P, HS, HP])
        xd = sb("ssd_xd", [P, HS, HP])
        state = sb("ssd_state", [P, HS, HP])
        y = sb("ssd_y", [P, 2, HS, HP])
        sq = sb("ssd_sq", [P, 512])
        yn = sb("ssd_yn", [P, DI])
        ss, rs = sb("ssd_ss", [P, NG]), sb("ssd_rs", [P, NG])
        da, dt = sb("ssd_da_now", [P, HS]), sb("ssd_dt_now", [P, HS])
        yc = sb("ssd_ycols", [P, 2, XT, P])
        hs = lambda g: slice(g * HPG, (g + 1) * HPG)
        gc = lambda g: slice(g * 512, (g + 1) * 512)
        bank = lambda b: ps[:, b, :].rearrange("p (h c) -> p h c", h=HPG)

        with nc.Block() as block:
            def over_chunks(eng, chunk):
                chunk(0, 0, 0)
                with eng.Fori(0, (NT - 2) // 2) as i:
                    chunk(i * 2 + 1, 1, i)
                    chunk(i * 2 + 2, 0, i + 1)
                chunk(NT - 1, 1, NT // 2 - 1)

            @block.sync
            def _(sp):
                def chunk(n, par, k):
                    for who in ("in_pe", "in_pool", "in_dve"):
                        sp.wait_ge(s[who], n + 1)
                    sp.dma_start(xb[:, par], e.xb_rows[bass.ds(n * P, P), :]).then_inc(s[f"in_ready{par}"], 16)
                    sp.dma_start(bcc[:, par], e.bc_cols[:, :, bass.ds(n * P, P)].rearrange("g p t -> p g t")).then_inc(s[f"in_ready{par}"], 16)
                    sp.dma_start(z[:, par], e.z_rows[bass.ds(n * P, P), :]).then_inc(s[f"in_ready{par}"], 16)
                over_chunks(sp, chunk)

            def wait_in(eng, par, k):
                eng.wait_ge(s[f"in_ready{par}"], k * 48 + 48)

            @block.gpsimd
            def _(pool):
                pool.memset(state[:, :, :], 0.0)
                pool.drain().then_inc(s["state_ready"], NG)
                pool.sem_inc(s["in_pool"], 2)
                pool.sem_inc(s["decays_pool"], 2)

                def chunk(n, par, k):
                    pool.tensor_copy(da[:, :], e.da[:, bass.ds(n, 1), :].rearrange("p o h -> p (o h)"))
                    pool.tensor_copy(dt[:, :], e.dt[:, bass.ds(n, 1), :].rearrange("p o h -> p (o h)"))
                    pool.drain()
                    x = xb[:, par, 0:DI].rearrange("p (h c) -> p h c", c=HP)

                    def running(g):
                        pool.wait_ge(s["rtri_free"], n * NG + (g + 1))
                        pool.tensor_tensor(rtri[:, g % 2], bc(e.tri[:, :].unsqueeze(1), [P, HPG, P]),
                                           bc(da[:, hs(g)].unsqueeze(2), [P, HPG, P]), ALU.mult).then_inc(s["rtri_ready"], 1)
                    running(0)
                    running(1)
                    wait_in(pool, par, k)
                    pool.wait_ge(s["xdt_free"], n + 1)
                    pool.tensor_tensor(xdt[:, par], x, bc(dt[:, :].unsqueeze(2), [P, HS, HP]), ALU.mult).then_inc(s["xdt_ready"], 1)
                    running(2)
                    pool.wait_ge(s["decays"], n + 1)
                    pool.wait_ge(s["xw_free"], n + 1)
                    pool.tensor_tensor(wdt[:, :], dec[:, par, HS:2 * HS], dt[:, :], ALU.mult)
                    pool.drain()
                    pool.tensor_tensor(xw[:, :, :], x, bc(wdt[:, :].unsqueeze(2), [P, HS, HP]), ALU.mult).then_inc(s["xw_ready"], 1)
                    running(3)
                    pool.wait_ge(s["xd_free"], n + 1)
                    pool.tensor_tensor(xd[:, :, :], x, bc(e.d_skip[:, :].unsqueeze(2), [P, HS, HP]), ALU.mult).then_inc(s["xd_ready"], 1)
                    pool.drain().then_inc(s["in_pool"], 1)
                    for g in range(NG):
                        pool.wait_ge(s["inter"], n * NG + (g + 1))
                        pool.wait_ge(s["state_ready"], n * NG + (g + 1))
                        pool.tensor_tensor(state[:, hs(g)], state[:, hs(g)],
                                           bc(dec[:, par, 2 * HS + g * HPG:2 * HS + (g + 1) * HPG].unsqueeze(2), [P, HPG, HP]),
                                           ALU.mult).then_inc(s["scaled"], 1)
                    pool.drain().then_inc(s["decays_pool"], 1)
                    pool.wait_ge(s["squared"], n + 1)
                    pool.tensor_tensor(ss[:, :], ss[:, :], e.eps[:, 0:NG], ALU.add)
                    pool.drain()
                    pool.tensor_tensor(rs[:, :], ss[:, :], e.mhalf[:, 0:NG], ALU.pow).then_inc(s["rooted"], 1)
                over_chunks(pool, chunk)

            @block.tensor
            def _(pe):
                pe.sem_inc(s["in_pe"], 2)
                pe.sem_inc(s["rtri_free"], 2)
                pe.sem_inc(s["m_free"], 2)
                pe.sem_inc(s["xdt_free"], 2)
                pe.sem_inc(s["xw_free"], 1)

                def turn(n):
                    pe.wait_ge(s["normed"], n + 1)
                    for q in range(XT // 4):
                        pe.wait_ge(s["turn_free"], n * (XT // 4) + (q + 1))
                        for k in range(4):
                            last = pe.transpose(ps[:, 7, k * P:(k + 1) * P], yn[:, (4 * q + k) * P:(4 * q + k + 1) * P], e.ident[:, :])
                        last.then_inc(s["turned"], 1)
                    pe.drain().then_inc(s["normed_free"], 1)

                def chunk(n, par, k, first=False):
                    da = e.da[:, bass.ds(n, 1), :].rearrange("p o h -> p (o h)")
                    wait_in(pe, par, k)
                    pe.wait_ge(s["sums_free"], n + 1)
                    pe.matmul(ps[:, 0, 0:HS], e.tri[:, :], da, start=True, stop=True)
                    pe.matmul(ps[:, 0, HS:2 * HS], e.below[:, :], da, start=True, stop=True)
                    pe.matmul(ps[:, 0, 2 * HS:3 * HS], e.ones[:, :], da, start=True, stop=True).then_inc(s["sums"], 1)
                    pe.wait_ge(s["cb_free"], n + 1)
                    for g in range(NG):
                        last = pe.matmul(ps[:, 3, g * P:(g + 1) * P], bcc[:, par, g], bcc[:, par, NG + g], start=True, stop=True)
                    last.then_inc(s["cb_ready"], 1)
                    for g in range(NG):
                        pe.wait_ge(s["rtri_ready"], n * NG + (g + 1))
                        pe.wait_ge(s["seg_free"], n * NG + (g + 1))
                        for b in range(2):
                            last = pe.matmul(ps[:, 1 + b, :], e.below[:, :], rtri[:, g % 2, 4 * b:4 * b + 4].rearrange("p h c -> p (h c)"),
                                             start=True, stop=True)
                        last.then_inc(s["seg_ready"], 1)
                        pe.drain().then_inc(s["rtri_free"], 1)
                        pe.wait_ge(s["state_ready"], n * NG + (g + 1))
                        pe.wait_ge(s["inter_free"], n * NG + (g + 1))
                        pe.matmul(ps[:, 5, :], bcc[:, par, NG + g], state[:, hs(g)].rearrange("p h c -> p (h c)"),
                                  start=True, stop=True).then_inc(s["inter"], 1)
                        pe.wait_ge(s["m_ready"], n * NG + (g + 1))
                        pe.wait_ge(s["xdt_ready"], n + 1)
                        pe.wait_ge(s["intra_free"], n * NG + (g + 1))
                        for h in range(HPG):
                            last = pe.matmul(ps[:, 4, h * HP:(h + 1) * HP], mm[:, g % 2, h], xdt[:, par, g * HPG + h], start=True, stop=True)
                        last.then_inc(s["intra"], 1)
                        pe.drain().then_inc(s["m_free"], 1)
                        pe.wait_ge(s["xw_ready"], n + 1)
                        pe.wait_ge(s["upd_free"], n * NG + (g + 1))
                        pe.matmul(ps[:, 6, :], xb[:, par, DI + g * NS:DI + (g + 1) * NS], xw[:, hs(g)].rearrange("p h c -> p (h c)"),
                                  start=True, stop=True).then_inc(s["upd"], 1)
                    pe.drain().then_inc(s["in_pe"], 1)
                    pe.sem_inc(s["xdt_free"], 1)
                    pe.sem_inc(s["xw_free"], 1)
                    if not first:
                        turn(n - 1)
                chunk(0, 0, 0, first=True)
                with pe.Fori(0, (NT - 2) // 2) as i:
                    chunk(i * 2 + 1, 1, i)
                    chunk(i * 2 + 2, 0, i + 1)
                chunk(NT - 1, 1, NT // 2 - 1)
                turn(NT - 1)

            @block.scalar
            def _(act):
                act.sem_inc(s["seg_free"], 1)
                act.sem_inc(s["sums_free"], 1)
                act.sem_inc(s["turn_free"], 1)
                act.sem_inc(s["gated_free"], 2)

                def columns(n, par, k):
                    act.wait_ge(s[f"y_stored{par}"], k * 16)
                    for q in range(XT // 4):
                        act.wait_ge(s["turned"], n * (XT // 4) + (q + 1))
                        for j in range(4):
                            f = 4 * q + j
                            last = act.activation(yc[:, par, f], ps[:, 7, j * P:(j + 1) * P], ACT.Copy,
                                                  scale=e.gvec[:, G_SSD + f:G_SSD + f + 1])
                        act.drain().then_inc(s["turn_free"], 1)
                    col = slice(n * P, (n + 1) * P) if isinstance(n, int) else bass.ds(n * P, P)
                    act.dma_start(e.y_cols[:, :, col].rearrange("f p t -> p f t"), yc[:, par]).then_inc(s[f"y_stored{par}"], 16)

                def chunk(n, par, k, first=False):
                    act.wait_ge(s["sums"], n + 1)
                    act.wait_ge(s["decays_pool"], n + 1)
                    act.wait_ge(s["decays_dve"], n + 1)
                    act.activation(dec[:, par], ps[:, 0, 0:3 * HS], ACT.Exp).then_inc(s["decays"], 1)
                    act.drain().then_inc(s["sums_free"], 1)
                    for g in range(NG):
                        act.wait_ge(s["seg_ready"], n * NG + (g + 1))
                        act.wait_ge(s["e_free"], n * NG + (g + 1))
                        act.activation(ee[:, g % 2].rearrange("p h c -> p (h c)"), ps[:, 1:3, :].rearrange("p b c -> p (b c)"),
                                       ACT.Exp).then_inc(s["e_ready"], 1)
                        act.drain().then_inc(s["seg_free"], 1)
                    if not first:
                        columns(n - 1, 1 - par, k if par else k - 1)
                    act.wait_ge(s["gated"], n + 1)
                    for g in range(NG):
                        last = act.activation(sq[:, :], y[:, par, hs(g)].rearrange("p h c -> p (h c)"), ACT.Square,
                                              scale=float(DI // NG) ** -0.5, accum_out=ss[:, g:g + 1])
                        if g < NG - 1:
                            act.drain()
                    last.then_inc(s["squared"], 1)
                    act.wait_ge(s["rooted"], n + 1)
                    act.wait_ge(s["normed_free"], n + 1)
                    for g in range(NG):
                        last = act.activation(yn[:, gc(g)], y[:, par, hs(g)].rearrange("p h c -> p (h c)"), ACT.Copy, scale=rs[:, g:g + 1])
                    last.then_inc(s["normed"], 1)
                    act.drain().then_inc(s["gated_free"], 1)
                chunk(0, 0, 0, first=True)
                with act.Fori(0, (NT - 2) // 2) as i:
                    chunk(i * 2 + 1, 1, i)
                    chunk(i * 2 + 2, 0, i + 1)
                chunk(NT - 1, 1, NT // 2 - 1)
                columns(NT - 1, 1, NT // 2 - 1)
                for b in range(2):
                    act.wait_ge(s[f"y_stored{b}"], 16 * NT // 2)

            @block.vector
            def _(dve):
                for name in ("e_free", "in_dve", "decays_dve"):
                    dve.sem_inc(s[name], 2)
                for name in ("cb_free", "inter_free", "intra_free", "upd_free", "xd_free", "normed_free"):
                    dve.sem_inc(s[name], 1)

                def chunk(n, par, k):
                    wait_in(dve, par, k)
                    dve.wait_ge(s["cb_ready"], n + 1)
                    dve.tensor_tensor(cbm[:, :, :], ps[:, 3, :].rearrange("p (g c) -> p g c", g=NG), bc(e.tri[:, :].unsqueeze(1), [P, NG, P]), ALU.mult)
                    dve.drain().then_inc(s["cb_free"], 1)
                    dve.wait_ge(s["gated_free"], n + 1)
                    for g in range(NG):
                        dve.wait_ge(s["e_ready"], n * NG + (g + 1))
                        dve.wait_ge(s["m_free"], n * NG + (g + 1))
                        dve.tensor_tensor(mm[:, g % 2], ee[:, g % 2], bc(cbm[:, g].unsqueeze(1), [P, HPG, P]), ALU.mult).then_inc(s["m_ready"], 1)
                        dve.drain().then_inc(s["e_free"], 1)
                        if g == 0:
                            dve.wait_ge(s["decays"], n + 1)
                        dve.wait_ge(s["inter"], n * NG + (g + 1))
                        yg = y[:, par, hs(g)]
                        dve.tensor_tensor(yg, bank(5), bc(dec[:, par, hs(g)].unsqueeze(2), [P, HPG, HP]), ALU.mult)
                        dve.drain().then_inc(s["inter_free"], 1)
                        if g == 0:
                            dve.wait_ge(s["xd_ready"], n + 1)
                        dve.tensor_tensor(yg, yg, xd[:, hs(g)], ALU.add)
                        dve.drain()
                        dve.wait_ge(s["intra"], n * NG + (g + 1))
                        dve.tensor_tensor(yg, yg, bank(4), ALU.add)
                        dve.drain().then_inc(s["intra_free"], 1)
                        last = dve.tensor_tensor(yg, yg, z[:, par, gc(g)].rearrange("p (h c) -> p h c", c=HP), ALU.mult)
                        dve.wait_ge(s["scaled"], n * NG + (g + 1))
                        dve.wait_ge(s["upd"], n * NG + (g + 1))
                        dve.tensor_tensor(state[:, hs(g)], state[:, hs(g)], bank(6), ALU.add).then_inc(s["state_ready"], 1)
                        dve.drain().then_inc(s["upd_free"], 1)
                    dve.drain().then_inc(s["gated"], 1)
                    dve.sem_inc(s["in_dve"], 1)
                    dve.sem_inc(s["decays_dve"], 1)
                    dve.sem_inc(s["xd_free"], 1)
                over_chunks(dve, chunk)
        ssd_state_out(e, state)


def ssd_state_out(e, state):
    nc, ps = e.nc, e.ps
    turned, copied, stored = e.sem("state_turned"), e.sem("state_copied"), e.sem("state_stored")
    with nc.sbuf_tensor("state_rows", [P, XT, NS], F32) as rows, nc.Block() as block:
        @block.tensor
        def _(pe):
            for k in range(XT):
                last = pe.transpose(ps[:, k // 4, (k % 4) * P:(k % 4 + 1) * P],
                                    state[:, 2 * k:2 * k + 2].rearrange("p h c -> p (h c)"), e.ident[:, :])
            last.then_inc(turned, 1)

        @block.vector
        def _(dve):
            dve.wait_ge(turned, 1)
            dve.tensor_copy(rows[:, :, :], ps[:, 0:4, :].rearrange("p b (k n) -> p (b k) n", k=4)).then_inc(copied, 1)

        @block.sync
        def _(sp):
            sp.wait_ge(copied, 1)
            sp.dma_start(e.o["p_state_ssd"].rearrange("o b h c n -> (o b h c) n").rearrange("(k p) n -> p k n", p=P),
                         rows[:, :, :]).then_inc(stored, 16)
            sp.wait_ge(stored, 16)


def pairs(eng, step):
    step(0, 0, 0)
    with eng.Fori(0, (NT - 2) // 2) as i:
        step(i * 2 + 1, 1, i)
        step(i * 2 + 2, 0, i + 1)
    step(NT - 1, 1, NT // 2 - 1)


def staggered(eng, front, back):
    front(0, 0, True)
    front(1, 1, False)
    back(0, 0, True)
    with eng.Fori(0, (NT - 2) // 2) as i:
        front(i * 2 + 2, 0, False)
        back(i * 2 + 1, 1, False)
        front(i * 2 + 3, 1, False)
        back(i * 2 + 2, 0, False)
    back(NT - 1, 1, False)


def window_attention(e):
    nc, a, ps = e.nc, e.a, e.ps
    e.att_cols = e.dram("att_cols", [KD, P, T])
    names = ("in_ready0", "in_ready1", "qk_free", "v_free", "bias_made", "bias_scaled", "bias_masked", "s_ready", "s_free", "max_ready",
             "exp_ready", "sc_free", "recip_ready", "p_ready", "t_ready", "t_low_free", "t_high_free", "pt_low", "pt_high", "pt_free",
             "o_ready", "o_free", "sink_ready", "out_ready", "stored0", "stored1")
    s = {n: e.sem("win_" + n) for n in names}
    SCALE = HD ** -0.5
    with ExitStack() as st:
        sb = lambda n, sh, dt=F32: st.enter_context(nc.sbuf_tensor(n, sh, dt))
        q = sb("win_q", [P, 2, NH // 2, W])
        kd = sb("win_k", [P, 2, NKV, 2 * W])
        v = sb("win_v", [P, 2, 2, NKV * HD])
        dist = sb("win_dist", [P, 2 * W])
        bias = sb("win_bias", [P, NH, 2 * W])
        sc = sb("win_scores", [P, 2, NH, 2 * W])
        pt = sb("win_pt", [P, NH, 2, W])
        sink = sb("win_sink", [P, NH])
        mx, nm = sb("win_max", [P, 2, NH]), sb("win_nmax", [P, 2, NH])
        den, es, rd = sb("win_den", [P, 2, NH]), sb("win_es", [P, 2, NH]), sb("win_rd", [P, 2, NH])
        oc = sb("win_out", [P, 2, KD, W])
        keys = lambda first: slice(W, 2 * W) if first else slice(0, 2 * W)
        with nc.Block() as block:
            @block.sync
            def _(sp):
                sp.dma_start(sink[:, :], a["attn_sinks"].to_broadcast([P, NH])).then_inc(s["sink_ready"], 16)
                k_src = e.qk_cols[NH // 2:QKT].rearrange("a (b d) t -> d (a b) t", d=HD)

                def load(n, par, k):
                    first = isinstance(n, int) and n == 0
                    sp.wait_ge(s["qk_free"], n + 1)
                    sp.wait_ge(s["v_free"], n + 1)
                    ready = s[f"in_ready{par}"]
                    sp.dma_start(q[:, par], e.qk_cols[0:NH // 2, :, bass.ds(n * W, W)].rearrange("h p t -> p h t")).then_inc(ready, 16)
                    for half in range(2):
                        src = k_src[:, :, 0:W] if first else k_src[:, :, bass.ds(n * W + (-W), 2 * W)]
                        sp.dma_start(kd[half * HD:(half + 1) * HD, par, :, keys(first)], src).then_inc(ready, 16)
                    if first:
                        sp.dma_start(v[:, par, 1], e.vdt_rows[0:W, 0:NKV * HD]).then_inc(ready, 16)
                    else:
                        sp.dma_start(v[:, par], e.vdt_rows[bass.ds(n * W + (-W), 2 * W), 0:NKV * HD].rearrange("(s p) c -> p s c", p=P)).then_inc(ready, 16)
                pairs(sp, load)

            @block.gpsimd
            def _(pool):
                pool.iota(dist[:, :], pattern=[[-1, 2 * W]], base=W, channel_multiplier=1, allow_small_or_imprecise_dtypes=True).then_inc(s["bias_made"], 1)
                pool.wait_ge(s["bias_scaled"], 1)
                pool.affine_select(out=bias[:, :, :], in_=bias[:, :, :], compare_op=ALU.is_ge, fill=NEG, base=W,
                                   pattern=[[0, NH], [-1, 2 * W]], channel_multiplier=1)
                pool.drain()
                pool.affine_select(out=bias[:, :, :], in_=bias[:, :, :], compare_op=ALU.is_ge, fill=NEG, base=0,
                                   pattern=[[0, NH], [1, 2 * W]], channel_multiplier=-1).then_inc(s["bias_masked"], 1)

                def scale(n, par, k):
                    ks = keys(isinstance(n, int) and n == 0)
                    pool.wait_ge(s["recip_ready"], n + 1)
                    pool.tensor_tensor(sc[:, par, :, ks], sc[:, par, :, ks], bc(rd[:, par].unsqueeze(2), [P, NH, ks.stop - ks.start]),
                                       ALU.mult).then_inc(s["p_ready"], 1)
                pairs(pool, scale)

            @block.tensor
            def _(pe):
                pe.sem_inc(s["qk_free"], 2)
                pe.sem_inc(s["v_free"], 2)
                pe.sem_inc(s["sc_free"], 2)

                def scores(n, par, first, k):
                    pe.wait_ge(s[f"in_ready{par}"], k * 64 + 64)
                    for g in range(NH // 2):
                        pe.wait_ge(s["s_free"], n * (NH // 2) + (g + 1))
                        for j in range(2):
                            h, half = 4 * (g // 2) + 2 * j + g % 2, slice(g % 2 * HD, (g % 2 + 1) * HD)
                            last = pe.matmul(ps[:, g % 4, j * 2 * W + keys(first).start:j * 2 * W + 2 * W], q[half, par, h // 2],
                                             kd[half, par, h // GQA, keys(first)], start=True, stop=True)
                        last.then_inc(s["s_ready"], 1)
                    pe.drain().then_inc(s["qk_free"], 1)

                def weigh(n, par, first):
                    pe.wait_ge(s["p_ready"], n + 1)
                    pe.wait_ge(s["pt_free"], n + 1)
                    for g in range(NH // 2):
                        low = g % 2 == 0
                        pe.wait_ge(s["t_low_free"] if low else s["t_high_free"], n * (NH // 4) + (g // 2 + 1))
                        for j in range(2):
                            for b in range(1 if first else 0, 2):
                                last = pe.transpose(ps[:, 4 + g % 2, (2 * j + b) * W:(2 * j + b + 1) * W],
                                                    sc[:, par, 2 * g + j, b * W:(b + 1) * W], e.ident[:, :])
                        last.then_inc(s["t_ready"], 1)
                    pe.drain().then_inc(s["sc_free"], 1)
                    pe.wait_ge(s["pt_low"], n * (NH // 4) + NH // 4)
                    pe.wait_ge(s["pt_high"], n * (NH // 4) + NH // 4)
                    pe.wait_ge(s["o_free"], n + 1)
                    for h in range(NH):
                        g, half = h // 2, slice((h % 2) * HD, (h % 2 + 1) * HD)
                        for b in range(1 if first else 0, 2):
                            last = pe.matmul(ps[half, 6 + g // 4, (g % 4) * W:(g % 4 + 1) * W],
                                             v[:, par, b, (h // GQA) * HD:(h // GQA + 1) * HD], pt[:, h, b],
                                             start=(b == 1 if first else b == 0), stop=(b == 1))
                    last.then_inc(s["o_ready"], 1)
                    pe.drain().then_inc(s["v_free"], 1)

                scores(0, 0, True, 0)
                scores(1, 1, False, 0)
                weigh(0, 0, True)
                with pe.Fori(0, (NT - 2) // 2) as i:
                    scores(i * 2 + 2, 0, False, i + 1)
                    weigh(i * 2 + 1, 1, False)
                    scores(i * 2 + 3, 1, False, i + 1)
                    weigh(i * 2 + 2, 0, False)
                weigh(NT - 1, 1, False)

            @block.scalar
            def _(act):
                act.sem_inc(s["t_high_free"], 1)
                act.sem_inc(s["o_free"], 1)

                def exps(n, par, first):
                    act.wait_ge(s["max_ready"], n + 1)
                    for h in range(NH):
                        act.activation(sc[:, par, h, keys(first)], sc[:, par, h, keys(first)], ACT.Exp,
                                       bias=nm[:, par, h:h + 1], accum_out=den[:, par, h:h + 1])
                    act.activation(es[:, par], es[:, par], ACT.Exp).then_inc(s["exp_ready"], 1)

                def out(n, par, first, earlier):
                    for g in range(NH // 4):
                        act.wait_ge(s["t_ready"], n * (NH // 2) + (2 * g + 2))
                        src = ps[:, 5, :].rearrange("p (h b c) -> p h b c", h=2, b=2)
                        b0 = 1 if first else 0
                        act.activation(pt[:, 4 * g + 2:4 * g + 4, b0:2], src[:, :, b0:2], ACT.Copy).then_inc(s["pt_high"], 1)
                        act.drain().then_inc(s["t_high_free"], 1)
                    act.wait_ge(s["o_ready"], n + 1)
                    act.wait_ge(s[f"stored{par}"], earlier * 16)
                    act.activation(oc[:, par].rearrange("p (b k) c -> p b (k c)", b=2), ps[:, 6:8, :], ACT.Copy).then_inc(s["out_ready"], 1)
                    act.drain().then_inc(s["o_free"], 1)
                    act.sem_inc(s["pt_free"], 1)
                    act.dma_start(e.att_cols[:, :, bass.ds(n * W, W)].rearrange("f p t -> p f t"), oc[:, par]).then_inc(s[f"stored{par}"], 16)

                act.sem_inc(s["pt_free"], 1)
                exps(0, 0, True)
                exps(1, 1, False)
                out(0, 0, True, 0)
                with act.Fori(0, (NT - 2) // 2) as i:
                    exps(i * 2 + 2, 0, False)
                    out(i * 2 + 1, 1, False, i)
                    exps(i * 2 + 3, 1, False)
                    out(i * 2 + 2, 0, False, i + 1)
                out(NT - 1, 1, False, NT // 2 - 1)
                for b in range(2):
                    act.wait_ge(s[f"stored{b}"], 16 * NT // 2)

            @block.vector
            def _(dve):
                dve.wait_ge(s["bias_made"], 1)
                for h in range(NH):
                    last = dve.tensor_scalar(bias[:, h], dist[:, :], -(2.0 ** (-8.0 * (h + 1) / NH)), None, ALU.mult)
                last.then_inc(s["bias_scaled"], 1)
                dve.wait_ge(s["bias_masked"], 1)
                dve.wait_ge(s["sink_ready"], 16)
                dve.sem_inc(s["s_free"], 4)
                dve.sem_inc(s["t_low_free"], 1)

                def maxima(n, par, first):
                    ks = keys(first)
                    dve.wait_ge(s["sc_free"], n + 1)
                    for g in range(NH // 2):
                        dve.wait_ge(s["s_ready"], n * (NH // 2) + (g + 1))
                        hh = slice(4 * (g // 2) + g % 2, 4 * (g // 2) + g % 2 + 3, 2)
                        dve.scalar_tensor_tensor(out=sc[:, par, hh, ks], in0=ps[:, g % 4, :].rearrange("p (h c) -> p h c", h=2)[:, :, ks],
                                                 scalar=SCALE, in1=bias[:, hh, ks], op0=ALU.mult, op1=ALU.add)
                        dve.drain().then_inc(s["s_free"], 1)
                    dve.tensor_reduce(mx[:, par], sc[:, par, :, ks], AX.X, ALU.max)
                    dve.drain()
                    dve.tensor_tensor(mx[:, par], mx[:, par], sink[:, :], ALU.max)
                    dve.drain()
                    dve.tensor_scalar(nm[:, par], mx[:, par], -1.0, None, ALU.mult)
                    dve.tensor_tensor(es[:, par], sink[:, :], mx[:, par], ALU.subtract).then_inc(s["max_ready"], 1)

                def normalise(n, par, first):
                    dve.wait_ge(s["exp_ready"], n + 1)
                    dve.tensor_tensor(den[:, par], den[:, par], es[:, par], ALU.add)
                    dve.drain()
                    dve.reciprocal(rd[:, par], den[:, par]).then_inc(s["recip_ready"], 1)
                    b0 = 1 if first else 0
                    for g in range(NH // 4):
                        dve.wait_ge(s["t_ready"], n * (NH // 2) + (2 * g + 1))
                        src = ps[:, 4, :].rearrange("p (h b c) -> p h b c", h=2, b=2)
                        dve.tensor_copy(pt[:, 4 * g:4 * g + 2, b0:2], src[:, :, b0:2]).then_inc(s["pt_low"], 1)
                        dve.drain().then_inc(s["t_low_free"], 1)
                staggered(dve, maxima, normalise)


def sample_states(e):
    nc, a, o, ps = e.nc, e.a, e.o, e.ps
    s = {n: e.sem("sconv_" + n) for n in ("u", "silu", "loaded", "turned", "rows", "stored", "copied")}
    keep = lambda n, sh: e.mix.enter_context(nc.sbuf_tensor(n, sh, F32))
    e.sc_cols = keep("sc_cols", [P, CT, NB])
    e.sqk_rows = keep("sqk_rows", [NB, (NH + NKV) * HD])
    e.sbc_rows = keep("sbc_rows", [NB, 2 * NG * NS])
    e.sv_rows = keep("sv_rows", [NB, NKV * HD])
    with ExitStack() as st:
        sb = lambda n, sh: st.enter_context(nc.sbuf_tensor(n, sh, F32))
        acc, term = sb("sconv_acc", [P, CT, NB]), sb("sconv_term", [P, CT, NB])
        trows = sb("tail_rows", [CK - 1 + NB, CD])
        qk_s = sb("qk_sample", [P, QKT, NB])
        k_last = sb("k_last", [P, 2, P])
        k_rows = sb("k_last_rows", [P, NKV * HD])
        block = st.enter_context(nc.Block())
        KW = NKV * HD

        @block.sync
        def _(sp):
            sp.dma_start(qk_s[:, :, :], e.qk_cols[:, :, SEQ:T].rearrange("f p t -> p f t")).then_inc(s["loaded"], 16)
            sp.dma_start(k_last[:, :, :], e.qk_cols[NH // 2:QKT, :, SEQ - W:SEQ].rearrange("f p t -> p f t")).then_inc(s["loaded"], 16)
            sp.dma_start(e.sv_rows[:, :], e.vdt_rows[SEQ:T, 0:KW]).then_inc(s["loaded"], 16)
            sp.dma_start(o["p_cache_win_v"].rearrange("o b s v d -> (o b s) (v d)"), e.vdt_rows[SEQ - W:SEQ, 0:KW]).then_inc(s["copied"], 16)
            for c in "kv":
                sp.dma_start(o["s_cache_win_" + c].rearrange("o b s v d -> (o b) s (v d)")[:, 0:W - 1],
                             a["cache_win_" + c].rearrange("o b s v d -> (o b) s (v d)")[:, 1:W]).then_inc(s["copied"], 16)
            sp.dma_start(o["s_cache_win_v"].rearrange("o b s v d -> (o b) s (v d)")[:, W - 1], e.vdt_rows[SEQ:T, 0:KW]).then_inc(s["copied"], 16)
            sp.dma_start(o["s_state_conv"][0, :, 0:CK - 2], a["state_conv"][0, :, 1:CK - 1]).then_inc(s["copied"], 16)
            sp.wait_ge(s["rows"], 1)
            sp.dma_start(o["p_state_conv"].rearrange("o b k c -> (o b k) c"), trows[0:CK - 1, :]).then_inc(s["copied"], 16)
            sp.dma_start(o["s_state_conv"][0, :, CK - 2], trows[CK - 1:CK - 1 + NB, :]).then_inc(s["copied"], 16)
            sp.wait_ge(s["rows"], 2)
            sp.dma_start(o["p_cache_win_k"].rearrange("o b s v d -> (o b s) (v d)"), k_rows[:, :]).then_inc(s["copied"], 16)
            sp.dma_start(o["s_cache_win_k"].rearrange("o b s v d -> (o b) s (v d)")[:, W - 1], e.sqk_rows[:, NH * HD:]).then_inc(s["copied"], 16)
            sp.wait_ge(s["copied"], 16 * 9)
            sp.wait_ge(s["loaded"], 48)

        @block.vector
        def _(dve):
            new = e.tails[:, :, CK - 1:]
            wt = lambda k: bc(e.cvec[:, :, CR_W + k:CR_W + k + 1], [P, CT, NB])
            dve.tensor_tensor(acc[:, :, :], new, wt(CK - 1), ALU.mult)
            dve.drain()
            dve.tensor_tensor(acc[:, :, :], acc[:, :, :], bc(e.cvec[:, :, CR_B:CR], [P, CT, NB]), ALU.add)
            for k in range(CK - 1):
                past = e.cvec[:, :, CR_STATE:CR_W].rearrange("p c (b k) -> p c b k", k=CK - 1)[:, :, :, k]
                dve.tensor_tensor(term[:, :, :], past, wt(k), ALU.mult)
                dve.drain()
                dve.tensor_tensor(acc[:, :, :], acc[:, :, :], term[:, :, :], ALU.add)
                dve.drain()
            dve.sem_inc(s["u"], 1)
            dve.wait_ge(s["turned"], 1)
            dve.tensor_copy(trows[:, :], ps[0:CK - 1 + NB, 0:6, :].rearrange("p b c -> p (b c)")).then_inc(s["rows"], 1)
            dve.drain()
            dve.wait_ge(s["turned"], 2)
            dve.tensor_copy(e.sqk_rows[:, 0:1024], ps[0:NB, 0:2, :].rearrange("p b c -> p (b c)"))
            dve.tensor_copy(e.sqk_rows[:, 1024:1280], ps[0:NB, 2, 0:256])
            dve.tensor_copy(k_rows[:, :], ps[:, 3, 0:256])
            dve.drain().then_inc(s["rows"], 1)
            dve.wait_ge(s["turned"], 3)
            dve.tensor_copy(e.sbc_rows[:, :], ps[0:NB, 4:6, :].rearrange("p b c -> p (b c)"))

        @block.scalar
        def _(act):
            act.wait_ge(s["u"], 1)
            act.activation(e.sc_cols[:, :, :], acc[:, :, :], ACT.Silu).then_inc(s["silu"], 1)

        @block.tensor
        def _(pe):
            for c in range(CT):
                last = pe.transpose(ps[0:CK - 1 + NB, c // 4, (c % 4) * P:(c % 4 + 1) * P], e.tails[:, c], e.ident[:, :])
            last.then_inc(s["turned"], 1)
            pe.wait_ge(s["loaded"], 48)
            pe.wait_ge(s["rows"], 1)
            for c in range(QKT):
                pe.transpose(ps[0:NB, c // 4, (c % 4) * P:(c % 4 + 1) * P], qk_s[:, c], e.ident[:, :])
            for c in range(2):
                last = pe.transpose(ps[:, 3, c * P:(c + 1) * P], k_last[:, c], e.ident[:, :])
            last.then_inc(s["turned"], 1)
            pe.wait_ge(s["silu"], 1)
            for c in range(2 * NG):
                last = pe.transpose(ps[0:NB, 4 + c // 4, (c % 4) * P:(c % 4 + 1) * P], e.sc_cols[:, XT + c], e.ident[:, :])
            last.then_inc(s["turned"], 1)


def sample_ssd(e):
    nc, a, o, ps = e.nc, e.a, e.o, e.ps
    names = ("sel_made", "loaded", "dec", "dtT", "dtT_copied", "spread", "spread_copied", "xdt_ready", "bc_ready", "bc_free",
             "h_ready0", "h_ready1", "h_scaled", "h_new", "h_stored0", "h_stored1", "zT", "zT_copied", "sq", "total", "meaned", "rooted", "y_ready", "y_stored")
    s = {n: e.sem("sssd_" + n) for n in names}
    e.onehot = e.mix.enter_context(nc.sbuf_tensor("onehot", [NB, NB, P], F32))
    with ExitStack() as st:
        sb = lambda n, sh: st.enter_context(nc.sbuf_tensor(n, sh, F32))
        sel = sb("head_sel", [HS, DI])
        decay = sb("sdecay", [NB, HS])
        dtT = sb("sdtT", [HS, 2 * NB + 1])
        spread = sb("sspread", [P, XT, 2 * NB + 1])
        zr = sb("sz_rows", [NB, DI])
        xdt = sb("sxdt", [P, XT, NB])
        h = sb("sh", [P, 2, XT, NS])
        t1 = sb("st1", [P, XT, NS])
        t2 = sb("st2", [P, XT, NS])
        y = sb("sy", [P, XT, NB])
        y2 = sb("sy2", [P, XT, NB])
        yb = sb("syb", [P, NB, XT])
        ms, rs = sb("sms", [P, NG, NB]), sb("srs", [P, NG, NB])
        mh = sb("smh", [P, NG, NB])
        block = st.enter_context(nc.Block())
        st_in = a["state_ssd"][0].rearrange("b h c n -> b (h c) n").rearrange("b (k p) n -> b p k n", p=P)
        st_out = o["s_state_ssd"][0].rearrange("b h c n -> b (h c) n").rearrange("b (k p) n -> b p k n", p=P)

        @block.gpsimd
        def _(pool):
            pool.memset(sel[:, :], 1.0)
            pool.memset(e.onehot[:, :, :], 0.0)
            pool.memset(mh[:, :, :], -0.5)
            pool.drain()
            pool.affine_select(out=sel[:, :], in_=sel[:, :], compare_op=ALU.is_ge, fill=0.0, base=0, pattern=[[1, DI]], channel_multiplier=-HP)
            pool.affine_select(out=e.onehot[:, :, :], in_=e.onehot[:, :, :], compare_op=ALU.not_equal, fill=1.0, base=0,
                               pattern=[[-1, NB], [0, P]], channel_multiplier=1)
            pool.drain()
            pool.affine_select(out=sel[:, :], in_=sel[:, :], compare_op=ALU.is_ge, fill=0.0, base=HP - 1, pattern=[[-1, DI]], channel_multiplier=HP)
            pool.drain().then_inc(s["sel_made"], 1)
            pool.wait_ge(s["spread_copied"], 1)
            for b in range(NB):
                pool.wait_ge(s[f"h_ready{b % 2}"], 16 * (b // 2 + 1))
                pool.tensor_tensor(h[:, b % 2], h[:, b % 2], bc(spread[:, :, NB + b:NB + b + 1], [P, XT, NS]), ALU.mult).then_inc(s["h_scaled"], 1)
            pool.wait_ge(s["meaned"], 1)
            pool.tensor_tensor(rs[:, :, :], ms[:, :, :], mh[:, :, :], ALU.pow).then_inc(s["rooted"], 1)

        @block.sync
        def _(sp):
            sp.dma_start(dtT[:, 2 * NB:2 * NB + 1], a["d_skip"].rearrange("o h -> h o")).then_inc(s["loaded"], 16)
            sp.dma_start(zr[:, :], e.z_rows[SEQ:T, :]).then_inc(s["loaded"], 16)
            for b in range(NB):
                if b >= 2:
                    sp.wait_ge(s[f"h_stored{b % 2}"], 16 * (b // 2))
                    sp.wait_ge(s["bc_free"], b + 1)
                sp.dma_start(h[:, b % 2], st_in[b]).then_inc(s[f"h_ready{b % 2}"], 16)
            sp.wait_ge(s["y_ready"], 1)
            sp.dma_start(e.y_cols[:, :, SEQ:T].rearrange("f p t -> p f t"), y2[:, :, :]).then_inc(s["y_stored"], 16)
            sp.wait_ge(s["y_stored"], 16)

        @block.scalar
        def _(act):
            act.activation(decay[:, :], e.da[0:NB, NT, :], ACT.Exp).then_inc(s["dec"], 1)
            for b in range(NB):
                act.wait_ge(s["h_new"], b + 1)
                act.dma_start(st_out[b], h[:, b % 2]).then_inc(s[f"h_stored{b % 2}"], 16)
            for q in range(2):
                act.wait_ge(s[f"h_stored{q}"], 16 * NB // 2)

        @block.tensor
        def _(pe):
            pe.wait_ge(s["dec"], 1)
            pe.transpose(ps[0:HS, 0, 0:NB], e.dt[0:NB, NT, :], e.ident[0:NB, 0:NB])
            pe.transpose(ps[0:HS, 0, NB:2 * NB], decay[:, :], e.ident[0:NB, 0:NB]).then_inc(s["dtT"], 1)
            pe.wait_ge(s["loaded"], 32)
            for k in range(XT):
                last = pe.transpose(ps[:, 2, k * NB:(k + 1) * NB], zr[:, k * P:(k + 1) * P], e.ident[0:NB, 0:NB])
            last.then_inc(s["zT"], 1)
            pe.wait_ge(s["dtT_copied"], 1)
            pe.wait_ge(s["sel_made"], 1)
            for k in range(XT):
                last = pe.matmul(ps[:, 1, k * 32:k * 32 + 2 * NB + 1], sel[:, k * P:(k + 1) * P], dtT[:, :], start=True, stop=True)
            last.then_inc(s["spread"], 1)
            for b in range(NB):
                pe.wait_ge(s["bc_free"], b + 1)
                for q in range(2):
                    last = pe.matmul(ps[:, 4 + 2 * (b % 2) + q, :], e.onehot[:, b], e.sbc_rows[:, q * 512:(q + 1) * 512], start=True, stop=True)
                last.then_inc(s["bc_ready"], 1)
            pe.wait_ge(s["sq"], 1)
            pe.matmul(ps[:, 3, 0:NG * NB], e.ones[:, :], ms[:, :, :].rearrange("p g b -> p (g b)"), start=True, stop=True).then_inc(s["total"], 1)

        @block.vector
        def _(dve):
            dve.sem_inc(s["bc_free"], 2)
            dve.wait_ge(s["dtT"], 1)
            dve.wait_ge(s["loaded"], 32)
            dve.tensor_copy(dtT[:, 0:2 * NB], ps[0:HS, 0, 0:2 * NB]).then_inc(s["dtT_copied"], 1)
            dve.wait_ge(s["spread"], 1)
            dve.tensor_copy(spread[:, :, :], ps[:, 1, :].rearrange("p (k c) -> p k c", c=32)[:, :, 0:2 * NB + 1])
            dve.drain().then_inc(s["spread_copied"], 1)
            dve.tensor_tensor(xdt[:, :, :], e.sc_cols[:, 0:XT, :], spread[:, :, 0:NB], ALU.mult)
            dve.drain()
            four = lambda ap: ap.rearrange("p (g k) n -> p g k n", g=NG)
            for b in range(NB):
                dve.wait_ge(s["bc_ready"], b + 1)
                bank = lambda q: bc(ps[:, 4 + 2 * (b % 2) + q, :].rearrange("p (g n) -> p g n", g=NG).unsqueeze(2), [P, NG, XT // NG, NS])
                dve.tensor_tensor(four(t1[:, :, :]), bank(0), bc(four(xdt[:, :, b:b + 1]), [P, NG, XT // NG, NS]), ALU.mult)
                dve.drain()
                dve.wait_ge(s["h_scaled"], b + 1)
                dve.tensor_tensor(h[:, b % 2], h[:, b % 2], t1[:, :, :], ALU.add).then_inc(s["h_new"], 1)
                dve.drain()
                dve.tensor_tensor(four(t2[:, :, :]), four(h[:, b % 2]), bank(1), ALU.mult)
                dve.drain().then_inc(s["bc_free"], 1)
                dve.tensor_reduce(yb[:, b], t2[:, :, :], AX.X, ALU.add)
                dve.drain()
            ybt = yb[:, :, :].rearrange("p b k -> p k b")
            dve.tensor_tensor(y[:, :, :], e.sc_cols[:, 0:XT, :], bc(spread[:, :, 2 * NB:2 * NB + 1], [P, XT, NB]), ALU.mult)
            dve.drain()
            dve.tensor_tensor(y[:, :, :], y[:, :, :], ybt, ALU.add)
            dve.drain()
            dve.wait_ge(s["zT"], 1)
            dve.tensor_tensor(y[:, :, :], y[:, :, :], ps[:, 2, 0:XT * NB].rearrange("p (k b) -> p k b", b=NB), ALU.mult)
            dve.drain()
            dve.tensor_tensor(y2[:, :, :], y[:, :, :], y[:, :, :], ALU.mult)
            dve.drain()
            dve.tensor_reduce(ms[:, :, :], y2[:, :, :].rearrange("p (g k) b -> p g b k", g=NG), AX.X, ALU.add).then_inc(s["sq"], 1)
            dve.wait_ge(s["total"], 1)
            dve.tensor_scalar(ms[:, :, :].rearrange("p g b -> p (g b)"), ps[:, 3, 0:NG * NB], NG / DI, EPS, ALU.mult, ALU.add).then_inc(s["meaned"], 1)
            dve.wait_ge(s["rooted"], 1)
            dve.tensor_tensor(y2[:, :, :].rearrange("p (g k) b -> p g k b", g=NG), y[:, :, :].rearrange("p (g k) b -> p g k b", g=NG),
                              bc(rs[:, :, :].unsqueeze(2), [P, NG, XT // NG, NB]), ALU.mult)
            dve.drain()
            dve.tensor_tensor(y2[:, :, :], y2[:, :, :], bc(e.gvec[:, G_SSD:G_SSD + XT].unsqueeze(2), [P, XT, NB]), ALU.mult).then_inc(s["y_ready"], 1)


def sample_window(e):
    nc, a, o, ps = e.nc, e.a, e.o, e.ps
    names = ("loaded", "dist", "q_ready", "q_free", "new_made", "sT", "turned", "cols", "maxed", "exped", "normed", "pT", "pT_copied",
             "pn", "pn_copied", "o_ready", "o_copied", "stored")
    s = {n: e.sem("swin_" + n) for n in names}
    SCALE = HD ** -0.5
    R = NB * NH
    with ExitStack() as st:
        sb = lambda n, sh: st.enter_context(nc.sbuf_tensor(n, sh, F32))
        kc, vc = sb("swin_k", [P, NB, NKV * HD]), sb("swin_v", [P, NB, NKV * HD])
        sink = sb("swin_sink", [NB, NH])
        prod = sb("swin_prod", [P, NKV, GQA, HD])
        prod_new = sb("swin_prod_new", [NB, NKV, GQA, HD])
        s_new = sb("swin_s_new", [NB, NH])
        own = sb("swin_own", [NB, 2, NB, NH])
        sT = sb("swin_sT", [P, NB, NH])
        dist, bias = sb("swin_dist", [P, 1]), sb("swin_bias", [P, NH])
        sc = sb("swin_sc", [R, W + 2])
        mx, nm, den, rd = sb("swin_mx", [R, 1]), sb("swin_nm", [R, 1]), sb("swin_den", [R, 1]), sb("swin_rd", [R, 1])
        pT = sb("swin_pT", [P, NB, NH])
        pn_row = sb("swin_pn_row", [1, R])
        pn = sb("swin_pn", [NB, NB, NH])
        oc = sb("swin_oc", [P, NH // 2, NB])
        block = st.enter_context(nc.Block())
        rows4 = lambda ap: ap.rearrange("p (v g d) -> p v g d", v=NKV, g=GQA)

        @block.sync
        def _(sp):
            sp.dma_start(kc[:, :, :], a["cache_win_k"][0].rearrange("b s v d -> s b (v d)")).then_inc(s["loaded"], 16)
            sp.dma_start(vc[:, :, :], a["cache_win_v"][0].rearrange("b s v d -> s b (v d)")).then_inc(s["loaded"], 16)
            sp.dma_start(sink[:, :], a["attn_sinks"].to_broadcast([NB, NH])).then_inc(s["loaded"], 16)
            sp.wait_ge(s["o_copied"], 1)
            sp.dma_start(e.att_cols[:, :, SEQ:T].rearrange("f p t -> p f t"), oc[:, :, :]).then_inc(s["stored"], 16)
            sp.wait_ge(s["stored"], 16)

        @block.gpsimd
        def _(pool):
            pool.iota(dist[:, :], pattern=[[0, 1]], base=W, channel_multiplier=-1, allow_small_or_imprecise_dtypes=True).then_inc(s["dist"], 1)

        @block.tensor
        def _(pe):
            for b in range(NB):
                pe.wait_ge(s["q_free"], b + 1)
                for q in range(2):
                    last = pe.matmul(ps[:, 2 * (b % 2) + q, :], e.onehot[:, b], e.sqk_rows[:, q * 512:(q + 1) * 512], start=True, stop=True)
                last.then_inc(s["q_ready"], 1)
            pe.wait_ge(s["new_made"], 1)
            for q in range(2):
                pe.matmul(ps[0:R, 4, q:q + 1], own[:, q].rearrange("p b h -> p (b h)"), e.ones[0:NB, 0:1], start=True, stop=True)
            pe.wait_ge(s["sT"], 1)
            pe.transpose(ps[0:R, 5, 0:W], sT[:, :, :].rearrange("p b h -> p (b h)"), e.ident[:, :]).then_inc(s["turned"], 1)
            pe.wait_ge(s["normed"], 1)
            pe.transpose(ps[:, 6, 0:R], sc[:, 0:W], e.ident[:, :])
            pe.transpose(ps[0:1, 7, 0:R], sc[:, W:W + 1], e.ident[:, :]).then_inc(s["pT"], 1)
            pe.wait_ge(s["pT_copied"], 1)
            pe.matmul(ps[0:NB, 4, 0:R], e.ones[0:1, 0:NB], pn_row[:, :], start=True, stop=True).then_inc(s["pn"], 1)
            pe.wait_ge(s["pn_copied"], 1)
            out = ps[:, 5, 0:(NH // 2) * NB].rearrange("p (k b) -> p k b", b=NB)
            for b in range(NB):
                for v in range(NKV):
                    for half in range(2):
                        dst = out[half * HD:(half + 1) * HD, 2 * v:2 * v + 2, b]
                        heads = slice(GQA * v + half, GQA * v + half + 3, 2)
                        pe.matmul(dst, vc[:, b, v * HD:(v + 1) * HD], pT[:, b, heads], start=True, stop=False)
                        last = pe.matmul(dst, e.sv_rows[:, v * HD:(v + 1) * HD], pn[:, b, heads], start=False, stop=True)
            last.then_inc(s["o_ready"], 1)

        @block.scalar
        def _(act):
            act.wait_ge(s["maxed"], 1)
            act.activation(sc[:, :], sc[:, :], ACT.Exp, bias=nm[:, :], accum_out=den[:, :]).then_inc(s["exped"], 1)

        @block.vector
        def _(dve):
            dve.sem_inc(s["q_free"], 2)
            dve.wait_ge(s["loaded"], 48)
            dve.wait_ge(s["dist"], 1)
            for hh in range(NH):
                dve.tensor_scalar(bias[:, hh:hh + 1], dist[:, :], -(2.0 ** (-8.0 * (hh + 1) / NH)), None, ALU.mult)
            dve.tensor_tensor(prod_new[:, :, :, :], rows4(e.sqk_rows[:, 0:NH * HD]),
                              bc(e.sqk_rows[:, NH * HD:].rearrange("p (v d) -> p v d", v=NKV).unsqueeze(2), [NB, NKV, GQA, HD]), ALU.mult)
            dve.drain()
            dve.tensor_reduce(s_new[:, :], prod_new[:, :, :, :].rearrange("p v g d -> p (v g) d"), AX.X, ALU.add)
            dve.drain()
            dve.tensor_scalar(s_new[:, :], s_new[:, :], SCALE, None, ALU.mult)
            dve.drain()
            diag = bc(e.onehot[:, :, 0:1], [NB, NB, NH])
            dve.tensor_tensor(own[:, 0], bc(s_new[:, :].unsqueeze(1), [NB, NB, NH]), diag, ALU.mult)
            dve.tensor_tensor(own[:, 1], bc(sink[:, :].unsqueeze(1), [NB, NB, NH]), diag, ALU.mult).then_inc(s["new_made"], 1)
            for b in range(NB):
                dve.wait_ge(s["q_ready"], b + 1)
                bank = rows4(ps[:, 2 * (b % 2):2 * (b % 2) + 2, :].rearrange("p b c -> p (b c)"))
                dve.tensor_tensor(prod[:, :, :, :], bank, bc(kc[:, b].rearrange("p (v d) -> p v d", v=NKV).unsqueeze(2), [P, NKV, GQA, HD]), ALU.mult)
                dve.drain().then_inc(s["q_free"], 1)
                dve.tensor_reduce(sT[:, b], prod[:, :, :, :].rearrange("p v g d -> p (v g) d"), AX.X, ALU.add)
                dve.drain()
            dve.scalar_tensor_tensor(out=sT[:, :, :], in0=sT[:, :, :], scalar=SCALE, in1=bc(bias[:, :].unsqueeze(1), [P, NB, NH]),
                                     op0=ALU.mult, op1=ALU.add).then_inc(s["sT"], 1)
            dve.wait_ge(s["turned"], 1)
            dve.tensor_copy(sc[:, 0:W], ps[0:R, 5, 0:W])
            dve.tensor_copy(sc[:, W:W + 2], ps[0:R, 4, 0:2])
            dve.drain()
            dve.tensor_reduce(mx[:, :], sc[:, :], AX.X, ALU.max)
            dve.drain()
            dve.tensor_scalar(nm[:, :], mx[:, :], -1.0, None, ALU.mult).then_inc(s["maxed"], 1)
            dve.wait_ge(s["exped"], 1)
            dve.reciprocal(rd[:, :], den[:, :])
            dve.drain()
            dve.tensor_scalar(sc[:, :], sc[:, :], rd[:, :], None, ALU.mult).then_inc(s["normed"], 1)
            dve.wait_ge(s["pT"], 1)
            dve.tensor_copy(pT[:, :, :].rearrange("p b h -> p (b h)"), ps[:, 6, 0:R])
            dve.tensor_copy(pn_row[:, :], ps[0:1, 7, 0:R]).then_inc(s["pT_copied"], 1)
            dve.wait_ge(s["pn"], 1)
            dve.tensor_tensor(pn[:, :, :], ps[0:NB, 4, 0:R].rearrange("p (b h) -> p b h", b=NB), bc(e.onehot[:, :, 0:1], [NB, NB, NH]), ALU.mult)\
                .then_inc(s["pn_copied"], 1)
            dve.wait_ge(s["o_ready"], 1)
            dve.tensor_copy(oc[:, :, :], ps[:, 5, 0:(NH // 2) * NB].rearrange("p (k b) -> p k b", b=NB)).then_inc(s["o_copied"], 1)


def mixer_out(e):
    nc, a, ps = e.nc, e.a, e.ps
    names = ("w_free", "g_free", "ps_ready", "ps_free", "att_ready", "mix_ready", "wm_ready")
    s = {n: e.sem("down_" + n) for n in names}
    w_ready = [e.sem(f"down_w_ready{i}") for i in range(2)]
    g_ready = [e.sem(f"down_g_ready{i}") for i in range(2)]
    y_ready = [e.sem(f"down_y_ready{i}") for i in range(4)]
    with ExitStack() as outer:
        merged = outer.enter_context(nc.sbuf_tensor("merged", [P, KD, TP], F32))
        with ExitStack() as st:
            sb = lambda n, sh: st.enter_context(nc.sbuf_tensor(n, sh, F32))
            y = sb("y_all", [P, XT, T])
            wd = sb("w_down", [P, 2, XT, P])
            gates = sb("gates", [P, 2, 3, T])
            block = st.enter_context(nc.Block())

            @block.sync
            def _(sp):
                def load(j, i):
                    n = i * 2 + j
                    sp.wait_ge(s["w_free"], n + 1)
                    sp.dma_start(wd[:, j], a["w_ssd_down"][0][:, bass.ds(n * P, P)].rearrange("(k p) c -> p k c", p=P)).then_inc(w_ready[j], 16)
                load(0, 0)
                for q in range(4):
                    sp.dma_start(y[:, 4 * q:4 * q + 4], e.y_cols[4 * q:4 * q + 4].rearrange("f p t -> p f t")).then_inc(y_ready[q], 16)
                load(1, 0)
                with sp.Fori(1, KD // 2) as i:
                    for j in range(2):
                        load(j, i)

            @block.gpsimd
            def _(pool):
                with pool.Fori(0, KD // 2) as i:
                    for j in range(2):
                        n = i * 2 + j
                        pool.wait_ge(s["g_free"], n + 1)
                        one = lambda ap, m: ap[bass.ds(m, 1)].rearrange("o p t -> (o p) t")
                        pool.dma_start(gates[:, j, 0], one(e.gate_cols, n)).then_inc(g_ready[j], 16)
                        pool.dma_start(gates[:, j, 1], one(e.gate_cols, i * 2 + (KD + j))).then_inc(g_ready[j], 16)
                        pool.dma_start(gates[:, j, 2], one(e.att_cols, n)).then_inc(g_ready[j], 16)

            @block.tensor
            def _(pe):
                pe.sem_inc(s["w_free"], 2)
                for q in range(4):
                    pe.wait_ge(y_ready[q], 16)
                with pe.Fori(0, KD // 2) as i:
                    for j in range(2):
                        pe.wait_ge(w_ready[j], i * 16 + 16)
                        pe.wait_ge(s["ps_free"], i * 2 + (j + 1))
                        for k in range(XT):
                            for q in range(NSPLIT):
                                last = pe.matmul(ps[:, 3 * j + q, 0:NW], wd[:, j, k], y[:, k, q * NW:(q + 1) * NW], start=(k == 0), stop=(k == XT - 1))
                        last.then_inc(s["ps_ready"], 1)
                        pe.drain().then_inc(s["w_free"], 1)

            @block.vector
            def _(dve):
                dve.sem_inc(s["ps_free"], 2)
                dve.sem_inc(s["g_free"], 2)
                dve.memset(merged[:, :, T:TP], 0.0)
                with dve.Fori(0, KD // 2) as i:
                    for j in range(2):
                        n = i * 2 + j
                        dve.wait_ge(g_ready[j], i * 48 + 48)
                        dve.tensor_tensor(gates[:, j, 2], gates[:, j, 2], gates[:, j, 1], ALU.mult)
                        dve.wait_ge(s["ps_ready"], n + 1)
                        three = lambda ap: ap.rearrange("p (q c) -> p q c", q=NSPLIT)
                        dve.tensor_tensor(three(gates[:, j, 0]), ps[:, 3 * j:3 * j + 3, 0:NW], three(gates[:, j, 0]), ALU.mult)
                        dve.drain().then_inc(s["ps_free"], 1)
                        dve.tensor_tensor(merged[:, bass.ds(n, 1), 0:T].rearrange("p o t -> p (o t)"), gates[:, j, 0], gates[:, j, 2], ALU.add)
                        dve.drain().then_inc(s["g_free"], 1)

        wm = outer.enter_context(nc.sbuf_tensor("w_mix", [P, KD, D], F32))
        padded, x_ready = e.sem("x_padded"), [e.sem(f"x_ready{i}") for i in range(3)]
        mixed, emptied = e.sem("mix_ps_ready"), e.sem("mix_ps_free")
        with nc.Block() as block:
            @block.gpsimd
            def _(pool):
                pool.memset(e.x[:, NT, :], 0.0).then_inc(padded, 1)

            @block.sync
            def _(sp):
                sp.dma_start(wm[:, :, :], a["w_mix_out"][0].rearrange("(k p) c -> p k c", p=P)).then_inc(s["wm_ready"], 16)
                rows = a["x_prompt"][0].rearrange("(t p) d -> p t d", p=P)
                for q in range(2):
                    sp.dma_start(e.x[:, 4 * q:4 * q + 4, :], rows[:, 4 * q:4 * q + 4]).then_inc(x_ready[q], 16)
                sp.wait_ge(padded, 1)
                sp.dma_start(e.x[0:NB, NT, :], a["x_sample"][:, 0, :]).then_inc(x_ready[2], 16)

            @block.tensor
            def _(pe):
                pe.wait_ge(s["wm_ready"], 16)
                for t in range(TILES):
                    for half in range(2):
                        u = 2 * t + half
                        if u >= 8:
                            pe.wait_ge(emptied, u - 7)
                        for k in range(KD):
                            last = pe.matmul(ps[:, u % 8, :], merged[:, k, t * P:(t + 1) * P], wm[:, k, half * 512:(half + 1) * 512],
                                             start=(k == 0), stop=(k == KD - 1))
                        last.then_inc(mixed, 1)

            @block.vector
            def _(dve):
                for t in range(TILES):
                    if t % 4 == 0:
                        dve.wait_ge(x_ready[t // 4], 16)
                    for half in range(2):
                        u = 2 * t + half
                        dve.wait_ge(mixed, u + 1)
                        xs = e.x[:, t, half * 512:(half + 1) * 512]
                        dve.tensor_tensor(xs, xs, ps[:, u % 8, :], ALU.add).then_inc(emptied, 1)


def cross_projections(e, xc, memT):
    nc, a, o, ps = e.nc, e.a, e.o, e.ps
    s = {n: e.sem("cproj_" + n) for n in ("w_ready", "wkv_ready", "q_ready", "q_free", "kv_ready", "kv_copied", "stored", "kT", "kT_copied")}
    with nc.sbuf_tensor("w_cq", [P, KD, CW], F32) as wq, nc.sbuf_tensor("w_ckv", [P, KD, 2 * CW], F32) as wkv, \
            nc.sbuf_tensor("mem_k_rows", [P, MT, CW], F32) as mk, nc.Block() as block:
        @block.sync
        def _(sp):
            sp.dma_start(wq[:, :, :], a["w_cq"][0].rearrange("(k p) c -> p k c", p=P)).then_inc(s["w_ready"], 16)
            sp.dma_start(wkv[:, :, :], a["w_ckv"][0].rearrange("(k p) c -> p k c", p=P)).then_inc(s["wkv_ready"], 16)
            sp.wait_ge(s["kv_copied"], 2 * MT)
            for name, rows in (("p_cache_mem_k", mk), ("p_cache_mem_v", e.mv)):
                sp.dma_start(o[name].rearrange("o b (m p) h d -> p (o b m) (h d)", p=P), rows[:, :, :]).then_inc(s["stored"], 16)
            sp.wait_ge(s["stored"], 32)

        @block.tensor
        def _(pe):
            pe.wait_ge(s["w_ready"], 16)
            for h in range(CH):
                if h >= 2:
                    pe.wait_ge(s["q_free"], h - 1)
                for k in range(KD):
                    for q in range(NSPLIT):
                        last = pe.matmul(ps[:, 3 * (h % 2) + q, 0:NW], wq[:, k, h * P:(h + 1) * P], xc[:, k, q * NW:(q + 1) * NW],
                                         start=(k == 0), stop=(k == KD - 1))
                last.then_inc(s["q_ready"], 1)
            pe.wait_ge(s["wkv_ready"], 16)
            pe.wait_ge(s["q_free"], CH)
            for m in range(MT):
                for half in range(2):
                    for k in range(KD):
                        last = pe.matmul(ps[:, 2 * m + half, :], memT[:, k, m * P:(m + 1) * P], wkv[:, k, half * CW:(half + 1) * CW],
                                         start=(k == 0), stop=(k == KD - 1))
                    last.then_inc(s["kv_ready"], 1)
            pe.wait_ge(s["kv_copied"], 2 * MT)
            for h in range(CH):
                for m in range(MT):
                    last = pe.transpose(ps[:, 4 + h // 2, (2 * (h % 2) + m) * P:(2 * (h % 2) + m + 1) * P], mk[:, m, h * P:(h + 1) * P], e.ident[:, :])
            last.then_inc(s["kT"], 1)

        @block.scalar
        def _(act):
            for h in range(CH):
                act.wait_ge(s["q_ready"], h + 1)
                act.activation(e.qc[:, h, 0:T].rearrange("p (q c) -> p q c", q=NSPLIT), ps[:, 3 * (h % 2):3 * (h % 2) + 3, 0:NW], ACT.Copy)\
                   .then_inc(s["q_free"], 1)

        @block.vector
        def _(dve):
            for m in range(MT):
                for half, rows in enumerate((mk, e.mv)):
                    dve.wait_ge(s["kv_ready"], 2 * m + half + 1)
                    dve.tensor_copy(rows[:, m], ps[:, 2 * m + half, :]).then_inc(s["kv_copied"], 1)
            dve.wait_ge(s["kT"], 1)
            dve.tensor_copy(e.mkT[:, :, :].rearrange("p (b h) m -> p b (h m)", b=2), ps[:, 4:6, :])


def cross_prompt(e, oc):
    nc, ps = e.nc, e.ps
    names = ("s_ready", "s_free", "maxed", "exped", "recip", "p_ready", "p_free", "t_ready", "t_free", "pt_ready", "pt_free", "o_ready", "o_free")
    s = {n: e.sem("cross_" + n) for n in names}
    SCALE = CHD ** -0.5
    with ExitStack() as st:
        sb = lambda n, sh: st.enter_context(nc.sbuf_tensor(n, sh, F32))
        p = sb("cross_p", [P, 2, CH, MEM])
        pt = sb("cross_pt", [P, 2, CH, MT, P])
        mx, nm, den, rd = (sb("cross_" + n, [P, 2, CH]) for n in ("mx", "nm", "den", "rd"))
        block = st.enter_context(nc.Block())

        @block.tensor
        def _(pe):
            def scores(t):
                if t >= 2:
                    pe.wait_ge(s["s_free"], t - 1)
                for h in range(CH):
                    last = pe.matmul(ps[:, 2 * (t % 2) + h // 2, (h % 2) * MEM:(h % 2 + 1) * MEM], e.qc[:, h, t * P:(t + 1) * P], e.mkT[:, h],
                                     start=True, stop=True)
                last.then_inc(s["s_ready"], 1)

            def weigh(t):
                pe.wait_ge(s["p_ready"], t + 1)
                if t >= 1:
                    pe.wait_ge(s["t_free"], t)
                for h in range(CH):
                    for m in range(MT):
                        last = pe.transpose(ps[:, 4 + h // 2, (2 * (h % 2) + m) * P:(2 * (h % 2) + m + 1) * P],
                                            p[:, t % 2, h, m * P:(m + 1) * P], e.ident[:, :])
                last.then_inc(s["t_ready"], 1)
                pe.drain().then_inc(s["p_free"], 1)

            def values(t):
                pe.wait_ge(s["pt_ready"], t + 1)
                if t >= 2:
                    pe.wait_ge(s["o_free"], t - 1)
                for h in range(CH):
                    for m in range(MT):
                        last = pe.matmul(ps[:, 6 + t % 2, h * P:(h + 1) * P], e.mv[:, m, h * CHD:(h + 1) * CHD], pt[:, t % 2, h, m],
                                         start=(m == 0), stop=(m == MT - 1))
                last.then_inc(s["o_ready"], 1)

            scores(0)
            scores(1)
            for t in range(NT):
                weigh(t)
                if t + 2 < NT:
                    scores(t + 2)
                values(t)

        @block.scalar
        def _(act):
            for t in range(NT):
                act.wait_ge(s["maxed"], t + 1)
                if t >= 2:
                    act.wait_ge(s["p_free"], t - 1)
                for h in range(CH):
                    last = act.activation(p[:, t % 2, h], ps[:, 2 * (t % 2) + h // 2, (h % 2) * MEM:(h % 2 + 1) * MEM], ACT.Exp,
                                          bias=nm[:, t % 2, h:h + 1], scale=SCALE, accum_out=den[:, t % 2, h:h + 1])
                last.then_inc(s["exped"], 1)
                act.drain().then_inc(s["s_free"], 1)
                if t >= 1:
                    act.wait_ge(s["o_ready"], t)
                    act.activation(oc[:, :, (t - 1) * P:t * P], ps[:, 6 + (t - 1) % 2, :].rearrange("p (h c) -> p h c", h=CH), ACT.Copy).then_inc(s["o_free"], 1)
            act.wait_ge(s["o_ready"], NT)
            act.activation(oc[:, :, SEQ - P:SEQ], ps[:, 6 + (NT - 1) % 2, :].rearrange("p (h c) -> p h c", h=CH), ACT.Copy)

        @block.gpsimd
        def _(pool):
            pool.memset(oc[:, :, T:TP], 0.0)
            for t in range(NT):
                pool.wait_ge(s["recip"], t + 1)
                pool.tensor_tensor(p[:, t % 2], p[:, t % 2], bc(rd[:, t % 2].unsqueeze(2), [P, CH, MEM]), ALU.mult).then_inc(s["p_ready"], 1)

        @block.vector
        def _(dve):
            def maxima(t):
                dve.wait_ge(s["s_ready"], t + 1)
                dve.tensor_reduce(mx[:, t % 2], ps[:, 2 * (t % 2):2 * (t % 2) + 2, :].rearrange("p b (h m) -> p (b h) m", m=MEM), AX.X, ALU.max)
                dve.drain()
                dve.tensor_scalar(nm[:, t % 2], mx[:, t % 2], -SCALE, None, ALU.mult).then_inc(s["maxed"], 1)
            maxima(0)
            for t in range(NT):
                dve.wait_ge(s["exped"], t + 1)
                dve.reciprocal(rd[:, t % 2], den[:, t % 2]).then_inc(s["recip"], 1)
                if t + 1 < NT:
                    maxima(t + 1)
                dve.wait_ge(s["t_ready"], t + 1)
                if t >= 2:
                    dve.wait_ge(s["o_ready"], t - 1)
                dve.tensor_copy(pt[:, t % 2].rearrange("p (b h) m c -> p b (h m c)", b=2), ps[:, 4:6, :]).then_inc(s["pt_ready"], 1)
                dve.drain().then_inc(s["t_free"], 1)


def cross_sample(e, oc):
    nc, a, ps = e.nc, e.a, e.ps
    names = ("v_ready", "k_free", "rows", "rows_copied", "q_ready", "q_free", "sT", "turned", "maxed", "exped", "normed", "pT", "pT_copied", "o_ready")
    s = {n: e.sem("csam_" + n) for n in names}
    k_ready = [e.sem(f"csam_k_ready{i}") for i in range(2)]
    SCALE = CHD ** -0.5
    R = NB * CH
    with ExitStack() as st:
        sb = lambda n, sh: st.enter_context(nc.sbuf_tensor(n, sh, F32))
        kc = sb("csam_k", [P, 2, MT, CW])
        vc = sb("csam_v", [P, NB, MT, CW])
        qr = sb("csam_q_rows", [NB, CW])
        prod = sb("csam_prod", [P, MT, CW])
        sT = sb("csam_sT", [P, MT, NB, CH])
        onehot = sb("csam_onehot", [NB, NB, P])
        sc = sb("csam_sc", [R, MEM])
        mx, nm, den, rd = (sb("csam_" + n, [R, 1]) for n in ("mx", "nm", "den", "rd"))
        pT = sb("csam_pT", [P, MT, NB, CH])
        made = e.sem("csam_onehot_made")
        block = st.enter_context(nc.Block())

        @block.gpsimd
        def _(pool):
            pool.memset(onehot[:, :, :], 0.0)
            pool.drain()
            pool.affine_select(out=onehot[:, :, :], in_=onehot[:, :, :], compare_op=ALU.not_equal, fill=1.0, base=0,
                               pattern=[[-1, NB], [0, P]], channel_multiplier=1).then_inc(made, 1)

        @block.sync
        def _(sp):
            mem = lambda name, b: a[name][0, b].rearrange("(m p) h d -> p m (h d)", p=P)
            for b in range(NB):
                if b >= 2:
                    sp.wait_ge(s["k_free"], b - 1)
                sp.dma_start(kc[:, b % 2], mem("cache_mem_k", b)).then_inc(k_ready[b % 2], 16)
                sp.dma_start(vc[:, b], mem("cache_mem_v", b)).then_inc(s["v_ready"], 16)

        @block.tensor
        def _(pe):
            for h in range(CH):
                last = pe.transpose(ps[0:NB, 0, h * P:(h + 1) * P], e.qc[:, h, SEQ:T], e.ident[:, :])
            last.then_inc(s["rows"], 1)
            pe.wait_ge(s["rows_copied"], 1)
            pe.wait_ge(made, 1)
            for b in range(NB):
                if b >= 2:
                    pe.wait_ge(s["q_free"], b - 1)
                pe.matmul(ps[:, 1 + b % 2, :], onehot[:, b], qr[:, :], start=True, stop=True).then_inc(s["q_ready"], 1)
            pe.wait_ge(s["sT"], 1)
            for m in range(MT):
                last = pe.transpose(ps[0:R, 3, m * P:(m + 1) * P], sT[:, m].rearrange("p b h -> p (b h)"), e.ident[:, :])
            last.then_inc(s["turned"], 1)
            pe.wait_ge(s["normed"], 1)
            for m in range(MT):
                last = pe.transpose(ps[:, 4, m * R:(m + 1) * R], sc[:, m * P:(m + 1) * P], e.ident[0:R, 0:R])
            last.then_inc(s["pT"], 1)
            pe.wait_ge(s["pT_copied"], 1)
            pe.wait_ge(s["v_ready"], 16 * NB)
            for b in range(NB):
                for h in range(CH):
                    for m in range(MT):
                        last = pe.matmul(ps[:, 5, h * NB + b:h * NB + b + 1], vc[:, b, m, h * CHD:(h + 1) * CHD], pT[:, m, b, h:h + 1],
                                         start=(m == 0), stop=(m == MT - 1))
            last.then_inc(s["o_ready"], 1)

        @block.scalar
        def _(act):
            act.wait_ge(s["maxed"], 1)
            act.activation(sc[:, :], ps[0:R, 3, 0:MEM], ACT.Exp, bias=nm[:, :], scale=SCALE, accum_out=den[:, :]).then_inc(s["exped"], 1)

        @block.vector
        def _(dve):
            dve.wait_ge(s["rows"], 1)
            dve.tensor_copy(qr[:, :], ps[0:NB, 0, :]).then_inc(s["rows_copied"], 1)
            for b in range(NB):
                dve.wait_ge(s["q_ready"], b + 1)
                dve.wait_ge(k_ready[b % 2], 16 * (b // 2 + 1))
                dve.tensor_tensor(prod[:, :, :], kc[:, b % 2], bc(ps[:, 1 + b % 2, :].unsqueeze(1), [P, MT, CW]), ALU.mult)
                dve.drain().then_inc(s["q_free"], 1)
                dve.sem_inc(s["k_free"], 1)
                dve.tensor_reduce(sT[:, :, b], prod[:, :, :].rearrange("p m (h d) -> p m h d", h=CH), AX.X, ALU.add)
                dve.drain()
            dve.sem_inc(s["sT"], 1)
            dve.wait_ge(s["turned"], 1)
            dve.tensor_reduce(mx[:, :], ps[0:R, 3, 0:MEM], AX.X, ALU.max)
            dve.drain()
            dve.tensor_scalar(nm[:, :], mx[:, :], -SCALE, None, ALU.mult).then_inc(s["maxed"], 1)
            dve.wait_ge(s["exped"], 1)
            dve.reciprocal(rd[:, :], den[:, :])
            dve.drain()
            dve.tensor_scalar(sc[:, :], sc[:, :], rd[:, :], None, ALU.mult).then_inc(s["normed"], 1)
            dve.wait_ge(s["pT"], 1)
            dve.tensor_copy(pT[:, :, :, :].rearrange("p m b h -> p (m b h)"), ps[:, 4, 0:MT * R]).then_inc(s["pT_copied"], 1)
            dve.wait_ge(s["o_ready"], 1)
            dve.tensor_copy(oc[:, :, SEQ:T], ps[:, 5, 0:CH * NB].rearrange("p (h b) -> p h b", h=CH))


def cross_out(e, oc):
    nc, a, ps = e.nc, e.a, e.ps
    w_ready, made, emptied = e.sem("co_w_ready"), e.sem("co_ready"), e.sem("co_free")
    with nc.sbuf_tensor("w_co", [P, CH, D], F32) as w, nc.Block() as block:
        @block.sync
        def _(sp):
            sp.dma_start(w[:, :, :], a["w_co"][0].rearrange("(k p) c -> p k c", p=P)).then_inc(w_ready, 16)

        @block.tensor
        def _(pe):
            pe.wait_ge(w_ready, 16)
            for u in range(2 * TILES):
                t, half = u // 2, u % 2
                if u >= 8:
                    pe.wait_ge(emptied, u - 7)
                for k in range(CH):
                    last = pe.matmul(ps[:, u % 8, :], oc[:, k, t * P:(t + 1) * P], w[:, k, half * 512:(half + 1) * 512],
                                     start=(k == 0), stop=(k == CH - 1))
                last.then_inc(made, 1)

        @block.vector
        def _(dve):
            for u in range(2 * TILES):
                dve.wait_ge(made, u + 1)
                xs = e.x[:, u // 2, (u % 2) * 512:(u % 2 + 1) * 512]
                dve.tensor_tensor(xs, xs, ps[:, u % 8, :], ALU.add).then_inc(emptied, 1)


def cross_attention(e):
    nc, a = e.nc, e.a
    with ExitStack() as st:
        sb = lambda n, sh: st.enter_context(nc.sbuf_tensor(n, sh, F32))
        e.qc = sb("qc", [P, CH, T])
        e.mkT = sb("mkT", [P, CH, MEM])
        e.mv = sb("mv", [P, MT, CW])
        with nc.sbuf_tensor("xc", [P, KD, TP], F32) as xc, nc.sbuf_tensor("memT", [P, KD, MEM], F32) as memT:
            rms_tiles(e, "cross", e.x, TILES, xc, grow=G_CROSS)
            with nc.sbuf_tensor("mem_rows", [P, MT, D], F32) as mem:
                rms_tiles(e, "mem", mem, MT, memT, grow=G_MEM,
                          load=[(mem[:, :, :], a["mem_prompt"][0].rearrange("(m p) d -> p m d", p=P))])
            cross_projections(e, xc, memT)
        with nc.sbuf_tensor("cross_oc", [P, CH, TP], F32) as oc:
            cross_prompt(e, oc)
            cross_sample(e, oc)
            cross_out(e, oc)


def resident_rows(e):
    e.x = e.ctx.enter_context(e.nc.sbuf_tensor("x_resident", [P, TILES, D], F32))


NBASE = NE
NMORE = TILES * P * 2 // P - 2
SLOTS = (NBASE + NMORE) * P


def routing(e, xT):
    nc, a, ps = e.nc, e.a, e.ps
    NR = NGR + NE
    s = {n: e.sem("route_" + n) for n in ("loaded", "logits", "pool_made", "chosen", "counted", "e0", "e1", "x0", "x1", "zeroed", "zero_made", "slots", "scattered0", "scattered1")}
    with ExitStack() as st:
        sb = lambda n, sh, dt=F32: st.enter_context(nc.sbuf_tensor("r_" + n, sh, dt))
        wr = sb("w", [P, KD, NR])
        bias = sb("bias", [P, NR])
        lg = sb("logits", [P, TILES, NR])
        gm = sb("gm", [P, TILES, 1])
        g4 = sb("g4", [P, TILES, NGR])
        ohg = sb("ohg", [P, TILES, NGR])
        wt = sb("wt", [P, EPG])
        pg = sb("pg", [P, TILES, 1])
        l4 = sb("l4", [P, TILES, NGR, EPG])
        le, key = sb("le", [P, TILES, EPG]), sb("key", [P, TILES, EPG])
        oh = [sb(f"oh{i}", [P, TILES, EPG]) for i in range(2)]
        m = [sb(f"m{i}", [P, TILES, 1]) for i in range(2)]
        km = sb("km", [P, TILES, 1])
        big = [sb(f"big{i}", [P, TILES, NE]) for i in range(2)]
        sel, rank = sb("sel", [P, TILES, NE]), sb("rank", [P, TILES, NE])
        valid = sb("valid", [P, TILES])
        off = sb("off", [P, TILES + 1, NE])
        more = [sb(f"more{i}", [P, NE]) for i in range(2)]
        nmore, delta, base_b = sb("nmore", [P, NE]), sb("delta", [P, NE]), sb("base_b", [P, NE])
        first = sb("first", [P, NE])
        below = sb("below_p", [P, TILES, NE])
        d = [sb(f"dest_f{i}", [P, TILES, 1]) for i in range(2)]
        tid = sb("tid", [P, TILES], I32)
        zero = sb("zero", [NBASE + NMORE, P], I32)
        jj = sb("jj", [1, NMORE, 1])
        ge = sb("ge", [1, NMORE, NE])
        ef = sb("ef", [1, NMORE])
        block = st.enter_context(nc.Block())

        @block.sync
        def _(sp):
            sp.dma_start(wr[:, :, 0:NGR], a["w_route_group"][0].rearrange("(k p) c -> p k c", p=P)).then_inc(s["loaded"], 16)
            sp.dma_start(wr[:, :, NGR:], a["w_route_expert"][0].rearrange("(k p) c -> p k c", p=P)).then_inc(s["loaded"], 16)
            sp.dma_start(bias[:, 0:NGR], a["b_route_group"].to_broadcast([P, NGR])).then_inc(s["loaded"], 16)
            sp.dma_start(bias[:, NGR:], a["b_route_expert"].to_broadcast([P, NE])).then_inc(s["loaded"], 16)
            sp.wait_ge(s["zero_made"], 1)
            sp.dma_start(e.slot_tok.rearrange("(b p) o -> b (p o)", p=P), zero[:, :]).then_inc(s["zeroed"], 16)
            sp.wait_ge(s["zeroed"], 16)

        @block.gpsimd
        def _(pool):
            pool.memset(zero[:, :], 0).then_inc(s["zero_made"], 1)
            pool.iota(wt[:, :], pattern=[[-1, EPG]], base=EPG, channel_multiplier=0, allow_small_or_imprecise_dtypes=True)
            pool.iota(first[:, :], pattern=[[P, NE]], base=0, channel_multiplier=0, allow_small_or_imprecise_dtypes=True)
            pool.iota(jj[:, :, :], pattern=[[1, NMORE], [0, 1]], base=0, channel_multiplier=0, allow_small_or_imprecise_dtypes=True)
            pool.iota(tid[:, :], pattern=[[P, TILES]], base=0, channel_multiplier=1)
            pool.memset(valid[:, :], 1.0)
            pool.drain()
            pool.affine_select(out=valid[:, NT:TILES], in_=valid[:, NT:TILES], compare_op=ALU.is_ge, fill=0.0, base=NB - 1,
                               pattern=[[0, 1]], channel_multiplier=-1)
            pool.drain().then_inc(s["pool_made"], 1)
            pool.wait_ge(s["slots"], 1)
            pool.wait_ge(s["zeroed"], 16)
            n = 0
            for i in range(2):
                for t in range(TILES):
                    rows = P if t < NT else NB
                    pool.indirect_dma_start(e.slot_tok, bass.IndirectOffsetOnAxis(ap=e.dest[0:rows, i, t:t + 1], axis=0),
                                            tid[0:rows, t:t + 1], None).then_inc(s[f"scattered{n % 2}"], 16)
                    n += 1
            for i in range(2):
                pool.wait_ge(s[f"scattered{i}"], 16 * TILES)

        @block.tensor
        def _(pe):
            pe.wait_ge(s["loaded"], 64)
            for t in range(TILES):
                for k in range(KD):
                    last = pe.matmul(ps[:, 0, t * NR:(t + 1) * NR], xT[:, k, t * P:(t + 1) * P], wr[:, k], start=(k == 0), stop=(k == KD - 1))
            last.then_inc(s["logits"], 1)
            pe.wait_ge(s["chosen"], 1)
            flat = sel[:, :, :].rearrange("p t e -> p (t e)")
            pe.matmul(ps[:, 1, 0:TILES * NE], e.tri[:, :], flat, start=True, stop=True)
            pe.matmul(ps[:, 2, 0:TILES * NE], e.ones[:, :], flat, start=True, stop=True).then_inc(s["counted"], 1)

        @block.scalar
        def _(act):
            act.wait_ge(s["e0"], 1)
            act.activation(g4[:, :, :], g4[:, :, :], ACT.Exp).then_inc(s["x0"], 1)
            act.wait_ge(s["e1"], 1)
            act.activation(m[1][:, :, :], m[1][:, :, :], ACT.Exp).then_inc(s["x1"], 1)

        @block.vector
        def _(dve):
            def tt(out, x, y, op):
                dve.tensor_tensor(out, x, y, op)
                dve.drain()

            def first_of(out, x, mx, width):
                tt(key[:, :, 0:width], x, bc(mx, [P, TILES, width]), ALU.is_equal)
                tt(key[:, :, 0:width], key[:, :, 0:width], bc(wt[:, EPG - width:].unsqueeze(1), [P, TILES, width]), ALU.mult)
                dve.tensor_reduce(km[:, :, :], key[:, :, 0:width].unsqueeze(2), AX.X, ALU.max)
                dve.drain()
                tt(out, key[:, :, 0:width], bc(km[:, :, :], [P, TILES, width]), ALU.is_equal)

            dve.wait_ge(s["loaded"], 64)
            dve.wait_ge(s["pool_made"], 1)
            dve.wait_ge(s["logits"], 1)
            tt(lg[:, :, :], ps[:, 0, 0:TILES * NR].rearrange("p (t c) -> p t c", c=NR), bc(bias[:, :].unsqueeze(1), [P, TILES, NR]), ALU.add)
            dve.tensor_reduce(gm[:, :, :], lg[:, :, 0:NGR].unsqueeze(2), AX.X, ALU.max)
            dve.drain()
            dve.tensor_tensor(g4[:, :, :], lg[:, :, 0:NGR], bc(gm[:, :, :], [P, TILES, NGR]), ALU.subtract).then_inc(s["e0"], 1)
            first_of(ohg[:, :, :], lg[:, :, 0:NGR], gm[:, :, :], NGR)
            tt(l4[:, :, :, :], lg[:, :, NGR:].rearrange("p t (g x) -> p t g x", g=NGR), bc(ohg[:, :, :].unsqueeze(3), [P, TILES, NGR, EPG]), ALU.mult)
            dve.tensor_reduce(le[:, :, :], l4[:, :, :, :].rearrange("p t g x -> p t x g"), AX.X, ALU.add)
            dve.drain()
            dve.tensor_reduce(m[0][:, :, :], le[:, :, :].unsqueeze(2), AX.X, ALU.max)
            dve.drain()
            first_of(oh[0][:, :, :], le[:, :, :], m[0][:, :, :], EPG)
            dve.scalar_tensor_tensor(out=le[:, :, :], in0=oh[0][:, :, :], scalar=NEG, in1=le[:, :, :], op0=ALU.mult, op1=ALU.add)
            dve.drain()
            dve.tensor_reduce(m[1][:, :, :], le[:, :, :].unsqueeze(2), AX.X, ALU.max)
            dve.drain()
            first_of(oh[1][:, :, :], le[:, :, :], m[1][:, :, :], EPG)
            dve.tensor_tensor(m[1][:, :, :], m[1][:, :, :], m[0][:, :, :], ALU.subtract).then_inc(s["e1"], 1)
            for i in range(2):
                tt(big[i][:, :, :].rearrange("p t (g x) -> p t g x", g=NGR), bc(ohg[:, :, :].unsqueeze(3), [P, TILES, NGR, EPG]),
                   bc(oh[i][:, :, :].unsqueeze(2), [P, TILES, NGR, EPG]), ALU.mult)
            tt(sel[:, :, :], big[0][:, :, :], big[1][:, :, :], ALU.add)
            tt(sel[:, :, :], sel[:, :, :], bc(valid[:, :].unsqueeze(2), [P, TILES, NE]), ALU.mult)
            dve.sem_inc(s["chosen"], 1)
            dve.wait_ge(s["x0"], 1)
            dve.tensor_reduce(pg[:, :, :], g4[:, :, :].unsqueeze(2), AX.X, ALU.add)
            dve.drain()
            dve.wait_ge(s["x1"], 1)
            dve.tensor_scalar(m[0][:, :, :], m[1][:, :, :], 1.0, None, ALU.add)
            dve.drain()
            tt(pg[:, :, :], pg[:, :, :], m[0][:, :, :], ALU.mult)
            dve.reciprocal(e.gate[:, 0].unsqueeze(2), pg[:, :, :])
            dve.drain()
            tt(e.gate[:, 1].unsqueeze(2), e.gate[:, 0].unsqueeze(2), m[1][:, :, :], ALU.mult)
            dve.wait_ge(s["counted"], 1)
            dve.memset(off[:, 0], 0.0)
            dve.drain()
            for t in range(TILES):
                tt(off[:, t + 1], off[:, t], ps[:, 2, t * NE:(t + 1) * NE], ALU.add)
            tt(rank[:, :, :], ps[:, 1, 0:TILES * NE].rearrange("p (t e) -> p t e", e=NE), sel[:, :, :], ALU.subtract)
            tt(rank[:, :, :], rank[:, :, :], off[:, 0:TILES], ALU.add)
            cnt = off[:, TILES]
            dve.tensor_scalar(nmore[:, :], cnt, float(P), None, ALU.is_gt)
            dve.drain()
            for j in range(2, T // P + 1):
                dve.scalar_tensor_tensor(out=nmore[:, :], in0=cnt, scalar=float(j * P), in1=nmore[:, :], op0=ALU.is_gt, op1=ALU.add)
                dve.drain()
            dve.tensor_copy(more[0][:, :], nmore[:, :])
            dve.drain()
            src = 0
            step = 1
            while step < NE:
                dve.tensor_copy(more[1 - src][:, 0:step], more[src][:, 0:step])
                dve.tensor_tensor(more[1 - src][:, step:], more[src][:, step:], more[src][:, 0:NE - step], ALU.add)
                dve.drain()
                src, step = 1 - src, 2 * step
            end = more[src]
            tt(base_b[:, :], end[:, :], nmore[:, :], ALU.subtract)
            dve.tensor_scalar(base_b[:, :], base_b[:, :], float(P), float((NBASE - 1) * P), ALU.mult, ALU.add)
            dve.drain()
            tt(delta[:, :], first[:, :], base_b[:, :], ALU.subtract)
            dve.tensor_scalar(below[:, :, :], rank[:, :, :], float(P), None, ALU.is_lt)
            dve.drain()
            tt(below[:, :, :], below[:, :, :], bc(delta[:, :].unsqueeze(1), [P, TILES, NE]), ALU.mult)
            tt(rank[:, :, :], rank[:, :, :], bc(base_b[:, :].unsqueeze(1), [P, TILES, NE]), ALU.add)
            tt(rank[:, :, :], rank[:, :, :], below[:, :, :], ALU.add)
            for i in range(2):
                tt(big[i][:, :, :], big[i][:, :, :], rank[:, :, :], ALU.mult)
                dve.tensor_reduce(d[i][:, :, :], big[i][:, :, :].unsqueeze(2), AX.X, ALU.add)
                dve.drain()
                dve.tensor_copy(e.dest[:, i].unsqueeze(2), d[i][:, :, :])
                dve.drain()
            tt(ge[:, :, :], bc(jj[:, :, :], [1, NMORE, NE]), bc(end[0:1, :].unsqueeze(1), [1, NMORE, NE]), ALU.is_ge)
            dve.tensor_reduce(ef[:, :], ge[:, :, :], AX.X, ALU.add)
            dve.drain()
            dve.tensor_scalar(ef[:, :], ef[:, :], float(NE - 1), None, ALU.min)
            dve.drain()
            dve.tensor_copy(e.more_expert[:, 0:NMORE], ef[:, :])
            dve.tensor_copy(e.more_expert[:, NMORE:NMORE + 1], end[0:1, NE - 1:NE])
            dve.drain().then_inc(s["slots"], 1)


def expert_blocks(e, name, first, count, expert_of):
    nc, a, ps = e.nc, e.a, e.ps
    names = ("wg_free", "wd_free", "idx_free", "x_free", "gather_go", "turned", "xt_low", "xt_high", "gu_ready", "silu_ready", "gu_free", "h_ready", "h_free",
             "ht_ready", "ht_copied", "down_ready", "down_free", "y_ready")
    s = {n: e.sem(f"{name}_{n}") for n in names}
    two = lambda n: [e.sem(f"{name}_{n}{i}") for i in range(2)]
    wg_ready, wd_ready, idx_ready, x_ready, stored = two("wg_ready"), two("wd_ready"), two("idx_ready"), two("x_ready"), two("stored")
    KE = DE // P
    with ExitStack() as st:
        sb = lambda n, sh, dt=F32: st.enter_context(nc.sbuf_tensor(f"{name}_{n}", sh, dt))
        wg, wu = sb("wg", [P, 2, KD, DE]), sb("wu", [P, 2, KD, DE])
        wd = sb("wd", [P, 2, KE, D])
        idx = [sb(f"idx{i}", [P, 1], I32) for i in range(2)]
        xg = [sb(f"x{i}", [P, D]) for i in range(2)]
        xt = sb("xt", [P, KD, P])
        act_g = sb("silu", [P, DE])
        h = sb("h", [P, 2, DE])
        ht = sb("ht", [P, 2, KE, P])
        y = sb("y", [P, 2, D])

        def in_pairs(eng, step):
            with eng.Fori(0, count // 2) as i:
                for j in range(2):
                    step(i * 2 + j, j, i)

        with nc.Block() as block:
            @block.sync
            def _(sp):
                def load(n, b, i):
                    x = expert_of(sp, n)
                    pick = lambda w: w[0][bass.ds(x, 1)].rearrange("o (k p) c -> p (o k) c", p=P)
                    sp.wait_ge(s["idx_free"], n + 1)
                    sp.dma_start(idx[b][:, :], e.slot_tok[bass.ds(n * P + first * P, P), :]).then_inc(idx_ready[b], 16)
                    sp.wait_ge(s["wg_free"], n + 1)
                    sp.dma_start(wg[:, b], pick(a["w_e_gate"])).then_inc(wg_ready[b], 16)
                    sp.dma_start(wu[:, b], pick(a["w_e_up"])).then_inc(wg_ready[b], 16)
                    sp.wait_ge(s["wd_free"], n + 1)
                    sp.dma_start(wd[:, b], pick(a["w_e_down"])).then_inc(wd_ready[b], 16)
                in_pairs(sp, load)

            @block.gpsimd
            def _(pool):
                pool.sem_inc(s["idx_free"], 2)

                def gather(n, b, i):
                    pool.wait_ge(idx_ready[b], i * 16 + 16)
                    pool.wait_ge(s["x_free"], n + 1)
                    pool.sem_inc(s["gather_go"], 1)
                    pool.indirect_dma_start(xg[b][:, :], None, e.xm_rows, bass.IndirectOffsetOnAxis(ap=idx[b][:, 0:1], axis=0)).then_inc(x_ready[b], 16)
                    pool.wait_ge(x_ready[b], i * 16 + 16)
                    pool.sem_inc(s["idx_free"], 1)
                in_pairs(pool, gather)

            @block.tensor
            def _(pe):
                pe.sem_inc(s["x_free"], 2)
                pe.sem_inc(s["wg_free"], 2)
                pe.sem_inc(s["wd_free"], 2)
                pe.sem_inc(s["h_free"], 2)

                def turn(n, b, i):
                    pe.wait_ge(x_ready[b], i * 16 + 16)
                    pe.wait_ge(s["xt_low"], n + 1)
                    pe.wait_ge(s["xt_high"], n + 1)
                    for k in range(KD):
                        last = pe.transpose(ps[:, k // 4, (k % 4) * P:(k % 4 + 1) * P], xg[b][:, k * P:(k + 1) * P], e.ident[:, :])
                    last.then_inc(s["turned"], 1)
                    pe.drain().then_inc(s["x_free"], 1)

                def gate_up(n, b, i):
                    pe.wait_ge(wg_ready[b], i * 32 + 32)
                    pe.wait_ge(s["gu_free"], n + 1)
                    pe.wait_ge(s["xt_low"], n + 2)
                    pe.wait_ge(s["xt_high"], n + 2)
                    for w, bank in ((wg, 2), (wu, 3)):
                        for k in range(KD):
                            last = pe.matmul(ps[:, bank, :], xt[:, k], w[:, b, k], start=(k == 0), stop=(k == KD - 1))
                    last.then_inc(s["gu_ready"], 1)
                    pe.drain().then_inc(s["wg_free"], 1)

                def turn_h(n, b):
                    pe.wait_ge(s["h_ready"], n + 1)
                    pe.wait_ge(s["ht_copied"], n + 1)
                    for k in range(KE):
                        last = pe.transpose(ps[:, 4, k * P:(k + 1) * P], h[:, b, k * P:(k + 1) * P], e.ident[:, :])
                    last.then_inc(s["ht_ready"], 1)
                    pe.drain().then_inc(s["h_free"], 1)

                def down(n, b, i):
                    pe.wait_ge(wd_ready[b], i * 16 + 16)
                    pe.wait_ge(s["ht_copied"], n + 2)
                    pe.wait_ge(s["down_free"], n + 1)
                    for half in range(2):
                        for k in range(KE):
                            last = pe.matmul(ps[:, 5 + half, :], ht[:, b, k], wd[:, b, k, half * 512:(half + 1) * 512], start=(k == 0), stop=(k == KE - 1))
                    last.then_inc(s["down_ready"], 1)
                    pe.drain().then_inc(s["wd_free"], 1)

                turn(0, 0, 0)
                gate_up(0, 0, 0)
                turn(1, 1, 0)
                turn_h(0, 0)
                with pe.Fori(0, count // 2 - 1) as i:
                    gate_up(i * 2 + 1, 1, i)
                    turn(i * 2 + 2, 0, i + 1)
                    down(i * 2, 0, i)
                    turn_h(i * 2 + 1, 1)
                    gate_up(i * 2 + 2, 0, i + 1)
                    turn(i * 2 + 3, 1, i + 1)
                    down(i * 2 + 1, 1, i)
                    turn_h(i * 2 + 2, 0)
                gate_up(count - 1, 1, count // 2 - 1)
                down(count - 2, 0, count // 2 - 1)
                turn_h(count - 1, 1)
                down(count - 1, 1, count // 2 - 1)

            @block.scalar
            def _(act):
                act.sem_inc(s["xt_high"], 1)

                def high(n):
                    act.wait_ge(s["turned"], n + 1)
                    act.wait_ge(s["gu_ready"], n) if not (isinstance(n, int) and n == 0) else None
                    act.activation(xt[:, 4:8].rearrange("p k c -> p (k c)"), ps[:, 1, :], ACT.Copy).then_inc(s["xt_high"], 1)

                def silu(n):
                    act.wait_ge(s["gu_ready"], n + 1)
                    act.wait_ge(s["gu_free"], n + 1)
                    act.activation(act_g[:, :], ps[:, 2, :], ACT.Silu).then_inc(s["silu_ready"], 1)

                def out(n, b, i):
                    act.wait_ge(s["y_ready"], n + 1)
                    act.dma_start(e.y_rows[bass.ds(n * P + first * P, P), :], y[:, b]).then_inc(stored[b], 16)

                high(0)
                silu(0)
                high(1)
                with act.Fori(0, count // 2 - 1) as i:
                    silu(i * 2 + 1)
                    high(i * 2 + 2)
                    out(i * 2, 0, i)
                    silu(i * 2 + 2)
                    high(i * 2 + 3)
                    out(i * 2 + 1, 1, i)
                silu(count - 1)
                out(count - 2, 0, 0)
                out(count - 1, 1, 0)
                for b in range(2):
                    act.wait_ge(stored[b], 16 * count // 2)

            @block.vector
            def _(dve):
                dve.sem_inc(s["xt_low"], 1)
                dve.sem_inc(s["gu_free"], 1)
                dve.sem_inc(s["ht_copied"], 1)
                dve.sem_inc(s["down_free"], 1)

                def low(n):
                    dve.wait_ge(s["turned"], n + 1)
                    dve.wait_ge(s["gu_ready"], n) if not (isinstance(n, int) and n == 0) else None
                    dve.tensor_copy(xt[:, 0:4].rearrange("p k c -> p (k c)"), ps[:, 0, :]).then_inc(s["xt_low"], 1)

                def product(n, b):
                    dve.wait_ge(s["silu_ready"], n + 1)
                    dve.wait_ge(s["h_free"], n + 1)
                    dve.tensor_tensor(h[:, b], act_g[:, :], ps[:, 3, :], ALU.mult).then_inc(s["h_ready"], 1)
                    dve.drain().then_inc(s["gu_free"], 1)

                def copy_h(n, b):
                    dve.wait_ge(s["ht_ready"], n + 1)
                    dve.wait_ge(s["down_ready"], n) if not (isinstance(n, int) and n == 0) else None
                    dve.tensor_copy(ht[:, b].rearrange("p k c -> p (k c)"), ps[:, 4, :]).then_inc(s["ht_copied"], 1)

                def rows(n, b, i):
                    dve.wait_ge(s["down_ready"], n + 1)
                    dve.wait_ge(stored[b], i * 16)
                    dve.tensor_copy(y[:, b].rearrange("p (h c) -> p h c", h=2), ps[:, 5:7, :]).then_inc(s["y_ready"], 1)
                    dve.drain().then_inc(s["down_free"], 1)

                low(0)
                product(0, 0)
                low(1)
                copy_h(0, 0)
                with dve.Fori(0, count // 2 - 1) as i:
                    product(i * 2 + 1, 1)
                    low(i * 2 + 2)
                    rows(i * 2, 0, i)
                    copy_h(i * 2 + 1, 1)
                    product(i * 2 + 2, 0)
                    low(i * 2 + 3)
                    rows(i * 2 + 1, 1, i)
                    copy_h(i * 2 + 2, 0)
                product(count - 1, 1)
                rows(count - 2, 0, count // 2 - 1)
                copy_h(count - 1, 1)
                rows(count - 1, 1, count // 2 - 1)


def moe(e):
    nc, a = e.nc, e.a
    e.xm_rows = e.dram("xm_rows", [TP, D])
    e.slot_tok = e.dram("slot_tok", [SLOTS, 1], I32)
    e.y_rows = e.dram("moe_rows", [SLOTS, D])
    keep = lambda n, sh, dt=F32: e.ctx.enter_context(nc.sbuf_tensor(n, sh, dt))
    e.gate = keep("gate", [P, 2, TILES])
    e.dest = keep("dest", [P, 2, TILES], I32)
    e.more_expert = keep("more_expert", [1, NMORE + 1], I32)
    g_ready = e.sem("g_moe_ready")
    with nc.sbuf_tensor("xmT", [P, KD, TP], F32) as xT:
        with nc.sbuf_tensor("g_moe_rows", [P, D], F32) as g:
            with nc.Block() as block:
                @block.sync
                def _(sp):
                    sp.dma_start(g[:, :], a["g_moe"].to_broadcast([P, D])).then_inc(g_ready, 16)
                    sp.wait_ge(g_ready, 16)
            rms_tiles(e, "moe", e.x, TILES, xT, gtok=g[:, :], store=e.xm_rows)
        routing(e, xT)
    expert_blocks(e, "own", 0, NBASE, lambda sp, n: n)
    expert_blocks(e, "more", NBASE, NMORE, lambda sp, n: sp.value_load(e.more_expert[0:1, bass.ds(n, 1)], min_val=0, max_val=NE - 1))


def output(e):
    nc, a, o = e.nc, e.a, e.o
    s = {n: e.sem("final_" + n) for n in ("g_ready", "added", "squared", "meaned", "rooted", "scaled")}
    row_ready = [[e.sem(f"final_rows{i}{b}") for b in range(2)] for i in range(2)]
    stored = [e.sem(f"final_stored{b}") for b in range(2)]
    with ExitStack() as st:
        sb = lambda n, sh: st.enter_context(nc.sbuf_tensor("f_" + n, sh, F32))
        y = [[sb(f"y{i}{b}", [P, D]) for b in range(2)] for i in range(2)]
        g, out = sb("g", [P, D]), sb("out", [P, 2, D])
        sq, ss, rs = sb("sq", [P, D]), sb("ss", [P, TILES]), sb("rs", [P, TILES])
        block = st.enter_context(nc.Block())
        rows = lambda t: P if t < NT else NB

        @block.sync
        def _(sp):
            sp.dma_start(g[:, :], a["g_final"].rearrange("(o d) -> o d", o=1).to_broadcast([P, D])).then_inc(s["g_ready"], 16)
            for t in range(TILES):
                sp.wait_ge(s["scaled"], t + 1)
                dst = o["y_prompt"][0, t * P:(t + 1) * P, :] if t < NT else o["y_sample"][:, 0, :]
                sp.dma_start(dst, out[0:rows(t), t % 2]).then_inc(stored[t % 2], 16)
            for b in range(2):
                sp.wait_ge(stored[b], 16 * ((TILES + 1 - b) // 2))

        @block.gpsimd
        def _(pool):
            def root(t):
                pool.wait_ge(s["meaned"], t + 1)
                pool.tensor_tensor(rs[0:rows(t), t:t + 1], ss[0:rows(t), t:t + 1], e.mhalf[0:rows(t), 0:1], ALU.pow).then_inc(s["rooted"], 1)
            for t in range(TILES):
                if t >= 2:
                    pool.wait_ge(s["added"], t - 1)
                for i in range(2):
                    pool.indirect_dma_start(y[i][t % 2][0:rows(t), :], None, e.y_rows,
                                            bass.IndirectOffsetOnAxis(ap=e.dest[0:rows(t), i, t:t + 1], axis=0)).then_inc(row_ready[i][t % 2], 16)
                if t >= 1:
                    root(t - 1)
            root(TILES - 1)

        @block.scalar
        def _(act):
            for t in range(TILES):
                act.wait_ge(s["added"], t + 1)
                act.activation(sq[0:rows(t), :], e.x[0:rows(t), t, :], ACT.Square, accum_out=ss[0:rows(t), t:t + 1]).then_inc(s["squared"], 1)
                act.drain()

        @block.vector
        def _(dve):
            def add(t):
                r = rows(t)
                for i in range(2):
                    dve.wait_ge(row_ready[i][t % 2], 16 * (t // 2 + 1))
                    last = dve.scalar_tensor_tensor(out=e.x[0:r, t, :], in0=y[i][t % 2][0:r, :], scalar=e.gate[0:r, i, t:t + 1], in1=e.x[0:r, t, :],
                                                    op0=ALU.mult, op1=ALU.add)
                    dve.drain()
                dve.sem_inc(s["added"], 1)

            def mean(t):
                r = rows(t)
                dve.wait_ge(s["squared"], t + 1)
                dve.tensor_scalar(ss[0:r, t:t + 1], ss[0:r, t:t + 1], 1.0 / D, EPS, ALU.mult, ALU.add).then_inc(s["meaned"], 1)

            def scale(t):
                r = rows(t)
                if t >= 2:
                    dve.wait_ge(stored[t % 2], 16 * (t // 2))
                dve.wait_ge(s["rooted"], t + 1)
                dve.scalar_tensor_tensor(out=out[0:r, t % 2, :], in0=e.x[0:r, t, :], scalar=rs[0:r, t:t + 1], in1=g[0:r, :],
                                         op0=ALU.mult, op1=ALU.mult).then_inc(s["scaled"], 1)
            dve.wait_ge(s["g_ready"], 16)
            add(0)
            for t in range(TILES):
                mean(t)
                if t + 1 < TILES:
                    add(t + 1)
                scale(t)


def hybrid_step(nc, a, o):
    with ExitStack() as ctx:
        e = Env(nc, ctx, a, o)
        with e.stage():
            constants(e)
        with nc.sbuf_tensor("x_turned", [P, KD, TP], F32) as x_turned, e.stage():
            mixer_norm(e, x_turned)
            project(e, x_turned)
        with e.stage():
            ssd_steps(e)
            ssd_chunks(e)
        with e.stage():
            window_attention(e)
        with ExitStack() as mix, e.stage():
            e.mix = mix
            sample_states(e)
            sample_ssd(e)
            sample_window(e)
        resident_rows(e)
        with e.stage():
            mixer_out(e)
        with e.stage():
            cross_attention(e)
        with e.stage():
            moe(e)
            output(e)


_INS = ["x_prompt", "x_sample", "state_ssd", "state_conv", "cache_win_k", "cache_win_v", "cache_mem_k", "cache_mem_v",
        "mem_prompt", "g_mix", "w_in", "conv_w", "conv_b", "dt_bias", "a_log", "d_skip", "g_ssd", "w_ssd_down", "attn_sinks",
        "w_mix_out", "g_cross", "g_mem", "w_cq", "w_ckv", "w_co", "g_moe", "w_route_group", "b_route_group",
        "w_route_expert", "b_route_expert", "w_e_gate", "w_e_up", "w_e_down", "g_final"]
_OUTS = [("y_prompt", (1, SEQ, D)), ("y_sample", (NB, 1, D)),
         ("p_state_ssd", (1, 1, HS, HP, NS)), ("p_state_conv", (1, 1, CK - 1, CD)),
         ("p_cache_win_k", (1, 1, W, NKV, HD)), ("p_cache_win_v", (1, 1, W, NKV, HD)),
         ("p_cache_mem_k", (1, 1, MEM, CH, CHD)), ("p_cache_mem_v", (1, 1, MEM, CH, CHD)),
         ("s_state_ssd", (1, NB, HS, HP, NS)), ("s_state_conv", (1, NB, CK - 1, CD)),
         ("s_cache_win_k", (1, NB, W, NKV, HD)), ("s_cache_win_v", (1, NB, W, NKV, HD))]


def kernel(**inputs):
    import numpy as np
    import concourse.bacc as bacc
    from concourse.bass_utils import run_bass_kernel_spmd

    nc = bacc.Bacc("TRN2", target_bir_lowering=False, num_devices=1)
    arrays, a, o = {}, {}, {}
    for name in _INS:
        x = np.ascontiguousarray(inputs[name])
        arrays["in_" + name] = x
        a[name] = nc.dram_tensor("in_" + name, x.shape, mybir.dt.from_np(x.dtype), kind="ExternalInput").ap()
    for name, shape in _OUTS:
        o[name] = nc.dram_tensor("out_" + name, shape, F32, kind="ExternalOutput").ap()
    hybrid_step(nc, a, o)
    r = run_bass_kernel_spmd(nc, [arrays], core_ids=[0])
    return tuple(r.results[0]["out_" + name] for name, _ in _OUTS)
```

```python
from contextlib import ExitStack, contextmanager

import concourse.bass as bass
from concourse import mybir

F32 = mybir.dt.float32
I32 = mybir.dt.int32
U32 = mybir.dt.uint32
ALU = mybir.AluOpType
ACT = mybir.ActivationFunctionType
AX = mybir.AxisListType

P = 128
D = 1024
KD = D // P
SEQ = 1024
NB = 8
NT = SEQ // P
TILES = NT + 1
T = SEQ + NB
TP = TILES * P
NSPLIT = 3
NW = T // NSPLIT
DI = 2048
HS, HP, NG, NS = 32, 64, 4, 128
HPG = HS // NG
CD = DI + 2 * NG * NS
CT = CD // P
XT = DI // P
XBT = XT + NG
CK = 4
NH, NKV, HD = 16, 4, 64
GQA = NH // NKV
W = 128
MEM, CH, CHD = 256, 4, 128
CW = CH * CHD
MT = MEM // P
NGR, EPG = 4, 8
NE = NGR * EPG
DE = 512
EPS = 1e-6
NEG = -1e30
Z0 = 0
XBC0 = DI
DT0 = XBC0 + CD
Q0 = DT0 + HS
K0 = Q0 + NH * HD
V0 = K0 + NKV * HD
GS0 = V0 + NKV * HD
VDT = NKV * HD + HS
QKT = (NH + NKV) * HD // P
GT = 2 * D // P

G_MIX, G_CROSS, G_MOE, G_MEM, G_SSD = 0, KD, 2 * KD, 3 * KD, 4 * KD
G_ROWS = 4 * KD + XT
CR_STATE, CR_W, CR_B = 0, NB * (CK - 1), NB * (CK - 1) + CK
CR = CR_B + 1


class Env:

    def __init__(self, nc, ctx, a, o):
        self.nc, self.ctx, self.a, self.o = nc, ctx, a, o

        self.stage_sems = []

    def sem(self, name):
        sem = self.nc.alloc_semaphore(name)
        self.stage_sems.append(sem)
        return sem

    @contextmanager
    def stage(self):
        self.stage_sems = []
        yield
        self.nc.clear_and_free_semaphores(self.stage_sems)
        self.nc.all_engine_barrier()

    def dram(self, name, shape, dt=F32):
        return self.nc.dram_tensor(name, shape, dt, kind="Internal").ap()


def bc(ap, shape):
    return ap.to_broadcast(shape)


def constants(e):
    nc, a = e.nc, e.a
    keep = lambda n, s, dt=F32: e.ctx.enter_context(nc.sbuf_tensor(n, s, dt))
    e.ident = keep("ident", [P, P])
    e.tri = keep("tri", [P, P])
    e.below = keep("below", [P, P])
    e.ones = keep("ones", [P, P])
    e.mhalf = keep("mhalf", [P, 16])
    e.eps = keep("eps", [P, 16])
    e.gvec = keep("gvec", [P, G_ROWS])
    e.cvec = keep("cvec", [P, CT, CR])
    e.tails = keep("tails", [P, CT, CK - 1 + NB])
    e.ps = e.ctx.enter_context(nc.psum_tensor("ps", [P, 8, 512], F32))
    ps = e.ps
    made, loaded, turned, copied = e.sem("const_made"), e.sem("const_loaded"), e.sem("const_turned"), e.sem("const_copied")
    with nc.sbuf_tensor("grows", [G_ROWS, P], F32) as grows, nc.sbuf_tensor("crows", [CR, CD], F32) as crows, \
            nc.Block() as block:
        @block.sync
        def _(sp):
            for n, (name, row, rows) in enumerate((("g_mix", G_MIX, KD), ("g_cross", G_CROSS, KD), ("g_moe", G_MOE, KD),
                                                   ("g_mem", G_MEM, KD), ("g_ssd", G_SSD, XT))):
                sp.dma_start(grows[row:row + rows, :], a[name].rearrange("o (k p) -> (o k) p", p=P)).then_inc(loaded, 16)
            sp.dma_start(crows[CR_STATE:CR_W, :], a["state_conv"].rearrange("o b k c -> (o b k) c")).then_inc(loaded, 16)
            sp.dma_start(crows[CR_W:CR_B, :], a["conv_w"][0]).then_inc(loaded, 16)
            sp.dma_start(crows[CR_B:CR, :], a["conv_b"]).then_inc(loaded, 16)

        @block.gpsimd
        def _(pool):
            pool.memset(e.ident[:, :], 0.0)
            pool.memset(e.tri[:, :], 1.0)
            pool.memset(e.below[:, :], 1.0)
            pool.memset(e.ones[:, :], 1.0)
            pool.memset(e.mhalf[:, :], -0.5)
            pool.memset(e.eps[:, :], EPS)
            pool.drain()
            pool.affine_select(out=e.ident[:, :], in_=e.ident[:, :], compare_op=ALU.not_equal, fill=1.0,
                               base=0, pattern=[[-1, P]], channel_multiplier=1)
            pool.affine_select(out=e.tri[:, :], in_=e.tri[:, :], compare_op=ALU.is_ge, fill=0.0,
                               base=0, pattern=[[1, P]], channel_multiplier=-1)
            pool.affine_select(out=e.below[:, :], in_=e.below[:, :], compare_op=ALU.is_ge, fill=0.0,
                               base=-1, pattern=[[-1, P]], channel_multiplier=1)
            pool.drain()
            pool.sem_inc(made, 1)

        @block.tensor
        def _(pe):
            pe.wait_ge(made, 1)
            pe.wait_ge(loaded, 8 * 16)
            pe.transpose(ps[:, 0, 0:G_ROWS], grows[:, :], e.ident[0:G_ROWS, 0:G_ROWS])
            for c in range(CT):
                last = pe.transpose(ps[:, 1 + c // 12, (c % 12) * 32:(c % 12) * 32 + CR],
                                    crows[:, c * P:(c + 1) * P], e.ident[0:CR, 0:CR])
            last.then_inc(turned, 1)

        @block.vector
        def _(dve):
            dve.wait_ge(turned, 1)
            dve.tensor_copy(e.gvec[:, :], ps[:, 0, 0:G_ROWS])
            for h in range(2):
                dve.tensor_copy(e.cvec[:, 12 * h:12 * h + 12, :],
                                ps[:, 1 + h, 0:12 * 32].rearrange("p (c r) -> p c r", r=32)[:, :, 0:CR])


def rms_tiles(e, name, x, n_tiles, out_turned, grow=None, load=None, gtok=None, store=None):
    nc, ps = e.nc, e.ps
    loaded, squared, meaned, rooted = (e.sem(f"{name}_{x}") for x in ("loaded", "squared", "meaned", "rooted"))
    scaled, turned, low_freed, high_freed = (e.sem(f"{name}_{x}") for x in ("scaled", "turned", "low_freed", "high_freed"))
    stored = [e.sem(f"{name}_stored{i}") for i in range(2)]
    with nc.sbuf_tensor(name + "_xn", [P, 2, D], F32) as xn, nc.sbuf_tensor(name + "_sq", [P, D], F32) as sq, \
            nc.sbuf_tensor(name + "_ss", [P, n_tiles], F32) as ss, nc.sbuf_tensor(name + "_rs", [P, n_tiles], F32) as rs, \
            nc.Block() as block:
        n_loads = len(load or [])

        @block.sync
        def _(sp):
            for dst, src in load or []:
                sp.dma_start(dst, src).then_inc(loaded, 16)
            if store is not None:
                for t in range(n_tiles):
                    sp.wait_ge(scaled, t + 1)
                    sp.dma_start(store[t * P:(t + 1) * P, :], xn[:, t % 2, :]).then_inc(stored[t % 2], 16)
                for b in range(2):
                    sp.wait_ge(stored[b], 16 * ((n_tiles + 1 - b) // 2))

        @block.scalar
        def _(act):
            if n_loads:
                act.wait_ge(loaded, 16 * n_loads)
            for t in range(n_tiles):
                act.activation(sq[:, :], x[:, t, :], ACT.Square, accum_out=ss[:, t:t + 1]).then_inc(squared, 1)
                act.drain()
            for t in range(n_tiles):
                act.wait_ge(turned, 2 * t + 2)
                for k in range(4, KD):
                    src, dst = ps[:, 2 * (t % 2) + 1, (k - 4) * P:(k - 3) * P], out_turned[:, k, t * P:(t + 1) * P]
                    if gtok is None:
                        last = act.activation(dst, src, ACT.Copy, scale=e.gvec[:, grow + k:grow + k + 1])
                    else:
                        last = act.activation(dst, src, ACT.Copy)
                last.then_inc(high_freed, 1)

        @block.gpsimd
        def _(pool):
            pool.wait_ge(meaned, 1)
            pool.tensor_tensor(rs[:, :], ss[:, :], e.mhalf[:, 0:n_tiles], ALU.pow).then_inc(rooted, 1)

        @block.vector
        def _(dve):
            if n_loads:
                dve.wait_ge(loaded, 16 * n_loads)
            dve.wait_ge(squared, n_tiles)
            dve.tensor_scalar(ss[:, :], ss[:, :], 1.0 / D, EPS, ALU.mult, ALU.add).then_inc(meaned, 1)
            dve.wait_ge(rooted, 1)

            def scale(t):
                if t >= 2:
                    dve.wait_ge(turned, 2 * (t - 1))
                    if store is not None:
                        dve.wait_ge(stored[t % 2], 16 * (t // 2))
                last = dve.tensor_scalar(xn[:, t % 2, :], x[:, t, :], rs[:, t:t + 1], None, ALU.mult)
                if gtok is not None:
                    dve.drain()
                    last = dve.tensor_tensor(xn[:, t % 2, :], xn[:, t % 2, :], gtok, ALU.mult)
                last.then_inc(scaled, 1)

            scale(0)
            for t in range(n_tiles):
                if t + 1 < n_tiles:
                    scale(t + 1)
                dve.wait_ge(turned, 2 * t + 1)
                src = ps[:, 2 * (t % 2), :].rearrange("p (k n) -> p k n", k=4)
                dst = out_turned[:, 0:4, t * P:(t + 1) * P]
                if gtok is None:
                    last = dve.tensor_tensor(dst, src, bc(e.gvec[:, grow:grow + 4].unsqueeze(2), [P, 4, P]), ALU.mult)
                else:
                    last = dve.tensor_copy(dst, src)
                last.then_inc(low_freed, 1)

        @block.tensor
        def _(pe):
            for t in range(n_tiles):
                pe.wait_ge(scaled, t + 1)
                if t >= 2:
                    pe.wait_ge(low_freed, t - 1)
                    pe.wait_ge(high_freed, t - 1)
                for k in range(KD):
                    last = pe.transpose(ps[:, 2 * (t % 2) + k // 4, (k % 4) * P:(k % 4 + 1) * P],
                                        xn[:, t % 2, k * P:(k + 1) * P], e.ident[:, :])
                    if k % 4 == 3:
                        last.then_inc(turned, 1)


def project(e, x_turned):
    nc, a, ps = e.nc, e.a, e.ps
    w_in = a["w_in"][0]
    e.xb_rows = e.dram("xb_rows", [SEQ, XBT * P])
    e.bc_cols = e.dram("bc_cols", [2 * NG, P, SEQ])
    e.qk_cols = e.dram("qk_cols", [QKT, P, T])
    e.z_rows = e.dram("z_rows", [TP, DI])
    e.vdt_rows = e.dram("vdt_rows", [TP, VDT])
    e.y_rows = e.dram("moe_rows", [SLOTS, D])

    w_ready, w_free = [e.sem(f"proj_w_ready{i}") for i in range(4)], e.sem("proj_w_free")
    ps_ready, ps_free = e.sem("proj_ps_ready"), e.sem("proj_ps_free")
    u_ready, u_free = e.sem("conv_u_ready"), e.sem("conv_u_free")
    conv_ready, conv_free = e.sem("conv_ready"), e.sem("conv_free")
    act_ready = e.sem("conv_act_ready")
    turned, turn_free = e.sem("conv_turned"), e.sem("conv_turn_free")
    rows_ready, rows_stored = e.sem("conv_rows_ready"), [e.sem(f"conv_rows_stored{i}") for i in range(2)]
    cols_stored = [e.sem(f"conv_cols_stored{i}") for i in range(2)]
    plain_ready, plain_stored = e.sem("plain_ready"), [e.sem(f"plain_stored{i}") for i in range(2)]
    zw_ready = [e.sem(f"zw_ready{i}") for i in range(3)]
    zw_free, z_ps, z_free = e.sem("zw_free"), e.sem("z_ps_ready"), e.sem("z_ps_free")
    z_out, z_stored = e.sem("z_out_ready"), [e.sem(f"z_stored{i}") for i in range(3)]

    WS = 4
    ZN = DI // 512
    with ExitStack() as st:
        sb = lambda n, s: st.enter_context(nc.sbuf_tensor(n, s, F32))
        wring = sb("wring", [P, WS, KD, P])
        zring = sb("zring", [P, 2, KD, 512])
        wv = sb("wv", [P, KD, VDT])
        u = sb("conv_u", [P, 2, CK - 1 + T])
        acc = sb("conv_acc", [P, 2, SEQ])
        y = sb("conv_y", [P, 2, SEQ])
        rows = sb("conv_rows", [P, 2, NT, P])
        plain = sb("plain", [P, 2, T])
        zout = sb("zout", [P, 3, 512])
        zero = sb("zero_rows", [P, D])
        zero_made, zero_stored = e.sem("zero_made"), e.sem("zero_stored")
        block = st.enter_context(nc.Block())

        def cols(c):
            return w_in[:, c].rearrange("(k p) c -> p k c", p=P)

        @block.sync
        def _(sp):
            def load(slot, n, col):
                sp.wait_ge(w_free, n + 1)
                sp.dma_start(wring[:, slot], cols(bass.ds(col, P))).then_inc(w_ready[slot], 16)
            with sp.Fori(0, CT // WS) as i:
                for j in range(WS):
                    load(j, i * WS + j, i * (WS * P) + (XBC0 + j * P))
            with sp.Fori(0, QKT // WS) as i:
                for j in range(WS):
                    load(j, i * WS + (CT + j), i * (WS * P) + (Q0 + j * P))
            for m in range(QKT // WS * WS, QKT):
                load((CT + m) % WS, CT + m, Q0 + m * P)
            with sp.Fori(0, ZN // 2) as i:
                for j in range(2):
                    sp.wait_ge(zw_free, i * 2 + (j + 1))
                    sp.dma_start(zring[:, j], cols(bass.ds(i * 1024 + (Z0 + j * 512), 512))).then_inc(zw_ready[j], 16)
            sp.dma_start(wv[:, :, 0:V0 + NKV * HD - V0], cols(slice(V0, V0 + NKV * HD))).then_inc(zw_ready[2], 16)
            sp.dma_start(wv[:, :, NKV * HD:VDT], cols(slice(DT0, DT0 + HS))).then_inc(zw_ready[2], 16)

        @block.tensor
        def _(pe):
            pe.sem_inc(w_free, WS)
            pe.sem_inc(zw_free, 2)

            def product(slot, par, n, turn_of_slot):
                pe.wait_ge(w_ready[slot], turn_of_slot * 16 + 16)
                pe.wait_ge(ps_free, n + 1)
                for k in range(KD):
                    for s in range(NSPLIT):
                        last = pe.matmul(ps[:, 3 * par + s, 0:NW], wring[:, slot, k], x_turned[:, k, s * NW:(s + 1) * NW],
                                         start=(k == 0), stop=(k == KD - 1))
                last.then_inc(ps_ready, 1)
                pe.drain().then_inc(w_free, 1)

            def turn(par, n):
                pe.wait_ge(act_ready, n + 1)
                pe.wait_ge(turn_free, n + 1)
                for t in range(NT):
                    last = pe.transpose(ps[:, 6 + t // 4, (t % 4) * P:(t % 4 + 1) * P], y[:, par, t * P:(t + 1) * P], e.ident[:, :])
                last.then_inc(turned, 1)

            product(0, 0, 0, 0)
            with pe.Fori(0, XBT // WS) as i:
                for j in range(WS):
                    product((j + 1) % WS, (j + 1) % 2, i * WS + (j + 1), i + (j + 1) // WS)
                    turn(j % 2, i * WS + j)
            for n in range(XBT + 1, CT):
                product(n % WS, n % 2, n, n // WS)
            with pe.Fori(0, QKT // WS) as i:
                for j in range(WS):
                    product(j, j % 2, i * WS + (CT + j), i + CT // WS)
            for m in range(QKT // WS * WS, QKT):
                product((CT + m) % WS, m % 2, CT + m, (CT + m) // WS)

            def row_product(bank, unit, t, w, width):
                pe.wait_ge(z_free, unit + 1)
                for k in range(KD):
                    last = pe.matmul(ps[:, bank, 0:width], x_turned[:, k, t * P:(t + 1) * P], w[:, k], start=(k == 0), stop=(k == KD - 1))
                last.then_inc(z_ps, 1)

            with pe.Fori(0, ZN // 2) as i:
                for j in range(2):
                    pe.wait_ge(zw_ready[j], i * 16 + 16)
                    for t in range(TILES):
                        row_product((j * TILES + t) % 6, i * (2 * TILES) + (j * TILES + t), t, zring[:, j], 512)
                    pe.drain().then_inc(zw_free, 1)
            pe.wait_ge(zw_ready[2], 32)
            for t in range(TILES):
                row_product((ZN * TILES + t) % 6, ZN * TILES + t, t, wv, VDT)

        @block.scalar
        def _(act):
            act.sem_inc(ps_free, 2)
            act.sem_inc(conv_free, 2)

            def empty(par, dst, func=ACT.Copy):
                for s in range(NSPLIT):
                    last = act.activation(dst[:, s * NW:(s + 1) * NW], ps[:, 3 * par + s, 0:NW], func)
                return last

            def conv_tile(par, n):
                act.wait_ge(ps_ready, n + 1)
                act.wait_ge(u_free, n + 1)
                empty(par, u[:, par, CK - 1:]).then_inc(u_ready, 1)
                act.drain().then_inc(ps_free, 1)
                act.wait_ge(conv_ready, n + 1)
                act.activation(y[:, par], acc[:, par], ACT.Silu).then_inc(act_ready, 1)
                act.drain().then_inc(conv_free, 1)

            def x_tile(par, n, first):
                if not first:
                    act.wait_ge(turned, n + (-1))
                conv_tile(par, n)
            x_tile(0, 0, True)
            x_tile(1, 1, True)
            for n in (2, 3):
                x_tile(n % 2, n, False)
            with act.Fori(1, XT // WS) as i:
                for j in range(WS):
                    x_tile(j % 2, i * WS + j, False)
            for n in range(XT, CT):
                if n - 2 < XBT:
                    act.wait_ge(turned, n - 1)
                if n - 2 >= XT:
                    act.wait_ge(cols_stored[n % 2], 16 * ((n - XT) // 2))
                conv_tile(n % 2, n)
                act.wait_ge(act_ready, n + 1)
                act.dma_start(e.bc_cols[n - XT], y[:, n % 2]).then_inc(cols_stored[n % 2], 16)

            def plain_tile(par, n, earlier, dst, func):
                act.wait_ge(ps_ready, n + (CT + 1))
                act.wait_ge(plain_stored[par], earlier * 16)
                empty(par, plain[:, par], func).then_inc(plain_ready, 1)
                act.drain().then_inc(ps_free, 1)
                act.dma_start(dst, plain[:, par]).then_inc(plain_stored[par], 16)

            with act.Fori(0, QKT // WS) as i:
                for j in range(WS):
                    plain_tile(j % 2, i * WS + j, i * 2 + j // 2, e.qk_cols[bass.ds(i * WS + j, 1)].rearrange("o p t -> (o p) t"), ACT.Copy)
            for m in range(QKT // WS * WS, QKT):
                plain_tile(m % 2, m, m // 2, e.qk_cols[m], ACT.Copy)
            act.drain().then_inc(z_free, 6)

            def row_tile(bank, buf, unit, earlier, dst, width, func):
                act.wait_ge(z_ps, unit + 1)
                act.wait_ge(z_stored[buf], earlier * 16)
                act.activation(zout[:, buf, 0:width], ps[:, bank, 0:width], func).then_inc(z_out, 1)
                act.drain().then_inc(z_free, 1)
                act.dma_start(dst, zout[:, buf, 0:width]).then_inc(z_stored[buf], 16)

            with act.Fori(0, ZN // 2) as i:
                for j in range(2):
                    for t in range(TILES):
                        n = j * TILES + t
                        row_tile(n % 6, n % 3, i * (2 * TILES) + n, i * (2 * TILES // 3) + n // 3, e.z_rows[t * P:(t + 1) * P, bass.ds(i * 1024 + j * 512, 512)], 512, ACT.Silu)
            for t in range(TILES):
                n = ZN * TILES + t
                row_tile(n % 6, n % 3, n, n // 3, e.vdt_rows[t * P:(t + 1) * P, :], VDT, ACT.Copy)
            for b in range(2):
                act.wait_ge(cols_stored[b], 16 * (CT - XT) // 2)
                act.wait_ge(plain_stored[b], 16 * QKT // 2)
            for b in range(3):
                act.wait_ge(z_stored[b], 16 * (ZN + 1) * TILES // 3)

        @block.vector
        def _(dve):
            dve.memset(u[:, :, 0:CK - 1], 0.0)
            dve.drain().then_inc(u_free, 2)
            dve.sem_inc(turn_free, 1)

            def conv(par, n):
                dve.wait_ge(u_ready, n + 1)
                dve.wait_ge(conv_free, n + 1)
                cv = e.cvec[:, bass.ds(n, 1), :].rearrange("p o r -> p (o r)")
                dve.tensor_scalar(acc[:, par], u[:, par, CK - 1:CK - 1 + SEQ], cv[:, CR_W + CK - 1:CR_W + CK], cv[:, CR_B:CR], ALU.mult, ALU.add)
                for k in range(CK - 1):
                    dve.drain()
                    last = dve.scalar_tensor_tensor(out=acc[:, par], in0=u[:, par, k:k + SEQ], scalar=cv[:, CR_W + k:CR_W + k + 1],
                                                    in1=acc[:, par], op0=ALU.mult, op1=ALU.add)
                last.then_inc(conv_ready, 1)
                dve.tensor_copy(e.tails[:, bass.ds(n, 1), :].rearrange("p o r -> p (o r)"), u[:, par, SEQ:SEQ + CK - 1 + NB])
                dve.drain().then_inc(u_free, 1)

            def rows_out(par, n, earlier):
                dve.wait_ge(turned, n + 1)
                dve.wait_ge(rows_stored[par], earlier * 16)
                dve.tensor_copy(rows[:, par], ps[:, 6:8, :].rearrange("p b (t c) -> p (b t) c", c=P)).then_inc(rows_ready, 1)
                dve.drain().then_inc(turn_free, 1)

            conv(0, 0)
            with dve.Fori(0, XBT // WS) as i:
                for j in range(WS):
                    conv((j + 1) % 2, i * WS + (j + 1))
                    rows_out(j % 2, i * WS + j, i * 2 + j // 2)
            for n in range(XBT + 1, CT):
                conv(n % 2, n)

        @block.gpsimd
        def _(pool):
            pool.memset(zero[:, :], 0.0).then_inc(zero_made, 1)
            pool.wait_ge(zero_made, 1)
            for b in range(NMORE):
                pool.dma_start(e.y_rows[(NBASE + b) * P:(NBASE + b + 1) * P, :], zero[:, :]).then_inc(zero_stored, 16)
            with pool.Fori(0, XBT // WS) as i:
                for j in range(WS):
                    pool.wait_ge(rows_ready, i * WS + (j + 1))
                    pool.dma_start(e.xb_rows[:, bass.ds(i * (WS * P) + j * P, P)].rearrange("(t p) c -> p t c", p=P),
                                   rows[:, j % 2]).then_inc(rows_stored[j % 2], 16)
            for b in range(2):
                pool.wait_ge(rows_stored[b], 16 * XBT // 2)
            pool.wait_ge(zero_stored, 16 * NMORE)


def mixer_norm(e, x_turned):
    nc, a = e.nc, e.a
    zeroed = e.sem("mixer_zeroed")
    with nc.sbuf_tensor("x_rows", [P, TILES, D], F32) as x:
        with nc.Block() as block:
            @block.vector
            def _(dve):
                dve.memset(x[:, NT, :], 0.0)
        rms_tiles(e, "mixer", x, TILES, x_turned, grow=G_MIX, load=x_loads(e, x))


def x_loads(e, x):
    return [(x[:, 0:NT, :], e.a["x_prompt"][0].rearrange("(t p) d -> p t d", p=P)),
            (x[0:NB, NT, :], e.a["x_sample"][:, 0, :])]


def ssd_vectors(e):
    keep = lambda n, s: e.ctx.enter_context(e.nc.sbuf_tensor(n, s, F32))
    e.dt = keep("dt", [P, TILES, HS])
    e.da = keep("da", [P, TILES, HS])
    e.d_skip = keep("d_skip", [P, HS])


def ssd_steps(e):
    nc, a = e.nc, e.a
    loaded, s_v, s_a = e.sem("dt_loaded"), e.sem("dt_vector_step"), e.sem("dt_scalar_step")
    with ExitStack() as st:
        sb = lambda n, s: st.enter_context(nc.sbuf_tensor(n, s, F32))
        raw, e1, ln = sb("dt_raw", [P, TILES, HS]), sb("dt_exp", [P, TILES, HS]), sb("dt_ln", [P, TILES, HS])
        u, d = sb("dt_u", [P, TILES, HS]), sb("dt_d", [P, TILES, HS])
        bias, alog = sb("dt_bias_all", [P, HS]), sb("a_log_all", [P, HS])
        block = st.enter_context(nc.Block())

        @block.sync
        def _(sp):
            sp.dma_start(raw[:, :, :], e.vdt_rows[:, NKV * HD:VDT].rearrange("(t p) c -> p t c", p=P)).then_inc(loaded, 16)
            for name, dst in (("dt_bias", bias), ("a_log", alog), ("d_skip", e.d_skip)):
                sp.dma_start(dst[:, :], a[name].to_broadcast([P, HS])).then_inc(loaded, 16)

        @block.scalar
        def _(act):
            act.wait_ge(loaded, 64)
            act.activation(alog[:, :], alog[:, :], ACT.Exp).then_inc(s_a, 1)
            act.wait_ge(s_v, 1)
            act.activation(e1[:, :, :], d[:, :, :], ACT.Exp).then_inc(s_a, 1)
            act.wait_ge(s_v, 2)
            act.activation(ln[:, :, :], u[:, :, :], ACT.Ln).then_inc(s_a, 1)

        @block.vector
        def _(dve):
            dve.wait_ge(loaded, 64)
            dve.tensor_tensor(raw[:, :, :], raw[:, :, :], bc(bias[:, :].unsqueeze(1), [P, TILES, HS]), ALU.add)
            dve.drain()
            dve.tensor_scalar(u[:, :, :], raw[:, :, :], -1.0, None, ALU.mult)
            dve.drain()
            dve.tensor_tensor(d[:, :, :], raw[:, :, :], u[:, :, :], ALU.min).then_inc(s_v, 1)
            dve.wait_ge(s_a, 2)
            dve.tensor_scalar(u[:, :, :], e1[:, :, :], 1.0, None, ALU.add).then_inc(s_v, 1)
            dve.drain()
            dve.tensor_scalar(d[:, :, :], u[:, :, :], -1.0, None, ALU.add)
            dve.drain()
            dve.tensor_scalar(e.dt[:, :, :], d[:, :, :], 0.0, None, ALU.is_equal)
            dve.tensor_scalar(raw[:, :, :], raw[:, :, :], 0.0, None, ALU.max)
            dve.drain()
            dve.tensor_tensor(d[:, :, :], d[:, :, :], e.dt[:, :, :], ALU.add)
            dve.tensor_tensor(e.dt[:, :, :], e.dt[:, :, :], e1[:, :, :], ALU.mult)
            dve.drain()
            dve.reciprocal(d[:, :, :], d[:, :, :])
            dve.tensor_tensor(raw[:, :, :], raw[:, :, :], e.dt[:, :, :], ALU.add)
            dve.drain()
            dve.tensor_tensor(d[:, :, :], d[:, :, :], e1[:, :, :], ALU.mult)
            dve.drain()
            dve.wait_ge(s_a, 3)
            dve.tensor_tensor(d[:, :, :], d[:, :, :], ln[:, :, :], ALU.mult)
            dve.tensor_scalar(alog[:, :], alog[:, :], -1.0, None, ALU.mult)
            dve.drain()
            dve.tensor_tensor(e.dt[:, :, :], raw[:, :, :], d[:, :, :], ALU.add)
            dve.drain()
            dve.tensor_tensor(e.da[:, :, :], e.dt[:, :, :], bc(alog[:, :].unsqueeze(1), [P, TILES, HS]), ALU.mult)


def ssd_chunks(e, x_turned):
    nc, a, ps = e.nc, e.a, e.ps
    e.gate_cols = e.dram("gate_cols", [GT, P, T])
    names = ("in_ready0", "in_ready1", "in_pe", "in_pool", "z_ready", "z_free", "gw_ready0", "gw_ready1", "gate_w_free", "gate_made", "gate_free",
             "gate_exp", "gate_out", "gate_stored0", "gate_stored1", "sums", "decays", "decays_pool", "decays_dve",
             "rtri_ready", "rtri_free", "seg_ready", "seg_free", "e_ready", "e_free", "cb_ready", "cb_free", "cbm_ready",
             "m_ready", "m_free", "xdt_ready", "xdt_free", "xw_ready", "xw_free", "xd_ready", "xd_free",
             "inter", "inter_free", "intra", "intra_free", "scaled", "upd", "state_ready", "gated", "gated_free", "sums_free", "upd_free",
             "squared", "rooted", "normed", "normed_free", "turned", "turn_free", "y_stored")
    s = {n: e.sem("ssd_" + n) for n in names}
    XW = XBT * P
    with ExitStack() as st:
        sb = lambda n, sh: st.enter_context(nc.sbuf_tensor(n, sh, F32))
        xb = sb("ssd_xb", [P, 2, XW])
        bcc = sb("ssd_bc", [P, 2, 2 * NG, P])
        z = sb("ssd_z", [P, DI])
        gw = sb("gate_w", [P, 2, KD, P])
        go = sb("gate_out", [P, 2, NW])
        rtri = sb("ssd_rtri", [P, 2, HPG, P])
        ee = sb("ssd_e", [P, 2, HPG, P])
        mm = sb("ssd_m", [P, 2, HPG, P])
        cbm = sb("ssd_cbm", [P, NG, P])
        dec = sb("ssd_dec", [P, 2, 3 * HS])
        wdt = sb("ssd_wdt", [P, HS])
        xdt = sb("ssd_xdt", [P, HS, HP])
        xw = sb("ssd_xw", [P, HS, HP])
        xd = sb("ssd_xd", [P, HS, HP])
        state = sb("ssd_state", [P, HS, HP])
        y = sb("ssd_y", [P, 2, HS, HP])
        sq = sb("ssd_sq", [P, 512])
        yn = sb("ssd_yn", [P, DI])
        ss, rs = sb("ssd_ss", [P, NG]), sb("ssd_rs", [P, NG])
        da, dt = sb("ssd_da_now", [P, HS]), sb("ssd_dt_now", [P, HS])
        yc = sb("ssd_ycols", [P, XT, P])
        hs = lambda g: slice(g * HPG, (g + 1) * HPG)
        GATE_PARTS = ((0,), (1, 2), (3,), (4, 5))
        gc = lambda g: slice(g * 512, (g + 1) * 512)
        bank = lambda b: ps[:, b, :].rearrange("p (h c) -> p h c", h=HPG)

        with nc.Block() as block:
            def over_chunks(eng, chunk):
                chunk(0, 0, 0)
                with eng.Fori(0, (NT - 2) // 2) as i:
                    chunk(i * 2 + 1, 1, i)
                    chunk(i * 2 + 2, 0, i + 1)
                chunk(NT - 1, 1, NT // 2 - 1)

            @block.sync
            def _(sp):
                for b in range(2):
                    sp.sem_inc(s[f"gate_stored{b}"], 16)

                def inputs(n, par):
                    for who in ("in_pe", "in_pool"):
                        sp.wait_ge(s[who], n + 1)
                    sp.dma_start(xb[:, par], e.xb_rows[bass.ds(n * P, P), :]).then_inc(s[f"in_ready{par}"], 16)
                    sp.dma_start(bcc[:, par], e.bc_cols[:, :, bass.ds(n * P, P)].rearrange("g p t -> p g t")).then_inc(s[f"in_ready{par}"], 16)

                def gate_weights(n, j):
                    sp.wait_ge(s["gate_w_free"], n * 2 + (j + 1))
                    sp.dma_start(gw[:, j], a["w_in"][0][:, bass.ds(n * (2 * P) + (GS0 + j * P), P)].rearrange("(k p) c -> p k c", p=P)).then_inc(s[f"gw_ready{j}"], 16)

                def load_z(n):
                    sp.wait_ge(s["z_free"], n + 1)
                    sp.dma_start(z[:, :], e.z_rows[bass.ds(n * P, P), :]).then_inc(s["z_ready"], 16)

                def chunk(n, par, k, last=False):
                    if not last:
                        inputs(n + 1, 1 - par)
                    for part in range(2 * NSPLIT):
                        j, q = part // NSPLIT, part % NSPLIT
                        sp.wait_ge(s["gate_out"], n * (2 * NSPLIT) + (part + 1))
                        tile = e.gate_cols[bass.ds(n * 2 + j, 1)].rearrange("o p t -> (o p) t")
                        sp.dma_start(tile[:, q * NW:(q + 1) * NW], go[:, part % 2]).then_inc(s[f"gate_stored{part % 2}"], 16)
                        if q == NSPLIT - 1 and not last:
                            gate_weights(n + 1, j)
                    if not last:
                        load_z(n + 1)
                inputs(0, 0)
                gate_weights(0, 0)
                gate_weights(0, 1)
                load_z(0)
                chunk(0, 0, 0)
                with sp.Fori(0, (NT - 2) // 2) as i:
                    chunk(i * 2 + 1, 1, i)
                    chunk(i * 2 + 2, 0, i + 1)
                chunk(NT - 1, 1, NT // 2 - 1, last=True)
                for b in range(2):
                    sp.wait_ge(s[f"gate_stored{b}"], 16 * (GT * NSPLIT // 2 + 1))

            def wait_in(eng, par, k):
                eng.wait_ge(s[f"in_ready{par}"], k * 32 + 32)

            @block.gpsimd
            def _(pool):
                pool.memset(state[:, :, :], 0.0)
                pool.drain().then_inc(s["state_ready"], NG)
                pool.sem_inc(s["in_pool"], 2)
                pool.sem_inc(s["decays_pool"], 2)

                def root(n):
                    pool.wait_ge(s["squared"], n + 1)
                    pool.tensor_tensor(ss[:, :], ss[:, :], e.eps[:, 0:NG], ALU.add)
                    pool.drain()
                    pool.tensor_tensor(rs[:, :], ss[:, :], e.mhalf[:, 0:NG], ALU.pow).then_inc(s["rooted"], 1)

                def chunk(n, par, k, first=False):
                    pool.tensor_copy(da[:, :], e.da[:, bass.ds(n, 1), :].rearrange("p o h -> p (o h)"))
                    pool.tensor_copy(dt[:, :], e.dt[:, bass.ds(n, 1), :].rearrange("p o h -> p (o h)"))
                    pool.drain()
                    x = xb[:, par, 0:DI].rearrange("p (h c) -> p h c", c=HP)

                    def running(g):
                        pool.wait_ge(s["rtri_free"], n * NG + (g + 1))
                        pool.tensor_tensor(rtri[:, g % 2], bc(e.tri[:, :].unsqueeze(1), [P, HPG, P]),
                                           bc(da[:, hs(g)].unsqueeze(2), [P, HPG, P]), ALU.mult).then_inc(s["rtri_ready"], 1)
                    running(0)
                    running(1)
                    wait_in(pool, par, k)
                    pool.wait_ge(s["xdt_free"], n + 1)
                    pool.tensor_tensor(xdt[:, :, :], x, bc(dt[:, :].unsqueeze(2), [P, HS, HP]), ALU.mult).then_inc(s["xdt_ready"], 1)
                    running(2)
                    pool.wait_ge(s["decays"], n + 1)
                    pool.wait_ge(s["xw_free"], n + 1)
                    pool.tensor_tensor(wdt[:, :], dec[:, par, HS:2 * HS], dt[:, :], ALU.mult)
                    pool.drain()
                    pool.tensor_tensor(xw[:, :, :], x, bc(wdt[:, :].unsqueeze(2), [P, HS, HP]), ALU.mult).then_inc(s["xw_ready"], 1)
                    running(3)
                    pool.wait_ge(s["xd_free"], n + 1)
                    pool.tensor_tensor(xd[:, :, :], x, bc(e.d_skip[:, :].unsqueeze(2), [P, HS, HP]), ALU.mult).then_inc(s["xd_ready"], 1)
                    pool.drain().then_inc(s["in_pool"], 1)
                    if not first:
                        root(n - 1)
                    for g in range(NG):
                        pool.wait_ge(s["inter"], n * NG + (g + 1))
                        pool.wait_ge(s["state_ready"], n * NG + (g + 1))
                        pool.tensor_tensor(state[:, hs(g)], state[:, hs(g)],
                                           bc(dec[:, par, 2 * HS + g * HPG:2 * HS + (g + 1) * HPG].unsqueeze(2), [P, HPG, HP]),
                                           ALU.mult).then_inc(s["scaled"], 1)
                    pool.drain().then_inc(s["decays_pool"], 1)

                chunk(0, 0, 0, first=True)
                with pool.Fori(0, (NT - 2) // 2) as i:
                    chunk(i * 2 + 1, 1, i)
                    chunk(i * 2 + 2, 0, i + 1)
                chunk(NT - 1, 1, NT // 2 - 1)
                root(NT - 1)

            @block.tensor
            def _(pe):
                pe.sem_inc(s["in_pe"], 2)
                pe.sem_inc(s["rtri_free"], 2)
                pe.sem_inc(s["m_free"], 2)
                pe.sem_inc(s["xdt_free"], 1)
                pe.sem_inc(s["gate_w_free"], 2)
                pe.sem_inc(s["xw_free"], 1)

                def turn(n, cb_done):
                    pe.wait_ge(s["normed"], n + 1)
                    pe.wait_ge(s["cb_free"], cb_done)
                    for q in range(XT // 4):
                        pe.wait_ge(s["turn_free"], n * (XT // 4) + (q + 1))
                        for k in range(4):
                            last = pe.transpose(ps[:, 3, k * P:(k + 1) * P], yn[:, (4 * q + k) * P:(4 * q + k + 1) * P], e.ident[:, :])
                        last.then_inc(s["turned"], 1)
                    pe.drain().then_inc(s["normed_free"], 1)

                def gate_part(n, part):
                    j, q = part // NSPLIT, part % NSPLIT
                    if q == 0:
                        pe.wait_ge(s[f"gw_ready{j}"], n * 16 + 16)
                    pe.wait_ge(s["gate_free"], n * (2 * NSPLIT) + (part + 1))
                    for k in range(KD):
                        last = pe.matmul(ps[:, 7, 0:NW], gw[:, j, k], x_turned[:, k, q * NW:(q + 1) * NW], start=(k == 0), stop=(k == KD - 1))
                    last.then_inc(s["gate_made"], 1)
                    if q == NSPLIT - 1:
                        pe.drain().then_inc(s["gate_w_free"], 1)

                def chunk(n, par, k, first=False):
                    da = e.da[:, bass.ds(n, 1), :].rearrange("p o h -> p (o h)")
                    wait_in(pe, par, k)
                    pe.wait_ge(s["sums_free"], n + 1)
                    pe.matmul(ps[:, 0, 0:HS], e.tri[:, :], da, start=True, stop=True)
                    pe.matmul(ps[:, 0, HS:2 * HS], e.below[:, :], da, start=True, stop=True)
                    pe.matmul(ps[:, 0, 2 * HS:3 * HS], e.ones[:, :], da, start=True, stop=True).then_inc(s["sums"], 1)
                    pe.wait_ge(s["cb_free"], n + 1)
                    if not first:
                        pe.wait_ge(s["turn_free"], n * (XT // 4) + (1 - XT // 4))
                    for g in range(NG):
                        last = pe.matmul(ps[:, 3, g * P:(g + 1) * P], bcc[:, par, g], bcc[:, par, NG + g], start=True, stop=True)
                    last.then_inc(s["cb_ready"], 1)

                    def segments(g):
                        pe.wait_ge(s["rtri_ready"], n * NG + (g + 1))
                        pe.wait_ge(s["seg_free"], n * NG + (g + 1))
                        for b in range(2):
                            last = pe.matmul(ps[:, 1 + b, :], e.below[:, :], rtri[:, g % 2, 4 * b:4 * b + 4].rearrange("p h c -> p (h c)"),
                                             start=True, stop=True)
                        last.then_inc(s["seg_ready"], 1)
                        pe.drain().then_inc(s["rtri_free"], 1)
                    segments(0)
                    for g in range(NG):
                        pe.wait_ge(s["state_ready"], n * NG + (g + 1))
                        pe.wait_ge(s["inter_free"], n * NG + (g + 1))
                        pe.matmul(ps[:, 5, :], bcc[:, par, NG + g], state[:, hs(g)].rearrange("p h c -> p (h c)"),
                                  start=True, stop=True).then_inc(s["inter"], 1)
                        for part in GATE_PARTS[g]:
                            gate_part(n, part)
                        if g < NG - 1:
                            segments(g + 1)
                        pe.wait_ge(s["m_ready"], n * NG + (g + 1))
                        pe.wait_ge(s["xdt_ready"], n + 1)
                        pe.wait_ge(s["intra_free"], n * NG + (g + 1))
                        for h in range(HPG):
                            last = pe.matmul(ps[:, 4, h * HP:(h + 1) * HP], mm[:, g % 2, h], xdt[:, g * HPG + h], start=True, stop=True)
                        last.then_inc(s["intra"], 1)
                        pe.drain().then_inc(s["m_free"], 1)
                        pe.wait_ge(s["xw_ready"], n + 1)
                        pe.wait_ge(s["upd_free"], n * NG + (g + 1))
                        pe.matmul(ps[:, 6, :], xb[:, par, DI + g * NS:DI + (g + 1) * NS], xw[:, hs(g)].rearrange("p h c -> p (h c)"),
                                  start=True, stop=True).then_inc(s["upd"], 1)
                    pe.drain().then_inc(s["in_pe"], 1)
                    pe.sem_inc(s["xdt_free"], 1)
                    pe.sem_inc(s["xw_free"], 1)
                    if not first:
                        turn(n - 1, n + 2)
                chunk(0, 0, 0, first=True)
                with pe.Fori(0, (NT - 2) // 2) as i:
                    chunk(i * 2 + 1, 1, i)
                    chunk(i * 2 + 2, 0, i + 1)
                chunk(NT - 1, 1, NT // 2 - 1)
                turn(NT - 1, NT + 1)

            @block.scalar
            def _(act):
                act.sem_inc(s["seg_free"], 1)
                act.sem_inc(s["sums_free"], 1)
                act.sem_inc(s["turn_free"], 1)
                act.sem_inc(s["gated_free"], 2)
                act.sem_inc(s["gate_free"], 1)
                act.sem_inc(s["y_stored"], 16)

                def gate_part(n, part):
                    b = part % 2
                    act.wait_ge(s["gate_made"], n * (2 * NSPLIT) + (part + 1))
                    act.wait_ge(s[f"gate_stored{b}"], n * (NSPLIT * 16) + (part // 2 + 1) * 16)
                    act.activation(go[:, b], ps[:, 7, 0:NW], ACT.Exp, scale=-1.0).then_inc(s["gate_exp"], 1)
                    act.drain().then_inc(s["gate_free"], 1)

                def columns(n):
                    act.wait_ge(s["y_stored"], n * 16 + 16)
                    for q in range(XT // 4):
                        act.wait_ge(s["turned"], n * (XT // 4) + (q + 1))
                        for j in range(4):
                            f = 4 * q + j
                            last = act.activation(yc[:, f], ps[:, 3, j * P:(j + 1) * P], ACT.Copy,
                                                  scale=e.gvec[:, G_SSD + f:G_SSD + f + 1])
                        act.drain().then_inc(s["turn_free"], 1)
                    col = slice(n * P, (n + 1) * P) if isinstance(n, int) else bass.ds(n * P, P)
                    act.dma_start(e.y_cols[:, :, col].rearrange("f p t -> p f t"), yc[:, :, :]).then_inc(s["y_stored"], 16)

                def squares(n, par):
                    act.wait_ge(s["gated"], n + 1)
                    for g in range(NG):
                        last = act.activation(sq[:, :], y[:, par, hs(g)].rearrange("p h c -> p (h c)"), ACT.Square,
                                              scale=float(DI // NG) ** -0.5, accum_out=ss[:, g:g + 1])
                        if g < NG - 1:
                            act.drain()
                    last.then_inc(s["squared"], 1)

                def norm(n, par):
                    act.wait_ge(s["rooted"], n + 1)
                    act.wait_ge(s["normed_free"], n + 1)
                    for g in range(NG):
                        last = act.activation(yn[:, gc(g)], y[:, par, hs(g)].rearrange("p h c -> p (h c)"), ACT.Copy, scale=rs[:, g:g + 1])
                    last.then_inc(s["normed"], 1)
                    act.drain().then_inc(s["gated_free"], 1)

                def chunk(n, par, k, first=False):
                    act.wait_ge(s["sums"], n + 1)
                    act.wait_ge(s["decays_pool"], n + 1)
                    act.wait_ge(s["decays_dve"], n + 1)
                    act.activation(dec[:, par], ps[:, 0, 0:3 * HS], ACT.Exp).then_inc(s["decays"], 1)
                    act.drain().then_inc(s["sums_free"], 1)
                    for g in range(NG):
                        act.wait_ge(s["seg_ready"], n * NG + (g + 1))
                        act.wait_ge(s["e_free"], n * NG + (g + 1))
                        act.activation(ee[:, g % 2].rearrange("p h c -> p (h c)"), ps[:, 1:3, :].rearrange("p b c -> p (b c)"),
                                       ACT.Exp).then_inc(s["e_ready"], 1)
                        act.drain().then_inc(s["seg_free"], 1)
                        for part in GATE_PARTS[g]:
                            gate_part(n, part)
                        if g == 0 and not first:
                            squares(n - 1, 1 - par)
                        if g == 2 and not first:
                            norm(n - 1, 1 - par)
                    if not first:
                        columns(n - 1)
                chunk(0, 0, 0, first=True)
                with act.Fori(0, (NT - 2) // 2) as i:
                    chunk(i * 2 + 1, 1, i)
                    chunk(i * 2 + 2, 0, i + 1)
                chunk(NT - 1, 1, NT // 2 - 1)
                squares(NT - 1, 1)
                norm(NT - 1, 1)
                columns(NT - 1)
                act.wait_ge(s["y_stored"], 16 * (NT + 1))

            @block.vector
            def _(dve):
                for name in ("e_free", "decays_dve"):
                    dve.sem_inc(s[name], 2)
                for name in ("cb_free", "inter_free", "intra_free", "upd_free", "xd_free", "normed_free", "z_free"):
                    dve.sem_inc(s[name], 1)

                def gate_part(n, part):
                    dve.wait_ge(s["gate_exp"], n * (2 * NSPLIT) + (part + 1))
                    dve.tensor_scalar(go[:, part % 2], go[:, part % 2], 1.0, None, ALU.add)
                    dve.drain()
                    dve.reciprocal(go[:, part % 2], go[:, part % 2]).then_inc(s["gate_out"], 1)

                def chunk(n, par, k):
                    dve.wait_ge(s["cb_ready"], n + 1)
                    dve.tensor_tensor(cbm[:, :, :], ps[:, 3, :].rearrange("p (g c) -> p g c", g=NG), bc(e.tri[:, :].unsqueeze(1), [P, NG, P]), ALU.mult)
                    dve.drain().then_inc(s["cb_free"], 1)
                    dve.wait_ge(s["gated_free"], n + 1)
                    for g in range(NG):
                        dve.wait_ge(s["e_ready"], n * NG + (g + 1))
                        dve.wait_ge(s["m_free"], n * NG + (g + 1))
                        dve.tensor_tensor(mm[:, g % 2], ee[:, g % 2], bc(cbm[:, g].unsqueeze(1), [P, HPG, P]), ALU.mult).then_inc(s["m_ready"], 1)
                        dve.drain().then_inc(s["e_free"], 1)
                        if g == 0:
                            dve.wait_ge(s["decays"], n + 1)
                        dve.wait_ge(s["inter"], n * NG + (g + 1))
                        yg = y[:, par, hs(g)]
                        dve.tensor_tensor(yg, bank(5), bc(dec[:, par, hs(g)].unsqueeze(2), [P, HPG, HP]), ALU.mult)
                        dve.drain().then_inc(s["inter_free"], 1)
                        if g == 0:
                            dve.wait_ge(s["xd_ready"], n + 1)
                        dve.tensor_tensor(yg, yg, xd[:, hs(g)], ALU.add)
                        dve.drain()
                        dve.wait_ge(s["intra"], n * NG + (g + 1))
                        dve.tensor_tensor(yg, yg, bank(4), ALU.add)
                        dve.drain().then_inc(s["intra_free"], 1)
                        if g == 0:
                            dve.wait_ge(s["z_ready"], n * 16 + 16)
                        dve.tensor_tensor(yg, yg, z[:, gc(g)].rearrange("p (h c) -> p h c", c=HP), ALU.mult)
                        dve.wait_ge(s["scaled"], n * NG + (g + 1))
                        dve.wait_ge(s["upd"], n * NG + (g + 1))
                        dve.tensor_tensor(state[:, hs(g)], state[:, hs(g)], bank(6), ALU.add).then_inc(s["state_ready"], 1)
                        dve.drain().then_inc(s["upd_free"], 1)
                        for part in GATE_PARTS[g]:
                            gate_part(n, part)
                    dve.drain().then_inc(s["gated"], 1)
                    dve.sem_inc(s["z_free"], 1)
                    dve.sem_inc(s["decays_dve"], 1)
                    dve.sem_inc(s["xd_free"], 1)
                over_chunks(dve, chunk)
        ssd_state_out(e, state)


def ssd_state_out(e, state):
    nc, ps = e.nc, e.ps
    turned, copied, stored = e.sem("state_turned"), e.sem("state_copied"), e.sem("state_stored")
    with nc.sbuf_tensor("state_rows", [P, XT, NS], F32) as rows, nc.Block() as block:
        @block.tensor
        def _(pe):
            for k in range(XT):
                last = pe.transpose(ps[:, k // 4, (k % 4) * P:(k % 4 + 1) * P],
                                    state[:, 2 * k:2 * k + 2].rearrange("p h c -> p (h c)"), e.ident[:, :])
            last.then_inc(turned, 1)

        @block.vector
        def _(dve):
            dve.wait_ge(turned, 1)
            dve.tensor_copy(rows[:, :, :], ps[:, 0:4, :].rearrange("p b (k n) -> p (b k) n", k=4)).then_inc(copied, 1)

        @block.sync
        def _(sp):
            sp.wait_ge(copied, 1)
            sp.dma_start(e.o["p_state_ssd"].rearrange("o b h c n -> (o b h c) n").rearrange("(k p) n -> p k n", p=P),
                         rows[:, :, :]).then_inc(stored, 16)
            sp.wait_ge(stored, 16)


def pairs(eng, step):
    step(0, 0, 0)
    with eng.Fori(0, (NT - 2) // 2) as i:
        step(i * 2 + 1, 1, i)
        step(i * 2 + 2, 0, i + 1)
    step(NT - 1, 1, NT // 2 - 1)


def staggered(eng, front, back):
    front(0, 0, True)
    front(1, 1, False)
    back(0, 0, True)
    with eng.Fori(0, (NT - 2) // 2) as i:
        front(i * 2 + 2, 0, False)
        back(i * 2 + 1, 1, False)
        front(i * 2 + 3, 1, False)
        back(i * 2 + 2, 0, False)
    back(NT - 1, 1, False)


def window_attention(e):
    nc, a, ps = e.nc, e.a, e.ps
    e.down_cols = e.dram("down_cols", [KD, P, T])
    y_ready = [e.sem(f"down_y_ready{i}") for i in range(4)]
    gate_ready = [e.sem(f"down_gate_ready{i}") for i in range(NSPLIT)]
    down_stored = [e.sem(f"down_stored{i}") for i in range(NSPLIT)]
    names = ("wd_ready0", "wd_ready1", "wd_free", "down_made", "down_free", "down_out", "qk_ready0", "qk_ready1", "v_ready0", "v_ready1", "qk_free", "v_free", "bias_made", "bias_scaled", "bias_masked", "s_ready", "s_free", "max_ready",
             "exp_ready", "sc_free", "recip_ready", "p_ready", "t_ready", "t_low_free", "t_high_free", "pt_low", "pt_high", "pt_free",
             "o_ready", "o_free", "sink_ready", "out_ready", "stored0", "stored1")
    s = {n: e.sem("win_" + n) for n in names}
    SCALE = HD ** -0.5
    with ExitStack() as st:
        sb = lambda n, sh, dt=F32: st.enter_context(nc.sbuf_tensor(n, sh, dt))
        q = sb("win_q", [P, 2, NH // 2, W])
        kd = sb("win_k", [P, 2, NKV, 2 * W])
        v = sb("win_v", [P, 2, 2, NKV * HD])
        dist = sb("win_dist", [P, 2 * W])
        bias = sb("win_bias", [P, NH, 2 * W])
        sc = sb("win_scores", [P, 2, NH, 2 * W])
        pt = sb("win_pt", [P, NH, 2, W])
        sink = sb("win_sink", [P, NH])
        mx, nm = sb("win_max", [P, 2, NH]), sb("win_nmax", [P, 2, NH])
        den, es, rd = sb("win_den", [P, 2, NH]), sb("win_es", [P, 2, NH]), sb("win_rd", [P, 2, NH])
        oc = sb("win_out", [P, 2, KD, W])
        y = sb("y_all", [P, XT, T])
        wd = sb("w_down", [P, 2, XT, P])
        dg = sb("down_gate", [P, NSPLIT, NW])
        keys = lambda first: slice(W, 2 * W) if first else slice(0, 2 * W)
        with nc.Block() as block:
            @block.sync
            def _(sp):
                sp.dma_start(sink[:, :], a["attn_sinks"].to_broadcast([P, NH])).then_inc(s["sink_ready"], 16)
                k_src = e.qk_cols[NH // 2:QKT].rearrange("a (b d) t -> d (a b) t", d=HD)

                def load_qk(n, par, first=False):
                    sp.wait_ge(s["qk_free"], n + 1)
                    ready = s[f"qk_ready{par}"]
                    sp.dma_start(q[:, par], e.qk_cols[0:NH // 2, :, bass.ds(n * W, W)].rearrange("h p t -> p h t")).then_inc(ready, 16)
                    for half in range(2):
                        src = k_src[:, :, 0:W] if first else k_src[:, :, bass.ds(n * W + (-W), 2 * W)]
                        sp.dma_start(kd[half * HD:(half + 1) * HD, par, :, keys(first)], src).then_inc(ready, 16)

                def load_v(n, par, first=False):
                    sp.wait_ge(s["v_free"], n + 1)
                    if first:
                        sp.dma_start(v[:, par, 1], e.vdt_rows[0:W, 0:NKV * HD]).then_inc(s[f"v_ready{par}"], 16)
                    else:
                        sp.dma_start(v[:, par], e.vdt_rows[bass.ds(n * W + (-W), 2 * W), 0:NKV * HD].rearrange("(s p) c -> p s c", p=P)).then_inc(s[f"v_ready{par}"], 16)

                def load_down(m, par):
                    sp.wait_ge(s["wd_free"], m + 1)
                    sp.dma_start(wd[:, par], a["w_ssd_down"][0][:, bass.ds(m * P, P)].rearrange("(k p) c -> p k c", p=P)).then_inc(s[f"wd_ready{par}"], 16)

                one = lambda ap, m, part: ap[bass.ds(m, 1)].rearrange("o p t -> (o p) t")[:, part * NW:(part + 1) * NW]

                def load_gate(m, part):
                    sp.dma_start(dg[:, part], one(e.gate_cols, m, part)).then_inc(gate_ready[part], 16)

                def step(n, par, more=True, last=False):
                    if more:
                        load_qk(n + 2, par)
                    if not last:
                        load_down(n + 1, 1 - par)
                    for part in range(NSPLIT):
                        sp.wait_ge(s["down_out"], n * NSPLIT + (part + 1))
                        sp.dma_start(one(e.down_cols, n, part), dg[:, part]).then_inc(down_stored[part], 16)
                    if more:
                        load_v(n + 2, par)
                    for part in range(NSPLIT):
                        sp.wait_ge(down_stored[part], n * 16 + 16)
                        if not last:
                            load_gate(n + 1, part)
                load_qk(0, 0, first=True)
                load_v(0, 0, first=True)
                load_qk(1, 1)
                load_down(0, 0)
                for i in range(4):
                    sp.dma_start(y[:, 4 * i:4 * i + 4], e.y_cols[4 * i:4 * i + 4].rearrange("f p t -> p f t")).then_inc(y_ready[i], 16)
                load_v(1, 1)
                for part in range(NSPLIT):
                    load_gate(0, part)
                with sp.Fori(0, (NT - 2) // 2) as i:
                    for par in range(2):
                        step(i * 2 + par, par)
                step(NT - 2, 0, more=False)
                step(NT - 1, 1, more=False, last=True)

            @block.gpsimd
            def _(pool):
                pool.iota(dist[:, :], pattern=[[-1, 2 * W]], base=W, channel_multiplier=1, allow_small_or_imprecise_dtypes=True).then_inc(s["bias_made"], 1)
                pool.wait_ge(s["bias_scaled"], 1)
                pool.affine_select(out=bias[:, :, :], in_=bias[:, :, :], compare_op=ALU.is_ge, fill=NEG, base=W,
                                   pattern=[[0, NH], [-1, 2 * W]], channel_multiplier=1)
                pool.drain()
                pool.affine_select(out=bias[:, :, :], in_=bias[:, :, :], compare_op=ALU.is_ge, fill=NEG, base=0,
                                   pattern=[[0, NH], [1, 2 * W]], channel_multiplier=-1).then_inc(s["bias_masked"], 1)

                def scale(n, par, k):
                    ks = keys(isinstance(n, int) and n == 0)
                    pool.wait_ge(s["recip_ready"], n + 1)
                    pool.tensor_tensor(sc[:, par, :, ks], sc[:, par, :, ks], bc(rd[:, par].unsqueeze(2), [P, NH, ks.stop - ks.start]),
                                       ALU.mult).then_inc(s["p_ready"], 1)
                pairs(pool, scale)

            @block.tensor
            def _(pe):
                pe.sem_inc(s["qk_free"], 2)
                pe.sem_inc(s["v_free"], 2)
                pe.sem_inc(s["sc_free"], 2)
                pe.sem_inc(s["wd_free"], 2)

                def down(m, par, part, ks, k=0):
                    for kk in ks:
                        if kk == 0:
                            pe.wait_ge(s["down_free"], m * NSPLIT + (part + 1))
                            if part == 0:
                                pe.wait_ge(s[f"wd_ready{par}"], k * 16 + 16)
                        if isinstance(m, int) and m == 0 and part == 0 and kk % 4 == 0:
                            pe.wait_ge(y_ready[kk // 4], 16)
                        last = pe.matmul(ps[:, 2 + (par + part) % 2, 0:NW], wd[:, par, kk], y[:, kk, part * NW:(part + 1) * NW],
                                         start=(kk == 0), stop=(kk == XT - 1))
                    if kk == XT - 1:
                        last.then_inc(s["down_made"], 1)
                        if part == NSPLIT - 1:
                            pe.drain().then_inc(s["wd_free"], 1)

                def scores(n, par, first, k):
                    pe.wait_ge(s[f"qk_ready{par}"], k * 48 + 48)
                    for g in range(NH // 2):
                        if not first:
                            down(n + (-1), 1 - par, 0, range(2 * g, 2 * g + 2), k - 1 + par)
                        pe.wait_ge(s["s_free"], n * (NH // 2) + (g + 1))
                        for j in range(2):
                            h, half = 4 * (g // 2) + 2 * j + g % 2, slice(g % 2 * HD, (g % 2 + 1) * HD)
                            last = pe.matmul(ps[:, g % 2, j * 2 * W + keys(first).start:j * 2 * W + 2 * W], q[half, par, h // 2],
                                             kd[half, par, h // GQA, keys(first)], start=True, stop=True)
                        last.then_inc(s["s_ready"], 1)
                    pe.drain().then_inc(s["qk_free"], 1)

                def weigh(n, par, first, k, final=False):
                    if final:
                        down(n, par, 0, range(XT), k)
                    pe.wait_ge(s["p_ready"], n + 1)
                    pe.wait_ge(s["pt_free"], n + 1)
                    for g in range(NH // 2):
                        low = g % 2 == 0
                        pe.wait_ge(s["t_low_free"] if low else s["t_high_free"], n * (NH // 4) + (g // 2 + 1))
                        for j in range(2):
                            for b in range(1 if first else 0, 2):
                                last = pe.transpose(ps[:, 4 + g % 2, (2 * j + b) * W:(2 * j + b + 1) * W],
                                                    sc[:, par, 2 * g + j, b * W:(b + 1) * W], e.ident[:, :])
                        last.then_inc(s["t_ready"], 1)
                        down(n, par, 1, range(2 * g, 2 * g + 2))
                    pe.drain().then_inc(s["sc_free"], 1)
                    down(n, par, 2, range(XT))
                    pe.wait_ge(s[f"v_ready{par}"], k * 16 + 16)
                    pe.wait_ge(s["pt_low"], n * (NH // 4) + NH // 4)
                    pe.wait_ge(s["pt_high"], n * (NH // 4) + NH // 4)
                    pe.wait_ge(s["o_free"], n + 1)
                    for h in range(NH):
                        g, half = h // 2, slice((h % 2) * HD, (h % 2 + 1) * HD)
                        for b in range(1 if first else 0, 2):
                            last = pe.matmul(ps[half, 6 + g // 4, (g % 4) * W:(g % 4 + 1) * W],
                                             v[:, par, b, (h // GQA) * HD:(h // GQA + 1) * HD], pt[:, h, b],
                                             start=(b == 1 if first else b == 0), stop=(b == 1))
                    last.then_inc(s["o_ready"], 1)
                    pe.drain().then_inc(s["v_free"], 1)

                scores(0, 0, True, 0)
                scores(1, 1, False, 0)
                weigh(0, 0, True, 0)
                with pe.Fori(0, (NT - 2) // 2) as i:
                    scores(i * 2 + 2, 0, False, i + 1)
                    weigh(i * 2 + 1, 1, False, i)
                    scores(i * 2 + 3, 1, False, i + 1)
                    weigh(i * 2 + 2, 0, False, i + 1)
                weigh(NT - 1, 1, False, NT // 2 - 1, final=True)

            @block.scalar
            def _(act):
                act.sem_inc(s["t_high_free"], 1)
                act.sem_inc(s["o_free"], 1)

                def exps(n, par, first):
                    act.wait_ge(s["max_ready"], n + 1)
                    for h in range(NH):
                        act.activation(sc[:, par, h, keys(first)], sc[:, par, h, keys(first)], ACT.Exp,
                                       bias=nm[:, par, h:h + 1], accum_out=den[:, par, h:h + 1])
                    act.activation(es[:, par], es[:, par], ACT.Exp).then_inc(s["exp_ready"], 1)

                def out(n, par, first, earlier):
                    for g in range(NH // 4):
                        act.wait_ge(s["t_ready"], n * (NH // 2) + (2 * g + 2))
                        src = ps[:, 5, :].rearrange("p (h b c) -> p h b c", h=2, b=2)
                        b0 = 1 if first else 0
                        act.activation(pt[:, 4 * g + 2:4 * g + 4, b0:2], src[:, :, b0:2], ACT.Copy).then_inc(s["pt_high"], 1)
                        act.drain().then_inc(s["t_high_free"], 1)
                    act.wait_ge(s["o_ready"], n + 1)
                    act.wait_ge(s[f"stored{par}"], earlier * 16)
                    act.activation(oc[:, par].rearrange("p (b k) c -> p b (k c)", b=2), ps[:, 6:8, :], ACT.Copy).then_inc(s["out_ready"], 1)
                    act.drain().then_inc(s["o_free"], 1)
                    act.sem_inc(s["pt_free"], 1)
                    act.dma_start(e.att_cols[:, :, bass.ds(n * W, W)].rearrange("f p t -> p f t"), oc[:, par]).then_inc(s[f"stored{par}"], 16)

                act.sem_inc(s["pt_free"], 1)
                exps(0, 0, True)
                exps(1, 1, False)
                out(0, 0, True, 0)
                with act.Fori(0, (NT - 2) // 2) as i:
                    exps(i * 2 + 2, 0, False)
                    out(i * 2 + 1, 1, False, i)
                    exps(i * 2 + 3, 1, False)
                    out(i * 2 + 2, 0, False, i + 1)
                out(NT - 1, 1, False, NT // 2 - 1)
                for b in range(2):
                    act.wait_ge(s[f"stored{b}"], 16 * NT // 2)

            @block.vector
            def _(dve):
                dve.wait_ge(s["bias_made"], 1)
                for h in range(NH):
                    last = dve.tensor_scalar(bias[:, h], dist[:, :], -(2.0 ** (-8.0 * (h + 1) / NH)), None, ALU.mult)
                last.then_inc(s["bias_scaled"], 1)
                dve.wait_ge(s["bias_masked"], 1)
                dve.wait_ge(s["sink_ready"], 16)
                dve.sem_inc(s["s_free"], 2)
                dve.sem_inc(s["down_free"], 2)
                dve.sem_inc(s["t_low_free"], 1)

                def gated(m, par, part):
                    dve.wait_ge(s["down_made"], m * NSPLIT + (part + 1))
                    dve.wait_ge(gate_ready[part], m * 16 + 16)
                    dve.tensor_tensor(dg[:, part], ps[:, 2 + (par + part) % 2, 0:NW], dg[:, part], ALU.mult).then_inc(s["down_out"], 1)
                    dve.drain().then_inc(s["down_free"], 1)

                def maxima(n, par, first):
                    ks = keys(first)
                    dve.wait_ge(s["sc_free"], n + 1)
                    for g in range(NH // 2):
                        dve.wait_ge(s["s_ready"], n * (NH // 2) + (g + 1))
                        hh = slice(4 * (g // 2) + g % 2, 4 * (g // 2) + g % 2 + 3, 2)
                        dve.scalar_tensor_tensor(out=sc[:, par, hh, ks], in0=ps[:, g % 2, :].rearrange("p (h c) -> p h c", h=2)[:, :, ks],
                                                 scalar=SCALE, in1=bias[:, hh, ks], op0=ALU.mult, op1=ALU.add)
                        dve.drain().then_inc(s["s_free"], 1)
                    dve.tensor_reduce(mx[:, par], sc[:, par, :, ks], AX.X, ALU.max)
                    dve.drain()
                    dve.tensor_tensor(mx[:, par], mx[:, par], sink[:, :], ALU.max)
                    dve.drain()
                    dve.tensor_scalar(nm[:, par], mx[:, par], -1.0, None, ALU.mult)
                    dve.tensor_tensor(es[:, par], sink[:, :], mx[:, par], ALU.subtract).then_inc(s["max_ready"], 1)
                    if not first:
                        gated(n + (-1), 1 - par, 0)

                def normalise(n, par):
                    dve.wait_ge(s["exp_ready"], n + 1)
                    dve.tensor_tensor(den[:, par], den[:, par], es[:, par], ALU.add)
                    dve.drain()
                    dve.reciprocal(rd[:, par], den[:, par]).then_inc(s["recip_ready"], 1)

                def copy(n, par, first):
                    final = isinstance(n, int) and n == NT - 1
                    if final:
                        gated(n, par, 0)
                    if first:
                        normalise(n, par)
                    b0 = 1 if first else 0
                    for g in range(NH // 4):
                        dve.wait_ge(s["t_ready"], n * (NH // 2) + (2 * g + 1))
                        src = ps[:, 4, :].rearrange("p (h b c) -> p h b c", h=2, b=2)
                        dve.tensor_copy(pt[:, 4 * g:4 * g + 2, b0:2], src[:, :, b0:2]).then_inc(s["pt_low"], 1)
                        dve.drain().then_inc(s["t_low_free"], 1)
                    if not final:
                        normalise(n + 1, 1 - par)
                    gated(n, par, 1)
                    gated(n, par, 2)
                staggered(dve, maxima, copy)


def sample_states(e):
    nc, a, o, ps = e.nc, e.a, e.o, e.ps
    s = {n: e.sem("sconv_" + n) for n in ("u", "silu", "loaded", "turned", "rows", "stored", "copied")}
    keep = lambda n, sh: e.mix.enter_context(nc.sbuf_tensor(n, sh, F32))
    e.sc_cols = keep("sc_cols", [P, CT, NB])
    e.sqk_rows = keep("sqk_rows", [NB, (NH + NKV) * HD])
    e.sbc_rows = keep("sbc_rows", [NB, 2 * NG * NS])
    e.sv_rows = keep("sv_rows", [NB, NKV * HD])
    with ExitStack() as st:
        sb = lambda n, sh: st.enter_context(nc.sbuf_tensor(n, sh, F32))
        acc, term = sb("sconv_acc", [P, CT, NB]), sb("sconv_term", [P, CT, NB])
        trows = sb("tail_rows", [CK - 1 + NB, CD])
        qk_s = sb("qk_sample", [P, QKT, NB])
        k_last = sb("k_last", [P, 2, P])
        k_rows = sb("k_last_rows", [P, NKV * HD])
        block = st.enter_context(nc.Block())
        KW = NKV * HD

        @block.sync
        def _(sp):
            sp.dma_start(qk_s[:, :, :], e.qk_cols[:, :, SEQ:T].rearrange("f p t -> p f t")).then_inc(s["loaded"], 16)
            sp.dma_start(k_last[:, :, :], e.qk_cols[NH // 2:QKT, :, SEQ - W:SEQ].rearrange("f p t -> p f t")).then_inc(s["loaded"], 16)
            sp.dma_start(e.sv_rows[:, :], e.vdt_rows[SEQ:T, 0:KW]).then_inc(s["loaded"], 16)
            sp.dma_start(o["p_cache_win_v"].rearrange("o b s v d -> (o b s) (v d)"), e.vdt_rows[SEQ - W:SEQ, 0:KW]).then_inc(s["copied"], 16)
            for c in "kv":
                sp.dma_start(o["s_cache_win_" + c].rearrange("o b s v d -> (o b) s (v d)")[:, 0:W - 1],
                             a["cache_win_" + c].rearrange("o b s v d -> (o b) s (v d)")[:, 1:W]).then_inc(s["copied"], 16)
            sp.dma_start(o["s_cache_win_v"].rearrange("o b s v d -> (o b) s (v d)")[:, W - 1], e.vdt_rows[SEQ:T, 0:KW]).then_inc(s["copied"], 16)
            sp.dma_start(o["s_state_conv"][0, :, 0:CK - 2], a["state_conv"][0, :, 1:CK - 1]).then_inc(s["copied"], 16)
            sp.wait_ge(s["rows"], 1)
            sp.dma_start(o["p_state_conv"].rearrange("o b k c -> (o b k) c"), trows[0:CK - 1, :]).then_inc(s["copied"], 16)
            sp.dma_start(o["s_state_conv"][0, :, CK - 2], trows[CK - 1:CK - 1 + NB, :]).then_inc(s["copied"], 16)
            sp.wait_ge(s["rows"], 2)
            sp.dma_start(o["p_cache_win_k"].rearrange("o b s v d -> (o b s) (v d)"), k_rows[:, :]).then_inc(s["copied"], 16)
            sp.dma_start(o["s_cache_win_k"].rearrange("o b s v d -> (o b) s (v d)")[:, W - 1], e.sqk_rows[:, NH * HD:]).then_inc(s["copied"], 16)
            sp.wait_ge(s["copied"], 16 * 9)
            sp.wait_ge(s["loaded"], 48)

        @block.vector
        def _(dve):
            new = e.tails[:, :, CK - 1:]
            wt = lambda k: bc(e.cvec[:, :, CR_W + k:CR_W + k + 1], [P, CT, NB])
            dve.tensor_tensor(acc[:, :, :], new, wt(CK - 1), ALU.mult)
            dve.drain()
            dve.tensor_tensor(acc[:, :, :], acc[:, :, :], bc(e.cvec[:, :, CR_B:CR], [P, CT, NB]), ALU.add)
            for k in range(CK - 1):
                past = e.cvec[:, :, CR_STATE:CR_W].rearrange("p c (b k) -> p c b k", k=CK - 1)[:, :, :, k]
                dve.tensor_tensor(term[:, :, :], past, wt(k), ALU.mult)
                dve.drain()
                dve.tensor_tensor(acc[:, :, :], acc[:, :, :], term[:, :, :], ALU.add)
                dve.drain()
            dve.sem_inc(s["u"], 1)
            dve.wait_ge(s["turned"], 1)
            dve.tensor_copy(trows[:, :], ps[0:CK - 1 + NB, 0:6, :].rearrange("p b c -> p (b c)")).then_inc(s["rows"], 1)
            dve.drain()
            dve.wait_ge(s["turned"], 2)
            dve.tensor_copy(e.sqk_rows[:, 0:1024], ps[0:NB, 0:2, :].rearrange("p b c -> p (b c)"))
            dve.tensor_copy(e.sqk_rows[:, 1024:1280], ps[0:NB, 2, 0:256])
            dve.tensor_copy(k_rows[:, :], ps[:, 3, 0:256])
            dve.drain().then_inc(s["rows"], 1)
            dve.wait_ge(s["turned"], 3)
            dve.tensor_copy(e.sbc_rows[:, :], ps[0:NB, 4:6, :].rearrange("p b c -> p (b c)"))

        @block.scalar
        def _(act):
            act.wait_ge(s["u"], 1)
            act.activation(e.sc_cols[:, :, :], acc[:, :, :], ACT.Silu).then_inc(s["silu"], 1)

        @block.tensor
        def _(pe):
            for c in range(CT):
                last = pe.transpose(ps[0:CK - 1 + NB, c // 4, (c % 4) * P:(c % 4 + 1) * P], e.tails[:, c], e.ident[:, :])
            last.then_inc(s["turned"], 1)
            pe.wait_ge(s["loaded"], 48)
            pe.wait_ge(s["rows"], 1)
            for c in range(QKT):
                pe.transpose(ps[0:NB, c // 4, (c % 4) * P:(c % 4 + 1) * P], qk_s[:, c], e.ident[:, :])
            for c in range(2):
                last = pe.transpose(ps[:, 3, c * P:(c + 1) * P], k_last[:, c], e.ident[:, :])
            last.then_inc(s["turned"], 1)
            pe.wait_ge(s["silu"], 1)
            for c in range(2 * NG):
                last = pe.transpose(ps[0:NB, 4 + c // 4, (c % 4) * P:(c % 4 + 1) * P], e.sc_cols[:, XT + c], e.ident[:, :])
            last.then_inc(s["turned"], 1)


def sample_ssd(e):
    nc, a, o, ps = e.nc, e.a, e.o, e.ps
    names = ("sel_made", "loaded", "dec", "dtT", "dtT_copied", "spread", "spread_copied", "xdt_ready", "bc_ready", "bc_free",
             "h_ready0", "h_ready1", "h_scaled", "h_new", "h_stored0", "h_stored1", "zT", "zT_copied", "sq", "total", "meaned", "rooted", "y_ready", "y_stored")
    s = {n: e.sem("sssd_" + n) for n in names}
    e.onehot = e.mix.enter_context(nc.sbuf_tensor("onehot", [NB, NB, P], F32))
    with ExitStack() as st:
        sb = lambda n, sh: st.enter_context(nc.sbuf_tensor(n, sh, F32))
        sel = sb("head_sel", [HS, DI])
        decay = sb("sdecay", [NB, HS])
        dtT = sb("sdtT", [HS, 2 * NB + 1])
        spread = sb("sspread", [P, XT, 2 * NB + 1])
        zr = sb("sz_rows", [NB, DI])
        xdt = sb("sxdt", [P, XT, NB])
        h = sb("sh", [P, 2, XT, NS])
        t1 = sb("st1", [P, XT, NS])
        t2 = sb("st2", [P, XT, NS])
        y = sb("sy", [P, XT, NB])
        y2 = sb("sy2", [P, XT, NB])
        yb = sb("syb", [P, NB, XT])
        ms, rs = sb("sms", [P, NG, NB]), sb("srs", [P, NG, NB])
        mh = sb("smh", [P, NG, NB])
        block = st.enter_context(nc.Block())
        st_in = a["state_ssd"][0].rearrange("b h c n -> b (h c) n").rearrange("b (k p) n -> b p k n", p=P)
        st_out = o["s_state_ssd"][0].rearrange("b h c n -> b (h c) n").rearrange("b (k p) n -> b p k n", p=P)

        @block.gpsimd
        def _(pool):
            pool.memset(sel[:, :], 1.0)
            pool.memset(e.onehot[:, :, :], 0.0)
            pool.memset(mh[:, :, :], -0.5)
            pool.drain()
            pool.affine_select(out=sel[:, :], in_=sel[:, :], compare_op=ALU.is_ge, fill=0.0, base=0, pattern=[[1, DI]], channel_multiplier=-HP)
            pool.affine_select(out=e.onehot[:, :, :], in_=e.onehot[:, :, :], compare_op=ALU.not_equal, fill=1.0, base=0,
                               pattern=[[-1, NB], [0, P]], channel_multiplier=1)
            pool.drain()
            pool.affine_select(out=sel[:, :], in_=sel[:, :], compare_op=ALU.is_ge, fill=0.0, base=HP - 1, pattern=[[-1, DI]], channel_multiplier=HP)
            pool.drain().then_inc(s["sel_made"], 1)
            pool.wait_ge(s["spread_copied"], 1)
            for b in range(NB):
                pool.wait_ge(s[f"h_ready{b % 2}"], 16 * (b // 2 + 1))
                pool.tensor_tensor(h[:, b % 2], h[:, b % 2], bc(spread[:, :, NB + b:NB + b + 1], [P, XT, NS]), ALU.mult).then_inc(s["h_scaled"], 1)
            pool.wait_ge(s["meaned"], 1)
            pool.tensor_tensor(rs[:, :, :], ms[:, :, :], mh[:, :, :], ALU.pow).then_inc(s["rooted"], 1)

        @block.sync
        def _(sp):
            sp.dma_start(dtT[:, 2 * NB:2 * NB + 1], a["d_skip"].rearrange("o h -> h o")).then_inc(s["loaded"], 16)
            sp.dma_start(zr[:, :], e.z_rows[SEQ:T, :]).then_inc(s["loaded"], 16)
            for b in range(NB):
                if b >= 2:
                    sp.wait_ge(s[f"h_stored{b % 2}"], 16 * (b // 2))
                    sp.wait_ge(s["bc_free"], b + 1)
                sp.dma_start(h[:, b % 2], st_in[b]).then_inc(s[f"h_ready{b % 2}"], 16)
            sp.wait_ge(s["y_ready"], 1)
            sp.dma_start(e.y_cols[:, :, SEQ:T].rearrange("f p t -> p f t"), y2[:, :, :]).then_inc(s["y_stored"], 16)
            sp.wait_ge(s["y_stored"], 16)

        @block.scalar
        def _(act):
            act.activation(decay[:, :], e.da[0:NB, NT, :], ACT.Exp).then_inc(s["dec"], 1)
            for b in range(NB):
                act.wait_ge(s["h_new"], b + 1)
                act.dma_start(st_out[b], h[:, b % 2]).then_inc(s[f"h_stored{b % 2}"], 16)
            for q in range(2):
                act.wait_ge(s[f"h_stored{q}"], 16 * NB // 2)

        @block.tensor
        def _(pe):
            pe.wait_ge(s["dec"], 1)
            pe.transpose(ps[0:HS, 0, 0:NB], e.dt[0:NB, NT, :], e.ident[0:NB, 0:NB])
            pe.transpose(ps[0:HS, 0, NB:2 * NB], decay[:, :], e.ident[0:NB, 0:NB]).then_inc(s["dtT"], 1)
            pe.wait_ge(s["loaded"], 32)
            for k in range(XT):
                last = pe.transpose(ps[:, 2, k * NB:(k + 1) * NB], zr[:, k * P:(k + 1) * P], e.ident[0:NB, 0:NB])
            last.then_inc(s["zT"], 1)
            pe.wait_ge(s["dtT_copied"], 1)
            pe.wait_ge(s["sel_made"], 1)
            for k in range(XT):
                last = pe.matmul(ps[:, 1, k * 32:k * 32 + 2 * NB + 1], sel[:, k * P:(k + 1) * P], dtT[:, :], start=True, stop=True)
            last.then_inc(s["spread"], 1)
            for b in range(NB):
                pe.wait_ge(s["bc_free"], b + 1)
                for q in range(2):
                    last = pe.matmul(ps[:, 4 + 2 * (b % 2) + q, :], e.onehot[:, b], e.sbc_rows[:, q * 512:(q + 1) * 512], start=True, stop=True)
                last.then_inc(s["bc_ready"], 1)
            pe.wait_ge(s["sq"], 1)
            pe.matmul(ps[:, 3, 0:NG * NB], e.ones[:, :], ms[:, :, :].rearrange("p g b -> p (g b)"), start=True, stop=True).then_inc(s["total"], 1)

        @block.vector
        def _(dve):
            dve.sem_inc(s["bc_free"], 2)
            dve.wait_ge(s["dtT"], 1)
            dve.wait_ge(s["loaded"], 32)
            dve.tensor_copy(dtT[:, 0:2 * NB], ps[0:HS, 0, 0:2 * NB]).then_inc(s["dtT_copied"], 1)
            dve.wait_ge(s["spread"], 1)
            dve.tensor_copy(spread[:, :, :], ps[:, 1, :].rearrange("p (k c) -> p k c", c=32)[:, :, 0:2 * NB + 1])
            dve.drain().then_inc(s["spread_copied"], 1)
            dve.tensor_tensor(xdt[:, :, :], e.sc_cols[:, 0:XT, :], spread[:, :, 0:NB], ALU.mult)
            dve.drain()
            four = lambda ap: ap.rearrange("p (g k) n -> p g k n", g=NG)
            for b in range(NB):
                dve.wait_ge(s["bc_ready"], b + 1)
                bank = lambda q: bc(ps[:, 4 + 2 * (b % 2) + q, :].rearrange("p (g n) -> p g n", g=NG).unsqueeze(2), [P, NG, XT // NG, NS])
                dve.tensor_tensor(four(t1[:, :, :]), bank(0), bc(four(xdt[:, :, b:b + 1]), [P, NG, XT // NG, NS]), ALU.mult)
                dve.drain()
                dve.wait_ge(s["h_scaled"], b + 1)
                dve.tensor_tensor(h[:, b % 2], h[:, b % 2], t1[:, :, :], ALU.add).then_inc(s["h_new"], 1)
                dve.drain()
                dve.tensor_tensor(four(t2[:, :, :]), four(h[:, b % 2]), bank(1), ALU.mult)
                dve.drain().then_inc(s["bc_free"], 1)
                dve.tensor_reduce(yb[:, b], t2[:, :, :], AX.X, ALU.add)
                dve.drain()
            ybt = yb[:, :, :].rearrange("p b k -> p k b")
            dve.tensor_tensor(y[:, :, :], e.sc_cols[:, 0:XT, :], bc(spread[:, :, 2 * NB:2 * NB + 1], [P, XT, NB]), ALU.mult)
            dve.drain()
            dve.tensor_tensor(y[:, :, :], y[:, :, :], ybt, ALU.add)
            dve.drain()
            dve.wait_ge(s["zT"], 1)
            dve.tensor_tensor(y[:, :, :], y[:, :, :], ps[:, 2, 0:XT * NB].rearrange("p (k b) -> p k b", b=NB), ALU.mult)
            dve.drain()
            dve.tensor_tensor(y2[:, :, :], y[:, :, :], y[:, :, :], ALU.mult)
            dve.drain()
            dve.tensor_reduce(ms[:, :, :], y2[:, :, :].rearrange("p (g k) b -> p g b k", g=NG), AX.X, ALU.add).then_inc(s["sq"], 1)
            dve.wait_ge(s["total"], 1)
            dve.tensor_scalar(ms[:, :, :].rearrange("p g b -> p (g b)"), ps[:, 3, 0:NG * NB], NG / DI, EPS, ALU.mult, ALU.add).then_inc(s["meaned"], 1)
            dve.wait_ge(s["rooted"], 1)
            dve.tensor_tensor(y2[:, :, :].rearrange("p (g k) b -> p g k b", g=NG), y[:, :, :].rearrange("p (g k) b -> p g k b", g=NG),
                              bc(rs[:, :, :].unsqueeze(2), [P, NG, XT // NG, NB]), ALU.mult)
            dve.drain()
            dve.tensor_tensor(y2[:, :, :], y2[:, :, :], bc(e.gvec[:, G_SSD:G_SSD + XT].unsqueeze(2), [P, XT, NB]), ALU.mult).then_inc(s["y_ready"], 1)


def sample_window(e):
    nc, a, o, ps = e.nc, e.a, e.o, e.ps
    names = ("loaded", "dist", "q_ready", "q_free", "new_made", "sT", "turned", "cols", "maxed", "exped", "normed", "pT", "pT_copied",
             "pn", "pn_copied", "o_ready", "o_copied", "stored")
    s = {n: e.sem("swin_" + n) for n in names}
    SCALE = HD ** -0.5
    R = NB * NH
    with ExitStack() as st:
        sb = lambda n, sh: st.enter_context(nc.sbuf_tensor(n, sh, F32))
        kc, vc = sb("swin_k", [P, NB, NKV * HD]), sb("swin_v", [P, NB, NKV * HD])
        sink = sb("swin_sink", [NB, NH])
        prod = sb("swin_prod", [P, NKV, GQA, HD])
        prod_new = sb("swin_prod_new", [NB, NKV, GQA, HD])
        s_new = sb("swin_s_new", [NB, NH])
        own = sb("swin_own", [NB, 2, NB, NH])
        sT = sb("swin_sT", [P, NB, NH])
        dist, bias = sb("swin_dist", [P, 1]), sb("swin_bias", [P, NH])
        sc = sb("swin_sc", [R, W + 2])
        mx, nm, den, rd = sb("swin_mx", [R, 1]), sb("swin_nm", [R, 1]), sb("swin_den", [R, 1]), sb("swin_rd", [R, 1])
        pT = sb("swin_pT", [P, NB, NH])
        pn_row = sb("swin_pn_row", [1, R])
        pn = sb("swin_pn", [NB, NB, NH])
        oc = sb("swin_oc", [P, NH // 2, NB])
        block = st.enter_context(nc.Block())
        rows4 = lambda ap: ap.rearrange("p (v g d) -> p v g d", v=NKV, g=GQA)

        @block.sync
        def _(sp):
            sp.dma_start(kc[:, :, :], a["cache_win_k"][0].rearrange("b s v d -> s b (v d)")).then_inc(s["loaded"], 16)
            sp.dma_start(vc[:, :, :], a["cache_win_v"][0].rearrange("b s v d -> s b (v d)")).then_inc(s["loaded"], 16)
            sp.dma_start(sink[:, :], a["attn_sinks"].to_broadcast([NB, NH])).then_inc(s["loaded"], 16)
            sp.wait_ge(s["o_copied"], 1)
            sp.dma_start(e.att_cols[:, :, SEQ:T].rearrange("f p t -> p f t"), oc[:, :, :]).then_inc(s["stored"], 16)
            sp.wait_ge(s["stored"], 16)

        @block.gpsimd
        def _(pool):
            pool.iota(dist[:, :], pattern=[[0, 1]], base=W, channel_multiplier=-1, allow_small_or_imprecise_dtypes=True).then_inc(s["dist"], 1)

        @block.tensor
        def _(pe):
            for b in range(NB):
                pe.wait_ge(s["q_free"], b + 1)
                for q in range(2):
                    last = pe.matmul(ps[:, 2 * (b % 2) + q, :], e.onehot[:, b], e.sqk_rows[:, q * 512:(q + 1) * 512], start=True, stop=True)
                last.then_inc(s["q_ready"], 1)
            pe.wait_ge(s["new_made"], 1)
            for q in range(2):
                pe.matmul(ps[0:R, 4, q:q + 1], own[:, q].rearrange("p b h -> p (b h)"), e.ones[0:NB, 0:1], start=True, stop=True)
            pe.wait_ge(s["sT"], 1)
            pe.transpose(ps[0:R, 5, 0:W], sT[:, :, :].rearrange("p b h -> p (b h)"), e.ident[:, :]).then_inc(s["turned"], 1)
            pe.wait_ge(s["normed"], 1)
            pe.transpose(ps[:, 6, 0:R], sc[:, 0:W], e.ident[:, :])
            pe.transpose(ps[0:1, 7, 0:R], sc[:, W:W + 1], e.ident[:, :]).then_inc(s["pT"], 1)
            pe.wait_ge(s["pT_copied"], 1)
            pe.matmul(ps[0:NB, 4, 0:R], e.ones[0:1, 0:NB], pn_row[:, :], start=True, stop=True).then_inc(s["pn"], 1)
            pe.wait_ge(s["pn_copied"], 1)
            out = ps[:, 5, 0:(NH // 2) * NB].rearrange("p (k b) -> p k b", b=NB)
            for b in range(NB):
                for v in range(NKV):
                    for half in range(2):
                        dst = out[half * HD:(half + 1) * HD, 2 * v:2 * v + 2, b]
                        heads = slice(GQA * v + half, GQA * v + half + 3, 2)
                        pe.matmul(dst, vc[:, b, v * HD:(v + 1) * HD], pT[:, b, heads], start=True, stop=False)
                        last = pe.matmul(dst, e.sv_rows[:, v * HD:(v + 1) * HD], pn[:, b, heads], start=False, stop=True)
            last.then_inc(s["o_ready"], 1)

        @block.scalar
        def _(act):
            act.wait_ge(s["maxed"], 1)
            act.activation(sc[:, :], sc[:, :], ACT.Exp, bias=nm[:, :], accum_out=den[:, :]).then_inc(s["exped"], 1)

        @block.vector
        def _(dve):
            dve.sem_inc(s["q_free"], 2)
            dve.wait_ge(s["loaded"], 48)
            dve.wait_ge(s["dist"], 1)
            for hh in range(NH):
                dve.tensor_scalar(bias[:, hh:hh + 1], dist[:, :], -(2.0 ** (-8.0 * (hh + 1) / NH)), None, ALU.mult)
            dve.tensor_tensor(prod_new[:, :, :, :], rows4(e.sqk_rows[:, 0:NH * HD]),
                              bc(e.sqk_rows[:, NH * HD:].rearrange("p (v d) -> p v d", v=NKV).unsqueeze(2), [NB, NKV, GQA, HD]), ALU.mult)
            dve.drain()
            dve.tensor_reduce(s_new[:, :], prod_new[:, :, :, :].rearrange("p v g d -> p (v g) d"), AX.X, ALU.add)
            dve.drain()
            dve.tensor_scalar(s_new[:, :], s_new[:, :], SCALE, None, ALU.mult)
            dve.drain()
            diag = bc(e.onehot[:, :, 0:1], [NB, NB, NH])
            dve.tensor_tensor(own[:, 0], bc(s_new[:, :].unsqueeze(1), [NB, NB, NH]), diag, ALU.mult)
            dve.tensor_tensor(own[:, 1], bc(sink[:, :].unsqueeze(1), [NB, NB, NH]), diag, ALU.mult).then_inc(s["new_made"], 1)
            for b in range(NB):
                dve.wait_ge(s["q_ready"], b + 1)
                bank = rows4(ps[:, 2 * (b % 2):2 * (b % 2) + 2, :].rearrange("p b c -> p (b c)"))
                dve.tensor_tensor(prod[:, :, :, :], bank, bc(kc[:, b].rearrange("p (v d) -> p v d", v=NKV).unsqueeze(2), [P, NKV, GQA, HD]), ALU.mult)
                dve.drain().then_inc(s["q_free"], 1)
                dve.tensor_reduce(sT[:, b], prod[:, :, :, :].rearrange("p v g d -> p (v g) d"), AX.X, ALU.add)
                dve.drain()
            dve.scalar_tensor_tensor(out=sT[:, :, :], in0=sT[:, :, :], scalar=SCALE, in1=bc(bias[:, :].unsqueeze(1), [P, NB, NH]),
                                     op0=ALU.mult, op1=ALU.add).then_inc(s["sT"], 1)
            dve.wait_ge(s["turned"], 1)
            dve.tensor_copy(sc[:, 0:W], ps[0:R, 5, 0:W])
            dve.tensor_copy(sc[:, W:W + 2], ps[0:R, 4, 0:2])
            dve.drain()
            dve.tensor_reduce(mx[:, :], sc[:, :], AX.X, ALU.max)
            dve.drain()
            dve.tensor_scalar(nm[:, :], mx[:, :], -1.0, None, ALU.mult).then_inc(s["maxed"], 1)
            dve.wait_ge(s["exped"], 1)
            dve.reciprocal(rd[:, :], den[:, :])
            dve.drain()
            dve.tensor_scalar(sc[:, :], sc[:, :], rd[:, :], None, ALU.mult).then_inc(s["normed"], 1)
            dve.wait_ge(s["pT"], 1)
            dve.tensor_copy(pT[:, :, :].rearrange("p b h -> p (b h)"), ps[:, 6, 0:R])
            dve.tensor_copy(pn_row[:, :], ps[0:1, 7, 0:R]).then_inc(s["pT_copied"], 1)
            dve.wait_ge(s["pn"], 1)
            dve.tensor_tensor(pn[:, :, :], ps[0:NB, 4, 0:R].rearrange("p (b h) -> p b h", b=NB), bc(e.onehot[:, :, 0:1], [NB, NB, NH]), ALU.mult)\
                .then_inc(s["pn_copied"], 1)
            dve.wait_ge(s["o_ready"], 1)
            dve.tensor_copy(oc[:, :, :], ps[:, 5, 0:(NH // 2) * NB].rearrange("p (k b) -> p k b", b=NB)).then_inc(s["o_copied"], 1)


def mixer_out(e):
    nc, a, ps = e.nc, e.a, e.ps
    names = ("in_free", "merged", "padded", "mixed", "emptied")
    s = {n: e.sem("mix_" + n) for n in names}
    in_ready = [e.sem(f"mix_in_ready{i}") for i in range(3)]
    w_ready = [e.sem(f"mix_w_ready{i}") for i in range(4)]
    x_ready = [e.sem(f"mix_x_ready{i}") for i in range(3)]
    width = lambda t: P if t < NT else T - SEQ
    with ExitStack() as st:
        sb = lambda n, sh: st.enter_context(nc.sbuf_tensor(n, sh, F32))
        parts = sb("mix_parts", [P, 3, 3, KD, P])
        merged = sb("merged", [P, KD, TP])
        wm = sb("w_mix", [P, KD, D])
        block = st.enter_context(nc.Block())

        @block.gpsimd
        def _(pool):
            pool.memset(e.x[:, NT, :], 0.0).then_inc(s["padded"], 1)
            pool.memset(merged[:, :, T:TP], 0.0).then_inc(s["padded"], 1)

        @block.sync
        def _(sp):
            def load_parts(t):
                if t >= 3:
                    sp.wait_ge(s["in_free"], t - 2)
                for i, src in enumerate((e.down_cols, e.gate_cols[KD:2 * KD], e.att_cols)):
                    sp.dma_start(parts[:, t % 3, i, :, 0:width(t)], src[:, :, t * P:t * P + width(t)].rearrange("f p t -> p f t")).then_inc(in_ready[t % 3], 16)
            load_parts(0)
            for q in range(4):
                sp.dma_start(wm[:, 2 * q:2 * q + 2, :], a["w_mix_out"][0][2 * q * P:(2 * q + 2) * P, :].rearrange("(k p) c -> p k c", p=P)).then_inc(w_ready[q], 16)
            rows = a["x_prompt"][0].rearrange("(t p) d -> p t d", p=P)
            load_parts(1)
            sp.dma_start(e.x[:, 0:4, :], rows[:, 0:4]).then_inc(x_ready[0], 16)
            load_parts(2)
            load_parts(3)
            sp.dma_start(e.x[:, 4:8, :], rows[:, 4:8]).then_inc(x_ready[1], 16)
            sp.wait_ge(s["padded"], 2)
            sp.dma_start(e.x[0:NB, NT, :], a["x_sample"][:, 0, :]).then_inc(x_ready[2], 16)
            for t in range(4, TILES):
                load_parts(t)

        @block.tensor
        def _(pe):
            for t in range(TILES):
                pe.wait_ge(s["merged"], t + 1)
                for half in range(2):
                    u = 2 * t + half
                    if u >= 8:
                        pe.wait_ge(s["emptied"], u - 7)
                    for k in range(KD):
                        if u == 0 and k % 2 == 0:
                            pe.wait_ge(w_ready[k // 2], 16)
                        last = pe.matmul(ps[:, u % 8, :], merged[:, k, t * P:(t + 1) * P], wm[:, k, half * 512:(half + 1) * 512],
                                         start=(k == 0), stop=(k == KD - 1))
                    last.then_inc(s["mixed"], 1)

        @block.vector
        def _(dve):
            def merge(t):
                dve.wait_ge(in_ready[t % 3], 48 * (t // 3 + 1))
                part = lambda i: parts[:, t % 3, i, :, 0:width(t)]
                dve.tensor_tensor(part(2), part(2), part(1), ALU.mult)
                dve.drain()
                dve.tensor_tensor(merged[:, :, t * P:t * P + width(t)], part(2), part(0), ALU.add).then_inc(s["merged"], 1)
                dve.drain().then_inc(s["in_free"], 1)
            dve.wait_ge(s["padded"], 2)
            merge(0)
            merge(1)
            for t in range(TILES):
                if t + 2 < TILES:
                    merge(t + 2)
                if t % 4 == 0:
                    dve.wait_ge(x_ready[t // 4], 16)
                for half in range(2):
                    u = 2 * t + half
                    dve.wait_ge(s["mixed"], u + 1)
                    xs = e.x[:, t, half * 512:(half + 1) * 512]
                    dve.tensor_tensor(xs, xs, ps[:, u % 8, :], ALU.add).then_inc(s["emptied"], 1)


def cross_projections(e, xc, memT):
    nc, a, o, ps = e.nc, e.a, e.o, e.ps
    s = {n: e.sem("cproj_" + n) for n in ("w_ready", "wkv_ready", "q_ready", "q_free", "kv_ready", "kv_copied", "stored", "kT", "kT_copied")}
    with nc.sbuf_tensor("w_cq", [P, KD, CW], F32) as wq, nc.sbuf_tensor("w_ckv", [P, KD, 2 * CW], F32) as wkv, \
            nc.sbuf_tensor("mem_k_rows", [P, MT, CW], F32) as mk, nc.Block() as block:
        @block.sync
        def _(sp):
            sp.dma_start(wq[:, :, :], a["w_cq"][0].rearrange("(k p) c -> p k c", p=P)).then_inc(s["w_ready"], 16)
            sp.dma_start(wkv[:, :, :], a["w_ckv"][0].rearrange("(k p) c -> p k c", p=P)).then_inc(s["wkv_ready"], 16)
            sp.wait_ge(s["kv_copied"], 2 * MT)
            for name, rows in (("p_cache_mem_k", mk), ("p_cache_mem_v", e.mv)):
                sp.dma_start(o[name].rearrange("o b (m p) h d -> p (o b m) (h d)", p=P), rows[:, :, :]).then_inc(s["stored"], 16)
            sp.wait_ge(s["stored"], 32)

        @block.tensor
        def _(pe):
            pe.wait_ge(s["w_ready"], 16)
            for h in range(CH):
                if h >= 2:
                    pe.wait_ge(s["q_free"], h - 1)
                for k in range(KD):
                    for q in range(NSPLIT):
                        last = pe.matmul(ps[:, 3 * (h % 2) + q, 0:NW], wq[:, k, h * P:(h + 1) * P], xc[:, k, q * NW:(q + 1) * NW],
                                         start=(k == 0), stop=(k == KD - 1))
                last.then_inc(s["q_ready"], 1)
            pe.wait_ge(s["wkv_ready"], 16)
            pe.wait_ge(s["q_free"], CH)
            for m in range(MT):
                for half in range(2):
                    for k in range(KD):
                        last = pe.matmul(ps[:, 2 * m + half, :], memT[:, k, m * P:(m + 1) * P], wkv[:, k, half * CW:(half + 1) * CW],
                                         start=(k == 0), stop=(k == KD - 1))
                    last.then_inc(s["kv_ready"], 1)
            pe.wait_ge(s["kv_copied"], 2 * MT)
            for h in range(CH):
                for m in range(MT):
                    last = pe.transpose(ps[:, 4 + h // 2, (2 * (h % 2) + m) * P:(2 * (h % 2) + m + 1) * P], mk[:, m, h * P:(h + 1) * P], e.ident[:, :])
            last.then_inc(s["kT"], 1)

        @block.scalar
        def _(act):
            for h in range(CH):
                act.wait_ge(s["q_ready"], h + 1)
                act.activation(e.qc[:, h, 0:T].rearrange("p (q c) -> p q c", q=NSPLIT), ps[:, 3 * (h % 2):3 * (h % 2) + 3, 0:NW], ACT.Copy)\
                   .then_inc(s["q_free"], 1)

        @block.vector
        def _(dve):
            for m in range(MT):
                for half, rows in enumerate((mk, e.mv)):
                    dve.wait_ge(s["kv_ready"], 2 * m + half + 1)
                    dve.tensor_copy(rows[:, m], ps[:, 2 * m + half, :]).then_inc(s["kv_copied"], 1)
            dve.wait_ge(s["kT"], 1)
            dve.tensor_copy(e.mkT[:, :, :].rearrange("p (b h) m -> p b (h m)", b=2), ps[:, 4:6, :])


def cross_prompt(e, oc):
    nc, ps = e.nc, e.ps
    names = ("s_ready", "s_free", "maxed", "exped", "recip", "p_ready", "p_free", "t_ready", "t_free", "pt_ready", "pt_free", "o_ready", "o_free")
    s = {n: e.sem("cross_" + n) for n in names}
    SCALE = CHD ** -0.5
    with ExitStack() as st:
        sb = lambda n, sh: st.enter_context(nc.sbuf_tensor(n, sh, F32))
        p = sb("cross_p", [P, 2, CH, MEM])
        pt = sb("cross_pt", [P, 2, CH, MT, P])
        mx, nm, den, rd = (sb("cross_" + n, [P, 2, CH]) for n in ("mx", "nm", "den", "rd"))
        block = st.enter_context(nc.Block())

        @block.tensor
        def _(pe):
            def scores(t):
                if t >= 2:
                    pe.wait_ge(s["s_free"], t - 1)
                for h in range(CH):
                    last = pe.matmul(ps[:, 2 * (t % 2) + h // 2, (h % 2) * MEM:(h % 2 + 1) * MEM], e.qc[:, h, t * P:(t + 1) * P], e.mkT[:, h],
                                     start=True, stop=True)
                last.then_inc(s["s_ready"], 1)

            def weigh(t):
                pe.wait_ge(s["p_ready"], t + 1)
                if t >= 1:
                    pe.wait_ge(s["t_free"], t)
                for h in range(CH):
                    for m in range(MT):
                        last = pe.transpose(ps[:, 4 + h // 2, (2 * (h % 2) + m) * P:(2 * (h % 2) + m + 1) * P],
                                            p[:, t % 2, h, m * P:(m + 1) * P], e.ident[:, :])
                last.then_inc(s["t_ready"], 1)
                pe.drain().then_inc(s["p_free"], 1)

            def values(t):
                pe.wait_ge(s["pt_ready"], t + 1)
                if t >= 2:
                    pe.wait_ge(s["o_free"], t - 1)
                for h in range(CH):
                    for m in range(MT):
                        last = pe.matmul(ps[:, 6 + t % 2, h * P:(h + 1) * P], e.mv[:, m, h * CHD:(h + 1) * CHD], pt[:, t % 2, h, m],
                                         start=(m == 0), stop=(m == MT - 1))
                last.then_inc(s["o_ready"], 1)

            scores(0)
            scores(1)
            for t in range(NT):
                weigh(t)
                if t + 2 < NT:
                    scores(t + 2)
                values(t)

        @block.scalar
        def _(act):
            for t in range(NT):
                act.wait_ge(s["maxed"], t + 1)
                if t >= 2:
                    act.wait_ge(s["p_free"], t - 1)
                for h in range(CH):
                    last = act.activation(p[:, t % 2, h], ps[:, 2 * (t % 2) + h // 2, (h % 2) * MEM:(h % 2 + 1) * MEM], ACT.Exp,
                                          bias=nm[:, t % 2, h:h + 1], scale=SCALE, accum_out=den[:, t % 2, h:h + 1])
                last.then_inc(s["exped"], 1)
                act.drain().then_inc(s["s_free"], 1)
                if t >= 1:
                    act.wait_ge(s["o_ready"], t)
                    act.activation(oc[:, :, (t - 1) * P:t * P], ps[:, 6 + (t - 1) % 2, :].rearrange("p (h c) -> p h c", h=CH), ACT.Copy).then_inc(s["o_free"], 1)
            act.wait_ge(s["o_ready"], NT)
            act.activation(oc[:, :, SEQ - P:SEQ], ps[:, 6 + (NT - 1) % 2, :].rearrange("p (h c) -> p h c", h=CH), ACT.Copy)

        @block.gpsimd
        def _(pool):
            pool.memset(oc[:, :, T:TP], 0.0)
            for t in range(NT):
                pool.wait_ge(s["recip"], t + 1)
                pool.tensor_tensor(p[:, t % 2], p[:, t % 2], bc(rd[:, t % 2].unsqueeze(2), [P, CH, MEM]), ALU.mult).then_inc(s["p_ready"], 1)

        @block.vector
        def _(dve):
            def maxima(t):
                dve.wait_ge(s["s_ready"], t + 1)
                dve.tensor_reduce(mx[:, t % 2], ps[:, 2 * (t % 2):2 * (t % 2) + 2, :].rearrange("p b (h m) -> p (b h) m", m=MEM), AX.X, ALU.max)
                dve.drain()
                dve.tensor_scalar(nm[:, t % 2], mx[:, t % 2], -SCALE, None, ALU.mult).then_inc(s["maxed"], 1)
            maxima(0)
            for t in range(NT):
                dve.wait_ge(s["exped"], t + 1)
                dve.reciprocal(rd[:, t % 2], den[:, t % 2]).then_inc(s["recip"], 1)
                if t + 1 < NT:
                    maxima(t + 1)
                dve.wait_ge(s["t_ready"], t + 1)
                if t >= 2:
                    dve.wait_ge(s["o_ready"], t - 1)
                dve.tensor_copy(pt[:, t % 2].rearrange("p (b h) m c -> p b (h m c)", b=2), ps[:, 4:6, :]).then_inc(s["pt_ready"], 1)
                dve.drain().then_inc(s["t_free"], 1)


def cross_sample(e, oc):
    nc, a, ps = e.nc, e.a, e.ps
    names = ("v_ready", "k_free", "rows", "rows_copied", "q_ready", "q_free", "sT", "turned", "maxed", "exped", "normed", "pT", "pT_copied", "o_ready")
    s = {n: e.sem("csam_" + n) for n in names}
    k_ready = [e.sem(f"csam_k_ready{i}") for i in range(2)]
    SCALE = CHD ** -0.5
    R = NB * CH
    with ExitStack() as st:
        sb = lambda n, sh: st.enter_context(nc.sbuf_tensor(n, sh, F32))
        kc = sb("csam_k", [P, 2, MT, CW])
        vc = sb("csam_v", [P, NB, MT, CW])
        qr = sb("csam_q_rows", [NB, CW])
        prod = sb("csam_prod", [P, MT, CW])
        sT = sb("csam_sT", [P, MT, NB, CH])
        onehot = sb("csam_onehot", [NB, NB, P])
        sc = sb("csam_sc", [R, MEM])
        mx, nm, den, rd = (sb("csam_" + n, [R, 1]) for n in ("mx", "nm", "den", "rd"))
        pT = sb("csam_pT", [P, MT, NB, CH])
        made = e.sem("csam_onehot_made")
        block = st.enter_context(nc.Block())

        @block.gpsimd
        def _(pool):
            pool.memset(onehot[:, :, :], 0.0)
            pool.drain()
            pool.affine_select(out=onehot[:, :, :], in_=onehot[:, :, :], compare_op=ALU.not_equal, fill=1.0, base=0,
                               pattern=[[-1, NB], [0, P]], channel_multiplier=1).then_inc(made, 1)

        @block.sync
        def _(sp):
            mem = lambda name, b: a[name][0, b].rearrange("(m p) h d -> p m (h d)", p=P)
            for b in range(NB):
                if b >= 2:
                    sp.wait_ge(s["k_free"], b - 1)
                sp.dma_start(kc[:, b % 2], mem("cache_mem_k", b)).then_inc(k_ready[b % 2], 16)
                sp.dma_start(vc[:, b], mem("cache_mem_v", b)).then_inc(s["v_ready"], 16)

        @block.tensor
        def _(pe):
            for h in range(CH):
                last = pe.transpose(ps[0:NB, 0, h * P:(h + 1) * P], e.qc[:, h, SEQ:T], e.ident[:, :])
            last.then_inc(s["rows"], 1)
            pe.wait_ge(s["rows_copied"], 1)
            pe.wait_ge(made, 1)
            for b in range(NB):
                if b >= 2:
                    pe.wait_ge(s["q_free"], b - 1)
                pe.matmul(ps[:, 1 + b % 2, :], onehot[:, b], qr[:, :], start=True, stop=True).then_inc(s["q_ready"], 1)
            pe.wait_ge(s["sT"], 1)
            for m in range(MT):
                last = pe.transpose(ps[0:R, 3, m * P:(m + 1) * P], sT[:, m].rearrange("p b h -> p (b h)"), e.ident[:, :])
            last.then_inc(s["turned"], 1)
            pe.wait_ge(s["normed"], 1)
            for m in range(MT):
                last = pe.transpose(ps[:, 4, m * R:(m + 1) * R], sc[:, m * P:(m + 1) * P], e.ident[0:R, 0:R])
            last.then_inc(s["pT"], 1)
            pe.wait_ge(s["pT_copied"], 1)
            pe.wait_ge(s["v_ready"], 16 * NB)
            for b in range(NB):
                for h in range(CH):
                    for m in range(MT):
                        last = pe.matmul(ps[:, 5, h * NB + b:h * NB + b + 1], vc[:, b, m, h * CHD:(h + 1) * CHD], pT[:, m, b, h:h + 1],
                                         start=(m == 0), stop=(m == MT - 1))
            last.then_inc(s["o_ready"], 1)

        @block.scalar
        def _(act):
            act.wait_ge(s["maxed"], 1)
            act.activation(sc[:, :], ps[0:R, 3, 0:MEM], ACT.Exp, bias=nm[:, :], scale=SCALE, accum_out=den[:, :]).then_inc(s["exped"], 1)

        @block.vector
        def _(dve):
            dve.wait_ge(s["rows"], 1)
            dve.tensor_copy(qr[:, :], ps[0:NB, 0, :]).then_inc(s["rows_copied"], 1)
            for b in range(NB):
                dve.wait_ge(s["q_ready"], b + 1)
                dve.wait_ge(k_ready[b % 2], 16 * (b // 2 + 1))
                dve.tensor_tensor(prod[:, :, :], kc[:, b % 2], bc(ps[:, 1 + b % 2, :].unsqueeze(1), [P, MT, CW]), ALU.mult)
                dve.drain().then_inc(s["q_free"], 1)
                dve.sem_inc(s["k_free"], 1)
                dve.tensor_reduce(sT[:, :, b], prod[:, :, :].rearrange("p m (h d) -> p m h d", h=CH), AX.X, ALU.add)
                dve.drain()
            dve.sem_inc(s["sT"], 1)
            dve.wait_ge(s["turned"], 1)
            dve.tensor_reduce(mx[:, :], ps[0:R, 3, 0:MEM], AX.X, ALU.max)
            dve.drain()
            dve.tensor_scalar(nm[:, :], mx[:, :], -SCALE, None, ALU.mult).then_inc(s["maxed"], 1)
            dve.wait_ge(s["exped"], 1)
            dve.reciprocal(rd[:, :], den[:, :])
            dve.drain()
            dve.tensor_scalar(sc[:, :], sc[:, :], rd[:, :], None, ALU.mult).then_inc(s["normed"], 1)
            dve.wait_ge(s["pT"], 1)
            dve.tensor_copy(pT[:, :, :, :].rearrange("p m b h -> p (m b h)"), ps[:, 4, 0:MT * R]).then_inc(s["pT_copied"], 1)
            dve.wait_ge(s["o_ready"], 1)
            dve.tensor_copy(oc[:, :, SEQ:T], ps[:, 5, 0:CH * NB].rearrange("p (h b) -> p h b", h=CH))


def cross_out(e, oc):
    nc, a, ps = e.nc, e.a, e.ps
    w_ready, made, emptied = e.sem("co_w_ready"), e.sem("co_ready"), e.sem("co_free")
    with nc.sbuf_tensor("w_co", [P, CH, D], F32) as w, nc.Block() as block:
        @block.sync
        def _(sp):
            sp.dma_start(w[:, :, :], a["w_co"][0].rearrange("(k p) c -> p k c", p=P)).then_inc(w_ready, 16)

        @block.tensor
        def _(pe):
            pe.wait_ge(w_ready, 16)
            for u in range(2 * TILES):
                t, half = u // 2, u % 2
                if u >= 8:
                    pe.wait_ge(emptied, u - 7)
                for k in range(CH):
                    last = pe.matmul(ps[:, u % 8, :], oc[:, k, t * P:(t + 1) * P], w[:, k, half * 512:(half + 1) * 512],
                                     start=(k == 0), stop=(k == CH - 1))
                last.then_inc(made, 1)

        @block.vector
        def _(dve):
            for u in range(2 * TILES):
                dve.wait_ge(made, u + 1)
                xs = e.x[:, u // 2, (u % 2) * 512:(u % 2 + 1) * 512]
                dve.tensor_tensor(xs, xs, ps[:, u % 8, :], ALU.add).then_inc(emptied, 1)


def cross_attention(e):
    nc, a = e.nc, e.a
    with ExitStack() as st:
        sb = lambda n, sh: st.enter_context(nc.sbuf_tensor(n, sh, F32))
        e.qc = sb("qc", [P, CH, T])
        e.mkT = sb("mkT", [P, CH, MEM])
        e.mv = sb("mv", [P, MT, CW])
        with nc.sbuf_tensor("xc", [P, KD, TP], F32) as xc, nc.sbuf_tensor("memT", [P, KD, MEM], F32) as memT:
            rms_tiles(e, "cross", e.x, TILES, xc, grow=G_CROSS)
            with nc.sbuf_tensor("mem_rows", [P, MT, D], F32) as mem:
                rms_tiles(e, "mem", mem, MT, memT, grow=G_MEM,
                          load=[(mem[:, :, :], a["mem_prompt"][0].rearrange("(m p) d -> p m d", p=P))])
            cross_projections(e, xc, memT)
        with nc.sbuf_tensor("cross_oc", [P, CH, TP], F32) as oc:
            cross_prompt(e, oc)
            cross_sample(e, oc)
            cross_out(e, oc)


def resident_rows(e):
    e.x = e.ctx.enter_context(e.nc.sbuf_tensor("x_resident", [P, TILES, D], F32))


NBASE = NE
NMORE = TILES * P * 2 // P - 2
SLOTS = (NBASE + NMORE) * P


def routing(e, xT):
    nc, a, ps = e.nc, e.a, e.ps
    NR = NGR + NE
    s = {n: e.sem("route_" + n) for n in ("loaded", "logits", "pool_made", "chosen", "counted", "e0", "e1", "x0", "x1", "zeroed", "zero_made", "slots", "scattered0", "scattered1")}
    with ExitStack() as st:
        sb = lambda n, sh, dt=F32: st.enter_context(nc.sbuf_tensor("r_" + n, sh, dt))
        wr = sb("w", [P, KD, NR])
        bias = sb("bias", [P, NR])
        lg = sb("logits", [P, TILES, NR])
        gm = sb("gm", [P, TILES, 1])
        g4 = sb("g4", [P, TILES, NGR])
        ohg = sb("ohg", [P, TILES, NGR])
        wt = sb("wt", [P, EPG])
        pg = sb("pg", [P, TILES, 1])
        l4 = sb("l4", [P, TILES, NGR, EPG])
        le, key = sb("le", [P, TILES, EPG]), sb("key", [P, TILES, EPG])
        oh = [sb(f"oh{i}", [P, TILES, EPG]) for i in range(2)]
        m = [sb(f"m{i}", [P, TILES, 1]) for i in range(2)]
        km = sb("km", [P, TILES, 1])
        big = [sb(f"big{i}", [P, TILES, NE]) for i in range(2)]
        sel, rank = sb("sel", [P, TILES, NE]), sb("rank", [P, TILES, NE])
        valid = sb("valid", [P, TILES])
        off = sb("off", [P, TILES + 1, NE])
        more = [sb(f"more{i}", [P, NE]) for i in range(2)]
        nmore, delta, base_b = sb("nmore", [P, NE]), sb("delta", [P, NE]), sb("base_b", [P, NE])
        first = sb("first", [P, NE])
        below = sb("below_p", [P, TILES, NE])
        d = [sb(f"dest_f{i}", [P, TILES, 1]) for i in range(2)]
        tid = sb("tid", [P, TILES], I32)
        zero = sb("zero", [NBASE + NMORE, P], I32)
        jj = sb("jj", [1, NMORE, 1])
        ge = sb("ge", [1, NMORE, NE])
        ef = sb("ef", [1, NMORE])
        block = st.enter_context(nc.Block())

        @block.sync
        def _(sp):
            sp.dma_start(wr[:, :, 0:NGR], a["w_route_group"][0].rearrange("(k p) c -> p k c", p=P)).then_inc(s["loaded"], 16)
            sp.dma_start(wr[:, :, NGR:], a["w_route_expert"][0].rearrange("(k p) c -> p k c", p=P)).then_inc(s["loaded"], 16)
            sp.dma_start(bias[:, 0:NGR], a["b_route_group"].to_broadcast([P, NGR])).then_inc(s["loaded"], 16)
            sp.dma_start(bias[:, NGR:], a["b_route_expert"].to_broadcast([P, NE])).then_inc(s["loaded"], 16)
            sp.wait_ge(s["zero_made"], 1)
            sp.dma_start(e.slot_tok.rearrange("(b p) o -> b (p o)", p=P), zero[:, :]).then_inc(s["zeroed"], 16)
            sp.wait_ge(s["zeroed"], 16)

        @block.gpsimd
        def _(pool):
            pool.memset(zero[:, :], 0).then_inc(s["zero_made"], 1)
            pool.iota(wt[:, :], pattern=[[-1, EPG]], base=EPG, channel_multiplier=0, allow_small_or_imprecise_dtypes=True)
            pool.iota(first[:, :], pattern=[[P, NE]], base=0, channel_multiplier=0, allow_small_or_imprecise_dtypes=True)
            pool.iota(jj[:, :, :], pattern=[[1, NMORE], [0, 1]], base=0, channel_multiplier=0, allow_small_or_imprecise_dtypes=True)
            pool.iota(tid[:, :], pattern=[[P, TILES]], base=0, channel_multiplier=1)
            pool.memset(valid[:, :], 1.0)
            pool.drain()
            pool.affine_select(out=valid[:, NT:TILES], in_=valid[:, NT:TILES], compare_op=ALU.is_ge, fill=0.0, base=NB - 1,
                               pattern=[[0, 1]], channel_multiplier=-1)
            pool.drain().then_inc(s["pool_made"], 1)
            pool.wait_ge(s["slots"], 1)
            pool.wait_ge(s["zeroed"], 16)
            n = 0
            for i in range(2):
                for t in range(TILES):
                    rows = P if t < NT else NB
                    pool.indirect_dma_start(e.slot_tok, bass.IndirectOffsetOnAxis(ap=e.dest[0:rows, i, t:t + 1], axis=0),
                                            tid[0:rows, t:t + 1], None).then_inc(s[f"scattered{n % 2}"], 16)
                    n += 1
            for i in range(2):
                pool.wait_ge(s[f"scattered{i}"], 16 * TILES)

        @block.tensor
        def _(pe):
            pe.wait_ge(s["loaded"], 64)
            for t in range(TILES):
                for k in range(KD):
                    last = pe.matmul(ps[:, 0, t * NR:(t + 1) * NR], xT[:, k, t * P:(t + 1) * P], wr[:, k], start=(k == 0), stop=(k == KD - 1))
            last.then_inc(s["logits"], 1)
            pe.wait_ge(s["chosen"], 1)
            flat = sel[:, :, :].rearrange("p t e -> p (t e)")
            pe.matmul(ps[:, 1, 0:TILES * NE], e.tri[:, :], flat, start=True, stop=True)
            pe.matmul(ps[:, 2, 0:TILES * NE], e.ones[:, :], flat, start=True, stop=True).then_inc(s["counted"], 1)

        @block.scalar
        def _(act):
            act.wait_ge(s["e0"], 1)
            act.activation(g4[:, :, :], g4[:, :, :], ACT.Exp).then_inc(s["x0"], 1)
            act.wait_ge(s["e1"], 1)
            act.activation(m[1][:, :, :], m[1][:, :, :], ACT.Exp).then_inc(s["x1"], 1)

        @block.vector
        def _(dve):
            def tt(out, x, y, op):
                dve.tensor_tensor(out, x, y, op)
                dve.drain()

            def first_of(out, x, mx, width):
                tt(key[:, :, 0:width], x, bc(mx, [P, TILES, width]), ALU.is_equal)
                tt(key[:, :, 0:width], key[:, :, 0:width], bc(wt[:, EPG - width:].unsqueeze(1), [P, TILES, width]), ALU.mult)
                dve.tensor_reduce(km[:, :, :], key[:, :, 0:width].unsqueeze(2), AX.X, ALU.max)
                dve.drain()
                tt(out, key[:, :, 0:width], bc(km[:, :, :], [P, TILES, width]), ALU.is_equal)

            dve.wait_ge(s["loaded"], 64)
            dve.wait_ge(s["pool_made"], 1)
            dve.wait_ge(s["logits"], 1)
            tt(lg[:, :, :], ps[:, 0, 0:TILES * NR].rearrange("p (t c) -> p t c", c=NR), bc(bias[:, :].unsqueeze(1), [P, TILES, NR]), ALU.add)
            dve.tensor_reduce(gm[:, :, :], lg[:, :, 0:NGR].unsqueeze(2), AX.X, ALU.max)
            dve.drain()
            dve.tensor_tensor(g4[:, :, :], lg[:, :, 0:NGR], bc(gm[:, :, :], [P, TILES, NGR]), ALU.subtract).then_inc(s["e0"], 1)
            first_of(ohg[:, :, :], lg[:, :, 0:NGR], gm[:, :, :], NGR)
            tt(l4[:, :, :, :], lg[:, :, NGR:].rearrange("p t (g x) -> p t g x", g=NGR), bc(ohg[:, :, :].unsqueeze(3), [P, TILES, NGR, EPG]), ALU.mult)
            dve.tensor_reduce(le[:, :, :], l4[:, :, :, :].rearrange("p t g x -> p t x g"), AX.X, ALU.add)
            dve.drain()
            dve.tensor_reduce(m[0][:, :, :], le[:, :, :].unsqueeze(2), AX.X, ALU.max)
            dve.drain()
            first_of(oh[0][:, :, :], le[:, :, :], m[0][:, :, :], EPG)
            dve.scalar_tensor_tensor(out=le[:, :, :], in0=oh[0][:, :, :], scalar=NEG, in1=le[:, :, :], op0=ALU.mult, op1=ALU.add)
            dve.drain()
            dve.tensor_reduce(m[1][:, :, :], le[:, :, :].unsqueeze(2), AX.X, ALU.max)
            dve.drain()
            first_of(oh[1][:, :, :], le[:, :, :], m[1][:, :, :], EPG)
            dve.tensor_tensor(m[1][:, :, :], m[1][:, :, :], m[0][:, :, :], ALU.subtract).then_inc(s["e1"], 1)
            for i in range(2):
                tt(big[i][:, :, :].rearrange("p t (g x) -> p t g x", g=NGR), bc(ohg[:, :, :].unsqueeze(3), [P, TILES, NGR, EPG]),
                   bc(oh[i][:, :, :].unsqueeze(2), [P, TILES, NGR, EPG]), ALU.mult)
            tt(sel[:, :, :], big[0][:, :, :], big[1][:, :, :], ALU.add)
            tt(sel[:, :, :], sel[:, :, :], bc(valid[:, :].unsqueeze(2), [P, TILES, NE]), ALU.mult)
            dve.sem_inc(s["chosen"], 1)
            dve.wait_ge(s["x0"], 1)
            dve.tensor_reduce(pg[:, :, :], g4[:, :, :].unsqueeze(2), AX.X, ALU.add)
            dve.drain()
            dve.wait_ge(s["x1"], 1)
            dve.tensor_scalar(m[0][:, :, :], m[1][:, :, :], 1.0, None, ALU.add)
            dve.drain()
            tt(pg[:, :, :], pg[:, :, :], m[0][:, :, :], ALU.mult)
            dve.reciprocal(e.gate[:, 0].unsqueeze(2), pg[:, :, :])
            dve.drain()
            tt(e.gate[:, 1].unsqueeze(2), e.gate[:, 0].unsqueeze(2), m[1][:, :, :], ALU.mult)
            dve.wait_ge(s["counted"], 1)
            dve.memset(off[:, 0], 0.0)
            dve.drain()
            for t in range(TILES):
                tt(off[:, t + 1], off[:, t], ps[:, 2, t * NE:(t + 1) * NE], ALU.add)
            tt(rank[:, :, :], ps[:, 1, 0:TILES * NE].rearrange("p (t e) -> p t e", e=NE), sel[:, :, :], ALU.subtract)
            tt(rank[:, :, :], rank[:, :, :], off[:, 0:TILES], ALU.add)
            cnt = off[:, TILES]
            dve.tensor_scalar(nmore[:, :], cnt, float(P), None, ALU.is_gt)
            dve.drain()
            for j in range(2, T // P + 1):
                dve.scalar_tensor_tensor(out=nmore[:, :], in0=cnt, scalar=float(j * P), in1=nmore[:, :], op0=ALU.is_gt, op1=ALU.add)
                dve.drain()
            dve.tensor_copy(more[0][:, :], nmore[:, :])
            dve.drain()
            src = 0
            step = 1
            while step < NE:
                dve.tensor_copy(more[1 - src][:, 0:step], more[src][:, 0:step])
                dve.tensor_tensor(more[1 - src][:, step:], more[src][:, step:], more[src][:, 0:NE - step], ALU.add)
                dve.drain()
                src, step = 1 - src, 2 * step
            end = more[src]
            tt(base_b[:, :], end[:, :], nmore[:, :], ALU.subtract)
            dve.tensor_scalar(base_b[:, :], base_b[:, :], float(P), float((NBASE - 1) * P), ALU.mult, ALU.add)
            dve.drain()
            tt(delta[:, :], first[:, :], base_b[:, :], ALU.subtract)
            dve.tensor_scalar(below[:, :, :], rank[:, :, :], float(P), None, ALU.is_lt)
            dve.drain()
            tt(below[:, :, :], below[:, :, :], bc(delta[:, :].unsqueeze(1), [P, TILES, NE]), ALU.mult)
            tt(rank[:, :, :], rank[:, :, :], bc(base_b[:, :].unsqueeze(1), [P, TILES, NE]), ALU.add)
            tt(rank[:, :, :], rank[:, :, :], below[:, :, :], ALU.add)
            for i in range(2):
                tt(big[i][:, :, :], big[i][:, :, :], rank[:, :, :], ALU.mult)
                dve.tensor_reduce(d[i][:, :, :], big[i][:, :, :].unsqueeze(2), AX.X, ALU.add)
                dve.drain()
                dve.tensor_copy(e.dest[:, i].unsqueeze(2), d[i][:, :, :])
                dve.drain()
            tt(ge[:, :, :], bc(jj[:, :, :], [1, NMORE, NE]), bc(end[0:1, :].unsqueeze(1), [1, NMORE, NE]), ALU.is_ge)
            dve.tensor_reduce(ef[:, :], ge[:, :, :], AX.X, ALU.add)
            dve.drain()
            dve.tensor_scalar(ef[:, :], ef[:, :], float(NE - 1), None, ALU.min)
            dve.drain()
            dve.tensor_copy(e.more_expert[:, 0:NMORE], ef[:, :])
            dve.tensor_copy(e.more_expert[:, NMORE:NMORE + 1], end[0:1, NE - 1:NE])
            dve.drain().then_inc(s["slots"], 1)


def expert_blocks(e, name, count):
    nc, a, ps = e.nc, e.a, e.ps
    names = ("wg_free", "idx_free", "x_free", "gather_go", "turned", "xt_low", "xt_high", "gu_ready", "silu_ready", "gu_free", "h_ready", "h_free",
             "ht_ready", "ht_copied", "down_ready", "down_free", "y_ready")
    s = {n: e.sem(f"{name}_{n}") for n in names}
    two = lambda n: [e.sem(f"{name}_{n}{i}") for i in range(2)]
    wg_ready, wd_ready, idx_ready, x_ready, stored = two("wg_ready"), two("wd_ready"), two("idx_ready"), two("x_ready"), two("stored")
    KE = DE // P
    with ExitStack() as st:
        sb = lambda n, sh, dt=F32: st.enter_context(nc.sbuf_tensor(f"{name}_{n}", sh, dt))
        wg, wu = sb("wg", [P, 2, KD, DE]), sb("wu", [P, 2, KD, DE])
        wd = sb("wd", [P, 2, KE, D])
        idx = [sb(f"idx{i}", [P, 1], I32) for i in range(2)]
        xg = [sb(f"x{i}", [P, D]) for i in range(2)]
        xt = sb("xt", [P, KD, P])
        act_g = sb("silu", [P, DE])
        h = sb("h", [P, 2, DE])
        ht = sb("ht", [P, 2, KE, P])
        y = sb("y", [P, 2, D])

        def in_pairs(eng, step):
            with eng.Fori(0, count // 2) as i:
                for j in range(2):
                    step(i * 2 + j, j, i)

        with nc.Block() as block:
            @block.sync
            def _(sp):
                def load(n, b, i):
                    pick = lambda w: w[0][bass.ds(n, 1)].rearrange("o (k p) c -> p (o k) c", p=P)
                    sp.wait_ge(s["idx_free"], n + 1)
                    sp.dma_start(idx[b][:, :], e.slot_tok[bass.ds(n * P, P), :]).then_inc(idx_ready[b], 16)
                    sp.wait_ge(s["wg_free"], n + 1)
                    sp.dma_start(wg[:, b], pick(a["w_e_gate"])).then_inc(wg_ready[b], 16)
                    sp.dma_start(wu[:, b], pick(a["w_e_up"])).then_inc(wg_ready[b], 16)
                in_pairs(sp, load)

            @block.gpsimd
            def _(pool):
                pool.sem_inc(s["idx_free"], 2)

                def gather(n, b, i):
                    pool.wait_ge(idx_ready[b], i * 16 + 16)
                    pool.wait_ge(s["x_free"], n + 1)
                    pool.sem_inc(s["gather_go"], 1)
                    pool.indirect_dma_start(xg[b][:, :], None, e.xm_rows, bass.IndirectOffsetOnAxis(ap=idx[b][:, 0:1], axis=0)).then_inc(x_ready[b], 16)
                    pool.wait_ge(x_ready[b], i * 16 + 16)
                    pool.sem_inc(s["idx_free"], 1)
                in_pairs(pool, gather)

            @block.tensor
            def _(pe):
                pe.sem_inc(s["x_free"], 2)
                pe.sem_inc(s["wg_free"], 2)
                pe.sem_inc(s["h_free"], 2)

                def turn(n, b, i):
                    pe.wait_ge(x_ready[b], i * 16 + 16)
                    pe.wait_ge(s["xt_low"], n + 1)
                    pe.wait_ge(s["xt_high"], n + 1)
                    for k in range(KD):
                        last = pe.transpose(ps[:, k // 4, (k % 4) * P:(k % 4 + 1) * P], xg[b][:, k * P:(k + 1) * P], e.ident[:, :])
                    last.then_inc(s["turned"], 1)
                    pe.drain().then_inc(s["x_free"], 1)

                def gate_up(n, b, i):
                    pe.wait_ge(wg_ready[b], i * 32 + 32)
                    pe.wait_ge(s["gu_free"], n + 1)
                    pe.wait_ge(s["xt_low"], n + 2)
                    pe.wait_ge(s["xt_high"], n + 2)
                    for w, bank in ((wg, 2), (wu, 3)):
                        for k in range(KD):
                            last = pe.matmul(ps[:, bank, :], xt[:, k], w[:, b, k], start=(k == 0), stop=(k == KD - 1))
                    last.then_inc(s["gu_ready"], 1)
                    pe.drain().then_inc(s["wg_free"], 1)

                def turn_h(n, b):
                    pe.wait_ge(s["h_ready"], n + 1)
                    pe.wait_ge(s["ht_copied"], n + 1)
                    for k in range(KE):
                        last = pe.transpose(ps[:, 4, k * P:(k + 1) * P], h[:, b, k * P:(k + 1) * P], e.ident[:, :])
                    last.then_inc(s["ht_ready"], 1)
                    pe.drain().then_inc(s["h_free"], 1)

                def down(n, b, i):
                    pe.wait_ge(wd_ready[b], i * 16 + 16)
                    pe.wait_ge(s["ht_copied"], n + 2)
                    pe.wait_ge(s["down_free"], n + 1)
                    for half in range(2):
                        for k in range(KE):
                            last = pe.matmul(ps[:, 5 + half, :], ht[:, b, k], wd[:, b, k, half * 512:(half + 1) * 512], start=(k == 0), stop=(k == KE - 1))
                    last.then_inc(s["down_ready"], 1)

                turn(0, 0, 0)
                gate_up(0, 0, 0)
                turn(1, 1, 0)
                turn_h(0, 0)
                with pe.Fori(0, count // 2 - 1) as i:
                    gate_up(i * 2 + 1, 1, i)
                    turn(i * 2 + 2, 0, i + 1)
                    down(i * 2, 0, i)
                    turn_h(i * 2 + 1, 1)
                    gate_up(i * 2 + 2, 0, i + 1)
                    turn(i * 2 + 3, 1, i + 1)
                    down(i * 2 + 1, 1, i)
                    turn_h(i * 2 + 2, 0)
                gate_up(count - 1, 1, count // 2 - 1)
                down(count - 2, 0, count // 2 - 1)
                turn_h(count - 1, 1)
                down(count - 1, 1, count // 2 - 1)

            @block.scalar
            def _(act):
                act.sem_inc(s["xt_high"], 1)

                def high(n):
                    act.wait_ge(s["turned"], n + 1)
                    act.wait_ge(s["gu_ready"], n) if not (isinstance(n, int) and n == 0) else None
                    act.activation(xt[:, 4:8].rearrange("p k c -> p (k c)"), ps[:, 1, :], ACT.Copy).then_inc(s["xt_high"], 1)

                def silu(n):
                    act.wait_ge(s["gu_ready"], n + 1)
                    act.wait_ge(s["gu_free"], n + 1)
                    act.activation(act_g[:, :], ps[:, 2, :], ACT.Silu).then_inc(s["silu_ready"], 1)

                def load_down(x, b):
                    act.dma_start(wd[:, b], a["w_e_down"][0][bass.ds(x, 1)].rearrange("o (k p) c -> p (o k) c", p=P)).then_inc(wd_ready[b], 16)

                def out(n, b, i, reload=True):
                    act.wait_ge(s["y_ready"], n + 1)
                    if reload:
                        load_down(n + 2, b)
                    act.dma_start(e.y_rows[bass.ds(n * P, P), :], y[:, b]).then_inc(stored[b], 16)

                load_down(0, 0)
                load_down(1, 1)
                high(0)
                silu(0)
                high(1)
                with act.Fori(0, count // 2 - 1) as i:
                    silu(i * 2 + 1)
                    high(i * 2 + 2)
                    out(i * 2, 0, i)
                    silu(i * 2 + 2)
                    high(i * 2 + 3)
                    out(i * 2 + 1, 1, i)
                silu(count - 1)
                out(count - 2, 0, 0, reload=False)
                out(count - 1, 1, 0, reload=False)
                for b in range(2):
                    act.wait_ge(stored[b], 16 * count // 2)

            @block.vector
            def _(dve):
                dve.sem_inc(s["xt_low"], 1)
                dve.sem_inc(s["gu_free"], 1)
                dve.sem_inc(s["ht_copied"], 1)
                dve.sem_inc(s["down_free"], 1)

                def low(n):
                    dve.wait_ge(s["turned"], n + 1)
                    dve.wait_ge(s["gu_ready"], n) if not (isinstance(n, int) and n == 0) else None
                    dve.tensor_copy(xt[:, 0:4].rearrange("p k c -> p (k c)"), ps[:, 0, :]).then_inc(s["xt_low"], 1)

                def product(n, b):
                    dve.wait_ge(s["silu_ready"], n + 1)
                    dve.wait_ge(s["h_free"], n + 1)
                    dve.tensor_tensor(h[:, b], act_g[:, :], ps[:, 3, :], ALU.mult).then_inc(s["h_ready"], 1)
                    dve.drain().then_inc(s["gu_free"], 1)

                def copy_h(n, b):
                    dve.wait_ge(s["ht_ready"], n + 1)
                    dve.wait_ge(s["down_ready"], n) if not (isinstance(n, int) and n == 0) else None
                    dve.tensor_copy(ht[:, b].rearrange("p k c -> p (k c)"), ps[:, 4, :]).then_inc(s["ht_copied"], 1)

                def rows(n, b, i):
                    dve.wait_ge(s["down_ready"], n + 1)
                    dve.wait_ge(stored[b], i * 16)
                    dve.tensor_copy(y[:, b].rearrange("p (h c) -> p h c", h=2), ps[:, 5:7, :]).then_inc(s["y_ready"], 1)
                    dve.drain().then_inc(s["down_free"], 1)

                low(0)
                product(0, 0)
                low(1)
                copy_h(0, 0)
                with dve.Fori(0, count // 2 - 1) as i:
                    product(i * 2 + 1, 1)
                    low(i * 2 + 2)
                    rows(i * 2, 0, i)
                    copy_h(i * 2 + 1, 1)
                    product(i * 2 + 2, 0)
                    low(i * 2 + 3)
                    rows(i * 2 + 1, 1, i)
                    copy_h(i * 2 + 2, 0)
                product(count - 1, 1)
                rows(count - 2, 0, count // 2 - 1)
                copy_h(count - 1, 1)
                rows(count - 1, 1, count // 2 - 1)


def further_blocks(e):
    nc, a, ps = e.nc, e.a, e.ps
    s = {n: e.sem("more_" + n) for n in ("idx_ready", "w_ready", "x_ready", "gather_go", "turned", "xt_low", "xt_high", "gu_ready", "silu_ready",
                                         "h_ready", "ht_ready", "ht_copied", "down_ready", "y_ready", "stored", "done")}
    KE = DE // P
    with ExitStack() as st:
        sb = lambda n, sh, dt=F32: st.enter_context(nc.sbuf_tensor(f"more_{n}", sh, dt))
        wg, wu, wd = sb("wg", [P, KD, DE]), sb("wu", [P, KD, DE]), sb("wd", [P, KE, D])
        idx, xg, xt = sb("idx", [P, 1], I32), sb("x", [P, D]), sb("xt", [P, KD, P])
        act_g, h, ht, y = sb("silu", [P, DE]), sb("h", [P, DE]), sb("ht", [P, KE, P]), sb("y", [P, D])
        block = st.enter_context(nc.Block())

        def each(eng, step):
            total = eng.value_load(e.more_expert[0:1, NMORE:NMORE + 1], min_val=0, max_val=NMORE)
            with eng.Fori(0, NMORE) as j:
                with eng.If(j < total):
                    step(j)

        @block.sync
        def _(sp):
            def load(j):
                x = sp.value_load(e.more_expert[0:1, bass.ds(j, 1)], min_val=0, max_val=NE - 1)
                pick = lambda w: w[0][bass.ds(x, 1)].rearrange("o (k p) c -> p (o k) c", p=P)
                sp.wait_ge(s["done"], j)
                sp.dma_start(idx[:, :], e.slot_tok[bass.ds(j * P + NBASE * P, P), :]).then_inc(s["idx_ready"], 16)
                for w, name in ((wg, "w_e_gate"), (wu, "w_e_up"), (wd, "w_e_down")):
                    sp.dma_start(w[:, :, :], pick(a[name])).then_inc(s["w_ready"], 16)
            each(sp, load)

        @block.gpsimd
        def _(pool):
            def gather(j):
                pool.wait_ge(s["idx_ready"], j * 16 + 16)
                pool.sem_inc(s["gather_go"], 1)
                pool.indirect_dma_start(xg[:, :], None, e.xm_rows, bass.IndirectOffsetOnAxis(ap=idx[:, 0:1], axis=0)).then_inc(s["x_ready"], 16)
                pool.wait_ge(s["x_ready"], j * 16 + 16)
                pool.sem_inc(s["gather_go"], 1)
            each(pool, gather)

        @block.tensor
        def _(pe):
            def products(j):
                pe.wait_ge(s["x_ready"], j * 16 + 16)
                for k in range(KD):
                    last = pe.transpose(ps[:, k // 4, (k % 4) * P:(k % 4 + 1) * P], xg[:, k * P:(k + 1) * P], e.ident[:, :])
                last.then_inc(s["turned"], 1)
                pe.wait_ge(s["w_ready"], j * 48 + 48)
                pe.wait_ge(s["xt_low"], j + 1)
                pe.wait_ge(s["xt_high"], j + 1)
                for w, bank in ((wg, 2), (wu, 3)):
                    for k in range(KD):
                        last = pe.matmul(ps[:, bank, :], xt[:, k], w[:, k], start=(k == 0), stop=(k == KD - 1))
                last.then_inc(s["gu_ready"], 1)
                pe.wait_ge(s["h_ready"], j + 1)
                for k in range(KE):
                    last = pe.transpose(ps[:, 4, k * P:(k + 1) * P], h[:, k * P:(k + 1) * P], e.ident[:, :])
                last.then_inc(s["ht_ready"], 1)
                pe.wait_ge(s["ht_copied"], j + 1)
                for half in range(2):
                    for k in range(KE):
                        last = pe.matmul(ps[:, 5 + half, :], ht[:, k], wd[:, k, half * 512:(half + 1) * 512], start=(k == 0), stop=(k == KE - 1))
                last.then_inc(s["down_ready"], 1)
            each(pe, products)

        @block.scalar
        def _(act):
            def step(j):
                act.wait_ge(s["turned"], j + 1)
                act.activation(xt[:, 4:8].rearrange("p k c -> p (k c)"), ps[:, 1, :], ACT.Copy).then_inc(s["xt_high"], 1)
                act.wait_ge(s["gu_ready"], j + 1)
                act.activation(act_g[:, :], ps[:, 2, :], ACT.Silu).then_inc(s["silu_ready"], 1)
                act.wait_ge(s["y_ready"], j + 1)
                act.dma_start(e.y_rows[bass.ds(j * P + NBASE * P, P), :], y[:, :]).then_inc(s["stored"], 16)
                act.wait_ge(s["stored"], j * 16 + 16)
                act.sem_inc(s["done"], 1)
            each(act, step)

        @block.vector
        def _(dve):
            def step(j):
                dve.wait_ge(s["turned"], j + 1)
                dve.tensor_copy(xt[:, 0:4].rearrange("p k c -> p (k c)"), ps[:, 0, :]).then_inc(s["xt_low"], 1)
                dve.wait_ge(s["silu_ready"], j + 1)
                dve.tensor_tensor(h[:, :], act_g[:, :], ps[:, 3, :], ALU.mult).then_inc(s["h_ready"], 1)
                dve.wait_ge(s["ht_ready"], j + 1)
                dve.tensor_copy(ht[:, :, :].rearrange("p k c -> p (k c)"), ps[:, 4, :]).then_inc(s["ht_copied"], 1)
                dve.wait_ge(s["down_ready"], j + 1)
                dve.tensor_copy(y[:, :].rearrange("p (h c) -> p h c", h=2), ps[:, 5:7, :]).then_inc(s["y_ready"], 1)
            each(dve, step)


def moe(e):
    nc, a = e.nc, e.a
    e.xm_rows = e.dram("xm_rows", [TP, D])
    e.slot_tok = e.dram("slot_tok", [SLOTS, 1], I32)
    keep = lambda n, sh, dt=F32: e.ctx.enter_context(nc.sbuf_tensor(n, sh, dt))
    e.gate = keep("gate", [P, 2, TILES])
    e.dest = keep("dest", [P, 2, TILES], I32)
    e.more_expert = keep("more_expert", [1, NMORE + 1], I32)
    g_ready = e.sem("g_moe_ready")
    with nc.sbuf_tensor("xmT", [P, KD, TP], F32) as xT:
        with nc.sbuf_tensor("g_moe_rows", [P, D], F32) as g:
            with nc.Block() as block:
                @block.sync
                def _(sp):
                    sp.dma_start(g[:, :], a["g_moe"].to_broadcast([P, D])).then_inc(g_ready, 16)
                    sp.wait_ge(g_ready, 16)
            rms_tiles(e, "moe", e.x, TILES, xT, gtok=g[:, :], store=e.xm_rows)
        routing(e, xT)
    expert_blocks(e, "own", NBASE)
    further_blocks(e)


def output(e):
    nc, a, o = e.nc, e.a, e.o
    s = {n: e.sem("final_" + n) for n in ("g_ready", "added", "squared", "meaned", "rooted", "scaled")}
    row_ready = [[e.sem(f"final_rows{i}{b}") for b in range(2)] for i in range(2)]
    stored = [e.sem(f"final_stored{b}") for b in range(2)]
    with ExitStack() as st:
        sb = lambda n, sh: st.enter_context(nc.sbuf_tensor("f_" + n, sh, F32))
        y = [[sb(f"y{i}{b}", [P, D]) for b in range(2)] for i in range(2)]
        g, out = sb("g", [P, D]), sb("out", [P, 2, D])
        sq, ss, rs = sb("sq", [P, D]), sb("ss", [P, TILES]), sb("rs", [P, TILES])
        block = st.enter_context(nc.Block())
        rows = lambda t: P if t < NT else NB

        @block.sync
        def _(sp):
            sp.dma_start(g[:, :], a["g_final"].rearrange("(o d) -> o d", o=1).to_broadcast([P, D])).then_inc(s["g_ready"], 16)
            for t in range(TILES):
                sp.wait_ge(s["scaled"], t + 1)
                dst = o["y_prompt"][0, t * P:(t + 1) * P, :] if t < NT else o["y_sample"][:, 0, :]
                sp.dma_start(dst, out[0:rows(t), t % 2]).then_inc(stored[t % 2], 16)
            for b in range(2):
                sp.wait_ge(stored[b], 16 * ((TILES + 1 - b) // 2))

        @block.gpsimd
        def _(pool):
            def root(t):
                pool.wait_ge(s["meaned"], t + 1)
                pool.tensor_tensor(rs[0:rows(t), t:t + 1], ss[0:rows(t), t:t + 1], e.mhalf[0:rows(t), 0:1], ALU.pow).then_inc(s["rooted"], 1)
            for t in range(TILES):
                if t >= 2:
                    pool.wait_ge(s["added"], t - 1)
                for i in range(2):
                    pool.indirect_dma_start(y[i][t % 2][0:rows(t), :], None, e.y_rows,
                                            bass.IndirectOffsetOnAxis(ap=e.dest[0:rows(t), i, t:t + 1], axis=0)).then_inc(row_ready[i][t % 2], 16)
                if t >= 1:
                    root(t - 1)
            root(TILES - 1)

        @block.scalar
        def _(act):
            for t in range(TILES):
                act.wait_ge(s["added"], t + 1)
                act.activation(sq[0:rows(t), :], e.x[0:rows(t), t, :], ACT.Square, accum_out=ss[0:rows(t), t:t + 1]).then_inc(s["squared"], 1)
                act.drain()

        @block.vector
        def _(dve):
            def add(t):
                r = rows(t)
                for i in range(2):
                    dve.wait_ge(row_ready[i][t % 2], 16 * (t // 2 + 1))
                    last = dve.scalar_tensor_tensor(out=e.x[0:r, t, :], in0=y[i][t % 2][0:r, :], scalar=e.gate[0:r, i, t:t + 1], in1=e.x[0:r, t, :],
                                                    op0=ALU.mult, op1=ALU.add)
                    dve.drain()
                dve.sem_inc(s["added"], 1)

            def mean(t):
                r = rows(t)
                dve.wait_ge(s["squared"], t + 1)
                dve.tensor_scalar(ss[0:r, t:t + 1], ss[0:r, t:t + 1], 1.0 / D, EPS, ALU.mult, ALU.add).then_inc(s["meaned"], 1)

            def scale(t):
                r = rows(t)
                if t >= 2:
                    dve.wait_ge(stored[t % 2], 16 * (t // 2))
                dve.wait_ge(s["rooted"], t + 1)
                dve.scalar_tensor_tensor(out=out[0:r, t % 2, :], in0=e.x[0:r, t, :], scalar=rs[0:r, t:t + 1], in1=g[0:r, :],
                                         op0=ALU.mult, op1=ALU.mult).then_inc(s["scaled"], 1)
            dve.wait_ge(s["g_ready"], 16)
            add(0)
            for t in range(TILES):
                mean(t)
                if t + 1 < TILES:
                    add(t + 1)
                scale(t)


def hybrid_step(nc, a, o):
    with ExitStack() as ctx:
        e = Env(nc, ctx, a, o)
        with e.stage():
            constants(e)
        e.y_cols = e.dram("y_cols", [XT, P, T])
        e.att_cols = e.dram("att_cols", [KD, P, T])
        ssd_vectors(e)
        with nc.sbuf_tensor("x_turned", [P, KD, TP], F32) as x_turned:
            with e.stage():
                mixer_norm(e, x_turned)
                project(e, x_turned)
            with e.stage():
                ssd_steps(e)
                ssd_chunks(e, x_turned)
        with ExitStack() as mix, e.stage():
            e.mix = mix
            sample_states(e)
            sample_ssd(e)
            sample_window(e)
        with e.stage():
            window_attention(e)
        resident_rows(e)
        with e.stage():
            mixer_out(e)
        with e.stage():
            cross_attention(e)
        with e.stage():
            moe(e)
            output(e)


_INS = ["x_prompt", "x_sample", "state_ssd", "state_conv", "cache_win_k", "cache_win_v", "cache_mem_k", "cache_mem_v",
        "mem_prompt", "g_mix", "w_in", "conv_w", "conv_b", "dt_bias", "a_log", "d_skip", "g_ssd", "w_ssd_down", "attn_sinks",
        "w_mix_out", "g_cross", "g_mem", "w_cq", "w_ckv", "w_co", "g_moe", "w_route_group", "b_route_group",
        "w_route_expert", "b_route_expert", "w_e_gate", "w_e_up", "w_e_down", "g_final"]
_OUTS = [("y_prompt", (1, SEQ, D)), ("y_sample", (NB, 1, D)),
         ("p_state_ssd", (1, 1, HS, HP, NS)), ("p_state_conv", (1, 1, CK - 1, CD)),
         ("p_cache_win_k", (1, 1, W, NKV, HD)), ("p_cache_win_v", (1, 1, W, NKV, HD)),
         ("p_cache_mem_k", (1, 1, MEM, CH, CHD)), ("p_cache_mem_v", (1, 1, MEM, CH, CHD)),
         ("s_state_ssd", (1, NB, HS, HP, NS)), ("s_state_conv", (1, NB, CK - 1, CD)),
         ("s_cache_win_k", (1, NB, W, NKV, HD)), ("s_cache_win_v", (1, NB, W, NKV, HD))]


def kernel(**inputs):
    import numpy as np
    import concourse.bacc as bacc
    from concourse.bass_utils import run_bass_kernel_spmd

    nc = bacc.Bacc("TRN2", target_bir_lowering=False, num_devices=1)
    arrays, a, o = {}, {}, {}
    for name in _INS:
        x = np.ascontiguousarray(inputs[name])
        arrays["in_" + name] = x
        a[name] = nc.dram_tensor("in_" + name, x.shape, mybir.dt.from_np(x.dtype), kind="ExternalInput").ap()
    for name, shape in _OUTS:
        o[name] = nc.dram_tensor("out_" + name, shape, F32, kind="ExternalOutput").ap()
    hybrid_step(nc, a, o)
    r = run_bass_kernel_spmd(nc, [arrays], core_ids=[0])
    return tuple(r.results[0]["out_" + name] for name, _ in _OUTS)
```

```python
from contextlib import ExitStack, contextmanager

import concourse.bass as bass
from concourse import mybir

F32 = mybir.dt.float32
I32 = mybir.dt.int32
U32 = mybir.dt.uint32
F32R = mybir.dt.float32r
ALU = mybir.AluOpType
ACT = mybir.ActivationFunctionType
AX = mybir.AxisListType

P = 128
D = 1024
KD = D // P
SEQ = 1024
NB = 8
NT = SEQ // P
TILES = NT + 1
T = SEQ + NB
TP = TILES * P
NSPLIT = 3
NW = T // NSPLIT
DI = 2048
HS, HP, NG, NS = 32, 64, 4, 128
HPG = HS // NG
CD = DI + 2 * NG * NS
CT = CD // P
XT = DI // P
XBT = XT + NG
CK = 4
NH, NKV, HD = 16, 4, 64
GQA = NH // NKV
W = 128
MEM, CH, CHD = 256, 4, 128
CW = CH * CHD
MT = MEM // P
NGR, EPG = 4, 8
NE = NGR * EPG
DE = 512
EPS = 1e-6
NEG = -1e30
Z0 = 0
XBC0 = DI
DT0 = XBC0 + CD
Q0 = DT0 + HS
K0 = Q0 + NH * HD
V0 = K0 + NKV * HD
GS0 = V0 + NKV * HD
VDT = NKV * HD + HS
QKT = (NH + NKV) * HD // P
GT = 2 * D // P

G_MIX, G_CROSS, G_MOE, G_MEM, G_SSD = 0, KD, 2 * KD, 3 * KD, 4 * KD
G_ROWS = 4 * KD + XT
CR_STATE, CR_W, CR_B = 0, NB * (CK - 1), NB * (CK - 1) + CK
CR = CR_B + 1


class Env:

    def __init__(self, nc, ctx, a, o):
        self.nc, self.ctx, self.a, self.o = nc, ctx, a, o

        self.stage_sems = []

    def sem(self, name):
        sem = self.nc.alloc_semaphore(name)
        self.stage_sems.append(sem)
        return sem

    @contextmanager
    def stage(self):
        self.stage_sems = []
        yield
        self.nc.clear_and_free_semaphores(self.stage_sems)
        self.nc.all_engine_barrier()

    def dram(self, name, shape, dt=F32):
        return self.nc.dram_tensor(name, shape, dt, kind="Internal").ap()


def bc(ap, shape):
    return ap.to_broadcast(shape)


def constants(e):
    nc, a = e.nc, e.a
    keep = lambda n, s, dt=F32: e.ctx.enter_context(nc.sbuf_tensor(n, s, dt))
    e.ident = keep("ident", [P, P])
    e.tri = keep("tri", [P, P])
    e.below = keep("below", [P, P])
    e.ones = keep("ones", [P, P])
    e.mhalf = keep("mhalf", [P, 16])
    e.eps = keep("eps", [P, 16])
    e.gvec = keep("gvec", [P, G_ROWS])
    e.cvec = keep("cvec", [P, CT, CR])
    e.tails = keep("tails", [P, CT, CK - 1 + NB])
    e.ps = e.ctx.enter_context(nc.psum_tensor("ps", [P, 8, 512], F32))
    ps = e.ps
    made, loaded, turned, copied = e.sem("const_made"), e.sem("const_loaded"), e.sem("const_turned"), e.sem("const_copied")
    with nc.sbuf_tensor("grows", [G_ROWS, P], F32) as grows, nc.sbuf_tensor("crows", [CR, CD], F32) as crows, \
            nc.Block() as block:
        @block.sync
        def _(sp):
            for n, (name, row, rows) in enumerate((("g_mix", G_MIX, KD), ("g_cross", G_CROSS, KD), ("g_moe", G_MOE, KD),
                                                   ("g_mem", G_MEM, KD), ("g_ssd", G_SSD, XT))):
                sp.dma_start(grows[row:row + rows, :], a[name].rearrange("o (k p) -> (o k) p", p=P)).then_inc(loaded, 16)
            sp.dma_start(crows[CR_STATE:CR_W, :], a["state_conv"].rearrange("o b k c -> (o b k) c")).then_inc(loaded, 16)
            sp.dma_start(crows[CR_W:CR_B, :], a["conv_w"][0]).then_inc(loaded, 16)
            sp.dma_start(crows[CR_B:CR, :], a["conv_b"]).then_inc(loaded, 16)

        @block.gpsimd
        def _(pool):
            pool.memset(e.ident[:, :], 0.0)
            pool.memset(e.tri[:, :], 1.0)
            pool.memset(e.below[:, :], 1.0)
            pool.memset(e.ones[:, :], 1.0)
            pool.memset(e.mhalf[:, :], -0.5)
            pool.memset(e.eps[:, :], EPS)
            pool.drain()
            pool.affine_select(out=e.ident[:, :], in_=e.ident[:, :], compare_op=ALU.not_equal, fill=1.0,
                               base=0, pattern=[[-1, P]], channel_multiplier=1)
            pool.affine_select(out=e.tri[:, :], in_=e.tri[:, :], compare_op=ALU.is_ge, fill=0.0,
                               base=0, pattern=[[1, P]], channel_multiplier=-1)
            pool.affine_select(out=e.below[:, :], in_=e.below[:, :], compare_op=ALU.is_ge, fill=0.0,
                               base=-1, pattern=[[-1, P]], channel_multiplier=1)
            pool.drain()
            pool.sem_inc(made, 1)

        @block.tensor
        def _(pe):
            pe.wait_ge(made, 1)
            pe.wait_ge(loaded, 8 * 16)
            pe.transpose(ps[:, 0, 0:G_ROWS], grows[:, :], e.ident[0:G_ROWS, 0:G_ROWS])
            for c in range(CT):
                last = pe.transpose(ps[:, 1 + c // 12, (c % 12) * 32:(c % 12) * 32 + CR],
                                    crows[:, c * P:(c + 1) * P], e.ident[0:CR, 0:CR])
            last.then_inc(turned, 1)

        @block.vector
        def _(dve):
            dve.wait_ge(turned, 1)
            dve.tensor_copy(e.gvec[:, :], ps[:, 0, 0:G_ROWS])
            for h in range(2):
                dve.tensor_copy(e.cvec[:, 12 * h:12 * h + 12, :],
                                ps[:, 1 + h, 0:12 * 32].rearrange("p (c r) -> p c r", r=32)[:, :, 0:CR])


def take_high(dve, high, x):
    return dve.tensor_copy(high.bitcast(F32R), x)


def take_low(eng, low, x, high):
    return eng.tensor_tensor(low.bitcast(F32R), x, high, ALU.subtract)


def split_product(pe, out, lhs, rhs, start, stop):
    r = lambda ap: ap.bitcast(F32R)
    pe.matmul(out, r(lhs[1]), r(rhs[1]), start=start, stop=False)
    pe.matmul(out, r(lhs[1]), r(rhs[0]), start=False, stop=False)
    return pe.matmul(out, r(lhs[0]), r(rhs[1]), start=False, stop=stop)


def rms_tiles(e, name, x, n_tiles, out_turned, grow=None, load=None, gtok=None, store=None, high=None,
              prefetch=(), ready=None, whole=None):
    nc, ps = e.nc, e.ps
    squared, meaned, rooted = (e.sem(f"{name}_{x}") for x in ("squared", "meaned", "rooted"))
    scaled, turned, low_freed, high_freed = (e.sem(f"{name}_{x}") for x in ("scaled", "turned", "low_freed", "high_freed"))
    high_made, split = e.sem(f"{name}_high_made"), e.sem(f"{name}_split")
    kept = [e.sem(f"{name}_kept{i}") for i in range(2)]
    tile = lambda t: slice(t * P, (t + 1) * P)
    GROUP = 2
    groups = [slice(t, min(t + GROUP, n_tiles)) for t in range(0, n_tiles, GROUP)]
    stored = [e.sem(f"{name}_stored{i}") for i in range(2)]
    with nc.sbuf_tensor(name + "_xn", [P, 2, D], F32) as xn, nc.sbuf_tensor(name + "_sq", [P, D], F32) as sq, \
            nc.sbuf_tensor(name + "_ss", [P, n_tiles], F32) as ss, nc.sbuf_tensor(name + "_rs", [P, n_tiles], F32) as rs, \
            ExitStack() as more:
        raw = None if high is None else more.enter_context(nc.sbuf_tensor(name + "_raw", [P, 2, KD, P], F32))
        block = more.enter_context(nc.Block())
        tile_loaded = {t: e.sem(f"{name}_loaded{i}") for i, (_, _, tiles) in enumerate(load or []) for t in tiles[:1]}

        @block.sync
        def _(sp):
            for dst, src, tiles in load or []:
                sp.dma_start(dst, src).then_inc(tile_loaded[tiles[0]], 16)
            if high is not None:
                for t in range(n_tiles):
                    sp.wait_ge(low_freed, t + 1)
                    sp.wait_ge(high_freed, t + 1)
                    sp.dma_start(whole[:, :, tile(t)], raw[:, t % 2]).then_inc(kept[t % 2], 16)
                for b in range(2):
                    sp.wait_ge(kept[b], 16 * ((n_tiles + 1 - b) // 2))
            if store is not None:
                for t in range(n_tiles):
                    sp.wait_ge(scaled, t + 1)
                    sp.dma_start(store[t * P:(t + 1) * P, :], xn[:, t % 2, :]).then_inc(stored[t % 2], 16)
            for dst, src, sem in prefetch:
                sp.dma_start(dst, src).then_inc(sem, 16)
            if store is not None:
                for b in range(2):
                    sp.wait_ge(stored[b], 16 * ((n_tiles + 1 - b) // 2))

        @block.scalar
        def _(act):
            if ready is not None:
                act.wait_ge(ready, 16)

            def square(t):
                if t in tile_loaded:
                    act.wait_ge(tile_loaded[t], 16)
                act.activation(sq[:, :], x[:, t, :], ACT.Square, accum_out=ss[:, t:t + 1]).then_inc(squared, 1)
                act.drain()
            for t in range(min(GROUP + 1, n_tiles)):
                square(t)
            for t in range(n_tiles):
                if t + GROUP + 1 < n_tiles:
                    square(t + GROUP + 1)
                act.wait_ge(turned, 2 * t + 2)
                if high is not None and t >= 2:
                    act.wait_ge(split, t - 1)
                    act.wait_ge(kept[t % 2], 16 * (t // 2))
                for k in range(4, KD):
                    src = ps[:, 2 * (t % 2) + 1, (k - 4) * P:(k - 3) * P]
                    dst = out_turned[:, k, tile(t)] if high is None else raw[:, t % 2, k]
                    if gtok is None:
                        last = act.activation(dst, src, ACT.Copy, scale=e.gvec[:, grow + k:grow + k + 1])
                    else:
                        last = act.activation(dst, src, ACT.Copy)
                last.then_inc(high_freed, 1)

        @block.gpsimd
        def _(pool):
            for t in range(n_tiles):
                for g in [0, 1] if t == 0 else [t // GROUP + 1] if t % GROUP == 0 else []:
                    if g < len(groups):
                        pool.wait_ge(meaned, g + 1)
                        pool.tensor_tensor(rs[:, groups[g]], ss[:, groups[g]], e.mhalf[:, groups[g]], ALU.pow).then_inc(rooted, 1)
                if high is not None:
                    pool.wait_ge(high_made, t + 1)
                    take_low(pool, out_turned[:, :, tile(t)], raw[:, t % 2], high[:, :, tile(t)]).then_inc(split, 1)

        @block.vector
        def _(dve):
            if ready is not None:
                dve.wait_ge(ready, 16)

            def mean(g):
                if g < len(groups):
                    dve.wait_ge(squared, groups[g].stop)
                    dve.tensor_scalar(ss[:, groups[g]], ss[:, groups[g]], 1.0 / D, EPS, ALU.mult, ALU.add).then_inc(meaned, 1)

            def scale(t):
                if t % GROUP == 0:
                    dve.wait_ge(rooted, t // GROUP + 1)
                if t >= 2:
                    dve.wait_ge(turned, 2 * (t - 1))
                    if store is not None:
                        dve.wait_ge(stored[t % 2], 16 * (t // 2))
                last = dve.tensor_scalar(xn[:, t % 2, :], x[:, t, :], rs[:, t:t + 1], None, ALU.mult)
                if gtok is not None:
                    dve.drain()
                    last = dve.tensor_tensor(xn[:, t % 2, :], xn[:, t % 2, :], gtok, ALU.mult)
                last.then_inc(scaled, 1)

            mean(0)
            scale(0)
            mean(1)
            for t in range(n_tiles):
                if t + 1 < n_tiles:
                    scale(t + 1)
                if t % GROUP == 0 and t > 0:
                    mean(t // GROUP + 1)
                dve.wait_ge(turned, 2 * t + 1)
                src = ps[:, 2 * (t % 2), :].rearrange("p (k n) -> p k n", k=4)
                if high is not None and t >= 2:
                    dve.wait_ge(split, t - 1)
                    dve.wait_ge(kept[t % 2], 16 * (t // 2))
                dst = out_turned[:, 0:4, tile(t)] if high is None else raw[:, t % 2, 0:4]
                if gtok is None:
                    last = dve.tensor_tensor(dst, src, bc(e.gvec[:, grow:grow + 4].unsqueeze(2), [P, 4, P]), ALU.mult)
                else:
                    last = dve.tensor_copy(dst, src)
                last.then_inc(low_freed, 1)
                if high is not None and t > 0:
                    dve.wait_ge(low_freed, t)
                    dve.wait_ge(high_freed, t)
                    take_high(dve, high[:, :, tile(t - 1)], raw[:, (t - 1) % 2]).then_inc(high_made, 1)
            if high is not None:
                dve.drain()
                dve.wait_ge(high_freed, n_tiles)
                take_high(dve, high[:, :, tile(n_tiles - 1)], raw[:, (n_tiles - 1) % 2]).then_inc(high_made, 1)

        @block.tensor
        def _(pe):
            for t in range(n_tiles):
                pe.wait_ge(scaled, t + 1)
                if t >= 2:
                    pe.wait_ge(low_freed, t - 1)
                    pe.wait_ge(high_freed, t - 1)
                for k in range(KD):
                    last = pe.transpose(ps[:, 2 * (t % 2) + k // 4, (k % 4) * P:(k % 4 + 1) * P],
                                        xn[:, t % 2, k * P:(k + 1) * P], e.ident[:, :])
                    if k % 4 == 3:
                        last.then_inc(turned, 1)


class ZRows:
    ZB = 256
    BLOCKS = DI // ZB
    TOKENS = [(NT,)] + [(t, t + 1) for t in range(0, NT, 2)]

    def __init__(self, e, st, x):
        self.e, self.x = e, x
        self.raw = st.enter_context(e.nc.sbuf_tensor("z_raw", [P, KD, self.ZB], F32))
        self.w = st.enter_context(e.nc.sbuf_tensor("z_weights", [P, 2, 2, KD, self.ZB], F32))
        self.out = st.enter_context(e.nc.sbuf_tensor("z_out", [P, 2, 2, self.ZB], F32))
        self.units = [(b, tokens) for b in range(self.BLOCKS) for tokens in self.TOKENS]
        self.made_by_pe = self.emptied_by_act = 0
        self.banks = (6, 7)
        e.z_rows = e.dram("z_rows", [TP, DI])
        self.loaded = e.sem("z_loaded")
        self.high_made, self.split, self.slot_free = e.sem("z_high_made"), e.sem("z_split"), e.sem("z_slot_free")
        self.made, self.free = e.sem("z_made"), e.sem("z_free")
        self.stored = [e.sem(f"z_stored{i}") for i in range(2)]

    def load(self, sp, b):
        if b >= 1:
            sp.wait_ge(self.split, b)
        cols = slice(Z0 + b * self.ZB, Z0 + (b + 1) * self.ZB)
        sp.dma_start(self.raw[:, :, :], self.e.a["w_in"][0][:, cols].rearrange("(k p) c -> p k c", p=P)).then_inc(self.loaded, 16)

    def high(self, dve, b):
        dve.wait_ge(self.loaded, 16 * (b + 1))
        if b >= 2:
            dve.wait_ge(self.slot_free, b - 1)
        take_high(dve, self.w[:, b % 2, 1], self.raw[:, :, :]).then_inc(self.high_made, 1)

    def low(self, pool, b):
        pool.wait_ge(self.high_made, b + 1)
        w = self.w[:, b % 2]
        take_low(pool, w[:, 0], self.raw[:, :, :], w[:, 1]).then_inc(self.split, 1)

    def make(self, pe, n):
        ps = self.e.ps
        for u in range(self.made_by_pe, self.made_by_pe + n):
            b, tokens = self.units[u]
            if tokens == self.TOKENS[0]:
                pe.wait_ge(self.split, b + 1)
            if u >= 2:
                pe.wait_ge(self.free, u - 1)
            w = self.w[:, b % 2]
            for i, t in enumerate(tokens):
                for k in range(KD):
                    last = split_product(pe, ps[:, self.banks[u % 2], i * self.ZB:(i + 1) * self.ZB], [x[:, k, t * P:(t + 1) * P] for x in self.x],
                                         [w[:, j, k] for j in range(2)], start=(k == 0), stop=(k == KD - 1))
            last.then_inc(self.made, 1)
            if tokens == self.TOKENS[-1]:
                pe.drain().then_inc(self.slot_free, 1)
        self.made_by_pe += n

    def store(self, act, n):
        ps = self.e.ps
        for u in range(self.emptied_by_act, self.emptied_by_act + n):
            b, tokens = self.units[u]
            act.wait_ge(self.made, u + 1)
            if u >= 2:
                act.wait_ge(self.stored[u % 2], 16 * (u // 2))
            n_t = len(tokens)
            src = ps[:, self.banks[u % 2], 0:n_t * self.ZB].rearrange("p (s c) -> p s c", s=n_t)
            act.activation(self.out[:, u % 2, 0:n_t], src, ACT.Silu).then_inc(self.free, 1)
            act.wait_ge(self.free, u + 1)
            act.dma_start(self.e.z_rows[tokens[0] * P:(tokens[-1] + 1) * P, b * self.ZB:(b + 1) * self.ZB].rearrange("(s p) c -> p s c", p=P),
                          self.out[:, u % 2, 0:n_t]).then_inc(self.stored[u % 2], 16)
        self.emptied_by_act += n

    def wait_sample(self, sp):
        for b in (self.BLOCKS - 2, self.BLOCKS - 1):
            u = self.units.index((b, self.TOKENS[0]))
            sp.wait_ge(self.stored[u % 2], 16 * (u // 2 + 1))

    def settle(self, act):
        for b in range(2):
            act.wait_ge(self.stored[b], 16 * ((self.emptied_by_act + 1 - b) // 2))


def project(e, x):
    nc, a, ps = e.nc, e.a, e.ps
    w_in = a["w_in"][0]
    e.xb_rows = e.dram("xb_rows", [SEQ, XBT * P])
    e.bc_cols = e.dram("bc_cols", [2 * NG, P, SEQ])
    e.qk_cols = e.dram("qk_cols", [QKT, P, T])
    e.vdt_rows = e.dram("vdt_rows", [TP, VDT])
    e.y_rows = e.dram("moe_rows", [SLOTS, D])

    w_ready, w_free = [e.sem(f"proj_w_ready{i}") for i in range(2)], e.sem("proj_w_free")
    w_high, w_split = e.sem("proj_w_high"), e.sem("proj_w_split")
    wv_high, wv_split = e.sem("wv_high"), e.sem("wv_split")
    ps_ready, ps_free = e.sem("proj_ps_ready"), e.sem("proj_ps_free")
    u_ready, u_free = e.sem("conv_u_ready"), e.sem("conv_u_free")
    conv_ready, conv_free = e.sem("conv_ready"), e.sem("conv_free")
    act_ready = e.sem("conv_act_ready")
    turned, turn_free = e.sem("conv_turned"), e.sem("conv_turn_free")
    rows_free = e.sem("conv_rows_free")
    rows_ready, rows_stored = e.sem("conv_rows_ready"), [e.sem(f"conv_rows_stored{i}") for i in range(2)]
    cols_stored = [e.sem(f"conv_cols_stored{i}") for i in range(2)]
    plain_ready, plain_stored = e.sem("plain_ready"), [e.sem(f"plain_stored{i}") for i in range(2)]
    wv_ready = e.sem("wv_ready")
    v_ps, v_free = e.sem("v_ps_ready"), e.sem("v_ps_free")
    v_stored = [e.sem(f"v_stored{i}") for i in range(3)]

    U = 4
    with ExitStack() as st:
        sb = lambda n, s: st.enter_context(nc.sbuf_tensor(n, s, F32))
        wraw = sb("w_raw", [P, 2, KD, P])
        wring = sb("wring", [P, 2, 2, KD, P])
        wv_raw = sb("wv_raw", [P, KD, VDT])
        wv = sb("wv", [P, 2, KD, VDT])
        u = sb("conv_u", [P, 2, CK - 1 + T])
        acc = sb("conv_acc", [P, 2, SEQ])
        y = sb("conv_y", [P, 2, SEQ])
        rows = sb("conv_rows", [P, 2, NT, P])
        plain = sb("plain", [P, 2, T])
        vout = sb("v_out", [P, 3, VDT])
        zero = sb("zero_rows", [P, D])
        zero_made, zero_stored = e.sem("zero_made"), e.sem("zero_stored")
        block = st.enter_context(nc.Block())

        def cols(c):
            return w_in[:, c].rearrange("(k p) c -> p k c", p=P)

        @block.sync
        def _(sp):
            def load(slot, n, col):
                sp.wait_ge(w_split, n + 1)
                sp.dma_start(wraw[:, slot], cols(bass.ds(col, P))).then_inc(w_ready[slot], 16)
            with sp.Fori(0, CT // U) as i:
                for j in range(U):
                    load(j % 2, i * U + j, i * (U * P) + (XBC0 + j * P))
            sp.dma_start(wv_raw[:, :, 0:NKV * HD], cols(slice(V0, V0 + NKV * HD))).then_inc(wv_ready, 16)
            sp.dma_start(wv_raw[:, :, NKV * HD:VDT], cols(slice(DT0, DT0 + HS))).then_inc(wv_ready, 16)
            with sp.Fori(0, QKT // U) as i:
                for j in range(U):
                    load(j % 2, i * U + (CT + j), i * (U * P) + (Q0 + j * P))
            for m in range(QKT // U * U, QKT):
                load(m % 2, CT + m, Q0 + m * P)

        @block.gpsimd
        def _(pool):
            pool.sem_inc(w_split, 2)
            pool.sem_inc(rows_free, 2)

            def low(par, n):
                pool.wait_ge(w_high, n + 1)
                take_low(pool, wring[:, par, 0], wraw[:, par], wring[:, par, 1]).then_inc(w_split, 1)

            for n in range(3):
                low(n % 2, n)
            with pool.Fori(0, XBT // U) as i:
                for j in range(U):
                    low((j + 3) % 2, i * U + (j + 3))
                    pool.wait_ge(rows_ready, i * U + (j + 1))
                    pool.dma_start(e.xb_rows[:, bass.ds(i * (U * P) + j * P, P)].rearrange("(t p) c -> p t c", p=P),
                                   rows[:, j % 2]).then_inc(rows_stored[j % 2], 16)
                    pool.wait_ge(rows_stored[j % 2], i * (U * 8) + (j // 2 * 16 + 16))
                    pool.sem_inc(rows_free, 1)
            for n in range(XBT + 3, CT + 2):
                low(n % 2, n)
            pool.wait_ge(wv_high, 1)
            take_low(pool, wv[:, 0], wv_raw[:, :, :], wv[:, 1]).then_inc(wv_split, 1)
            with pool.Fori(CT // 2 + 1, (CT + QKT) // 2) as use:
                for par in range(2):
                    low(par, use * 2 + par)
            pool.memset(zero[:, :], 0.0).then_inc(zero_made, 1)
            pool.wait_ge(zero_made, 1)
            for b in range(NMORE):
                pool.dma_start(e.y_rows[(NBASE + b) * P:(NBASE + b + 1) * P, :], zero[:, :]).then_inc(zero_stored, 16)
            pool.wait_ge(zero_stored, 16 * NMORE)

        @block.vector
        def _(dve):
            dve.memset(u[:, :, 0:CK - 1], 0.0)
            dve.drain().then_inc(u_free, 2)
            dve.sem_inc(turn_free, 1)

            def conv(par, n):
                dve.wait_ge(u_ready, n + 1)
                dve.wait_ge(conv_free, n + 1)
                cv = e.cvec[:, bass.ds(n, 1), :].rearrange("p o r -> p (o r)")
                dve.tensor_scalar(acc[:, par], u[:, par, CK - 1:CK - 1 + SEQ], cv[:, CR_W + CK - 1:CR_W + CK], cv[:, CR_B:CR], ALU.mult, ALU.add)
                for k in range(CK - 1):
                    dve.drain()
                    last = dve.scalar_tensor_tensor(out=acc[:, par], in0=u[:, par, k:k + SEQ], scalar=cv[:, CR_W + k:CR_W + k + 1],
                                                    in1=acc[:, par], op0=ALU.mult, op1=ALU.add)
                last.then_inc(conv_ready, 1)
                dve.tensor_copy(e.tails[:, bass.ds(n, 1), :].rearrange("p o r -> p (o r)"), u[:, par, SEQ:SEQ + CK - 1 + NB])
                dve.drain().then_inc(u_free, 1)

            def rows_out(par, n):
                dve.wait_ge(turned, n + 1)
                dve.wait_ge(rows_free, n + 1)
                dve.tensor_copy(rows[:, par], ps[:, 6:8, :].rearrange("p b (t c) -> p (b t) c", c=P)).then_inc(rows_ready, 1)
                dve.drain().then_inc(turn_free, 1)

            def high(par, use):
                dve.wait_ge(w_ready[par], use * 16 + 16)
                dve.wait_ge(w_free, use * 2 + (par + 1))
                take_high(dve, wring[:, par, 1], wraw[:, par]).then_inc(w_high, 1)

            high(0, 0)
            high(1, 0)
            conv(0, 0)
            high(0, 1)
            with dve.Fori(0, XBT // U) as i:
                for j in range(U):
                    conv((j + 1) % 2, i * U + (j + 1))
                    high((j + 3) % 2, i * (U // 2) + (j + 3) // 2)
                    rows_out(j % 2, i * U + j)
            for n in range(XBT + 1, CT):
                conv(n % 2, n)
                high(n % 2, (n + 2) // 2)
            dve.wait_ge(wv_ready, 32)
            take_high(dve, wv[:, 1], wv_raw[:, :, :]).then_inc(wv_high, 1)
            with dve.Fori(CT // 2 + 1, (CT + QKT) // 2) as use:
                for par in range(2):
                    high(par, use)

        @block.tensor
        def _(pe):
            pe.sem_inc(w_free, 2)

            def product(par, n):
                pe.wait_ge(w_split, n + 3)
                pe.wait_ge(ps_free, n + 1)
                for k in range(KD):
                    for s in range(NSPLIT):
                        last = split_product(pe, ps[:, 3 * par + s, 0:NW], [wring[:, par, j, k] for j in range(2)],
                                             [xs[:, k, s * NW:(s + 1) * NW] for xs in x], start=(k == 0), stop=(k == KD - 1))
                last.then_inc(ps_ready, 1)
                pe.drain().then_inc(w_free, 1)

            def turn(par, n):
                pe.wait_ge(act_ready, n + 1)
                pe.wait_ge(turn_free, n + 1)
                for t in range(NT):
                    last = pe.transpose(ps[:, 6 + t // 4, (t % 4) * P:(t % 4 + 1) * P], y[:, par, t * P:(t + 1) * P], e.ident[:, :])
                last.then_inc(turned, 1)

            product(0, 0)
            with pe.Fori(0, XBT // U) as i:
                for j in range(U):
                    product((j + 1) % 2, i * U + (j + 1))
                    turn(j % 2, i * U + j)
            for n in range(XBT + 1, CT):
                product(n % 2, n)
            with pe.Fori(0, QKT // U) as i:
                for j in range(U):
                    product(j % 2, i * U + (CT + j))
            for m in range(QKT // U * U, QKT):
                product(m % 2, CT + m)

            pe.wait_ge(wv_split, 1)
            for t in range(TILES):
                pe.wait_ge(v_free, t + 1)
                for k in range(KD):
                    last = split_product(pe, ps[:, t % 6, 0:VDT], [xs[:, k, t * P:(t + 1) * P] for xs in x], [wv[:, j, k] for j in range(2)],
                                         start=(k == 0), stop=(k == KD - 1))
                last.then_inc(v_ps, 1)

        @block.scalar
        def _(act):
            act.sem_inc(ps_free, 2)
            act.sem_inc(conv_free, 2)
            for b in range(2):
                act.sem_inc(plain_stored[b], 16)

            def empty(par, dst, func=ACT.Copy):
                for s in range(NSPLIT):
                    last = act.activation(dst[:, s * NW:(s + 1) * NW], ps[:, 3 * par + s, 0:NW], func)
                return last

            def conv_tile(par, n):
                act.wait_ge(ps_ready, n + 1)
                act.wait_ge(u_free, n + 1)
                empty(par, u[:, par, CK - 1:]).then_inc(u_ready, 1)
                act.drain().then_inc(ps_free, 1)
                act.wait_ge(conv_ready, n + 1)
                act.activation(y[:, par], acc[:, par], ACT.Silu).then_inc(act_ready, 1)
                act.drain().then_inc(conv_free, 1)

            def x_tile(par, n, first):
                if not first:
                    act.wait_ge(turned, n + (-1))
                conv_tile(par, n)
            x_tile(0, 0, True)
            x_tile(1, 1, True)
            for n in (2, 3):
                x_tile(n % 2, n, False)
            with act.Fori(1, XT // U) as i:
                for j in range(U):
                    x_tile(j % 2, i * U + j, False)
            for n in range(XT, CT):
                if n - 2 < XBT:
                    act.wait_ge(turned, n - 1)
                if n - 2 >= XT:
                    act.wait_ge(cols_stored[n % 2], 16 * ((n - XT) // 2))
                conv_tile(n % 2, n)
                act.wait_ge(act_ready, n + 1)
                act.dma_start(e.bc_cols[n - XT], y[:, n % 2]).then_inc(cols_stored[n % 2], 16)

            def plain_tile(par, n, earlier, dst, func):
                act.wait_ge(ps_ready, n + (CT + 1))
                act.wait_ge(plain_stored[par], earlier * 16 + 16)
                empty(par, plain[:, par], func).then_inc(plain_ready, 1)
                act.drain().then_inc(ps_free, 1)
                act.dma_start(dst, plain[:, par]).then_inc(plain_stored[par], 16)

            with act.Fori(0, QKT // U) as i:
                for j in range(U):
                    plain_tile(j % 2, i * U + j, i * 2 + j // 2, e.qk_cols[bass.ds(i * U + j, 1)].rearrange("o p t -> (o p) t"), ACT.Copy)
            for m in range(QKT // U * U, QKT):
                plain_tile(m % 2, m, m // 2, e.qk_cols[m], ACT.Copy)
            act.drain().then_inc(v_free, 6)
            for t in range(TILES):
                act.wait_ge(v_ps, t + 1)
                if t >= 3:
                    act.wait_ge(v_stored[t % 3], 16 * (t // 3))
                act.activation(vout[:, t % 3], ps[:, t % 6, 0:VDT], ACT.Copy)
                act.drain().then_inc(v_free, 1)
                act.dma_start(e.vdt_rows[t * P:(t + 1) * P, :], vout[:, t % 3]).then_inc(v_stored[t % 3], 16)
            for b in range(2):
                act.wait_ge(cols_stored[b], 16 * (CT - XT) // 2)
                act.wait_ge(plain_stored[b], 16 * (QKT // 2 + 1))
            for b in range(3):
                act.wait_ge(v_stored[b], 16 * TILES // 3)



def mixer_norm(e, x_low, x_high):
    nc, a = e.nc, e.a
    zeroed = e.sem("mixer_zeroed")
    with nc.sbuf_tensor("x_rows", [P, TILES, D], F32) as x:
        with nc.Block() as block:
            @block.vector
            def _(dve):
                dve.memset(x[:, NT, :], 0.0)
        rms_tiles(e, "mixer", x, TILES, x_low, grow=G_MIX, load=x_loads(e, x), high=x_high, whole=e.x_cols)


def x_loads(e, x):
    rows = e.a["x_prompt"][0].rearrange("(t p) d -> p t d", p=P)
    return [(x[0:NB, NT, :], e.a["x_sample"][:, 0, :], (NT,))] + [(x[:, t:t + 2, :], rows[:, t:t + 2], (t, t + 1)) for t in range(0, NT, 2)]


def ssd_vectors(e):
    keep = lambda n, s: e.ctx.enter_context(e.nc.sbuf_tensor(n, s, F32))
    e.dt = keep("dt", [P, TILES, HS])
    e.da = keep("da", [P, TILES, HS])
    e.d_skip = keep("d_skip", [P, HS])


def ssd_steps(e, z):
    nc, a = e.nc, e.a
    loaded, s_v, s_a = e.sem("dt_loaded"), e.sem("dt_vector_step"), e.sem("dt_scalar_step")
    with ExitStack() as st:
        sb = lambda n, s: st.enter_context(nc.sbuf_tensor(n, s, F32))
        raw, e1, ln = sb("dt_raw", [P, TILES, HS]), sb("dt_exp", [P, TILES, HS]), sb("dt_ln", [P, TILES, HS])
        u, d = sb("dt_u", [P, TILES, HS]), sb("dt_d", [P, TILES, HS])
        bias, alog = sb("dt_bias_all", [P, HS]), sb("a_log_all", [P, HS])
        block = st.enter_context(nc.Block())

        @block.sync
        def _(sp):
            z.load(sp, 0)
            sp.dma_start(raw[:, :, :], e.vdt_rows[:, NKV * HD:VDT].rearrange("(t p) c -> p t c", p=P)).then_inc(loaded, 16)
            for name, dst in (("dt_bias", bias), ("a_log", alog), ("d_skip", e.d_skip)):
                sp.dma_start(dst[:, :], a[name].to_broadcast([P, HS])).then_inc(loaded, 16)
            z.load(sp, 1)

        @block.gpsimd
        def _(pool):
            z.low(pool, 0)
            z.low(pool, 1)

        @block.vector
        def _(dve):
            z.high(dve, 0)
            dve.wait_ge(loaded, 64)
            dve.tensor_tensor(raw[:, :, :], raw[:, :, :], bc(bias[:, :].unsqueeze(1), [P, TILES, HS]), ALU.add)
            dve.drain()
            dve.tensor_scalar(u[:, :, :], raw[:, :, :], -1.0, None, ALU.mult)
            dve.drain()
            dve.tensor_tensor(d[:, :, :], raw[:, :, :], u[:, :, :], ALU.min).then_inc(s_v, 1)
            dve.wait_ge(s_a, 2)
            dve.tensor_scalar(u[:, :, :], e1[:, :, :], 1.0, None, ALU.add).then_inc(s_v, 1)
            dve.drain()
            dve.tensor_scalar(d[:, :, :], u[:, :, :], -1.0, None, ALU.add)
            dve.drain()
            dve.tensor_scalar(e.dt[:, :, :], d[:, :, :], 0.0, None, ALU.is_equal)
            dve.tensor_scalar(raw[:, :, :], raw[:, :, :], 0.0, None, ALU.max)
            dve.drain()
            dve.tensor_tensor(d[:, :, :], d[:, :, :], e.dt[:, :, :], ALU.add)
            dve.tensor_tensor(e.dt[:, :, :], e.dt[:, :, :], e1[:, :, :], ALU.mult)
            dve.drain()
            dve.reciprocal(d[:, :, :], d[:, :, :])
            dve.tensor_tensor(raw[:, :, :], raw[:, :, :], e.dt[:, :, :], ALU.add)
            dve.drain()
            dve.tensor_tensor(d[:, :, :], d[:, :, :], e1[:, :, :], ALU.mult)
            dve.drain()
            dve.wait_ge(s_a, 3)
            dve.tensor_tensor(d[:, :, :], d[:, :, :], ln[:, :, :], ALU.mult)
            dve.tensor_scalar(alog[:, :], alog[:, :], -1.0, None, ALU.mult)
            dve.drain()
            dve.tensor_tensor(e.dt[:, :, :], raw[:, :, :], d[:, :, :], ALU.add)
            dve.drain()
            dve.tensor_tensor(e.da[:, :, :], e.dt[:, :, :], bc(alog[:, :].unsqueeze(1), [P, TILES, HS]), ALU.mult)
            z.high(dve, 1)

        @block.tensor
        def _(pe):
            z.make(pe, 3)

        @block.scalar
        def _(act):
            act.wait_ge(loaded, 64)
            act.activation(alog[:, :], alog[:, :], ACT.Exp).then_inc(s_a, 1)
            act.wait_ge(s_v, 1)
            act.activation(e1[:, :, :], d[:, :, :], ACT.Exp).then_inc(s_a, 1)
            act.wait_ge(s_v, 2)
            act.activation(ln[:, :, :], u[:, :, :], ACT.Ln).then_inc(s_a, 1)
            z.store(act, 3)



def ssd_chunks(e):
    nc, a, ps = e.nc, e.a, e.ps
    e.gate_cols = e.dram("gate_cols", [GT, P, T])
    names = ("in_ready0", "in_ready1", "in_pe", "in_pool", "z_ready", "z_free", "gw_ready0", "gw_ready1", "gate_w_free", "gate_made", "gate_free",
             "gate_exp", "gate_out", "gate_stored0", "gate_stored1", "sums", "decays", "decays_pool", "decays_dve",
             "rtri_ready", "rtri_free", "seg_ready", "seg_free", "e_ready", "e_free", "cb_ready", "cb_free", 
             "m_ready", "m_free", "xdt_ready", "xdt_free", "xw_ready", "xw_free", "xd_ready", "xd_free",
             "inter", "inter_free", "intra", "intra_free", "scaled", "upd", "state_ready", "gated", "gated_free", "sums_free", "upd_free",
             "squared", "rooted", "normed", "normed_free", "turned", "turn_free", "y_stored")
    s = {n: e.sem("ssd_" + n) for n in names}
    x_ready = [e.sem(f"ssd_x_ready{i}") for i in range(NSPLIT)]
    XW = XBT * P
    with ExitStack() as st:
        sb = lambda n, sh: st.enter_context(nc.sbuf_tensor(n, sh, F32))
        xb = sb("ssd_xb", [P, 2, XW])
        bcc = sb("ssd_bc", [P, 2, 2 * NG, P])
        z = sb("ssd_z", [P, DI])
        gw = sb("gate_w", [P, 2, KD, P])
        x_turned = sb("x_turned", [P, KD, T])
        go = sb("gate_out", [P, 2, NW])
        rtri = sb("ssd_rtri", [P, 2, HPG, P])
        ee = sb("ssd_e", [P, 2, HPG, P])
        mm = sb("ssd_m", [P, 2, HPG, P])
        cbm = sb("ssd_cbm", [P, NG, P])
        dec = sb("ssd_dec", [P, 2, 3 * HS])
        wdt = sb("ssd_wdt", [P, HS])
        xdt = sb("ssd_xdt", [P, HS, HP])
        xw = sb("ssd_xw", [P, HS, HP])
        xd = sb("ssd_xd", [P, HS, HP])
        state = sb("ssd_state", [P, HS, HP])
        y = sb("ssd_y", [P, 2, HS, HP])
        sq = sb("ssd_sq", [P, 512])
        yn = sb("ssd_yn", [P, DI])
        ss, rs = sb("ssd_ss", [P, NG]), sb("ssd_rs", [P, NG])
        da, dt = sb("ssd_da_now", [P, HS]), sb("ssd_dt_now", [P, HS])
        yc = sb("ssd_ycols", [P, XT, P])
        hs = lambda g: slice(g * HPG, (g + 1) * HPG)
        TURN_BANKS = (3, 0)
        GATE_BEFORE, GATE_AFTER = ((0,), (1,), (3,), (4,)), ((), (2,), (), (5,))
        gc = lambda g: slice(g * 512, (g + 1) * 512)
        bank = lambda b: ps[:, b, :].rearrange("p (h c) -> p h c", h=HPG)

        with nc.Block() as block:
            @block.sync
            def _(sp):
                for b in range(2):
                    sp.sem_inc(s[f"gate_stored{b}"], 16)

                def inputs(n, par):
                    for who in ("in_pe", "in_pool"):
                        sp.wait_ge(s[who], n + 1)
                    sp.dma_start(xb[:, par], e.xb_rows[bass.ds(n * P, P), :]).then_inc(s[f"in_ready{par}"], 16)
                    sp.dma_start(bcc[:, par], e.bc_cols[:, :, bass.ds(n * P, P)].rearrange("g p t -> p g t")).then_inc(s[f"in_ready{par}"], 16)

                def gate_weights(n, j):
                    sp.wait_ge(s["gate_w_free"], n * 2 + (j + 1))
                    sp.dma_start(gw[:, j], a["w_in"][0][:, bass.ds(n * (2 * P) + (GS0 + j * P), P)].rearrange("(k p) c -> p k c", p=P)).then_inc(s[f"gw_ready{j}"], 16)

                def load_z(n):
                    sp.wait_ge(s["z_free"], n + 1)
                    sp.dma_start(z[:, :], e.z_rows[bass.ds(n * P, P), :]).then_inc(s["z_ready"], 16)

                def chunk(n, par, k, last=False):
                    if not last:
                        inputs(n + 1, 1 - par)
                    for part in range(2 * NSPLIT):
                        j, q = part // NSPLIT, part % NSPLIT
                        sp.wait_ge(s["gate_out"], n * (2 * NSPLIT) + (part + 1))
                        tile = e.gate_cols[bass.ds(n * 2 + j, 1)].rearrange("o p t -> (o p) t")
                        sp.dma_start(tile[:, q * NW:(q + 1) * NW], go[:, part % 2]).then_inc(s[f"gate_stored{part % 2}"], 16)
                        if q == NSPLIT - 1 and not last:
                            gate_weights(n + 1, j)
                    if not last:
                        load_z(n + 1)
                inputs(0, 0)
                gate_weights(0, 0)
                for q in range(NSPLIT):
                    cols = slice(q * NW, (q + 1) * NW)
                    sp.dma_start(x_turned[:, :, cols], e.x_cols[:, :, cols]).then_inc(x_ready[q], 16)
                    if q == 0:
                        load_z(0)
                gate_weights(0, 1)
                chunk(0, 0, 0)
                with sp.Fori(0, (NT - 2) // 2) as i:
                    chunk(i * 2 + 1, 1, i)
                    chunk(i * 2 + 2, 0, i + 1)
                chunk(NT - 1, 1, NT // 2 - 1, last=True)
                for b in range(2):
                    sp.wait_ge(s[f"gate_stored{b}"], 16 * (GT * NSPLIT // 2 + 1))

            def wait_in(eng, par, k):
                eng.wait_ge(s[f"in_ready{par}"], k * 32 + 32)

            @block.gpsimd
            def _(pool):
                pool.memset(state[:, :, :], 0.0)
                pool.drain().then_inc(s["state_ready"], NG)
                pool.sem_inc(s["in_pool"], 2)
                pool.sem_inc(s["decays_pool"], 2)

                def root(n):
                    pool.wait_ge(s["squared"], n + 1)
                    pool.tensor_tensor(ss[:, :], ss[:, :], e.eps[:, 0:NG], ALU.add)
                    pool.drain()
                    pool.tensor_tensor(rs[:, :], ss[:, :], e.mhalf[:, 0:NG], ALU.pow).then_inc(s["rooted"], 1)

                def chunk(n, par, k, first=False):
                    pool.tensor_copy(da[:, :], e.da[:, bass.ds(n, 1), :].rearrange("p o h -> p (o h)"))
                    pool.tensor_copy(dt[:, :], e.dt[:, bass.ds(n, 1), :].rearrange("p o h -> p (o h)"))
                    pool.drain()
                    x = xb[:, par, 0:DI].rearrange("p (h c) -> p h c", c=HP)

                    def running(g):
                        pool.wait_ge(s["rtri_free"], n * NG + (g + 1))
                        pool.tensor_tensor(rtri[:, g % 2], bc(e.tri[:, :].unsqueeze(1), [P, HPG, P]),
                                           bc(da[:, hs(g)].unsqueeze(2), [P, HPG, P]), ALU.mult).then_inc(s["rtri_ready"], 1)
                    running(0)
                    running(1)
                    wait_in(pool, par, k)
                    pool.wait_ge(s["xdt_free"], n + 1)
                    pool.tensor_tensor(xdt[:, :, :], x, bc(dt[:, :].unsqueeze(2), [P, HS, HP]), ALU.mult).then_inc(s["xdt_ready"], 1)
                    running(2)
                    pool.wait_ge(s["decays"], n + 1)
                    pool.wait_ge(s["xw_free"], n + 1)
                    pool.tensor_tensor(wdt[:, :], dec[:, par, HS:2 * HS], dt[:, :], ALU.mult)
                    pool.drain()
                    pool.tensor_tensor(xw[:, :, :], x, bc(wdt[:, :].unsqueeze(2), [P, HS, HP]), ALU.mult).then_inc(s["xw_ready"], 1)
                    running(3)
                    pool.wait_ge(s["xd_free"], n + 1)
                    pool.tensor_tensor(xd[:, :, :], x, bc(e.d_skip[:, :].unsqueeze(2), [P, HS, HP]), ALU.mult).then_inc(s["xd_ready"], 1)
                    pool.drain().then_inc(s["in_pool"], 1)
                    if not first:
                        root(n - 1)
                    for g in range(NG):
                        pool.wait_ge(s["inter"], n * NG + (g + 1))
                        pool.wait_ge(s["state_ready"], n * NG + (g + 1))
                        pool.tensor_tensor(state[:, hs(g)], state[:, hs(g)],
                                           bc(dec[:, par, 2 * HS + g * HPG:2 * HS + (g + 1) * HPG].unsqueeze(2), [P, HPG, HP]),
                                           ALU.mult).then_inc(s["scaled"], 1)
                    pool.drain().then_inc(s["decays_pool"], 1)

                chunk(0, 0, 0, first=True)
                with pool.Fori(0, (NT - 2) // 2) as i:
                    chunk(i * 2 + 1, 1, i)
                    chunk(i * 2 + 2, 0, i + 1)
                chunk(NT - 1, 1, NT // 2 - 1)
                root(NT - 1)

            @block.tensor
            def _(pe):
                pe.sem_inc(s["in_pe"], 2)
                pe.sem_inc(s["rtri_free"], 2)
                pe.sem_inc(s["m_free"], 2)
                pe.sem_inc(s["xdt_free"], 1)
                pe.sem_inc(s["gate_w_free"], 2)
                pe.sem_inc(s["xw_free"], 1)

                def turn(n, chunks):
                    pe.wait_ge(s["normed"], n + 1)
                    pe.wait_ge(s["cb_free"], chunks + 1)
                    pe.wait_ge(s["sums_free"], chunks + 1)
                    for q in range(XT // 4):
                        pe.wait_ge(s["turn_free"], n * (XT // 4) + (q + 1))
                        for k in range(4):
                            last = pe.transpose(ps[:, TURN_BANKS[q % 2], k * P:(k + 1) * P], yn[:, (4 * q + k) * P:(4 * q + k + 1) * P], e.ident[:, :])
                        last.then_inc(s["turned"], 1)
                    pe.drain().then_inc(s["normed_free"], 1)

                def gate_part(n, part):
                    j, q = part // NSPLIT, part % NSPLIT
                    if q == 0:
                        pe.wait_ge(s[f"gw_ready{j}"], n * 16 + 16)
                    if isinstance(n, int) and n == 0 and j == 0:
                        pe.wait_ge(x_ready[q], 16)
                    pe.wait_ge(s["gate_free"], n * (2 * NSPLIT) + (part + 1))
                    for k in range(KD):
                        last = pe.matmul(ps[:, 7, 0:NW], gw[:, j, k], x_turned[:, k, q * NW:(q + 1) * NW], start=(k == 0), stop=(k == KD - 1))
                    last.then_inc(s["gate_made"], 1)
                    if q == NSPLIT - 1:
                        pe.drain().then_inc(s["gate_w_free"], 1)

                def chunk(n, par, k, first=False):
                    da = e.da[:, bass.ds(n, 1), :].rearrange("p o h -> p (o h)")
                    wait_in(pe, par, k)
                    pe.wait_ge(s["cb_free"], n + 1)
                    if not first:
                        pe.wait_ge(s["turn_free"], n * (XT // 4) + (1 - XT // 4))
                    for g in range(NG):
                        last = pe.matmul(ps[:, 3, g * P:(g + 1) * P], bcc[:, par, g], bcc[:, par, NG + g], start=True, stop=True)
                    last.then_inc(s["cb_ready"], 1)
                    pe.wait_ge(s["sums_free"], n + 1)
                    if not first:
                        pe.wait_ge(s["turn_free"], n * (XT // 4) + (2 - XT // 4))
                    pe.matmul(ps[:, 0, 0:HS], e.tri[:, :], da, start=True, stop=True)
                    pe.matmul(ps[:, 0, HS:2 * HS], e.below[:, :], da, start=True, stop=True)
                    pe.matmul(ps[:, 0, 2 * HS:3 * HS], e.ones[:, :], da, start=True, stop=True).then_inc(s["sums"], 1)

                    def segments(g):
                        pe.wait_ge(s["rtri_ready"], n * NG + (g + 1))
                        pe.wait_ge(s["seg_free"], n * NG + (g + 1))
                        for b in range(2):
                            last = pe.matmul(ps[:, 1 + b, :], e.below[:, :], rtri[:, g % 2, 4 * b:4 * b + 4].rearrange("p h c -> p (h c)"),
                                             start=True, stop=True)
                        last.then_inc(s["seg_ready"], 1)
                        pe.drain().then_inc(s["rtri_free"], 1)
                    segments(0)
                    for g in range(NG):
                        pe.wait_ge(s["state_ready"], n * NG + (g + 1))
                        pe.wait_ge(s["inter_free"], n * NG + (g + 1))
                        pe.matmul(ps[:, 5, :], bcc[:, par, NG + g], state[:, hs(g)].rearrange("p h c -> p (h c)"),
                                  start=True, stop=True).then_inc(s["inter"], 1)
                        for part in GATE_BEFORE[g]:
                            gate_part(n, part)
                        if g < NG - 1:
                            segments(g + 1)
                        pe.wait_ge(s["m_ready"], n * NG + (g + 1))
                        pe.wait_ge(s["xdt_ready"], n + 1)
                        pe.wait_ge(s["intra_free"], n * NG + (g + 1))
                        for h in range(HPG):
                            last = pe.matmul(ps[:, 4, h * HP:(h + 1) * HP], mm[:, g % 2, h], xdt[:, g * HPG + h], start=True, stop=True)
                        last.then_inc(s["intra"], 1)
                        pe.drain().then_inc(s["m_free"], 1)
                        pe.wait_ge(s["xw_ready"], n + 1)
                        pe.wait_ge(s["upd_free"], n * NG + (g + 1))
                        pe.matmul(ps[:, 6, :], xb[:, par, DI + g * NS:DI + (g + 1) * NS], xw[:, hs(g)].rearrange("p h c -> p (h c)"),
                                  start=True, stop=True).then_inc(s["upd"], 1)
                        for part in GATE_AFTER[g]:
                            gate_part(n, part)
                    pe.drain().then_inc(s["in_pe"], 1)
                    pe.sem_inc(s["xdt_free"], 1)
                    pe.sem_inc(s["xw_free"], 1)
                    if not first:
                        turn(n - 1, n + 1)
                chunk(0, 0, 0, first=True)
                with pe.Fori(0, (NT - 2) // 2) as i:
                    chunk(i * 2 + 1, 1, i)
                    chunk(i * 2 + 2, 0, i + 1)
                chunk(NT - 1, 1, NT // 2 - 1)
                turn(NT - 1, NT)

            @block.scalar
            def _(act):
                act.sem_inc(s["seg_free"], 1)
                act.sem_inc(s["sums_free"], 1)
                act.sem_inc(s["turn_free"], 2)
                act.sem_inc(s["gated_free"], 2)
                act.sem_inc(s["gate_free"], 1)
                act.sem_inc(s["y_stored"], 16)

                def gate_part(n, part):
                    b = part % 2
                    act.wait_ge(s["gate_made"], n * (2 * NSPLIT) + (part + 1))
                    act.wait_ge(s[f"gate_stored{b}"], n * (NSPLIT * 16) + (part // 2 + 1) * 16)
                    act.activation(go[:, b], ps[:, 7, 0:NW], ACT.Exp, scale=-1.0).then_inc(s["gate_exp"], 1)
                    act.drain().then_inc(s["gate_free"], 1)

                def columns(n):
                    act.wait_ge(s["y_stored"], n * 16 + 16)
                    for q in range(XT // 4):
                        act.wait_ge(s["turned"], n * (XT // 4) + (q + 1))
                        for j in range(4):
                            f = 4 * q + j
                            last = act.activation(yc[:, f], ps[:, TURN_BANKS[q % 2], j * P:(j + 1) * P], ACT.Copy,
                                                  scale=e.gvec[:, G_SSD + f:G_SSD + f + 1])
                        act.drain().then_inc(s["turn_free"], 1)
                    col = slice(n * P, (n + 1) * P) if isinstance(n, int) else bass.ds(n * P, P)
                    act.dma_start(e.y_cols[:, :, col].rearrange("f p t -> p f t"), yc[:, :, :]).then_inc(s["y_stored"], 16)

                def squares(n, par):
                    act.wait_ge(s["gated"], n + 1)
                    for g in range(NG):
                        last = act.activation(sq[:, :], y[:, par, hs(g)].rearrange("p h c -> p (h c)"), ACT.Square,
                                              scale=float(DI // NG) ** -0.5, accum_out=ss[:, g:g + 1])
                        if g < NG - 1:
                            act.drain()
                    last.then_inc(s["squared"], 1)

                def norm(n, par):
                    act.wait_ge(s["rooted"], n + 1)
                    act.wait_ge(s["normed_free"], n + 1)
                    for g in range(NG):
                        last = act.activation(yn[:, gc(g)], y[:, par, hs(g)].rearrange("p h c -> p (h c)"), ACT.Copy, scale=rs[:, g:g + 1])
                    last.then_inc(s["normed"], 1)
                    act.drain().then_inc(s["gated_free"], 1)

                def chunk(n, par, k, first=False):
                    act.wait_ge(s["sums"], n + 1)
                    act.wait_ge(s["decays_pool"], n + 1)
                    act.wait_ge(s["decays_dve"], n + 1)
                    act.activation(dec[:, par], ps[:, 0, 0:3 * HS], ACT.Exp).then_inc(s["decays"], 1)
                    act.drain().then_inc(s["sums_free"], 1)
                    for g in range(NG):
                        act.wait_ge(s["seg_ready"], n * NG + (g + 1))
                        act.wait_ge(s["e_free"], n * NG + (g + 1))
                        act.activation(ee[:, g % 2].rearrange("p h c -> p (h c)"), ps[:, 1:3, :].rearrange("p b c -> p (b c)"),
                                       ACT.Exp).then_inc(s["e_ready"], 1)
                        act.drain().then_inc(s["seg_free"], 1)
                        for part in (GATE_AFTER[g - 1] if g > 0 else ()) + GATE_BEFORE[g]:
                            gate_part(n, part)
                        if g == 0 and not first:
                            squares(n - 1, 1 - par)
                        if g == 2 and not first:
                            norm(n - 1, 1 - par)
                    for part in GATE_AFTER[NG - 1]:
                        gate_part(n, part)
                    if not first:
                        columns(n - 1)
                chunk(0, 0, 0, first=True)
                with act.Fori(0, (NT - 2) // 2) as i:
                    chunk(i * 2 + 1, 1, i)
                    chunk(i * 2 + 2, 0, i + 1)
                chunk(NT - 1, 1, NT // 2 - 1)
                squares(NT - 1, 1)
                norm(NT - 1, 1)
                columns(NT - 1)
                act.wait_ge(s["y_stored"], 16 * (NT + 1))

            @block.vector
            def _(dve):
                for name in ("e_free", "decays_dve"):
                    dve.sem_inc(s[name], 2)
                for name in ("cb_free", "inter_free", "intra_free", "upd_free", "xd_free", "normed_free", "z_free"):
                    dve.sem_inc(s[name], 1)

                def gate_part(n, part):
                    dve.wait_ge(s["gate_exp"], n * (2 * NSPLIT) + (part + 1))
                    dve.tensor_scalar(go[:, part % 2], go[:, part % 2], 1.0, None, ALU.add)
                    dve.drain()
                    dve.reciprocal(go[:, part % 2], go[:, part % 2]).then_inc(s["gate_out"], 1)

                def chunk(n, par, k):
                    dve.wait_ge(s["cb_ready"], n + 1)
                    dve.tensor_tensor(cbm[:, :, :], ps[:, 3, :].rearrange("p (g c) -> p g c", g=NG), bc(e.tri[:, :].unsqueeze(1), [P, NG, P]), ALU.mult)
                    dve.drain().then_inc(s["cb_free"], 1)
                    dve.wait_ge(s["gated_free"], n + 1)

                    def masked(g):
                        dve.wait_ge(s["e_ready"], n * NG + (g + 1))
                        dve.wait_ge(s["m_free"], n * NG + (g + 1))
                        dve.tensor_tensor(mm[:, g % 2], ee[:, g % 2], bc(cbm[:, g].unsqueeze(1), [P, HPG, P]), ALU.mult).then_inc(s["m_ready"], 1)
                        dve.drain().then_inc(s["e_free"], 1)
                    masked(0)
                    for g in range(NG):
                        if g == 0:
                            dve.wait_ge(s["decays"], n + 1)
                        dve.wait_ge(s["inter"], n * NG + (g + 1))
                        yg = y[:, par, hs(g)]
                        dve.tensor_tensor(yg, bank(5), bc(dec[:, par, hs(g)].unsqueeze(2), [P, HPG, HP]), ALU.mult)
                        dve.drain().then_inc(s["inter_free"], 1)
                        if g == 0:
                            dve.wait_ge(s["xd_ready"], n + 1)
                        dve.tensor_tensor(yg, yg, xd[:, hs(g)], ALU.add)
                        dve.drain()
                        if g < NG - 1:
                            masked(g + 1)
                        dve.wait_ge(s["intra"], n * NG + (g + 1))
                        dve.tensor_tensor(yg, yg, bank(4), ALU.add)
                        dve.drain().then_inc(s["intra_free"], 1)
                        if g == 0:
                            dve.wait_ge(s["z_ready"], n * 16 + 16)
                        dve.tensor_tensor(yg, yg, z[:, gc(g)].rearrange("p (h c) -> p h c", c=HP), ALU.mult)
                        dve.wait_ge(s["scaled"], n * NG + (g + 1))
                        dve.wait_ge(s["upd"], n * NG + (g + 1))
                        dve.tensor_tensor(state[:, hs(g)], state[:, hs(g)], bank(6), ALU.add).then_inc(s["state_ready"], 1)
                        dve.drain().then_inc(s["upd_free"], 1)
                        for part in (GATE_AFTER[g - 1] if g > 0 else ()) + GATE_BEFORE[g] + (GATE_AFTER[g] if g == NG - 1 else ()):
                            gate_part(n, part)
                    dve.drain().then_inc(s["gated"], 1)
                    dve.sem_inc(s["z_free"], 1)
                    dve.sem_inc(s["decays_dve"], 1)
                    dve.sem_inc(s["xd_free"], 1)
                pairs(dve, chunk)
        ssd_state_out(e, state)


def ssd_state_out(e, state):
    nc, ps = e.nc, e.ps
    turned, copied, stored = e.sem("state_turned"), e.sem("state_copied"), e.sem("state_stored")
    with nc.sbuf_tensor("state_rows", [P, XT, NS], F32) as rows, nc.Block() as block:
        @block.tensor
        def _(pe):
            for k in range(XT):
                last = pe.transpose(ps[:, k // 4, (k % 4) * P:(k % 4 + 1) * P],
                                    state[:, 2 * k:2 * k + 2].rearrange("p h c -> p (h c)"), e.ident[:, :])
            last.then_inc(turned, 1)

        @block.vector
        def _(dve):
            dve.wait_ge(turned, 1)
            dve.tensor_copy(rows[:, :, :], ps[:, 0:4, :].rearrange("p b (k n) -> p (b k) n", k=4)).then_inc(copied, 1)

        @block.sync
        def _(sp):
            sp.wait_ge(copied, 1)
            sp.dma_start(e.o["p_state_ssd"].rearrange("o b h c n -> (o b h c) n").rearrange("(k p) n -> p k n", p=P),
                         rows[:, :, :]).then_inc(stored, 16)
            sp.wait_ge(stored, 16)


def pairs(eng, step):
    step(0, 0, 0)
    with eng.Fori(0, (NT - 2) // 2) as i:
        step(i * 2 + 1, 1, i)
        step(i * 2 + 2, 0, i + 1)
    step(NT - 1, 1, NT // 2 - 1)


def staggered(eng, front, back):
    front(0, 0, True)
    front(1, 1, False)
    back(0, 0, True)
    with eng.Fori(0, (NT - 2) // 2) as i:
        front(i * 2 + 2, 0, False)
        back(i * 2 + 1, 1, False)
        front(i * 2 + 3, 1, False)
        back(i * 2 + 2, 0, False)
    back(NT - 1, 1, False)


def window_attention(e):
    nc, a, ps = e.nc, e.a, e.ps
    e.down_cols = e.dram("down_cols", [KD, P, T])
    y_ready = [e.sem(f"down_y_ready{i}") for i in range(4)]
    gate_ready = [e.sem(f"down_gate_ready{i}") for i in range(NSPLIT)]
    down_stored = [e.sem(f"down_stored{i}") for i in range(NSPLIT)]
    names = ("wd_ready0", "wd_ready1", "wd_free", "down_made", "down_free", "down_out", "qk_ready0", "qk_ready1", "v_ready0", "v_ready1", "qk_free", "v_free", "bias_made", "bias_scaled", "bias_masked", "s_ready", "s_free", "max_ready",
             "exp_ready", "sc_free", "recip_ready", "p_ready", "t_ready", "t_low_free", "t_high_free", "pt_low", "pt_high", "pt_free",
             "o_ready", "o_free", "sink_ready", "out_ready", "stored0", "stored1")
    s = {n: e.sem("win_" + n) for n in names}
    SCALE = HD ** -0.5
    with ExitStack() as st:
        sb = lambda n, sh, dt=F32: st.enter_context(nc.sbuf_tensor(n, sh, dt))
        q = sb("win_q", [P, 2, NH // 2, W])
        kd = sb("win_k", [P, 2, NKV, 2 * W])
        v = sb("win_v", [P, 2, 2, NKV * HD])
        dist = sb("win_dist", [P, 2 * W])
        bias = sb("win_bias", [P, NH, 2 * W])
        sc = sb("win_scores", [P, 2, NH, 2 * W])
        pt = sb("win_pt", [P, NH, 2, W])
        sink = sb("win_sink", [P, NH])
        mx, nm = sb("win_max", [P, 2, NH]), sb("win_nmax", [P, 2, NH])
        den, es, rd = sb("win_den", [P, 2, NH]), sb("win_es", [P, 2, NH]), sb("win_rd", [P, 2, NH])
        oc = sb("win_out", [P, 2, KD, W])
        y = sb("y_all", [P, XT, T])
        wd = sb("w_down", [P, 2, XT, P])
        dg = sb("down_gate", [P, NSPLIT, NW])
        keys = lambda first: slice(W, 2 * W) if first else slice(0, 2 * W)
        with nc.Block() as block:
            @block.sync
            def _(sp):
                sp.dma_start(sink[:, :], a["attn_sinks"].to_broadcast([P, NH])).then_inc(s["sink_ready"], 16)
                k_src = e.qk_cols[NH // 2:QKT].rearrange("a (b d) t -> d (a b) t", d=HD)

                def load_qk(n, par, first=False):
                    sp.wait_ge(s["qk_free"], n + 1)
                    ready = s[f"qk_ready{par}"]
                    sp.dma_start(q[:, par], e.qk_cols[0:NH // 2, :, bass.ds(n * W, W)].rearrange("h p t -> p h t")).then_inc(ready, 16)
                    for half in range(2):
                        src = k_src[:, :, 0:W] if first else k_src[:, :, bass.ds(n * W + (-W), 2 * W)]
                        sp.dma_start(kd[half * HD:(half + 1) * HD, par, :, keys(first)], src).then_inc(ready, 16)

                def load_v(n, par, first=False):
                    sp.wait_ge(s["v_free"], n + 1)
                    if first:
                        sp.dma_start(v[:, par, 1], e.vdt_rows[0:W, 0:NKV * HD]).then_inc(s[f"v_ready{par}"], 16)
                    else:
                        sp.dma_start(v[:, par], e.vdt_rows[bass.ds(n * W + (-W), 2 * W), 0:NKV * HD].rearrange("(s p) c -> p s c", p=P)).then_inc(s[f"v_ready{par}"], 16)

                def load_down(m, par):
                    sp.wait_ge(s["wd_free"], m + 1)
                    sp.dma_start(wd[:, par], a["w_ssd_down"][0][:, bass.ds(m * P, P)].rearrange("(k p) c -> p k c", p=P)).then_inc(s[f"wd_ready{par}"], 16)

                one = lambda ap, m, part: ap[bass.ds(m, 1)].rearrange("o p t -> (o p) t")[:, part * NW:(part + 1) * NW]

                def load_gate(m, part):
                    sp.dma_start(dg[:, part], one(e.gate_cols, m, part)).then_inc(gate_ready[part], 16)

                def step(n, par, more=True, last=False):
                    if more:
                        load_qk(n + 2, par)
                    if not last:
                        load_down(n + 1, 1 - par)
                    for part in range(NSPLIT):
                        sp.wait_ge(s["down_out"], n * NSPLIT + (part + 1))
                        sp.dma_start(one(e.down_cols, n, part), dg[:, part]).then_inc(down_stored[part], 16)
                    if more:
                        load_v(n + 2, par)
                    for part in range(NSPLIT):
                        sp.wait_ge(down_stored[part], n * 16 + 16)
                        if not last:
                            load_gate(n + 1, part)
                load_qk(0, 0, first=True)
                load_v(0, 0, first=True)
                load_qk(1, 1)
                load_down(0, 0)
                for i in range(4):
                    sp.dma_start(y[:, 4 * i:4 * i + 4], e.y_cols[4 * i:4 * i + 4].rearrange("f p t -> p f t")).then_inc(y_ready[i], 16)
                load_v(1, 1)
                for part in range(NSPLIT):
                    load_gate(0, part)
                with sp.Fori(0, (NT - 2) // 2) as i:
                    for par in range(2):
                        step(i * 2 + par, par)
                step(NT - 2, 0, more=False)
                step(NT - 1, 1, more=False, last=True)

            @block.gpsimd
            def _(pool):
                pool.iota(dist[:, :], pattern=[[-1, 2 * W]], base=W, channel_multiplier=1, allow_small_or_imprecise_dtypes=True).then_inc(s["bias_made"], 1)
                pool.wait_ge(s["bias_scaled"], 1)
                pool.affine_select(out=bias[:, :, :], in_=bias[:, :, :], compare_op=ALU.is_ge, fill=NEG, base=W,
                                   pattern=[[0, NH], [-1, 2 * W]], channel_multiplier=1)
                pool.drain()
                pool.affine_select(out=bias[:, :, :], in_=bias[:, :, :], compare_op=ALU.is_ge, fill=NEG, base=0,
                                   pattern=[[0, NH], [1, 2 * W]], channel_multiplier=-1).then_inc(s["bias_masked"], 1)

                def scale(n, par, k):
                    ks = keys(isinstance(n, int) and n == 0)
                    pool.wait_ge(s["recip_ready"], n + 1)
                    pool.tensor_tensor(sc[:, par, :, ks], sc[:, par, :, ks], bc(rd[:, par].unsqueeze(2), [P, NH, ks.stop - ks.start]),
                                       ALU.mult).then_inc(s["p_ready"], 1)
                pairs(pool, scale)

            @block.tensor
            def _(pe):
                pe.sem_inc(s["qk_free"], 2)
                pe.sem_inc(s["v_free"], 2)
                pe.sem_inc(s["sc_free"], 2)
                pe.sem_inc(s["wd_free"], 2)

                def down(m, par, part, ks, k=0):
                    for kk in ks:
                        if kk == 0:
                            pe.wait_ge(s["down_free"], m * NSPLIT + (part + 1))
                            if part == 0:
                                pe.wait_ge(s[f"wd_ready{par}"], k * 16 + 16)
                        if isinstance(m, int) and m == 0 and part == 0 and kk % 4 == 0:
                            pe.wait_ge(y_ready[kk // 4], 16)
                        last = pe.matmul(ps[:, 2 + (par + part) % 2, 0:NW], wd[:, par, kk], y[:, kk, part * NW:(part + 1) * NW],
                                         start=(kk == 0), stop=(kk == XT - 1))
                    if len(ks) > 0 and ks[-1] == XT - 1:
                        last.then_inc(s["down_made"], 1)
                        if part == NSPLIT - 1:
                            pe.drain().then_inc(s["wd_free"], 1)

                def scores(n, par, first, k):
                    pe.wait_ge(s[f"qk_ready{par}"], k * 48 + 48)
                    for g in range(NH // 2):
                        if not first:
                            down(n + (-1), 1 - par, 0, range(2 * g, 2 * g + 2), k - 1 + par)
                        pe.wait_ge(s["s_free"], n * (NH // 2) + (g + 1))
                        for j in range(2):
                            h, half = 4 * (g // 2) + 2 * j + g % 2, slice(g % 2 * HD, (g % 2 + 1) * HD)
                            last = pe.matmul(ps[:, g % 2, j * 2 * W + keys(first).start:j * 2 * W + 2 * W], q[half, par, h // 2],
                                             kd[half, par, h // GQA, keys(first)], start=True, stop=True)
                        last.then_inc(s["s_ready"], 1)
                    pe.drain().then_inc(s["qk_free"], 1)

                BEFORE = XT // 2

                def weigh(n, par, first, k, final=False):
                    if final:
                        down(n, par, 0, range(XT), k)
                    down(n, par, 1, range(XT))
                    down(n, par, 2, range(BEFORE))
                    pe.wait_ge(s["p_ready"], n + 1)
                    pe.wait_ge(s["pt_free"], n + 1)
                    for g in range(NH // 2):
                        low = g % 2 == 0
                        pe.wait_ge(s["t_low_free"] if low else s["t_high_free"], n * (NH // 4) + (g // 2 + 1))
                        for j in range(2):
                            for b in range(1 if first else 0, 2):
                                last = pe.transpose(ps[:, 4 + g % 2, (2 * j + b) * W:(2 * j + b + 1) * W],
                                                    sc[:, par, 2 * g + j, b * W:(b + 1) * W], e.ident[:, :])
                        last.then_inc(s["t_ready"], 1)
                        down(n, par, 2, range(BEFORE + g * (XT - BEFORE) // (NH // 2), BEFORE + (g + 1) * (XT - BEFORE) // (NH // 2)))
                    pe.drain().then_inc(s["sc_free"], 1)
                    pe.wait_ge(s[f"v_ready{par}"], k * 16 + 16)
                    pe.wait_ge(s["pt_low"], n * (NH // 4) + NH // 4)
                    pe.wait_ge(s["pt_high"], n * (NH // 4) + NH // 4)
                    pe.wait_ge(s["o_free"], n + 1)
                    for h in range(NH):
                        g, half = h // 2, slice((h % 2) * HD, (h % 2 + 1) * HD)
                        for b in range(1 if first else 0, 2):
                            last = pe.matmul(ps[half, 6 + g // 4, (g % 4) * W:(g % 4 + 1) * W],
                                             v[:, par, b, (h // GQA) * HD:(h // GQA + 1) * HD], pt[:, h, b],
                                             start=(b == 1 if first else b == 0), stop=(b == 1))
                    last.then_inc(s["o_ready"], 1)
                    pe.drain().then_inc(s["v_free"], 1)

                scores(0, 0, True, 0)
                scores(1, 1, False, 0)
                weigh(0, 0, True, 0)
                with pe.Fori(0, (NT - 2) // 2) as i:
                    scores(i * 2 + 2, 0, False, i + 1)
                    weigh(i * 2 + 1, 1, False, i)
                    scores(i * 2 + 3, 1, False, i + 1)
                    weigh(i * 2 + 2, 0, False, i + 1)
                weigh(NT - 1, 1, False, NT // 2 - 1, final=True)

            @block.scalar
            def _(act):
                act.sem_inc(s["t_high_free"], 1)
                act.sem_inc(s["o_free"], 1)
                for b in range(2):
                    act.sem_inc(s[f"stored{b}"], 16)

                def exps(n, par, first):
                    act.wait_ge(s["max_ready"], n + 1)
                    for h in range(NH):
                        act.activation(sc[:, par, h, keys(first)], sc[:, par, h, keys(first)], ACT.Exp,
                                       bias=nm[:, par, h:h + 1], accum_out=den[:, par, h:h + 1])
                    act.activation(es[:, par], es[:, par], ACT.Exp).then_inc(s["exp_ready"], 1)

                def out(n, par, first, earlier):
                    for g in range(NH // 4):
                        act.wait_ge(s["t_ready"], n * (NH // 2) + (2 * g + 2))
                        src = ps[:, 5, :].rearrange("p (h b c) -> p h b c", h=2, b=2)
                        b0 = 1 if first else 0
                        act.activation(pt[:, 4 * g + 2:4 * g + 4, b0:2], src[:, :, b0:2], ACT.Copy).then_inc(s["pt_high"], 1)
                        act.drain().then_inc(s["t_high_free"], 1)
                    act.wait_ge(s["o_ready"], n + 1)
                    act.wait_ge(s[f"stored{par}"], earlier * 16 + 16)
                    act.activation(oc[:, par].rearrange("p (b k) c -> p b (k c)", b=2), ps[:, 6:8, :], ACT.Copy).then_inc(s["out_ready"], 1)
                    act.drain().then_inc(s["o_free"], 1)
                    act.sem_inc(s["pt_free"], 1)
                    act.dma_start(e.att_cols[:, :, bass.ds(n * W, W)].rearrange("f p t -> p f t"), oc[:, par]).then_inc(s[f"stored{par}"], 16)

                act.sem_inc(s["pt_free"], 1)
                exps(0, 0, True)
                exps(1, 1, False)
                out(0, 0, True, 0)
                with act.Fori(0, (NT - 2) // 2) as i:
                    exps(i * 2 + 2, 0, False)
                    out(i * 2 + 1, 1, False, i)
                    exps(i * 2 + 3, 1, False)
                    out(i * 2 + 2, 0, False, i + 1)
                out(NT - 1, 1, False, NT // 2 - 1)
                for b in range(2):
                    act.wait_ge(s[f"stored{b}"], 16 * (NT // 2 + 1))

            @block.vector
            def _(dve):
                dve.wait_ge(s["bias_made"], 1)
                for h in range(NH):
                    last = dve.tensor_scalar(bias[:, h], dist[:, :], -(2.0 ** (-8.0 * (h + 1) / NH)), None, ALU.mult)
                last.then_inc(s["bias_scaled"], 1)
                dve.wait_ge(s["bias_masked"], 1)
                dve.wait_ge(s["sink_ready"], 16)
                dve.sem_inc(s["s_free"], 2)
                dve.sem_inc(s["down_free"], 2)
                dve.sem_inc(s["t_low_free"], 1)

                def gated(m, par, part):
                    dve.wait_ge(s["down_made"], m * NSPLIT + (part + 1))
                    dve.wait_ge(gate_ready[part], m * 16 + 16)
                    dve.tensor_tensor(dg[:, part], ps[:, 2 + (par + part) % 2, 0:NW], dg[:, part], ALU.mult).then_inc(s["down_out"], 1)
                    dve.drain().then_inc(s["down_free"], 1)

                def maxima(n, par, first):
                    ks = keys(first)
                    dve.wait_ge(s["sc_free"], n + 1)
                    for g in range(NH // 2):
                        dve.wait_ge(s["s_ready"], n * (NH // 2) + (g + 1))
                        hh = slice(4 * (g // 2) + g % 2, 4 * (g // 2) + g % 2 + 3, 2)
                        dve.scalar_tensor_tensor(out=sc[:, par, hh, ks], in0=ps[:, g % 2, :].rearrange("p (h c) -> p h c", h=2)[:, :, ks],
                                                 scalar=SCALE, in1=bias[:, hh, ks], op0=ALU.mult, op1=ALU.add)
                        dve.drain().then_inc(s["s_free"], 1)
                    dve.tensor_reduce(mx[:, par], sc[:, par, :, ks], AX.X, ALU.max)
                    dve.drain()
                    dve.tensor_tensor(mx[:, par], mx[:, par], sink[:, :], ALU.max)
                    dve.drain()
                    dve.tensor_scalar(nm[:, par], mx[:, par], -1.0, None, ALU.mult)
                    dve.tensor_tensor(es[:, par], sink[:, :], mx[:, par], ALU.subtract).then_inc(s["max_ready"], 1)
                    if not first:
                        gated(n + (-1), 1 - par, 0)

                def normalise(n, par):
                    dve.wait_ge(s["exp_ready"], n + 1)
                    dve.tensor_tensor(den[:, par], den[:, par], es[:, par], ALU.add)
                    dve.drain()
                    dve.reciprocal(rd[:, par], den[:, par]).then_inc(s["recip_ready"], 1)

                def copy(n, par, first):
                    final = isinstance(n, int) and n == NT - 1
                    if final:
                        gated(n, par, 0)
                    if first:
                        normalise(n, par)
                    b0 = 1 if first else 0
                    for g in range(NH // 4):
                        dve.wait_ge(s["t_ready"], n * (NH // 2) + (2 * g + 1))
                        src = ps[:, 4, :].rearrange("p (h b c) -> p h b c", h=2, b=2)
                        dve.tensor_copy(pt[:, 4 * g:4 * g + 2, b0:2], src[:, :, b0:2]).then_inc(s["pt_low"], 1)
                        dve.drain().then_inc(s["t_low_free"], 1)
                    if not final:
                        normalise(n + 1, 1 - par)
                    gated(n, par, 1)
                    gated(n, par, 2)
                staggered(dve, maxima, copy)


def sample_states(e, z):
    nc, a, o, ps = e.nc, e.a, e.o, e.ps
    s = {n: e.sem("sconv_" + n) for n in ("u", "silu", "loaded", "turned", "rows", "copied")}
    keep = lambda n, sh: e.mix.enter_context(nc.sbuf_tensor(n, sh, F32))
    e.sc_cols = keep("sc_cols", [P, CT, NB])
    e.sqk_rows = keep("sqk_rows", [NB, (NH + NKV) * HD])
    e.sbc_rows = keep("sbc_rows", [NB, 2 * NG * NS])
    e.sv_rows = keep("sv_rows", [NB, NKV * HD])
    e.onehot = keep("onehot", [NB, NB, P])
    with ExitStack() as st:
        sb = lambda n, sh: st.enter_context(nc.sbuf_tensor(n, sh, F32))
        acc, term = sb("sconv_acc", [P, CT, NB]), sb("sconv_term", [P, CT, NB])
        trows = sb("tail_rows", [CK - 1 + NB, CD])
        qk_s = sb("qk_sample", [P, QKT, NB])
        k_last = sb("k_last", [P, 2, P])
        k_rows = sb("k_last_rows", [P, NKV * HD])
        block = st.enter_context(nc.Block())
        KW = NKV * HD

        @block.sync
        def _(sp):
            sp.dma_start(qk_s[:, :, :], e.qk_cols[:, :, SEQ:T].rearrange("f p t -> p f t")).then_inc(s["loaded"], 16)
            sp.dma_start(k_last[:, :, :], e.qk_cols[NH // 2:QKT, :, SEQ - W:SEQ].rearrange("f p t -> p f t")).then_inc(s["loaded"], 16)
            sp.dma_start(e.sv_rows[:, :], e.vdt_rows[SEQ:T, 0:KW]).then_inc(s["loaded"], 16)
            sp.dma_start(o["p_cache_win_v"].rearrange("o b s v d -> (o b s) (v d)"), e.vdt_rows[SEQ - W:SEQ, 0:KW]).then_inc(s["copied"], 16)
            for c in "kv":
                sp.dma_start(o["s_cache_win_" + c].rearrange("o b s v d -> (o b) s (v d)")[:, 0:W - 1],
                             a["cache_win_" + c].rearrange("o b s v d -> (o b) s (v d)")[:, 1:W]).then_inc(s["copied"], 16)
            sp.dma_start(o["s_cache_win_v"].rearrange("o b s v d -> (o b) s (v d)")[:, W - 1], e.vdt_rows[SEQ:T, 0:KW]).then_inc(s["copied"], 16)
            sp.dma_start(o["s_state_conv"][0, :, 0:CK - 2], a["state_conv"][0, :, 1:CK - 1]).then_inc(s["copied"], 16)
            z.load(sp, 2)
            sp.wait_ge(s["rows"], 1)
            sp.dma_start(o["p_state_conv"].rearrange("o b k c -> (o b k) c"), trows[0:CK - 1, :]).then_inc(s["copied"], 16)
            sp.dma_start(o["s_state_conv"][0, :, CK - 2], trows[CK - 1:CK - 1 + NB, :]).then_inc(s["copied"], 16)
            sp.wait_ge(s["rows"], 2)
            sp.dma_start(o["p_cache_win_k"].rearrange("o b s v d -> (o b s) (v d)"), k_rows[:, :]).then_inc(s["copied"], 16)
            sp.dma_start(o["s_cache_win_k"].rearrange("o b s v d -> (o b) s (v d)")[:, W - 1], e.sqk_rows[:, NH * HD:]).then_inc(s["copied"], 16)
            sp.wait_ge(s["copied"], 16 * 9)
            sp.wait_ge(s["loaded"], 48)

        @block.gpsimd
        def _(pool):
            pool.memset(e.onehot[:, :, :], 0.0)
            pool.drain()
            pool.affine_select(out=e.onehot[:, :, :], in_=e.onehot[:, :, :], compare_op=ALU.not_equal, fill=1.0, base=0,
                               pattern=[[-1, NB], [0, P]], channel_multiplier=1)
            z.low(pool, 2)

        @block.vector
        def _(dve):
            new = e.tails[:, :, CK - 1:]
            wt = lambda k: bc(e.cvec[:, :, CR_W + k:CR_W + k + 1], [P, CT, NB])
            dve.tensor_tensor(acc[:, :, :], new, wt(CK - 1), ALU.mult)
            dve.drain()
            dve.tensor_tensor(acc[:, :, :], acc[:, :, :], bc(e.cvec[:, :, CR_B:CR], [P, CT, NB]), ALU.add)
            for k in range(CK - 1):
                past = e.cvec[:, :, CR_STATE:CR_W].rearrange("p c (b k) -> p c b k", k=CK - 1)[:, :, :, k]
                dve.tensor_tensor(term[:, :, :], past, wt(k), ALU.mult)
                dve.drain()
                dve.tensor_tensor(acc[:, :, :], acc[:, :, :], term[:, :, :], ALU.add)
                dve.drain()
            dve.sem_inc(s["u"], 1)
            dve.wait_ge(s["turned"], 1)
            dve.tensor_copy(trows[:, :], ps[0:CK - 1 + NB, 0:6, :].rearrange("p b c -> p (b c)")).then_inc(s["rows"], 1)
            dve.drain()
            dve.wait_ge(s["turned"], 2)
            dve.tensor_copy(e.sqk_rows[:, 0:1024], ps[0:NB, 0:2, :].rearrange("p b c -> p (b c)"))
            dve.tensor_copy(e.sqk_rows[:, 1024:1280], ps[0:NB, 2, 0:256])
            dve.tensor_copy(k_rows[:, :], ps[:, 3, 0:256])
            dve.drain().then_inc(s["rows"], 1)
            dve.wait_ge(s["turned"], 3)
            dve.tensor_copy(e.sbc_rows[:, :], ps[0:NB, 4:6, :].rearrange("p b c -> p (b c)"))
            z.high(dve, 2)

        @block.tensor
        def _(pe):
            for c in range(CT):
                last = pe.transpose(ps[0:CK - 1 + NB, c // 4, (c % 4) * P:(c % 4 + 1) * P], e.tails[:, c], e.ident[:, :])
            last.then_inc(s["turned"], 1)
            z.make(pe, 2)
            pe.wait_ge(s["loaded"], 48)
            pe.wait_ge(s["rows"], 1)
            for c in range(QKT):
                pe.transpose(ps[0:NB, c // 4, (c % 4) * P:(c % 4 + 1) * P], qk_s[:, c], e.ident[:, :])
            for c in range(2):
                last = pe.transpose(ps[:, 3, c * P:(c + 1) * P], k_last[:, c], e.ident[:, :])
            last.then_inc(s["turned"], 1)
            z.make(pe, 3)
            pe.wait_ge(s["silu"], 1)
            for c in range(2 * NG):
                last = pe.transpose(ps[0:NB, 4 + c // 4, (c % 4) * P:(c % 4 + 1) * P], e.sc_cols[:, XT + c], e.ident[:, :])
            last.then_inc(s["turned"], 1)
            z.make(pe, 2)

        @block.scalar
        def _(act):
            act.wait_ge(s["u"], 1)
            act.activation(e.sc_cols[:, :, :], acc[:, :, :], ACT.Silu).then_inc(s["silu"], 1)
            z.store(act, 7)



def sample_ssd(e, z):
    nc, a, o, ps = e.nc, e.a, e.o, e.ps
    names = ("sel_made", "loaded", "z_loaded", "dec", "dtT", "dtT_copied", "spread", "spread_copied", "bc_ready", "bc_free",
             "h_ready0", "h_ready1", "h_scaled", "h_new", "h_stored0", "h_stored1", "zT", "sq", "total", "meaned", "rooted", "y_ready", "y_stored")
    s = {n: e.sem("sssd_" + n) for n in names}
    z.banks = (2, 3)
    with ExitStack() as st:
        sb = lambda n, sh: st.enter_context(nc.sbuf_tensor(n, sh, F32))
        sel = sb("head_sel", [HS, DI])
        decay = sb("sdecay", [NB, HS])
        dtT = sb("sdtT", [HS, 2 * NB + 1])
        spread = sb("sspread", [P, XT, 2 * NB + 1])
        xdt = sb("sxdt", [P, XT, NB])
        h = sb("sh", [P, 2, XT, NS])
        t1 = sb("st1", [P, XT, NS])
        t2 = sb("st2", [P, XT, NS])
        zr = t1[0:NB, :, :].rearrange("p k n -> p (k n)")
        y = sb("sy", [P, XT, NB])
        y2 = sb("sy2", [P, XT, NB])
        yb = sb("syb", [P, NB, XT])
        ms, rs = sb("sms", [P, NG, NB]), sb("srs", [P, NG, NB])
        mh = sb("smh", [P, NG, NB])
        block = st.enter_context(nc.Block())
        st_in = a["state_ssd"][0].rearrange("b h c n -> b (h c) n").rearrange("b (k p) n -> b p k n", p=P)
        st_out = o["s_state_ssd"][0].rearrange("b h c n -> b (h c) n").rearrange("b (k p) n -> b p k n", p=P)

        @block.sync
        def _(sp):
            sp.dma_start(dtT[:, 2 * NB:2 * NB + 1], a["d_skip"].rearrange("o h -> h o")).then_inc(s["loaded"], 16)
            for b in range(NB):
                if b >= 2:
                    sp.wait_ge(s[f"h_stored{b % 2}"], 16 * (b // 2))
                    sp.wait_ge(s["bc_free"], b + 1)
                sp.dma_start(h[:, b % 2], st_in[b]).then_inc(s[f"h_ready{b % 2}"], 16)
                if b in (1, 4):
                    z.load(sp, 6 + b // 4)
            z.wait_sample(sp)
            sp.wait_ge(s["h_new"], NB)
            sp.dma_start(zr[:, :], e.z_rows[SEQ:T, :]).then_inc(s["z_loaded"], 16)
            sp.wait_ge(s["y_ready"], 1)
            sp.dma_start(e.y_cols[:, :, SEQ:T].rearrange("f p t -> p f t"), y2[:, :, :]).then_inc(s["y_stored"], 16)
            sp.wait_ge(s["y_stored"], 16)

        @block.gpsimd
        def _(pool):
            pool.memset(sel[:, :], 1.0)
            pool.memset(mh[:, :, :], -0.5)
            pool.drain()
            pool.affine_select(out=sel[:, :], in_=sel[:, :], compare_op=ALU.is_ge, fill=0.0, base=0, pattern=[[1, DI]], channel_multiplier=-HP)
            pool.drain()
            pool.affine_select(out=sel[:, :], in_=sel[:, :], compare_op=ALU.is_ge, fill=0.0, base=HP - 1, pattern=[[-1, DI]], channel_multiplier=HP)
            pool.drain().then_inc(s["sel_made"], 1)
            z.low(pool, 5)
            pool.wait_ge(s["spread_copied"], 1)
            for b in range(NB):
                pool.wait_ge(s[f"h_ready{b % 2}"], 16 * (b // 2 + 1))
                pool.tensor_tensor(h[:, b % 2], h[:, b % 2], bc(spread[:, :, NB + b:NB + b + 1], [P, XT, NS]), ALU.mult).then_inc(s["h_scaled"], 1)
                if b in (2, 5):
                    z.low(pool, 6 + b // 4)
            pool.wait_ge(s["meaned"], 1)
            pool.tensor_tensor(rs[:, :, :], ms[:, :, :], mh[:, :, :], ALU.pow).then_inc(s["rooted"], 1)

        @block.vector
        def _(dve):
            dve.sem_inc(s["bc_free"], 2)
            dve.wait_ge(s["dtT"], 1)
            dve.wait_ge(s["loaded"], 16)
            z.high(dve, 5)
            dve.tensor_copy(dtT[:, 0:2 * NB], ps[0:HS, 0, 0:2 * NB]).then_inc(s["dtT_copied"], 1)
            dve.wait_ge(s["spread"], 1)
            dve.tensor_copy(spread[:, :, :], ps[:, 1, :].rearrange("p (k c) -> p k c", c=32)[:, :, 0:2 * NB + 1])
            dve.drain().then_inc(s["spread_copied"], 1)
            dve.tensor_tensor(xdt[:, :, :], e.sc_cols[:, 0:XT, :], spread[:, :, 0:NB], ALU.mult)
            dve.drain()
            four = lambda ap: ap.rearrange("p (g k) n -> p g k n", g=NG)
            for b in range(NB):
                dve.wait_ge(s["bc_ready"], b + 1)
                bank = lambda q: bc(ps[:, 4 + 2 * (b % 2) + q, :].rearrange("p (g n) -> p g n", g=NG).unsqueeze(2), [P, NG, XT // NG, NS])
                dve.tensor_tensor(four(t1[:, :, :]), bank(0), bc(four(xdt[:, :, b:b + 1]), [P, NG, XT // NG, NS]), ALU.mult)
                dve.drain()
                dve.wait_ge(s["h_scaled"], b + 1)
                dve.tensor_tensor(h[:, b % 2], h[:, b % 2], t1[:, :, :], ALU.add).then_inc(s["h_new"], 1)
                dve.drain()
                dve.tensor_tensor(four(t2[:, :, :]), four(h[:, b % 2]), bank(1), ALU.mult)
                dve.drain().then_inc(s["bc_free"], 1)
                dve.tensor_reduce(yb[:, b], t2[:, :, :], AX.X, ALU.add)
                dve.drain()
                if b in (1, 4):
                    z.high(dve, 6 + b // 4)
            ybt = yb[:, :, :].rearrange("p b k -> p k b")
            dve.tensor_tensor(y[:, :, :], e.sc_cols[:, 0:XT, :], bc(spread[:, :, 2 * NB:2 * NB + 1], [P, XT, NB]), ALU.mult)
            dve.drain()
            dve.tensor_tensor(y[:, :, :], y[:, :, :], ybt, ALU.add)
            dve.drain()
            dve.wait_ge(s["zT"], 1)
            dve.tensor_tensor(y[:, :, :], y[:, :, :], ps[:, 0, HS:HS + XT * NB].rearrange("p (k b) -> p k b", b=NB), ALU.mult)
            dve.drain()
            dve.tensor_tensor(y2[:, :, :], y[:, :, :], y[:, :, :], ALU.mult)
            dve.drain()
            dve.tensor_reduce(ms[:, :, :], y2[:, :, :].rearrange("p (g k) b -> p g b k", g=NG), AX.X, ALU.add).then_inc(s["sq"], 1)
            dve.wait_ge(s["total"], 1)
            dve.tensor_scalar(ms[:, :, :].rearrange("p g b -> p (g b)"), ps[:, 0, 2 * P:2 * P + NG * NB], NG / DI, EPS, ALU.mult, ALU.add).then_inc(s["meaned"], 1)
            dve.wait_ge(s["rooted"], 1)
            dve.tensor_tensor(y2[:, :, :].rearrange("p (g k) b -> p g k b", g=NG), y[:, :, :].rearrange("p (g k) b -> p g k b", g=NG),
                              bc(rs[:, :, :].unsqueeze(2), [P, NG, XT // NG, NB]), ALU.mult)
            dve.drain()
            dve.tensor_tensor(y2[:, :, :], y2[:, :, :], bc(e.gvec[:, G_SSD:G_SSD + XT].unsqueeze(2), [P, XT, NB]), ALU.mult).then_inc(s["y_ready"], 1)

        @block.tensor
        def _(pe):
            pe.wait_ge(s["dec"], 1)
            pe.transpose(ps[0:HS, 0, 0:NB], e.dt[0:NB, NT, :], e.ident[0:NB, 0:NB])
            pe.transpose(ps[0:HS, 0, NB:2 * NB], decay[:, :], e.ident[0:NB, 0:NB]).then_inc(s["dtT"], 1)
            z.make(pe, 2)
            pe.wait_ge(s["dtT_copied"], 1)
            pe.wait_ge(s["sel_made"], 1)
            for k in range(XT):
                last = pe.matmul(ps[:, 1, k * 32:k * 32 + 2 * NB + 1], sel[:, k * P:(k + 1) * P], dtT[:, :], start=True, stop=True)
            last.then_inc(s["spread"], 1)
            z.make(pe, 1)
            for b in range(NB):
                pe.wait_ge(s["bc_free"], b + 1)
                for q in range(2):
                    last = pe.matmul(ps[:, 4 + 2 * (b % 2) + q, :], e.onehot[:, b], e.sbc_rows[:, q * 512:(q + 1) * 512], start=True, stop=True)
                last.then_inc(s["bc_ready"], 1)
                z.make(pe, 2)
            pe.wait_ge(s["z_loaded"], 16)
            for k in range(XT):
                last = pe.transpose(ps[:, 0, HS + k * NB:HS + (k + 1) * NB], zr[:, k * P:(k + 1) * P], e.ident[0:NB, 0:NB])
            last.then_inc(s["zT"], 1)
            pe.wait_ge(s["sq"], 1)
            pe.matmul(ps[:, 0, 2 * P:2 * P + NG * NB], e.ones[:, :], ms[:, :, :].rearrange("p g b -> p (g b)"), start=True, stop=True).then_inc(s["total"], 1)

        @block.scalar
        def _(act):
            act.activation(decay[:, :], e.da[0:NB, NT, :], ACT.Exp).then_inc(s["dec"], 1)
            z.store(act, 3)
            for b in range(NB):
                z.store(act, 2)
                act.wait_ge(s["h_new"], b + 1)
                act.dma_start(st_out[b], h[:, b % 2]).then_inc(s[f"h_stored{b % 2}"], 16)
            z.settle(act)
            for q in range(2):
                act.wait_ge(s[f"h_stored{q}"], 16 * NB // 2)



def sample_window(e, z):
    nc, a, o, ps = e.nc, e.a, e.o, e.ps
    names = ("loaded", "dist", "q_ready", "q_free", "new_made", "sT", "turned", "maxed", "exped", "normed", "pT", "pT_copied",
             "pn", "pn_copied", "o_ready", "o_copied", "stored")
    s = {n: e.sem("swin_" + n) for n in names}
    z.banks = (6, 7)
    SCALE = HD ** -0.5
    R = NB * NH
    with ExitStack() as st:
        sb = lambda n, sh: st.enter_context(nc.sbuf_tensor(n, sh, F32))
        kc, vc = sb("swin_k", [P, NB, NKV * HD]), sb("swin_v", [P, NB, NKV * HD])
        sink = sb("swin_sink", [NB, NH])
        prod = sb("swin_prod", [P, NKV, GQA, HD])
        prod_new = sb("swin_prod_new", [NB, NKV, GQA, HD])
        s_new = sb("swin_s_new", [NB, NH])
        own = sb("swin_own", [NB, 2, NB, NH])
        sT = sb("swin_sT", [P, NB, NH])
        dist, bias = sb("swin_dist", [P, 1]), sb("swin_bias", [P, NH])
        sc = sb("swin_sc", [R, W + 2])
        mx, nm, den, rd = sb("swin_mx", [R, 1]), sb("swin_nm", [R, 1]), sb("swin_den", [R, 1]), sb("swin_rd", [R, 1])
        pT = sb("swin_pT", [P, NB, NH])
        pn_row = sb("swin_pn_row", [1, R])
        pn = sb("swin_pn", [NB, NB, NH])
        oc = sb("swin_oc", [P, 2, GQA, NB])
        block = st.enter_context(nc.Block())
        rows4 = lambda ap: ap.rearrange("p (v g d) -> p v g d", v=NKV, g=GQA)

        @block.sync
        def _(sp):
            sp.dma_start(kc[:, :, :], a["cache_win_k"][0].rearrange("b s v d -> s b (v d)")).then_inc(s["loaded"], 16)
            sp.dma_start(vc[:, :, :], a["cache_win_v"][0].rearrange("b s v d -> s b (v d)")).then_inc(s["loaded"], 16)
            sp.dma_start(sink[:, :], a["attn_sinks"].to_broadcast([NB, NH])).then_inc(s["loaded"], 16)
            for block_of_z in (3, 4, 5):
                z.load(sp, block_of_z)
            sp.wait_ge(s["o_copied"], 1)
            att = e.att_cols[:, :, SEQ:T].rearrange("(u v j) (q d) t -> u v q d j t", u=2, v=2, d=HD)
            for u in range(2):
                for v in range(2):
                    for q in range(2):
                        sp.dma_start(att[u, v, q], oc[v * HD:(v + 1) * HD, u, q:GQA:2]).then_inc(s["stored"], 16)
            sp.wait_ge(s["stored"], 16 * 8)

        @block.gpsimd
        def _(pool):
            pool.iota(dist[:, :], pattern=[[0, 1]], base=W, channel_multiplier=-1, allow_small_or_imprecise_dtypes=True).then_inc(s["dist"], 1)
            for block_of_z in (3, 4):
                z.low(pool, block_of_z)

        @block.vector
        def _(dve):
            dve.sem_inc(s["q_free"], 2)
            dve.wait_ge(s["loaded"], 48)
            dve.wait_ge(s["dist"], 1)
            z.high(dve, 3)
            for hh in range(NH):
                dve.tensor_scalar(bias[:, hh:hh + 1], dist[:, :], -(2.0 ** (-8.0 * (hh + 1) / NH)), None, ALU.mult)
            dve.tensor_tensor(prod_new[:, :, :, :], rows4(e.sqk_rows[:, 0:NH * HD]),
                              bc(e.sqk_rows[:, NH * HD:].rearrange("p (v d) -> p v d", v=NKV).unsqueeze(2), [NB, NKV, GQA, HD]), ALU.mult)
            dve.drain()
            dve.tensor_reduce(s_new[:, :], prod_new[:, :, :, :].rearrange("p v g d -> p (v g) d"), AX.X, ALU.add)
            dve.drain()
            dve.tensor_scalar(s_new[:, :], s_new[:, :], SCALE, None, ALU.mult)
            dve.drain()
            diag = bc(e.onehot[:, :, 0:1], [NB, NB, NH])
            dve.tensor_tensor(own[:, 0], bc(s_new[:, :].unsqueeze(1), [NB, NB, NH]), diag, ALU.mult)
            dve.tensor_tensor(own[:, 1], bc(sink[:, :].unsqueeze(1), [NB, NB, NH]), diag, ALU.mult).then_inc(s["new_made"], 1)
            for b in range(NB):
                dve.wait_ge(s["q_ready"], b + 1)
                bank = rows4(ps[:, 2 * (b % 2):2 * (b % 2) + 2, :].rearrange("p b c -> p (b c)"))
                dve.tensor_tensor(prod[:, :, :, :], bank, bc(kc[:, b].rearrange("p (v d) -> p v d", v=NKV).unsqueeze(2), [P, NKV, GQA, HD]), ALU.mult)
                dve.drain().then_inc(s["q_free"], 1)
                dve.tensor_reduce(sT[:, b], prod[:, :, :, :].rearrange("p v g d -> p (v g) d"), AX.X, ALU.add)
                dve.drain()
                if b == NB - 1:
                    z.high(dve, 4)
            dve.scalar_tensor_tensor(out=sT[:, :, :], in0=sT[:, :, :], scalar=SCALE, in1=bc(bias[:, :].unsqueeze(1), [P, NB, NH]),
                                     op0=ALU.mult, op1=ALU.add).then_inc(s["sT"], 1)
            dve.wait_ge(s["turned"], 1)
            dve.tensor_copy(sc[:, 0:W], ps[0:R, 4, 0:W])
            dve.tensor_copy(sc[:, W:W + 2], ps[0:R, 4, W:W + 2])
            dve.drain()
            dve.tensor_reduce(mx[:, :], sc[:, :], AX.X, ALU.max)
            dve.drain()
            dve.tensor_scalar(nm[:, :], mx[:, :], -1.0, None, ALU.mult).then_inc(s["maxed"], 1)
            dve.wait_ge(s["exped"], 1)
            dve.reciprocal(rd[:, :], den[:, :])
            dve.drain()
            dve.tensor_scalar(sc[:, :], sc[:, :], rd[:, :], None, ALU.mult).then_inc(s["normed"], 1)
            dve.wait_ge(s["pT"], 1)
            dve.tensor_copy(pT[:, :, :].rearrange("p b h -> p (b h)"), ps[:, 5, 0:R])
            dve.tensor_copy(pn_row[:, :], ps[0:1, 5, R:2 * R]).then_inc(s["pT_copied"], 1)
            dve.wait_ge(s["pn"], 1)
            dve.tensor_tensor(pn[:, :, :], ps[0:NB, 4, 2 * R:3 * R].rearrange("p (b h) -> p b h", b=NB), bc(e.onehot[:, :, 0:1], [NB, NB, NH]), ALU.mult)\
                .then_inc(s["pn_copied"], 1)
            dve.wait_ge(s["o_ready"], 1)
            for v in range(2):
                half = slice(v * HD, (v + 1) * HD)
                src = ps[half, 5, 2 * R:3 * R].rearrange("p (u b h) -> p u h b", u=2, b=NB)
                last = dve.tensor_copy(oc[half], src[:, :, v * GQA:(v + 1) * GQA])
            last.then_inc(s["o_copied"], 1)

        @block.tensor
        def _(pe):
            for b in range(NB):
                pe.wait_ge(s["q_free"], b + 1)
                for q in range(2):
                    last = pe.matmul(ps[:, 2 * (b % 2) + q, :], e.onehot[:, b], e.sqk_rows[:, q * 512:(q + 1) * 512], start=True, stop=True)
                last.then_inc(s["q_ready"], 1)
                if b < 6:
                    z.make(pe, 1)
            pe.wait_ge(s["new_made"], 1)
            for q in range(2):
                pe.matmul(ps[0:R, 4, W + q:W + q + 1], own[:, q].rearrange("p b h -> p (b h)"), e.ones[0:NB, 0:1], start=True, stop=True)
            z.make(pe, 1)
            pe.wait_ge(s["sT"], 1)
            pe.transpose(ps[0:R, 4, 0:W], sT[:, :, :].rearrange("p b h -> p (b h)"), e.ident[:, :]).then_inc(s["turned"], 1)
            z.make(pe, 1)
            pe.wait_ge(s["normed"], 1)
            pe.transpose(ps[:, 5, 0:R], sc[:, 0:W], e.ident[:, :])
            pe.transpose(ps[0:1, 5, R:2 * R], sc[:, W:W + 1], e.ident[:, :]).then_inc(s["pT"], 1)
            pe.wait_ge(s["pT_copied"], 1)
            pe.matmul(ps[0:NB, 4, 2 * R:3 * R], e.ones[0:1, 0:NB], pn_row[:, :], start=True, stop=True).then_inc(s["pn"], 1)
            pe.wait_ge(s["pn_copied"], 1)
            out = ps[:, 5, 2 * R:3 * R].rearrange("p (u b h) -> p u b h", u=2, b=NB)
            for b in range(NB):
                for u in range(2):
                    heads, values = slice(2 * GQA * u, 2 * GQA * (u + 1)), slice(u * P, (u + 1) * P)
                    pe.matmul(out[:, u, b], vc[:, b, values], pT[:, b, heads], start=True, stop=False)
                    last = pe.matmul(out[:, u, b], e.sv_rows[:, values], pn[:, b, heads], start=False, stop=True)
            last.then_inc(s["o_ready"], 1)
            z.make(pe, 3)

        @block.scalar
        def _(act):
            z.store(act, 7)
            act.wait_ge(s["maxed"], 1)
            act.activation(sc[:, :], sc[:, :], ACT.Exp, bias=nm[:, :], accum_out=den[:, :]).then_inc(s["exped"], 1)
            z.store(act, 4)



def mixer_out(e):
    nc, a, ps = e.nc, e.a, e.ps
    names = ("m_high", "m_split", "w_high", "w_split0", "w_split1", "padded", "mixed", "emptied")
    s = {n: e.sem("mix_" + n) for n in names}
    in_ready = [e.sem(f"mix_in_ready{i}") for i in range(3)]
    w_ready = [e.sem(f"mix_w_ready{i}") for i in range(4)]
    x_ready = [e.sem(f"mix_x_ready{i}") for i in range(3)]
    width = lambda t: P if t < NT else T - SEQ
    with ExitStack() as st:
        sb = lambda n, sh: st.enter_context(nc.sbuf_tensor(n, sh, F32))
        parts = sb("mix_parts", [P, 3, 3, KD, P])
        merged = sb("merged", [P, 3, 2, KD, P])
        wraw = sb("w_mix_raw", [P, 2, 2, D])
        wm = sb("w_mix", [P, 2, KD, D])
        block = st.enter_context(nc.Block())

        @block.sync
        def _(sp):
            def load_parts(t):
                if t >= 3:
                    sp.wait_ge(s["m_split"], t - 2)
                for i, src in enumerate((e.down_cols, e.gate_cols[KD:2 * KD], e.att_cols)):
                    sp.dma_start(parts[:, t % 3, i, :, 0:width(t)], src[:, :, t * P:t * P + width(t)].rearrange("f p t -> p f t")).then_inc(in_ready[t % 3], 16)
            load_parts(0)
            for q in range(4):
                if q >= 2:
                    sp.wait_ge(s[f"w_split{q % 2}"], 1)
                sp.dma_start(wraw[:, q % 2], a["w_mix_out"][0][2 * q * P:(2 * q + 2) * P, :].rearrange("(k p) c -> p k c", p=P)).then_inc(w_ready[q], 16)
            rows = a["x_prompt"][0].rearrange("(t p) d -> p t d", p=P)
            load_parts(1)
            sp.dma_start(e.x[:, 0:4, :], rows[:, 0:4]).then_inc(x_ready[0], 16)
            load_parts(2)
            load_parts(3)
            sp.dma_start(e.x[:, 4:8, :], rows[:, 4:8]).then_inc(x_ready[1], 16)
            sp.wait_ge(s["padded"], 1)
            sp.dma_start(e.x[0:NB, NT, :], a["x_sample"][:, 0, :]).then_inc(x_ready[2], 16)
            for t in range(4, TILES):
                load_parts(t)

        @block.gpsimd
        def _(pool):
            pool.memset(e.x[:, NT, :], 0.0).then_inc(s["padded"], 1)

            def weights(q):
                k = slice(2 * q, 2 * q + 2)
                pool.wait_ge(s["w_high"], q + 1)
                take_low(pool, wm[:, 0, k], wraw[:, q % 2], wm[:, 1, k]).then_inc(s["w_split0"], 1)
            weights(0)
            for t in range(TILES):
                if t == 1:
                    weights(2)
                pool.wait_ge(s["m_high"], t + 1)
                m = merged[:, t % 3]
                take_low(pool, m[:, 0], parts[:, t % 3, 2], m[:, 1]).then_inc(s["m_split"], 1)

        @block.vector
        def _(dve):
            def merge(t):
                dve.wait_ge(in_ready[t % 3], 48 * (t // 3 + 1))
                part = lambda i: parts[:, t % 3, i, :, 0:width(t)]
                dve.tensor_tensor(part(2), part(2), part(1), ALU.mult)
                if t >= 3:
                    dve.wait_ge(s["mixed"], 2 * (t - 2))
                dve.drain()
                dve.tensor_tensor(part(2), part(2), part(0), ALU.add)
                if width(t) < P:
                    dve.memset(parts[:, t % 3, 2, :, width(t):P], 0.0)
                dve.drain()
                take_high(dve, merged[:, t % 3, 1], parts[:, t % 3, 2]).then_inc(s["m_high"], 1)

            def weights(q):
                dve.wait_ge(w_ready[q], 16)
                k = slice(2 * q, 2 * q + 2)
                take_high(dve, wm[:, 1, k], wraw[:, q % 2]).then_inc(s["w_high"], 1)
                if q % 2 == 1:
                    dve.drain()
                    take_low(dve, wm[:, 0, k], wraw[:, q % 2], wm[:, 1, k]).then_inc(s["w_split1"], 1)
            weights(0)
            merge(0)
            for q in range(1, 4):
                weights(q)
            merge(1)
            for t in range(TILES):
                if t + 2 < TILES:
                    merge(t + 2)
                if t % 4 == 0:
                    dve.wait_ge(x_ready[t // 4], 16)
                for half in range(2):
                    u = 2 * t + half
                    dve.wait_ge(s["mixed"], u + 1)
                    xs = e.x[:, t, half * 512:(half + 1) * 512]
                    dve.tensor_tensor(xs, xs, ps[:, u % 8, :], ALU.add).then_inc(s["emptied"], 1)

        @block.tensor
        def _(pe):
            for t in range(TILES):
                pe.wait_ge(s["m_split"], t + 1)
                for half in range(2):
                    u = 2 * t + half
                    if u >= 8:
                        pe.wait_ge(s["emptied"], u - 7)
                    for k in range(KD):
                        if u == 0 and k % 2 == 0:
                            pe.wait_ge(s[f"w_split{k // 2 % 2}"], k // 4 + 1)
                        last = split_product(pe, ps[:, u % 8, :], [merged[:, t % 3, j, k] for j in range(2)],
                                             [wm[:, j, k, half * 512:(half + 1) * 512] for j in range(2)], start=(k == 0), stop=(k == KD - 1))
                    last.then_inc(s["mixed"], 1)



def cross_projections(e, xc, memT, wq, wq_ready, wkv, wkv_ready):
    nc, a, o, ps = e.nc, e.a, e.o, e.ps
    s = {n: e.sem("cproj_" + n) for n in ("q_ready", "q_free", "kv_ready", "kv_copied", "stored", "kT")}
    with nc.sbuf_tensor("mem_k_rows", [P, MT, CW], F32) as mk, nc.Block() as block:
        @block.sync
        def _(sp):
            sp.wait_ge(s["kv_copied"], 2 * MT)
            for name, rows in (("p_cache_mem_k", mk), ("p_cache_mem_v", e.mv)):
                sp.dma_start(o[name].rearrange("o b (m p) h d -> p (o b m) (h d)", p=P), rows[:, :, :]).then_inc(s["stored"], 16)
            sp.wait_ge(s["stored"], 32)

        @block.tensor
        def _(pe):
            pe.wait_ge(wq_ready, 16)
            for h in range(CH):
                if h >= 2:
                    pe.wait_ge(s["q_free"], h - 1)
                for k in range(KD):
                    for q in range(NSPLIT):
                        last = pe.matmul(ps[:, 3 * (h % 2) + q, 0:NW], wq[:, k, h * P:(h + 1) * P], xc[:, k, q * NW:(q + 1) * NW],
                                         start=(k == 0), stop=(k == KD - 1))
                last.then_inc(s["q_ready"], 1)
            pe.wait_ge(wkv_ready, 16)
            pe.wait_ge(s["q_free"], CH)
            for m in range(MT):
                for half in range(2):
                    for k in range(KD):
                        last = pe.matmul(ps[:, 2 * m + half, :], memT[:, k, m * P:(m + 1) * P], wkv[:, k, half * CW:(half + 1) * CW],
                                         start=(k == 0), stop=(k == KD - 1))
                    last.then_inc(s["kv_ready"], 1)
            pe.wait_ge(s["kv_copied"], 2 * MT)
            for h in range(CH):
                for m in range(MT):
                    last = pe.transpose(ps[:, 4 + h // 2, (2 * (h % 2) + m) * P:(2 * (h % 2) + m + 1) * P], mk[:, m, h * P:(h + 1) * P], e.ident[:, :])
            last.then_inc(s["kT"], 1)

        @block.scalar
        def _(act):
            for h in range(CH):
                act.wait_ge(s["q_ready"], h + 1)
                act.activation(e.qc[:, h, 0:T].rearrange("p (q c) -> p q c", q=NSPLIT), ps[:, 3 * (h % 2):3 * (h % 2) + 3, 0:NW], ACT.Copy)\
                   .then_inc(s["q_free"], 1)

        @block.vector
        def _(dve):
            for m in range(MT):
                for half, rows in enumerate((mk, e.mv)):
                    dve.wait_ge(s["kv_ready"], 2 * m + half + 1)
                    dve.tensor_copy(rows[:, m], ps[:, 2 * m + half, :]).then_inc(s["kv_copied"], 1)
            dve.wait_ge(s["kT"], 1)
            dve.tensor_copy(e.mkT[:, :, :].rearrange("p (b h) m -> p b (h m)", b=2), ps[:, 4:6, :])


def cross_prompt(e, oc, w_out, w_ready):
    nc, ps = e.nc, e.ps
    names = ("s_ready", "s_free", "maxed", "exped", "recip", "p_ready", "p_free", "t_ready", "t_free", "pt_ready", "o_ready", "o_free")
    s = {n: e.sem("cross_" + n) for n in names}
    SCALE = CHD ** -0.5
    with ExitStack() as st:
        sb = lambda n, sh: st.enter_context(nc.sbuf_tensor(n, sh, F32))
        p = sb("cross_p", [P, 2, CH, MEM])
        pt = sb("cross_pt", [P, 2, CH, MT, P])
        mx, nm, den, rd = (sb("cross_" + n, [P, 2, CH]) for n in ("mx", "nm", "den", "rd"))
        block = st.enter_context(nc.Block())

        @block.sync
        def _(sp):
            sp.dma_start(w_out[:, :, :], e.a["w_co"][0].rearrange("(k p) c -> p k c", p=P)).then_inc(w_ready, 16)

        @block.tensor
        def _(pe):
            def scores(t):
                if t >= 2:
                    pe.wait_ge(s["s_free"], t - 1)
                for h in range(CH):
                    last = pe.matmul(ps[:, 2 * (t % 2) + h // 2, (h % 2) * MEM:(h % 2 + 1) * MEM], e.qc[:, h, t * P:(t + 1) * P], e.mkT[:, h],
                                     start=True, stop=True)
                last.then_inc(s["s_ready"], 1)

            def weigh(t):
                pe.wait_ge(s["p_ready"], t + 1)
                if t >= 1:
                    pe.wait_ge(s["t_free"], t)
                for h in range(CH):
                    for m in range(MT):
                        last = pe.transpose(ps[:, 4 + h // 2, (2 * (h % 2) + m) * P:(2 * (h % 2) + m + 1) * P],
                                            p[:, t % 2, h, m * P:(m + 1) * P], e.ident[:, :])
                last.then_inc(s["t_ready"], 1)
                pe.drain().then_inc(s["p_free"], 1)

            def values(t):
                pe.wait_ge(s["pt_ready"], t + 1)
                if t >= 2:
                    pe.wait_ge(s["o_free"], t - 1)
                for h in range(CH):
                    for m in range(MT):
                        last = pe.matmul(ps[:, 6 + t % 2, h * P:(h + 1) * P], e.mv[:, m, h * CHD:(h + 1) * CHD], pt[:, t % 2, h, m],
                                         start=(m == 0), stop=(m == MT - 1))
                last.then_inc(s["o_ready"], 1)

            scores(0)
            scores(1)
            for t in range(NT):
                weigh(t)
                if t + 2 < NT:
                    scores(t + 2)
                values(t)

        @block.scalar
        def _(act):
            for t in range(NT):
                act.wait_ge(s["maxed"], t + 1)
                if t >= 2:
                    act.wait_ge(s["p_free"], t - 1)
                for h in range(CH):
                    last = act.activation(p[:, t % 2, h], ps[:, 2 * (t % 2) + h // 2, (h % 2) * MEM:(h % 2 + 1) * MEM], ACT.Exp,
                                          bias=nm[:, t % 2, h:h + 1], scale=SCALE, accum_out=den[:, t % 2, h:h + 1])
                last.then_inc(s["exped"], 1)
                act.drain().then_inc(s["s_free"], 1)
                if t >= 1:
                    act.wait_ge(s["o_ready"], t)
                    act.activation(oc[:, :, (t - 1) * P:t * P], ps[:, 6 + (t - 1) % 2, :].rearrange("p (h c) -> p h c", h=CH), ACT.Copy).then_inc(s["o_free"], 1)
            act.wait_ge(s["o_ready"], NT)
            act.activation(oc[:, :, SEQ - P:SEQ], ps[:, 6 + (NT - 1) % 2, :].rearrange("p (h c) -> p h c", h=CH), ACT.Copy)

        @block.gpsimd
        def _(pool):
            pool.memset(oc[:, :, T:TP], 0.0)
            for t in range(NT):
                pool.wait_ge(s["recip"], t + 1)
                pool.tensor_tensor(p[:, t % 2], p[:, t % 2], bc(rd[:, t % 2].unsqueeze(2), [P, CH, MEM]), ALU.mult).then_inc(s["p_ready"], 1)

        @block.vector
        def _(dve):
            def maxima(t):
                dve.wait_ge(s["s_ready"], t + 1)
                dve.tensor_reduce(mx[:, t % 2], ps[:, 2 * (t % 2):2 * (t % 2) + 2, :].rearrange("p b (h m) -> p (b h) m", m=MEM), AX.X, ALU.max)
                dve.drain()
                dve.tensor_scalar(nm[:, t % 2], mx[:, t % 2], -SCALE, None, ALU.mult).then_inc(s["maxed"], 1)
            maxima(0)
            for t in range(NT):
                dve.wait_ge(s["exped"], t + 1)
                dve.reciprocal(rd[:, t % 2], den[:, t % 2]).then_inc(s["recip"], 1)
                if t + 1 < NT:
                    maxima(t + 1)
                dve.wait_ge(s["t_ready"], t + 1)
                if t >= 2:
                    dve.wait_ge(s["o_ready"], t - 1)
                dve.tensor_copy(pt[:, t % 2].rearrange("p (b h) m c -> p b (h m c)", b=2), ps[:, 4:6, :]).then_inc(s["pt_ready"], 1)
                dve.drain().then_inc(s["t_free"], 1)


def cross_sample(e, oc, w, w_ready):
    nc, a, ps = e.nc, e.a, e.ps
    names = ("v_ready", "k_free", "rows", "rows_copied", "q_ready", "q_free", "sT", "turned", "maxed", "exped", "normed", "pT", "pT_copied", "o_ready", "o_copied", "made", "emptied")
    s = {n: e.sem("csam_" + n) for n in names}
    k_ready = [e.sem(f"csam_k_ready{i}") for i in range(2)]
    SCALE = CHD ** -0.5
    R = NB * CH
    with ExitStack() as st:
        sb = lambda n, sh: st.enter_context(nc.sbuf_tensor(n, sh, F32))
        kc = sb("csam_k", [P, 2, MT, CW])
        vc = sb("csam_v", [P, NB, MT, CW])
        qr = sb("csam_q_rows", [NB, CW])
        prod = sb("csam_prod", [P, MT, CW])
        sT = sb("csam_sT", [P, MT, NB, CH])
        onehot = sb("csam_onehot", [NB, NB, P])
        sc = sb("csam_sc", [R, MEM])
        mx, nm, den, rd = (sb("csam_" + n, [R, 1]) for n in ("mx", "nm", "den", "rd"))
        pT = sb("csam_pT", [P, MT, NB, CH])
        made = e.sem("csam_onehot_made")
        block = st.enter_context(nc.Block())
        EARLY, UNITS = 3, 2 * TILES
        after = [range(0, EARLY)] + [range(EARLY + b, EARLY + b + 1) for b in range(NB)]
        after += [range(EARLY + NB, 12), range(12, 14), range(14, 2 * NT), range(2 * NT, UNITS)]

        @block.gpsimd
        def _(pool):
            pool.memset(onehot[:, :, :], 0.0)
            pool.drain()
            pool.affine_select(out=onehot[:, :, :], in_=onehot[:, :, :], compare_op=ALU.not_equal, fill=1.0, base=0,
                               pattern=[[-1, NB], [0, P]], channel_multiplier=1).then_inc(made, 1)

        @block.sync
        def _(sp):
            mem = lambda name, b: a[name][0, b].rearrange("(m p) h d -> p m (h d)", p=P)
            for b in range(NB):
                if b >= 2:
                    sp.wait_ge(s["k_free"], b - 1)
                sp.dma_start(kc[:, b % 2], mem("cache_mem_k", b)).then_inc(k_ready[b % 2], 16)
                sp.dma_start(vc[:, b], mem("cache_mem_v", b)).then_inc(s["v_ready"], 16)

        @block.tensor
        def _(pe):
            def make(units):
                for u in units:
                    t, half = u // 2, u % 2
                    if u >= 2:
                        pe.wait_ge(s["emptied"], u - 1)
                    for k in range(CH):
                        last = pe.matmul(ps[:, 6 + u % 2, :], oc[:, k, t * P:(t + 1) * P], w[:, k, half * 512:(half + 1) * 512],
                                         start=(k == 0), stop=(k == CH - 1))
                    last.then_inc(s["made"], 1)

            for h in range(CH):
                last = pe.transpose(ps[0:NB, 0, h * P:(h + 1) * P], e.qc[:, h, SEQ:T], e.ident[:, :])
            last.then_inc(s["rows"], 1)
            pe.wait_ge(w_ready, 16)
            make(after[0])
            pe.wait_ge(s["rows_copied"], 1)
            pe.wait_ge(made, 1)
            for b in range(NB):
                if b >= 2:
                    pe.wait_ge(s["q_free"], b - 1)
                pe.matmul(ps[:, 1 + b % 2, :], onehot[:, b], qr[:, :], start=True, stop=True).then_inc(s["q_ready"], 1)
                make(after[1 + b])
            make(after[1 + NB])
            pe.wait_ge(s["sT"], 1)
            for m in range(MT):
                last = pe.transpose(ps[0:R, 3, m * P:(m + 1) * P], sT[:, m].rearrange("p b h -> p (b h)"), e.ident[:, :])
            last.then_inc(s["turned"], 1)
            make(after[2 + NB])
            pe.wait_ge(s["normed"], 1)
            for m in range(MT):
                last = pe.transpose(ps[:, 4, m * R:(m + 1) * R], sc[:, m * P:(m + 1) * P], e.ident[0:R, 0:R])
            last.then_inc(s["pT"], 1)
            make(after[3 + NB])
            pe.wait_ge(s["pT_copied"], 1)
            pe.wait_ge(s["v_ready"], 16 * NB)
            for b in range(NB):
                for h in range(CH):
                    for m in range(MT):
                        last = pe.matmul(ps[:, 5, h * NB + b:h * NB + b + 1], vc[:, b, m, h * CHD:(h + 1) * CHD], pT[:, m, b, h:h + 1],
                                         start=(m == 0), stop=(m == MT - 1))
            last.then_inc(s["o_ready"], 1)
            pe.wait_ge(s["o_copied"], 1)
            make(after[4 + NB])

        @block.scalar
        def _(act):
            act.wait_ge(s["maxed"], 1)
            act.activation(sc[:, :], ps[0:R, 3, 0:MEM], ACT.Exp, bias=nm[:, :], scale=SCALE, accum_out=den[:, :]).then_inc(s["exped"], 1)

        @block.vector
        def _(dve):
            def add(units):
                for u in units:
                    dve.wait_ge(s["made"], u + 1)
                    xs = e.x[:, u // 2, (u % 2) * 512:(u % 2 + 1) * 512]
                    dve.tensor_tensor(xs, xs, ps[:, 6 + u % 2, :], ALU.add).then_inc(s["emptied"], 1)

            dve.wait_ge(s["rows"], 1)
            dve.tensor_copy(qr[:, :], ps[0:NB, 0, :]).then_inc(s["rows_copied"], 1)
            add(after[0])
            for b in range(NB):
                dve.wait_ge(s["q_ready"], b + 1)
                dve.wait_ge(k_ready[b % 2], 16 * (b // 2 + 1))
                dve.tensor_tensor(prod[:, :, :], kc[:, b % 2], bc(ps[:, 1 + b % 2, :].unsqueeze(1), [P, MT, CW]), ALU.mult)
                dve.drain().then_inc(s["q_free"], 1)
                dve.sem_inc(s["k_free"], 1)
                dve.tensor_reduce(sT[:, :, b], prod[:, :, :].rearrange("p m (h d) -> p m h d", h=CH), AX.X, ALU.add)
                dve.drain()
                if b == NB - 1:
                    dve.sem_inc(s["sT"], 1)
                add(after[1 + b])
            add(after[1 + NB])
            dve.wait_ge(s["turned"], 1)
            dve.tensor_reduce(mx[:, :], ps[0:R, 3, 0:MEM], AX.X, ALU.max)
            dve.drain()
            dve.tensor_scalar(nm[:, :], mx[:, :], -SCALE, None, ALU.mult).then_inc(s["maxed"], 1)
            add(after[2 + NB])
            dve.wait_ge(s["exped"], 1)
            dve.reciprocal(rd[:, :], den[:, :])
            dve.drain()
            dve.tensor_scalar(sc[:, :], sc[:, :], rd[:, :], None, ALU.mult).then_inc(s["normed"], 1)
            dve.wait_ge(s["pT"], 1)
            dve.tensor_copy(pT[:, :, :, :].rearrange("p m b h -> p (m b h)"), ps[:, 4, 0:MT * R]).then_inc(s["pT_copied"], 1)
            add(after[3 + NB])
            dve.wait_ge(s["o_ready"], 1)
            dve.tensor_copy(oc[:, :, SEQ:T], ps[:, 5, 0:CH * NB].rearrange("p (h b) -> p h b", h=CH)).then_inc(s["o_copied"], 1)
            add(after[4 + NB])


def cross_attention(e):
    nc, a = e.nc, e.a
    with ExitStack() as st:
        sb = lambda n, sh: st.enter_context(nc.sbuf_tensor(n, sh, F32))
        e.qc = sb("qc", [P, CH, T])
        e.mkT = sb("mkT", [P, CH, MEM])
        e.mv = sb("mv", [P, MT, CW])
        rows = lambda w: w.rearrange("(k p) c -> p k c", p=P)
        with nc.sbuf_tensor("xc", [P, KD, TP], F32) as xc, nc.sbuf_tensor("memT", [P, KD, MEM], F32) as memT, \
                nc.sbuf_tensor("w_cq", [P, KD, CW], F32) as wq, nc.sbuf_tensor("w_ckv", [P, KD, 2 * CW], F32) as wkv:
            with nc.sbuf_tensor("mem_rows", [P, MT, D], F32) as mem:
                mem_ready, wq_ready, wkv_ready = (e.sem(n) for n in ("mem_ready", "wq_ready", "wkv_ready"))
                rms_tiles(e, "cross", e.x, TILES, xc, grow=G_CROSS,
                          prefetch=[(mem[:, :, :], rows(a["mem_prompt"][0]), mem_ready), (wq[:, :, :], rows(a["w_cq"][0]), wq_ready),
                                    (wkv[:, :, :], rows(a["w_ckv"][0]), wkv_ready)])
                rms_tiles(e, "mem", mem, MT, memT, grow=G_MEM, ready=mem_ready)
            cross_projections(e, xc, memT, wq, wq_ready, wkv, wkv_ready)
        with nc.sbuf_tensor("cross_oc", [P, CH, TP], F32) as oc, nc.sbuf_tensor("w_co", [P, CH, D], F32) as w_out:
            w_ready = e.sem("co_w_ready")
            cross_prompt(e, oc, w_out, w_ready)
            cross_sample(e, oc, w_out, w_ready)


def resident_rows(e):
    e.x = e.ctx.enter_context(e.nc.sbuf_tensor("x_resident", [P, TILES, D], F32))


NBASE = NE
NMORE = TILES * P * 2 // P - 2
SLOTS = (NBASE + NMORE) * P


NR = NGR + NE


def routing(e, xT, wr, bias, loaded):
    nc, a, ps = e.nc, e.a, e.ps
    s = {n: e.sem("route_" + n) for n in ("columns", "copied", "logits", "pool_made", "chosen", "counted", "e0", "e1", "x0", "x1", "zeroed", "zero_made", "slots", "scattered0", "scattered1")}
    with ExitStack() as st:
        sb = lambda n, sh, dt=F32: st.enter_context(nc.sbuf_tensor("r_" + n, sh, dt))
        lg = sb("logits", [P, TILES, NR])
        lgT = sb("logit_cols", [NR, TP])
        LOGIT_COLS = [slice(0, 512), slice(512, 1024), slice(1024, TP)]
        gm = sb("gm", [P, TILES, 1])
        g4 = sb("g4", [P, TILES, NGR])
        ohg = sb("ohg", [P, TILES, NGR])
        wt = sb("wt", [P, EPG])
        pg = sb("pg", [P, TILES, 1])
        l4 = sb("l4", [P, TILES, NGR, EPG])
        le, key = sb("le", [P, TILES, EPG]), sb("key", [P, TILES, EPG])
        oh = [sb(f"oh{i}", [P, TILES, EPG]) for i in range(2)]
        m = [sb(f"m{i}", [P, TILES, 1]) for i in range(2)]
        km = sb("km", [P, TILES, 1])
        big = [sb(f"big{i}", [P, TILES, NE]) for i in range(2)]
        sel, rank = sb("sel", [P, TILES, NE]), sb("rank", [P, TILES, NE])
        valid = sb("valid", [P, TILES])
        off = sb("off", [P, TILES + 1, NE])
        more = [sb(f"more{i}", [P, NE]) for i in range(2)]
        nmore, delta, base_b = sb("nmore", [P, NE]), sb("delta", [P, NE]), sb("base_b", [P, NE])
        first = sb("first", [P, NE])
        below = sb("below_p", [P, TILES, NE])
        d = [sb(f"dest_f{i}", [P, TILES, 1]) for i in range(2)]
        tid = sb("tid", [P, TILES], I32)
        zero = sb("zero", [NBASE + NMORE, P], I32)
        jj = sb("jj", [1, NMORE, 1])
        ge = sb("ge", [1, NMORE, NE])
        ef = sb("ef", [1, NMORE])
        block = st.enter_context(nc.Block())

        @block.sync
        def _(sp):
            sp.wait_ge(s["zero_made"], 1)
            sp.dma_start(e.slot_tok.rearrange("(b p) o -> b (p o)", p=P), zero[:, :]).then_inc(s["zeroed"], 16)
            sp.wait_ge(s["zeroed"], 16)

        @block.gpsimd
        def _(pool):
            pool.memset(zero[:, :], 0).then_inc(s["zero_made"], 1)
            pool.iota(wt[:, :], pattern=[[-1, EPG]], base=EPG, channel_multiplier=0, allow_small_or_imprecise_dtypes=True)
            pool.iota(first[:, :], pattern=[[P, NE]], base=0, channel_multiplier=0, allow_small_or_imprecise_dtypes=True)
            pool.iota(jj[:, :, :], pattern=[[1, NMORE], [0, 1]], base=0, channel_multiplier=0, allow_small_or_imprecise_dtypes=True)
            pool.iota(tid[:, :], pattern=[[P, TILES]], base=0, channel_multiplier=1)
            pool.memset(valid[:, :], 1.0)
            pool.drain()
            pool.affine_select(out=valid[:, NT:TILES], in_=valid[:, NT:TILES], compare_op=ALU.is_ge, fill=0.0, base=NB - 1,
                               pattern=[[0, 1]], channel_multiplier=-1)
            pool.drain().then_inc(s["pool_made"], 1)
            pool.wait_ge(s["slots"], 1)
            pool.wait_ge(s["zeroed"], 16)
            n = 0
            for i in range(2):
                for t in range(TILES):
                    rows = P if t < NT else NB
                    pool.indirect_dma_start(e.slot_tok, bass.IndirectOffsetOnAxis(ap=e.dest[0:rows, i, t:t + 1], axis=0),
                                            tid[0:rows, t:t + 1], None).then_inc(s[f"scattered{n % 2}"], 16)
                    n += 1
            for i in range(2):
                pool.wait_ge(s[f"scattered{i}"], 16 * TILES)

        @block.tensor
        def _(pe):
            pe.wait_ge(loaded, 64)
            for i, c in enumerate(LOGIT_COLS):
                for k in range(KD):
                    last = pe.matmul(ps[0:NR, 1 + i, 0:c.stop - c.start], wr[:, k], xT[:, k, c], start=(k == 0), stop=(k == KD - 1))
                last.then_inc(s["columns"], 1)
            pe.wait_ge(s["copied"], len(LOGIT_COLS))
            for t in range(TILES):
                last = pe.transpose(ps[:, 0, t * NR:(t + 1) * NR], lgT[:, t * P:(t + 1) * P], e.ident[0:NR, 0:NR])
            last.then_inc(s["logits"], 1)
            pe.wait_ge(s["chosen"], 1)
            flat = sel[:, :, :].rearrange("p t e -> p (t e)")
            pe.matmul(ps[:, 1, 0:TILES * NE], e.tri[:, :], flat, start=True, stop=True)
            pe.matmul(ps[:, 2, 0:TILES * NE], e.ones[:, :], flat, start=True, stop=True).then_inc(s["counted"], 1)

        @block.scalar
        def _(act):
            act.wait_ge(s["e0"], 1)
            act.activation(g4[:, :, :], g4[:, :, :], ACT.Exp).then_inc(s["x0"], 1)
            act.wait_ge(s["e1"], 1)
            act.activation(m[1][:, :, :], m[1][:, :, :], ACT.Exp).then_inc(s["x1"], 1)

        @block.vector
        def _(dve):
            def tt(out, x, y, op):
                dve.tensor_tensor(out, x, y, op)
                dve.drain()

            def first_of(out, x, mx, width):
                tt(key[:, :, 0:width], x, bc(mx, [P, TILES, width]), ALU.is_equal)
                tt(key[:, :, 0:width], key[:, :, 0:width], bc(wt[:, EPG - width:].unsqueeze(1), [P, TILES, width]), ALU.mult)
                dve.tensor_reduce(km[:, :, :], key[:, :, 0:width].unsqueeze(2), AX.X, ALU.max)
                dve.drain()
                tt(out, key[:, :, 0:width], bc(km[:, :, :], [P, TILES, width]), ALU.is_equal)

            dve.wait_ge(loaded, 64)
            dve.wait_ge(s["pool_made"], 1)
            for i, c in enumerate(LOGIT_COLS):
                dve.wait_ge(s["columns"], i + 1)
                dve.tensor_copy(lgT[:, c], ps[0:NR, 1 + i, 0:c.stop - c.start]).then_inc(s["copied"], 1)
            dve.wait_ge(s["logits"], 1)
            tt(lg[:, :, :], ps[:, 0, 0:TILES * NR].rearrange("p (t c) -> p t c", c=NR), bc(bias[:, :].unsqueeze(1), [P, TILES, NR]), ALU.add)
            dve.tensor_reduce(gm[:, :, :], lg[:, :, 0:NGR].unsqueeze(2), AX.X, ALU.max)
            dve.drain()
            dve.tensor_tensor(g4[:, :, :], lg[:, :, 0:NGR], bc(gm[:, :, :], [P, TILES, NGR]), ALU.subtract).then_inc(s["e0"], 1)
            first_of(ohg[:, :, :], lg[:, :, 0:NGR], gm[:, :, :], NGR)
            tt(l4[:, :, :, :], lg[:, :, NGR:].rearrange("p t (g x) -> p t g x", g=NGR), bc(ohg[:, :, :].unsqueeze(3), [P, TILES, NGR, EPG]), ALU.mult)
            dve.tensor_reduce(le[:, :, :], l4[:, :, :, :].rearrange("p t g x -> p t x g"), AX.X, ALU.add)
            dve.drain()
            dve.tensor_reduce(m[0][:, :, :], le[:, :, :].unsqueeze(2), AX.X, ALU.max)
            dve.drain()
            first_of(oh[0][:, :, :], le[:, :, :], m[0][:, :, :], EPG)
            dve.scalar_tensor_tensor(out=le[:, :, :], in0=oh[0][:, :, :], scalar=NEG, in1=le[:, :, :], op0=ALU.mult, op1=ALU.add)
            dve.drain()
            dve.tensor_reduce(m[1][:, :, :], le[:, :, :].unsqueeze(2), AX.X, ALU.max)
            dve.drain()
            first_of(oh[1][:, :, :], le[:, :, :], m[1][:, :, :], EPG)
            dve.tensor_tensor(m[1][:, :, :], m[1][:, :, :], m[0][:, :, :], ALU.subtract).then_inc(s["e1"], 1)
            for i in range(2):
                tt(big[i][:, :, :].rearrange("p t (g x) -> p t g x", g=NGR), bc(ohg[:, :, :].unsqueeze(3), [P, TILES, NGR, EPG]),
                   bc(oh[i][:, :, :].unsqueeze(2), [P, TILES, NGR, EPG]), ALU.mult)
            tt(sel[:, :, :], big[0][:, :, :], big[1][:, :, :], ALU.add)
            tt(sel[:, :, :], sel[:, :, :], bc(valid[:, :].unsqueeze(2), [P, TILES, NE]), ALU.mult)
            dve.sem_inc(s["chosen"], 1)
            dve.wait_ge(s["x0"], 1)
            dve.tensor_reduce(pg[:, :, :], g4[:, :, :].unsqueeze(2), AX.X, ALU.add)
            dve.drain()
            dve.wait_ge(s["x1"], 1)
            dve.tensor_scalar(m[0][:, :, :], m[1][:, :, :], 1.0, None, ALU.add)
            dve.drain()
            tt(pg[:, :, :], pg[:, :, :], m[0][:, :, :], ALU.mult)
            dve.reciprocal(e.gate[:, 0].unsqueeze(2), pg[:, :, :])
            dve.drain()
            tt(e.gate[:, 1].unsqueeze(2), e.gate[:, 0].unsqueeze(2), m[1][:, :, :], ALU.mult)
            dve.wait_ge(s["counted"], 1)
            dve.memset(off[:, 0], 0.0)
            dve.drain()
            for t in range(TILES):
                tt(off[:, t + 1], off[:, t], ps[:, 2, t * NE:(t + 1) * NE], ALU.add)
            tt(rank[:, :, :], ps[:, 1, 0:TILES * NE].rearrange("p (t e) -> p t e", e=NE), sel[:, :, :], ALU.subtract)
            tt(rank[:, :, :], rank[:, :, :], off[:, 0:TILES], ALU.add)
            cnt = off[:, TILES]
            dve.tensor_scalar(nmore[:, :], cnt, float(P), None, ALU.is_gt)
            dve.drain()
            for j in range(2, T // P + 1):
                dve.scalar_tensor_tensor(out=nmore[:, :], in0=cnt, scalar=float(j * P), in1=nmore[:, :], op0=ALU.is_gt, op1=ALU.add)
                dve.drain()
            dve.tensor_copy(more[0][:, :], nmore[:, :])
            dve.drain()
            src = 0
            step = 1
            while step < NE:
                dve.tensor_copy(more[1 - src][:, 0:step], more[src][:, 0:step])
                dve.tensor_tensor(more[1 - src][:, step:], more[src][:, step:], more[src][:, 0:NE - step], ALU.add)
                dve.drain()
                src, step = 1 - src, 2 * step
            end = more[src]
            tt(base_b[:, :], end[:, :], nmore[:, :], ALU.subtract)
            dve.tensor_scalar(base_b[:, :], base_b[:, :], float(P), float((NBASE - 1) * P), ALU.mult, ALU.add)
            dve.drain()
            tt(delta[:, :], first[:, :], base_b[:, :], ALU.subtract)
            dve.tensor_scalar(below[:, :, :], rank[:, :, :], float(P), None, ALU.is_lt)
            dve.drain()
            tt(below[:, :, :], below[:, :, :], bc(delta[:, :].unsqueeze(1), [P, TILES, NE]), ALU.mult)
            tt(rank[:, :, :], rank[:, :, :], bc(base_b[:, :].unsqueeze(1), [P, TILES, NE]), ALU.add)
            tt(rank[:, :, :], rank[:, :, :], below[:, :, :], ALU.add)
            for i in range(2):
                tt(big[i][:, :, :], big[i][:, :, :], rank[:, :, :], ALU.mult)
                dve.tensor_reduce(d[i][:, :, :], big[i][:, :, :].unsqueeze(2), AX.X, ALU.add)
                dve.drain()
                dve.tensor_copy(e.dest[:, i].unsqueeze(2), d[i][:, :, :])
                dve.drain()
            dve.sem_inc(s["slots"], 1)
            tt(ge[:, :, :], bc(jj[:, :, :], [1, NMORE, NE]), bc(end[0:1, :].unsqueeze(1), [1, NMORE, NE]), ALU.is_ge)
            dve.tensor_reduce(ef[:, :], ge[:, :, :], AX.X, ALU.add)
            dve.drain()
            dve.tensor_scalar(ef[:, :], ef[:, :], float(NE - 1), None, ALU.min)
            dve.drain()
            dve.tensor_copy(e.more_expert[:, 0:NMORE], ef[:, :])
            dve.tensor_copy(e.more_expert[:, NMORE:NMORE + 1], end[0:1, NE - 1:NE])


def expert_weights(e, n, names):
    return [e.a[name][0][bass.ds(n, 1)].rearrange("o (k p) c -> p (o k) c", p=P) for name in names]


def expert_blocks(e, name, count, wg, wu, wg_ready):
    nc, a, ps = e.nc, e.a, e.ps
    names = ("wg_free", "idx_free", "x_free", "gather_go", "turned", "xt_low", "xt_high", "gu_ready", "silu_ready", "gu_free", "h_ready", "h_free",
             "ht_ready", "ht_copied", "down_ready", "down_free", "y_ready")
    s = {n: e.sem(f"{name}_{n}") for n in names}
    two = lambda n: [e.sem(f"{name}_{n}{i}") for i in range(2)]
    wd_ready, idx_ready, x_ready, stored = two("wd_ready"), two("idx_ready"), two("x_ready"), two("stored")
    KE = DE // P
    with ExitStack() as st:
        sb = lambda n, sh, dt=F32: st.enter_context(nc.sbuf_tensor(f"{name}_{n}", sh, dt))
        wd = sb("wd", [P, 2, KE, D])
        idx = [sb(f"idx{i}", [P, 1], I32) for i in range(2)]
        xg = [sb(f"x{i}", [P, D]) for i in range(2)]
        xt = sb("xt", [P, KD, P])
        act_g = sb("silu", [P, DE])
        h = sb("h", [P, 2, DE])
        ht = sb("ht", [P, 2, KE, P])
        y = sb("y", [P, 2, D])

        def in_pairs(eng, step):
            with eng.Fori(0, count // 2) as i:
                for j in range(2):
                    step(i * 2 + j, j, i)

        with nc.Block() as block:
            @block.sync
            def _(sp):
                def load_index(n, b):
                    sp.wait_ge(s["idx_free"], n + 1)
                    sp.dma_start(idx[b][:, :], e.slot_tok[bass.ds(n * P, P), :]).then_inc(idx_ready[b], 16)
                load_index(0, 0)
                load_index(1, 1)
                with sp.Fori(1, count // 2) as i:
                    for b in range(2):
                        n = i * 2 + b
                        load_index(n, b)
                        sp.wait_ge(s["wg_free"], n + 1)
                        for dst, src in zip((wg, wu), expert_weights(e, n, ("w_e_gate", "w_e_up"))):
                            sp.dma_start(dst[:, b], src).then_inc(wg_ready[b], 16)

            @block.gpsimd
            def _(pool):
                pool.sem_inc(s["idx_free"], 2)

                def gather(n, b, i):
                    pool.wait_ge(idx_ready[b], i * 16 + 16)
                    pool.wait_ge(s["x_free"], n + 1)
                    pool.sem_inc(s["gather_go"], 1)
                    pool.indirect_dma_start(xg[b][:, :], None, e.xm_rows, bass.IndirectOffsetOnAxis(ap=idx[b][:, 0:1], axis=0)).then_inc(x_ready[b], 16)
                    pool.wait_ge(x_ready[b], i * 16 + 16)
                    pool.sem_inc(s["idx_free"], 1)
                in_pairs(pool, gather)

            @block.tensor
            def _(pe):
                pe.sem_inc(s["x_free"], 2)
                pe.sem_inc(s["wg_free"], 2)
                pe.sem_inc(s["h_free"], 2)

                def turn(n, b, i):
                    pe.wait_ge(x_ready[b], i * 16 + 16)
                    pe.wait_ge(s["xt_low"], n + 1)
                    pe.wait_ge(s["xt_high"], n + 1)
                    for k in range(KD):
                        last = pe.transpose(ps[:, k // 4, (k % 4) * P:(k % 4 + 1) * P], xg[b][:, k * P:(k + 1) * P], e.ident[:, :])
                    last.then_inc(s["turned"], 1)
                    pe.drain().then_inc(s["x_free"], 1)

                def gate_up(n, b, i):
                    pe.wait_ge(wg_ready[b], i * 32 + 32)
                    pe.wait_ge(s["gu_free"], n + 1)
                    pe.wait_ge(s["xt_low"], n + 2)
                    pe.wait_ge(s["xt_high"], n + 2)
                    for w, bank in ((wg, 2), (wu, 3)):
                        for k in range(KD):
                            last = pe.matmul(ps[:, bank, :], xt[:, k], w[:, b, k], start=(k == 0), stop=(k == KD - 1))
                    last.then_inc(s["gu_ready"], 1)
                    pe.drain().then_inc(s["wg_free"], 1)

                def turn_h(n, b):
                    pe.wait_ge(s["h_ready"], n + 1)
                    pe.wait_ge(s["ht_copied"], n + 1)
                    for k in range(KE):
                        last = pe.transpose(ps[:, 4, k * P:(k + 1) * P], h[:, b, k * P:(k + 1) * P], e.ident[:, :])
                    last.then_inc(s["ht_ready"], 1)
                    pe.drain().then_inc(s["h_free"], 1)

                def down(n, b, i):
                    pe.wait_ge(wd_ready[b], i * 16 + 16)
                    pe.wait_ge(s["ht_copied"], n + 2)
                    pe.wait_ge(s["down_free"], n + 1)
                    for half in range(2):
                        for k in range(KE):
                            last = pe.matmul(ps[:, 5 + half, :], ht[:, b, k], wd[:, b, k, half * 512:(half + 1) * 512], start=(k == 0), stop=(k == KE - 1))
                    last.then_inc(s["down_ready"], 1)

                turn(0, 0, 0)
                gate_up(0, 0, 0)
                turn(1, 1, 0)
                turn_h(0, 0)
                with pe.Fori(0, count // 2 - 1) as i:
                    gate_up(i * 2 + 1, 1, i)
                    turn(i * 2 + 2, 0, i + 1)
                    down(i * 2, 0, i)
                    turn_h(i * 2 + 1, 1)
                    gate_up(i * 2 + 2, 0, i + 1)
                    turn(i * 2 + 3, 1, i + 1)
                    down(i * 2 + 1, 1, i)
                    turn_h(i * 2 + 2, 0)
                gate_up(count - 1, 1, count // 2 - 1)
                down(count - 2, 0, count // 2 - 1)
                turn_h(count - 1, 1)
                down(count - 1, 1, count // 2 - 1)

            @block.scalar
            def _(act):
                act.sem_inc(s["xt_high"], 1)
                for b in range(2):
                    act.sem_inc(stored[b], 16)

                def high(n):
                    act.wait_ge(s["turned"], n + 1)
                    act.wait_ge(s["gu_ready"], n) if not (isinstance(n, int) and n == 0) else None
                    act.activation(xt[:, 4:8].rearrange("p k c -> p (k c)"), ps[:, 1, :], ACT.Copy).then_inc(s["xt_high"], 1)

                def silu(n):
                    act.wait_ge(s["gu_ready"], n + 1)
                    act.wait_ge(s["gu_free"], n + 1)
                    act.activation(act_g[:, :], ps[:, 2, :], ACT.Silu).then_inc(s["silu_ready"], 1)

                def load_down(x, b):
                    act.dma_start(wd[:, b], a["w_e_down"][0][bass.ds(x, 1)].rearrange("o (k p) c -> p (o k) c", p=P)).then_inc(wd_ready[b], 16)

                def out(n, b, i, reload=True):
                    act.wait_ge(s["y_ready"], n + 1)
                    if reload:
                        load_down(n + 2, b)
                    act.dma_start(e.y_rows[bass.ds(n * P, P), :], y[:, b]).then_inc(stored[b], 16)

                load_down(0, 0)
                load_down(1, 1)
                high(0)
                silu(0)
                high(1)
                with act.Fori(0, count // 2 - 1) as i:
                    silu(i * 2 + 1)
                    high(i * 2 + 2)
                    out(i * 2, 0, i)
                    silu(i * 2 + 2)
                    high(i * 2 + 3)
                    out(i * 2 + 1, 1, i)
                silu(count - 1)
                out(count - 2, 0, 0, reload=False)
                out(count - 1, 1, 0, reload=False)
                for b in range(2):
                    act.wait_ge(stored[b], 16 * (count // 2 + 1))

            @block.vector
            def _(dve):
                dve.sem_inc(s["xt_low"], 1)
                dve.sem_inc(s["gu_free"], 1)
                dve.sem_inc(s["ht_copied"], 1)
                dve.sem_inc(s["down_free"], 1)

                def low(n):
                    dve.wait_ge(s["turned"], n + 1)
                    dve.wait_ge(s["gu_ready"], n) if not (isinstance(n, int) and n == 0) else None
                    dve.tensor_copy(xt[:, 0:4].rearrange("p k c -> p (k c)"), ps[:, 0, :]).then_inc(s["xt_low"], 1)

                def product(n, b):
                    dve.wait_ge(s["silu_ready"], n + 1)
                    dve.wait_ge(s["h_free"], n + 1)
                    dve.tensor_tensor(h[:, b], act_g[:, :], ps[:, 3, :], ALU.mult).then_inc(s["h_ready"], 1)
                    dve.drain().then_inc(s["gu_free"], 1)

                def copy_h(n, b):
                    dve.wait_ge(s["ht_ready"], n + 1)
                    dve.wait_ge(s["down_ready"], n) if not (isinstance(n, int) and n == 0) else None
                    dve.tensor_copy(ht[:, b].rearrange("p k c -> p (k c)"), ps[:, 4, :]).then_inc(s["ht_copied"], 1)

                def rows(n, b, i):
                    dve.wait_ge(s["down_ready"], n + 1)
                    dve.wait_ge(stored[b], i * 16 + 16)
                    dve.tensor_copy(y[:, b].rearrange("p (h c) -> p h c", h=2), ps[:, 5:7, :]).then_inc(s["y_ready"], 1)
                    dve.drain().then_inc(s["down_free"], 1)

                low(0)
                product(0, 0)
                low(1)
                copy_h(0, 0)
                with dve.Fori(0, count // 2 - 1) as i:
                    product(i * 2 + 1, 1)
                    low(i * 2 + 2)
                    rows(i * 2, 0, i)
                    copy_h(i * 2 + 1, 1)
                    product(i * 2 + 2, 0)
                    low(i * 2 + 3)
                    rows(i * 2 + 1, 1, i)
                    copy_h(i * 2 + 2, 0)
                product(count - 1, 1)
                rows(count - 2, 0, count // 2 - 1)
                copy_h(count - 1, 1)
                rows(count - 1, 1, count // 2 - 1)


def further_blocks(e):
    nc, a, ps = e.nc, e.a, e.ps
    s = {n: e.sem("more_" + n) for n in ("idx_ready", "w_ready", "x_ready", "gather_go", "turned", "xt_low", "xt_high", "gu_ready", "silu_ready",
                                         "h_ready", "ht_ready", "ht_copied", "down_ready", "y_ready", "stored", "done")}
    KE = DE // P
    with ExitStack() as st:
        sb = lambda n, sh, dt=F32: st.enter_context(nc.sbuf_tensor(f"more_{n}", sh, dt))
        wg, wu, wd = sb("wg", [P, KD, DE]), sb("wu", [P, KD, DE]), sb("wd", [P, KE, D])
        idx, xg, xt = sb("idx", [P, 1], I32), sb("x", [P, D]), sb("xt", [P, KD, P])
        act_g, h, ht, y = sb("silu", [P, DE]), sb("h", [P, DE]), sb("ht", [P, KE, P]), sb("y", [P, D])
        block = st.enter_context(nc.Block())

        def each(eng, step):
            total = eng.value_load(e.more_expert[0:1, NMORE:NMORE + 1], min_val=0, max_val=NMORE)
            with eng.Fori(0, NMORE) as j:
                with eng.If(j < total):
                    step(j)

        @block.sync
        def _(sp):
            def load(j):
                x = sp.value_load(e.more_expert[0:1, bass.ds(j, 1)], min_val=0, max_val=NE - 1)
                pick = lambda w: w[0][bass.ds(x, 1)].rearrange("o (k p) c -> p (o k) c", p=P)
                sp.wait_ge(s["done"], j + 1)
                sp.dma_start(idx[:, :], e.slot_tok[bass.ds(j * P + NBASE * P, P), :]).then_inc(s["idx_ready"], 16)
                for w, name in ((wg, "w_e_gate"), (wu, "w_e_up"), (wd, "w_e_down")):
                    sp.dma_start(w[:, :, :], pick(a[name])).then_inc(s["w_ready"], 16)
            each(sp, load)

        @block.gpsimd
        def _(pool):
            def gather(j):
                pool.wait_ge(s["idx_ready"], j * 16 + 16)
                pool.sem_inc(s["gather_go"], 1)
                pool.indirect_dma_start(xg[:, :], None, e.xm_rows, bass.IndirectOffsetOnAxis(ap=idx[:, 0:1], axis=0)).then_inc(s["x_ready"], 16)
                pool.wait_ge(s["x_ready"], j * 16 + 16)
                pool.sem_inc(s["gather_go"], 1)
            each(pool, gather)

        @block.tensor
        def _(pe):
            def products(j):
                pe.wait_ge(s["x_ready"], j * 16 + 16)
                for k in range(KD):
                    last = pe.transpose(ps[:, k // 4, (k % 4) * P:(k % 4 + 1) * P], xg[:, k * P:(k + 1) * P], e.ident[:, :])
                last.then_inc(s["turned"], 1)
                pe.wait_ge(s["w_ready"], j * 48 + 48)
                pe.wait_ge(s["xt_low"], j + 1)
                pe.wait_ge(s["xt_high"], j + 1)
                for w, bank in ((wg, 2), (wu, 3)):
                    for k in range(KD):
                        last = pe.matmul(ps[:, bank, :], xt[:, k], w[:, k], start=(k == 0), stop=(k == KD - 1))
                last.then_inc(s["gu_ready"], 1)
                pe.wait_ge(s["h_ready"], j + 1)
                for k in range(KE):
                    last = pe.transpose(ps[:, 4, k * P:(k + 1) * P], h[:, k * P:(k + 1) * P], e.ident[:, :])
                last.then_inc(s["ht_ready"], 1)
                pe.wait_ge(s["ht_copied"], j + 1)
                for half in range(2):
                    for k in range(KE):
                        last = pe.matmul(ps[:, 5 + half, :], ht[:, k], wd[:, k, half * 512:(half + 1) * 512], start=(k == 0), stop=(k == KE - 1))
                last.then_inc(s["down_ready"], 1)
            each(pe, products)

        @block.scalar
        def _(act):
            act.sem_inc(s["done"], 1)

            def step(j):
                act.wait_ge(s["turned"], j + 1)
                act.activation(xt[:, 4:8].rearrange("p k c -> p (k c)"), ps[:, 1, :], ACT.Copy).then_inc(s["xt_high"], 1)
                act.wait_ge(s["gu_ready"], j + 1)
                act.activation(act_g[:, :], ps[:, 2, :], ACT.Silu).then_inc(s["silu_ready"], 1)
                act.wait_ge(s["y_ready"], j + 1)
                act.dma_start(e.y_rows[bass.ds(j * P + NBASE * P, P), :], y[:, :]).then_inc(s["stored"], 16)
                act.wait_ge(s["stored"], j * 16 + 16)
                act.sem_inc(s["done"], 1)
            each(act, step)

        @block.vector
        def _(dve):
            def step(j):
                dve.wait_ge(s["turned"], j + 1)
                dve.tensor_copy(xt[:, 0:4].rearrange("p k c -> p (k c)"), ps[:, 0, :]).then_inc(s["xt_low"], 1)
                dve.wait_ge(s["silu_ready"], j + 1)
                dve.tensor_tensor(h[:, :], act_g[:, :], ps[:, 3, :], ALU.mult).then_inc(s["h_ready"], 1)
                dve.wait_ge(s["ht_ready"], j + 1)
                dve.tensor_copy(ht[:, :, :].rearrange("p k c -> p (k c)"), ps[:, 4, :]).then_inc(s["ht_copied"], 1)
                dve.wait_ge(s["down_ready"], j + 1)
                dve.tensor_copy(y[:, :].rearrange("p (h c) -> p h c", h=2), ps[:, 5:7, :]).then_inc(s["y_ready"], 1)
            each(dve, step)


def moe(e):
    nc, a = e.nc, e.a
    e.xm_rows = e.dram("xm_rows", [TP, D])
    e.slot_tok = e.dram("slot_tok", [SLOTS, 1], I32)
    keep = lambda n, sh, dt=F32: e.ctx.enter_context(nc.sbuf_tensor(n, sh, dt))
    e.gate = keep("gate", [P, 2, TILES])
    e.dest = keep("dest", [P, 2, TILES], I32)
    e.more_expert = keep("more_expert", [1, NMORE + 1], I32)
    g_ready = e.sem("g_moe_ready")
    with nc.sbuf_tensor("expert_gate", [P, 2, KD, DE], F32) as wg, nc.sbuf_tensor("expert_up", [P, 2, KD, DE], F32) as wu:
        wg_ready = [e.sem(f"own_wg_ready{i}") for i in range(2)]
        first = [(dst[:, n], src, wg_ready[n]) for n in range(2) for dst, src in zip((wg, wu), expert_weights(e, n, ("w_e_gate", "w_e_up")))]
        with nc.sbuf_tensor("xmT", [P, KD, TP], F32) as xT, nc.sbuf_tensor("w_route", [P, KD, NR], F32) as wr, \
                nc.sbuf_tensor("b_route", [P, NR], F32) as bias:
            route_loaded = e.sem("route_loaded")
            with nc.sbuf_tensor("g_moe_rows", [P, D], F32) as g:
                with nc.Block() as block:
                    @block.sync
                    def _(sp):
                        sp.dma_start(g[:, :], a["g_moe"].to_broadcast([P, D])).then_inc(g_ready, 16)
                        sp.dma_start(wr[:, :, 0:NGR], a["w_route_group"][0].rearrange("(k p) c -> p k c", p=P)).then_inc(route_loaded, 16)
                        sp.dma_start(wr[:, :, NGR:], a["w_route_expert"][0].rearrange("(k p) c -> p k c", p=P)).then_inc(route_loaded, 16)
                        sp.dma_start(bias[:, 0:NGR], a["b_route_group"].to_broadcast([P, NGR])).then_inc(route_loaded, 16)
                        sp.dma_start(bias[:, NGR:], a["b_route_expert"].to_broadcast([P, NE])).then_inc(route_loaded, 16)
                        sp.wait_ge(g_ready, 16)
                rms_tiles(e, "moe", e.x, TILES, xT, gtok=g[:, :], store=e.xm_rows, prefetch=first)
            routing(e, xT, wr, bias, route_loaded)
        expert_blocks(e, "own", NBASE, wg, wu, wg_ready)
    further_blocks(e)


def output(e):
    nc, a, o = e.nc, e.a, e.o
    s = {n: e.sem("final_" + n) for n in ("g_ready", "added", "squared", "meaned", "rooted", "scaled")}
    row_ready = [[e.sem(f"final_rows{i}{b}") for b in range(2)] for i in range(2)]
    stored = [e.sem(f"final_stored{b}") for b in range(2)]
    with ExitStack() as st:
        sb = lambda n, sh: st.enter_context(nc.sbuf_tensor("f_" + n, sh, F32))
        y = [[sb(f"y{i}{b}", [P, D]) for b in range(2)] for i in range(2)]
        g, out = sb("g", [P, D]), sb("out", [P, 2, D])
        sq, ss, rs = sb("sq", [P, D]), sb("ss", [P, TILES]), sb("rs", [P, TILES])
        block = st.enter_context(nc.Block())
        rows = lambda t: P if t < NT else NB

        @block.sync
        def _(sp):
            sp.dma_start(g[:, :], a["g_final"].rearrange("(o d) -> o d", o=1).to_broadcast([P, D])).then_inc(s["g_ready"], 16)
            for t in range(TILES):
                sp.wait_ge(s["scaled"], t + 1)
                dst = o["y_prompt"][0, t * P:(t + 1) * P, :] if t < NT else o["y_sample"][:, 0, :]
                sp.dma_start(dst, out[0:rows(t), t % 2]).then_inc(stored[t % 2], 16)
            for b in range(2):
                sp.wait_ge(stored[b], 16 * ((TILES + 1 - b) // 2))

        @block.gpsimd
        def _(pool):
            def root(t):
                pool.wait_ge(s["meaned"], t + 1)
                pool.tensor_tensor(rs[0:rows(t), t:t + 1], ss[0:rows(t), t:t + 1], e.mhalf[0:rows(t), 0:1], ALU.pow).then_inc(s["rooted"], 1)
            for t in range(TILES):
                if t >= 2:
                    pool.wait_ge(s["added"], t - 1)
                for i in range(2):
                    pool.indirect_dma_start(y[i][t % 2][0:rows(t), :], None, e.y_rows,
                                            bass.IndirectOffsetOnAxis(ap=e.dest[0:rows(t), i, t:t + 1], axis=0)).then_inc(row_ready[i][t % 2], 16)
                if t >= 1:
                    root(t - 1)
            root(TILES - 1)

        @block.scalar
        def _(act):
            for t in range(TILES):
                act.wait_ge(s["added"], t + 1)
                act.activation(sq[0:rows(t), :], e.x[0:rows(t), t, :], ACT.Square, accum_out=ss[0:rows(t), t:t + 1]).then_inc(s["squared"], 1)
                act.drain()

        @block.vector
        def _(dve):
            def add(t):
                r = rows(t)
                for i in range(2):
                    dve.wait_ge(row_ready[i][t % 2], 16 * (t // 2 + 1))
                    last = dve.scalar_tensor_tensor(out=e.x[0:r, t, :], in0=y[i][t % 2][0:r, :], scalar=e.gate[0:r, i, t:t + 1], in1=e.x[0:r, t, :],
                                                    op0=ALU.mult, op1=ALU.add)
                    dve.drain()
                dve.sem_inc(s["added"], 1)

            def mean(t):
                r = rows(t)
                dve.wait_ge(s["squared"], t + 1)
                dve.tensor_scalar(ss[0:r, t:t + 1], ss[0:r, t:t + 1], 1.0 / D, EPS, ALU.mult, ALU.add).then_inc(s["meaned"], 1)

            def scale(t):
                r = rows(t)
                if t >= 2:
                    dve.wait_ge(stored[t % 2], 16 * (t // 2))
                dve.wait_ge(s["rooted"], t + 1)
                dve.scalar_tensor_tensor(out=out[0:r, t % 2, :], in0=e.x[0:r, t, :], scalar=rs[0:r, t:t + 1], in1=g[0:r, :],
                                         op0=ALU.mult, op1=ALU.mult).then_inc(s["scaled"], 1)
            dve.wait_ge(s["g_ready"], 16)
            add(0)
            for t in range(TILES):
                mean(t)
                if t + 1 < TILES:
                    add(t + 1)
                scale(t)


def hybrid_step(nc, a, o):
    with ExitStack() as ctx:
        e = Env(nc, ctx, a, o)
        with e.stage():
            constants(e)
        e.y_cols = e.dram("y_cols", [XT, P, T])
        e.att_cols = e.dram("att_cols", [KD, P, T])
        ssd_vectors(e)
        e.x_cols = e.dram("x_cols", [P, KD, TP])
        with nc.sbuf_tensor("x_low", [P, KD, TP], F32) as x_low, nc.sbuf_tensor("x_high", [P, KD, TP], F32) as x_high:
            x = (x_low, x_high)
            with e.stage():
                mixer_norm(e, x_low, x_high)
                project(e, x)
            with ExitStack() as mix, e.stage():
                e.mix = mix
                z = ZRows(e, mix, x)
                ssd_steps(e, z)
                sample_states(e, z)
                sample_window(e, z)
                sample_ssd(e, z)
        with e.stage():
            ssd_chunks(e)
        with e.stage():
            window_attention(e)
        resident_rows(e)
        with e.stage():
            mixer_out(e)
        with e.stage():
            cross_attention(e)
        with e.stage():
            moe(e)
            output(e)


_INS = ["x_prompt", "x_sample", "state_ssd", "state_conv", "cache_win_k", "cache_win_v", "cache_mem_k", "cache_mem_v",
        "mem_prompt", "g_mix", "w_in", "conv_w", "conv_b", "dt_bias", "a_log", "d_skip", "g_ssd", "w_ssd_down", "attn_sinks",
        "w_mix_out", "g_cross", "g_mem", "w_cq", "w_ckv", "w_co", "g_moe", "w_route_group", "b_route_group",
        "w_route_expert", "b_route_expert", "w_e_gate", "w_e_up", "w_e_down", "g_final"]
_OUTS = [("y_prompt", (1, SEQ, D)), ("y_sample", (NB, 1, D)),
         ("p_state_ssd", (1, 1, HS, HP, NS)), ("p_state_conv", (1, 1, CK - 1, CD)),
         ("p_cache_win_k", (1, 1, W, NKV, HD)), ("p_cache_win_v", (1, 1, W, NKV, HD)),
         ("p_cache_mem_k", (1, 1, MEM, CH, CHD)), ("p_cache_mem_v", (1, 1, MEM, CH, CHD)),
         ("s_state_ssd", (1, NB, HS, HP, NS)), ("s_state_conv", (1, NB, CK - 1, CD)),
         ("s_cache_win_k", (1, NB, W, NKV, HD)), ("s_cache_win_v", (1, NB, W, NKV, HD))]


def kernel(**inputs):
    import numpy as np
    import concourse.bacc as bacc
    from concourse.bass_utils import run_bass_kernel_spmd

    nc = bacc.Bacc("TRN2", target_bir_lowering=False, num_devices=1)
    arrays, a, o = {}, {}, {}
    for name in _INS:
        x = np.ascontiguousarray(inputs[name])
        arrays["in_" + name] = x
        a[name] = nc.dram_tensor("in_" + name, x.shape, mybir.dt.from_np(x.dtype), kind="ExternalInput").ap()
    for name, shape in _OUTS:
        o[name] = nc.dram_tensor("out_" + name, shape, F32, kind="ExternalOutput").ap()
    hybrid_step(nc, a, o)
    r = run_bass_kernel_spmd(nc, [arrays], core_ids=[0])
    return tuple(r.results[0]["out_" + name] for name, _ in _OUTS)
```
